# Optimizing a Trainium2 kernel written in Bass

```python
import math
import jax
import jax.numpy as jnp
from jax import lax
import numpy as np
import jax, jax.numpy as jnp

D_MODEL = 1024
BATCH = 1
SEQ = 256
DEPTH = 2

EPS = 1e-6
ROPE_THETA = 10000.0
D_FF = 2816
GDN_HEADS = 4
GDN_DK = 128
GDN_DV = 128
GDN_CONV = 4
GDN_CHUNK = 64
RET_HEADS = 4
RET_DK = 64
RET_DV = 128
RET_CHUNK = 64
DIL_HEADS = 4
DIL_DH = 128
DIL_PATTERNS = ((128, 1), (512, 4), (2048, 16))
DIFF_HEADS = 4
DIFF_DK = 64
DIFF_DV = 128
Q_BLOCK = 128

GDN_QK_W = GDN_HEADS * GDN_DK
GDN_V_W = GDN_HEADS * GDN_DV
GDN_CONV_W = 2 * GDN_QK_W + GDN_V_W
RET_QK_W = RET_HEADS * RET_DK
RET_V_W = RET_HEADS * RET_DV
IN0_SPLITS = (GDN_CONV_W, GDN_V_W, GDN_HEADS, GDN_HEADS, RET_QK_W, RET_QK_W, RET_V_W, RET_V_W)
IN0_W = sum(IN0_SPLITS)
MIX0_W = GDN_V_W + RET_V_W
DIL_W = DIL_HEADS * DIL_DH
DIFF_QK_W = DIFF_HEADS * 2 * DIFF_DK
DIFF_V_W = DIFF_HEADS * DIFF_DV
IN1_SPLITS = (DIL_W, DIL_W, DIL_W, DIFF_QK_W, DIFF_QK_W, DIFF_V_W)
IN1_W = sum(IN1_SPLITS)
MIX1_W = DIL_W + DIFF_V_W


def rmsnorm(x, w=None):
    xf = x.astype(jnp.float32)
    y = xf * lax.rsqrt(jnp.mean(xf * xf, axis=-1, keepdims=True) + EPS)
    if w is not None:
        y = y * w.astype(jnp.float32)
    return y.astype(x.dtype)

def l2norm(t):
    tf = t.astype(jnp.float32)
    return (tf * lax.rsqrt(jnp.sum(tf * tf, axis=-1, keepdims=True) + EPS)).astype(t.dtype)

def split_cols(t, sizes):
    offs = np.cumsum(sizes)[:-1].tolist()
    return jnp.split(t, offs, axis=-1)

def swiglu(h, w_up, w_down):
    gate, up = jnp.split(h @ w_up, 2, axis=-1)
    return (jax.nn.silu(gate) * up) @ w_down

def rope_tables(seq, dim):
    inv = ROPE_THETA ** (-jnp.arange(0, dim, 2, dtype=jnp.float32) / dim)
    ang = jnp.arange(seq, dtype=jnp.float32)[:, None] * inv[None, :]
    return jnp.cos(ang), jnp.sin(ang)

def apply_rope(x, cos, sin):
    x1, x2 = jnp.split(x, 2, axis=-1)
    c = cos[None, :, None, :].astype(x.dtype)
    s = sin[None, :, None, :].astype(x.dtype)
    return jnp.concatenate([x1 * c - x2 * s, x1 * s + x2 * c], axis=-1)

def causal_depthwise_conv(x, w):
    K, C = w.shape
    return lax.conv_general_dilated(x, w[:, None, :].astype(x.dtype), window_strides=(1,),
                                    padding=[(K - 1, 0)], dimension_numbers=('NWC', 'WIO', 'NWC'),
                                    feature_group_count=C)

def to_chunks(t, c):
    B, S = t.shape[:2]
    t = t.reshape(B, S // c, c, *t.shape[2:])
    return jnp.swapaxes(t, 2, 3)

def from_chunks(t):
    t = jnp.swapaxes(t, 2, 3)
    return t.reshape(t.shape[0], t.shape[1] * t.shape[2], *t.shape[3:])

def gated_delta_rule_chunked(q, k, v, g, beta):
    B, S, H, dk = q.shape
    dv = v.shape[-1]
    C = GDN_CHUNK
    f32 = jnp.float32
    qc, kc, vc = (to_chunks(t.astype(f32), C) for t in (q, k, v))
    gc, bc = (to_chunks(t.astype(f32), C) for t in (g, beta))
    gcum = jnp.cumsum(gc, axis=-1)
    idx = jnp.arange(C)
    causal = idx[:, None] >= idx[None, :]
    strict = idx[:, None] > idx[None, :]
    gdiff = gcum[..., :, None] - gcum[..., None, :]
    decay = jnp.where(causal, jnp.exp(jnp.where(causal, gdiff, 0.0)), 0.0)
    a_strict = jnp.where(strict, jnp.einsum('bnhid,bnhjd->bnhij', kc, kc) * decay * bc[..., :, None], 0.0)
    rhs = jnp.concatenate([vc * bc[..., None], kc * (bc * jnp.exp(gcum))[..., None]], axis=-1)
    sol = lax.linalg.triangular_solve(a_strict + jnp.eye(C, dtype=f32), rhs, left_side=True,
                                      lower=True, unit_diagonal=True)
    u, w = sol[..., :dv], sol[..., dv:]
    qk = jnp.einsum('bnhid,bnhjd->bnhij', qc, kc) * decay
    q_dec = qc * jnp.exp(gcum)[..., None]
    g_last = gcum[..., -1]
    k_dec = kc * jnp.exp(g_last[..., None] - gcum)[..., None]

    def step(state, xs):
        qk_n, q_n, w_n, u_n, k_n, gl_n = xs
        v_new = u_n - jnp.einsum('bhcd,bhde->bhce', w_n, state)
        o_n = jnp.einsum('bhcd,bhde->bhce', q_n, state) + jnp.einsum('bhij,bhje->bhie', qk_n, v_new)
        state = state * jnp.exp(gl_n)[..., None, None] + jnp.einsum('bhcd,bhce->bhde', k_n, v_new)
        return state, o_n

    xs = tuple(jnp.moveaxis(t, 1, 0) for t in (qk, q_dec, w, u, k_dec, g_last))
    _, o = lax.scan(step, jnp.zeros((B, H, dk, dv), f32), xs)
    return from_chunks(jnp.moveaxis(o, 0, 1)).astype(v.dtype)

def retention_chunked(q, k, v):
    B, S, H, dk = q.shape
    dv = v.shape[-1]
    C = RET_CHUNK
    f32 = jnp.float32
    log_gamma = jnp.log(1.0 - 2.0 ** (-5.0 - jnp.arange(H, dtype=f32)))
    qc, kc, vc = (to_chunks(t.astype(f32), C) for t in (q, k, v))
    idx = jnp.arange(C, dtype=f32)
    rel = idx[:, None] - idx[None, :]
    causal = rel >= 0
    dmask = jnp.where(causal, jnp.exp(jnp.where(causal, rel, 0.0)[None] * log_gamma[:, None, None]), 0.0)
    intra = jnp.einsum('bnhij,bnhje->bnhie', jnp.einsum('bnhid,bnhjd->bnhij', qc, kc) * dmask, vc)
    k_scale = jnp.exp((C - 1 - idx)[None, :] * log_gamma[:, None])
    q_scale = jnp.exp((idx + 1)[None, :] * log_gamma[:, None])
    chunk_decay = jnp.exp(C * log_gamma)
    kv = jnp.einsum('bnhcd,bnhce->bnhde', kc * k_scale[..., None], vc)

    def step(state, kv_n):
        return state * chunk_decay[:, None, None] + kv_n, state

    _, prev = lax.scan(step, jnp.zeros((B, H, dk, dv), f32), jnp.moveaxis(kv, 1, 0))
    prev = jnp.moveaxis(prev, 0, 1)
    inter = jnp.einsum('bnhcd,bnhde->bnhce', qc, prev) * q_scale[..., None]
    return from_chunks(intra + inter).astype(v.dtype)

def dilated_branch(q, k, v, window, dilation):
    B, S, H, d = q.shape
    L = S // dilation
    n_keys = window // dilation
    blk = min(n_keys, L)
    nb = -(-L // blk)
    Lp = nb * blk

    def strided(t):
        t = t.reshape(B, L, dilation, H, d).swapaxes(1, 2)
        t = jnp.pad(t, ((0, 0), (0, 0), (0, Lp - L), (0, 0), (0, 0)))
        return t.reshape(B, dilation, nb, blk, H, d)

    def with_prev(t):
        prev = jnp.pad(t, ((0, 0), (0, 0), (1, 0), (0, 0), (0, 0), (0, 0)))[:, :, :-1]
        return jnp.concatenate([prev, t], axis=3)

    qs = strided(q)
    kb, vb = with_prev(strided(k)), with_prev(strided(v))
    s = jnp.einsum('brnqhd,brnkhd->brnhqk', qs, kb).astype(jnp.float32)
    qi = jnp.arange(blk)[:, None] + blk
    kj = jnp.arange(2 * blk)[None, :]
    dist = qi - kj
    band = (dist >= 0) & (dist <= n_keys)
    has_prev = (jnp.arange(nb) > 0)[:, None, None] | (kj >= blk)[None]
    valid = band[None] & has_prev
    s = jnp.where(valid[:, None], s, -jnp.inf)
    m = jnp.max(s, axis=-1)
    p = jnp.exp(s - m[..., None])
    l = jnp.sum(p, axis=-1)
    o = jnp.einsum('brnhqk,brnkhd->brnqhd', p.astype(v.dtype), vb).astype(jnp.float32)

    def unstrided(t):
        t = t.reshape(B, dilation, Lp, *t.shape[4:])[:, :, :L]
        return t.swapaxes(1, 2).reshape(B, S, *t.shape[3:])

    return unstrided(o), unstrided(m.swapaxes(3, 4)), unstrided(l.swapaxes(3, 4))

def dilated_attention(q, k, v):
    outs = [dilated_branch(q, k, v, w, r) for (w, r) in DIL_PATTERNS]
    m_all = jnp.max(jnp.stack([o[1] for o in outs]), axis=0)
    num = jnp.zeros_like(outs[0][0])
    den = jnp.zeros_like(outs[0][2])
    for o_g, m_g, l_g in outs:
        scale = jnp.exp(m_g - m_all)
        num = num + o_g * scale[..., None]
        den = den + l_g * scale
    return (num / den[..., None]).astype(v.dtype)

def differential_attention(q1, q2, k1, k2, v, lam):
    B, S, H, dk = q1.shape
    nq = S // Q_BLOCK

    def blocks(t):
        return jnp.moveaxis(t.reshape(B, nq, Q_BLOCK, H, t.shape[-1]), 1, 0)

    key_pos = jnp.arange(S)

    def one_block(args):
        i, qa, qb = args
        q_pos = i * Q_BLOCK + jnp.arange(Q_BLOCK)
        causal = (q_pos[:, None] >= key_pos[None, :])[None, None]
        s1 = jnp.where(causal, jnp.einsum('bqhd,bkhd->bhqk', qa, k1).astype(jnp.float32), -jnp.inf)
        s2 = jnp.where(causal, jnp.einsum('bqhd,bkhd->bhqk', qb, k2).astype(jnp.float32), -jnp.inf)
        attn = jax.nn.softmax(s1, axis=-1) - lam * jax.nn.softmax(s2, axis=-1)
        return jnp.einsum('bhqk,bkhe->bqhe', attn.astype(v.dtype), v)

    o = lax.map(one_block, (jnp.arange(nq), blocks(q1), blocks(q2)))
    return jnp.moveaxis(o, 0, 1).reshape(B, S, H, v.shape[-1])

def mixer_delta_retention(h, w_in, conv_w, a_log, dt_bias, gdn_norm, w_out, cos, sin):
    B, S, _ = h.shape
    qkv, z, b, a, rq, rk, rv, rg = split_cols(h @ w_in, IN0_SPLITS)
    qkv = jax.nn.silu(causal_depthwise_conv(qkv, conv_w))
    q, k, v = split_cols(qkv, (GDN_QK_W, GDN_QK_W, GDN_V_W))
    q = l2norm(q.reshape(B, S, GDN_HEADS, GDN_DK)) * GDN_DK ** -0.5
    k = l2norm(k.reshape(B, S, GDN_HEADS, GDN_DK))
    v = v.reshape(B, S, GDN_HEADS, GDN_DV)
    beta = jax.nn.sigmoid(b)
    g = -jnp.exp(a_log) * jax.nn.softplus(a + dt_bias)
    o_a = gated_delta_rule_chunked(q, k, v, g, beta)
    o_a = rmsnorm(o_a, gdn_norm) * jax.nn.silu(z.reshape(B, S, GDN_HEADS, GDN_DV))
    rq = apply_rope(rq.reshape(B, S, RET_HEADS, RET_DK), cos, sin) * RET_DK ** -0.5
    rk = apply_rope(rk.reshape(B, S, RET_HEADS, RET_DK), cos, sin)
    o_b = retention_chunked(rq, rk, rv.reshape(B, S, RET_HEADS, RET_DV))
    o_b = rmsnorm(o_b) * jax.nn.silu(rg.reshape(B, S, RET_HEADS, RET_DV))
    o = jnp.concatenate([o_a.reshape(B, S, GDN_V_W), o_b.reshape(B, S, RET_V_W)], axis=-1)
    return o @ w_out

def mixer_dilated_differential(h, w_in, lambda_q1, lambda_k1, lambda_q2, lambda_k2, diff_norm, w_out,
                               cos128, sin128, cos64, sin64, lambda_init):
    B, S, _ = h.shape
    cq, ck, cv, dq, dk, dv = split_cols(h @ w_in, IN1_SPLITS)
    cq = apply_rope(cq.reshape(B, S, DIL_HEADS, DIL_DH), cos128, sin128) * DIL_DH ** -0.5
    ck = apply_rope(ck.reshape(B, S, DIL_HEADS, DIL_DH), cos128, sin128)
    o_c = dilated_attention(cq, ck, cv.reshape(B, S, DIL_HEADS, DIL_DH))
    dq = dq.reshape(B, S, DIFF_HEADS, 2, DIFF_DK)
    dk = dk.reshape(B, S, DIFF_HEADS, 2, DIFF_DK)
    q1 = apply_rope(dq[..., 0, :], cos64, sin64) * DIFF_DK ** -0.5
    q2 = apply_rope(dq[..., 1, :], cos64, sin64) * DIFF_DK ** -0.5
    k1 = apply_rope(dk[..., 0, :], cos64, sin64)
    k2 = apply_rope(dk[..., 1, :], cos64, sin64)
    lam = (jnp.exp(jnp.sum(lambda_q1 * lambda_k1).astype(jnp.float32))
           - jnp.exp(jnp.sum(lambda_q2 * lambda_k2).astype(jnp.float32)) + lambda_init)
    o_d = differential_attention(q1, q2, k1, k2, dv.reshape(B, S, DIFF_HEADS, DIFF_DV), lam)
    o_d = rmsnorm(o_d, diff_norm) * (1.0 - lambda_init)
    o = jnp.concatenate([o_c.reshape(B, S, DIL_W), o_d.reshape(B, S, DIFF_V_W)], axis=-1)
    return o @ w_out

def first_inputs(seed: int = 0) -> dict:
    key = jax.random.key(seed)
    ks = iter(jax.random.split(key, 64))

    def nrm(shape, scale):
        return jax.random.normal(next(ks), shape, jnp.float32) * scale

    def gain(n):
        return 1.0 + 0.02 * jax.random.normal(next(ks), (n,), jnp.float32)

    inp = {}
    inp['x'] = nrm((BATCH, SEQ, D_MODEL), 1.0)

    def ffn(prefix):
        inp[prefix + '_norm'] = gain(D_MODEL)
        inp[prefix + '_w_up'] = nrm((D_MODEL, 2 * D_FF), D_MODEL ** -0.5)
        inp[prefix + '_w_down'] = nrm((D_FF, D_MODEL), D_FF ** -0.5)

    ffn('l0_ffn1')
    inp['l0_mix_norm'] = gain(D_MODEL)
    inp['l0_w_in'] = nrm((D_MODEL, IN0_W), D_MODEL ** -0.5)
    inp['l0_conv_w'] = nrm((GDN_CONV, GDN_CONV_W), GDN_CONV ** -0.5)
    inp['l0_a_log'] = jnp.log(jax.random.uniform(next(ks), (GDN_HEADS,), jnp.float32, 1.0, 16.0))
    dt = jnp.exp(jax.random.uniform(next(ks), (GDN_HEADS,), jnp.float32, math.log(1e-3), math.log(1e-1)))
    inp['l0_dt_bias'] = dt + jnp.log(-jnp.expm1(-dt))
    inp['l0_gdn_norm'] = gain(GDN_DV)
    inp['l0_w_out'] = nrm((MIX0_W, D_MODEL), MIX0_W ** -0.5)
    ffn('l0_ffn2')
    ffn('l1_ffn1')
    inp['l1_mix_norm'] = gain(D_MODEL)
    inp['l1_w_in'] = nrm((D_MODEL, IN1_W), D_MODEL ** -0.5)
    inp['l1_lambda_q1'] = nrm((DIFF_DK,), 0.1)
    inp['l1_lambda_k1'] = nrm((DIFF_DK,), 0.1)
    inp['l1_lambda_q2'] = nrm((DIFF_DK,), 0.1)
    inp['l1_lambda_k2'] = nrm((DIFF_DK,), 0.1)
    inp['l1_diff_norm'] = gain(DIFF_DV)
    inp['l1_w_out'] = nrm((MIX1_W, D_MODEL), MIX1_W ** -0.5)
    ffn('l1_ffn2')
    inp['final_norm'] = gain(D_MODEL)
    return inp

def first_block(x, l0_ffn1_norm, l0_ffn1_w_up, l0_ffn1_w_down, l0_mix_norm, l0_w_in, l0_conv_w, l0_a_log,
              l0_dt_bias, l0_gdn_norm, l0_w_out, l0_ffn2_norm, l0_ffn2_w_up, l0_ffn2_w_down,
              l1_ffn1_norm, l1_ffn1_w_up, l1_ffn1_w_down, l1_mix_norm, l1_w_in, l1_lambda_q1, l1_lambda_k1,
              l1_lambda_q2, l1_lambda_k2, l1_diff_norm, l1_w_out, l1_ffn2_norm, l1_ffn2_w_up, l1_ffn2_w_down,
              final_norm):
    S = x.shape[1]
    cos64, sin64 = rope_tables(S, 64)
    cos128, sin128 = rope_tables(S, 128)
    ffn1 = ((l0_ffn1_norm, l0_ffn1_w_up, l0_ffn1_w_down), (l1_ffn1_norm, l1_ffn1_w_up, l1_ffn1_w_down))
    ffn2 = ((l0_ffn2_norm, l0_ffn2_w_up, l0_ffn2_w_down), (l1_ffn2_norm, l1_ffn2_w_up, l1_ffn2_w_down))
    mix_norm = (l0_mix_norm, l1_mix_norm)
    for i in range(DEPTH):
        n1, wu1, wd1 = ffn1[i]
        x = x + 0.5 * swiglu(rmsnorm(x, n1), wu1, wd1)
        h = rmsnorm(x, mix_norm[i])
        if i % 2 == 0:
            mix = mixer_delta_retention(h, l0_w_in, l0_conv_w, l0_a_log, l0_dt_bias, l0_gdn_norm, l0_w_out,
                                        cos64, sin64)
        else:
            lambda_init = 0.8 - 0.6 * math.exp(-0.3 * i)
            mix = mixer_dilated_differential(h, l1_w_in, l1_lambda_q1, l1_lambda_k1, l1_lambda_q2, l1_lambda_k2,
                                             l1_diff_norm, l1_w_out, cos128, sin128, cos64, sin64, lambda_init)
        x = x + mix
        n2, wu2, wd2 = ffn2[i]
        x = x + 0.5 * swiglu(rmsnorm(x, n2), wu2, wd2)
    return rmsnorm(x, final_norm)


N_EVEN = (DEPTH + 1) // 2
N_ODD = DEPTH // 2

MIX_WIDTH = 1024
A_GROUPS = 4
A_GROUP_DIM = 128
A_WIDTH = A_GROUPS * A_GROUP_DIM
CHUNK = 128
SGU_LN_EPS = 1e-5
B_HEADS = 8
B_HEAD_DIM = 64
B_WIDTH = B_HEADS * B_HEAD_DIM
DECAY_LORA = 64
ICLR_LORA = 64
GATE_LORA = 128
B_IN = 3 * B_WIDTH + DECAY_LORA + ICLR_LORA + GATE_LORA
RWKV_GN_EPS = 64e-5
IN0 = 2 * A_WIDTH + B_IN
C_HEADS = 8
C_KV_HEADS = 2
C_GROUP = C_HEADS // C_KV_HEADS
C_HEAD_DIM = 64
C_WIDTH = C_HEADS * C_HEAD_DIM
KV_WIDTH = C_KV_HEADS * C_HEAD_DIM
N_BRANCH = 3
CMP_LEN = 32
CMP_STRIDE = 16
CMP_HIDDEN = 256
SLC_BLK = 64
SEL_TOPK = 8
WIN = 512
QBLK = 128
ROT_DIM = C_HEAD_DIM // 4
ROPE_THETA_2 = 500000.0
D_WIDTH = 512
CONV_W = 3
IN1 = C_WIDTH + 6 * KV_WIDTH + C_HEADS * N_BRANCH + 3 * D_WIDTH
FFN_DIM = 2816
N_EXPERTS = 8
TOP_K = 2
EXPERT_DIM = 1408
MOE_BLK = 256
NORM_EPS = 1e-6
NEG_INF = -1e30
FORCE_BONUS = 1e6


def _split(p, sizes):
    offs = [int(o) for o in np.cumsum(sizes)[:-1]]
    return jnp.split(p, offs, axis=-1)

def _rms_norm(x, g):
    xf = x.astype(jnp.float32)
    y = xf * lax.rsqrt(jnp.mean(xf * xf, axis=-1, keepdims=True) + NORM_EPS)
    return (y * g.astype(jnp.float32)).astype(x.dtype)

def _masked_softmax(s, mask):
    s = jnp.where(mask, s, NEG_INF)
    m = jnp.max(s, axis=-1, keepdims=True)
    p = jnp.where(mask, jnp.exp(s - m), 0.0)
    return p / jnp.maximum(jnp.sum(p, axis=-1, keepdims=True), 1e-30)

def _rope_partial(x, cos, sin):
    half = ROT_DIM // 2
    c = cos[None, :, None, :].astype(x.dtype)
    s = sin[None, :, None, :].astype(x.dtype)
    x1 = x[..., :half]
    x2 = x[..., half:ROT_DIM]
    return jnp.concatenate([x1 * c - x2 * s, x1 * s + x2 * c, x[..., ROT_DIM:]], axis=-1)

def _chunked_sgu(u, v, ln_g, ln_b, w_s, b_s):
    bsz, t, _ = v.shape
    vf = v.reshape(bsz, t, A_GROUPS, A_GROUP_DIM).astype(jnp.float32)
    mu = jnp.mean(vf, axis=-1, keepdims=True)
    var = jnp.mean(jnp.square(vf - mu), axis=-1, keepdims=True)
    vn = ((vf - mu) * lax.rsqrt(var + SGU_LN_EPS)).reshape(bsz, t, A_WIDTH)
    vn = (vn * ln_g + ln_b).astype(v.dtype)
    vc = vn.reshape(bsz, t // CHUNK, CHUNK, A_GROUPS, A_GROUP_DIM)
    causal = jnp.tril(jnp.ones((CHUNK, CHUNK), dtype=bool))
    wm = jnp.where(causal[None], w_s, 0.0).astype(v.dtype)
    mixed = jnp.einsum('gts,bcsgd->bctgd', wm, vc) + b_s.T[:, :, None]
    return u * mixed.reshape(bsz, t, A_WIDTH)

def _rwkv7_scan(r, w, k, v, kk, a):
    bsz, _, h, n = r.shape

    def step(S, inp):
        r_t, w_t, k_t, v_t, kk_t, a_t = inp
        sa = jnp.einsum('bhij,bhj->bhi', S, kk_t)
        S = (S * w_t[:, :, None, :]
             - sa[..., None] * (kk_t * a_t)[:, :, None, :]
             + v_t[..., None] * k_t[:, :, None, :])
        return S, jnp.einsum('bhij,bhj->bhi', S, r_t)

    xs = tuple(jnp.moveaxis(z, 1, 0) for z in (r, w, k, v, kk, a))
    S0 = jnp.zeros((bsz, h, n, n), jnp.float32)
    _, ys = lax.scan(step, S0, xs)
    return jnp.moveaxis(ys, 0, 1)

def _rwkv7_time_mix(pb, mu, w0, w2, a0, a2, g2, k_k, k_a, r_k, gn_g, gn_b):
    bsz, t, _ = pb.shape
    prev = jnp.pad(pb, ((0, 0), (1, 0), (0, 0)))[:, :-1]
    pb = pb + (prev - pb) * mu
    r, k, v, wl, al, gl = _split(pb, [B_WIDTH, B_WIDTH, B_WIDTH, DECAY_LORA, ICLR_LORA, GATE_LORA])
    w = -jax.nn.softplus(-(w0 + jnp.tanh(wl) @ w2)) - 0.5
    decay = jnp.exp(-jnp.exp(w.astype(jnp.float32)))
    a = jax.nn.sigmoid(a0 + al @ a2)
    g = jax.nn.sigmoid(gl) @ g2

    def heads(z):
        return z.reshape(bsz, t, B_HEADS, B_HEAD_DIM).astype(jnp.float32)

    kk = heads(k * k_k)
    kk = kk / jnp.maximum(jnp.sqrt(jnp.sum(kk * kk, axis=-1, keepdims=True)), 1e-12)
    k = k * (1.0 + (a - 1.0) * k_a)
    rh, kh, vh, ah, wh = heads(r), heads(k), heads(v), heads(a), heads(decay)
    y = _rwkv7_scan(rh, wh, kh, vh, kk, ah)
    ym = jnp.mean(y, axis=-1, keepdims=True)
    yv = jnp.mean(jnp.square(y - ym), axis=-1, keepdims=True)
    y = ((y - ym) * lax.rsqrt(yv + RWKV_GN_EPS)).reshape(bsz, t, B_WIDTH)
    y = y * gn_g.astype(jnp.float32) + gn_b.astype(jnp.float32)
    bonus = jnp.sum(rh * kh * r_k.astype(jnp.float32), axis=-1, keepdims=True) * vh
    y = (y + bonus.reshape(bsz, t, B_WIDTH)) * g.astype(jnp.float32)
    return y.astype(pb.dtype)

def _nsa(q, kc, vc, ks, vs, kw, vw, gl, pos_k, pos_v, ck1, ck2, cv1, cv2, cos, sin):
    bsz, t, _ = q.shape
    f32 = jnp.float32
    scale = C_HEAD_DIM ** -0.5
    q = q.reshape(bsz, t, C_HEADS, C_HEAD_DIM)
    kc, vc, ks, vs, kw, vw = (z.reshape(bsz, t, C_KV_HEADS, C_HEAD_DIM) for z in (kc, vc, ks, vs, kw, vw))

    n_cmp = (t - CMP_LEN) // CMP_STRIDE + 1
    idx = np.arange(n_cmp)[:, None] * CMP_STRIDE + np.arange(CMP_LEN)[None, :]

    def compress(z, pos, w1, w2):
        zb = z[:, idx] + pos[None, None, :, None, :]
        zb = zb.transpose(0, 3, 1, 2, 4).reshape(bsz, C_KV_HEADS, n_cmp, CMP_LEN * C_HEAD_DIM)
        return jax.nn.gelu(zb @ w1) @ w2

    k_cmp = compress(kc, pos_k, ck1, ck2)
    v_cmp = compress(vc, pos_v, cv1, cv2).astype(f32)
    cmp_end = jnp.arange(n_cmp) * CMP_STRIDE + CMP_LEN - 1
    n_slc = t // SLC_BLK
    ci = jnp.arange(n_cmp)[:, None] * CMP_STRIDE
    sj = jnp.arange(n_slc)[None, :] * SLC_BLK
    overlap = ((ci < sj + SLC_BLK) & (ci + CMP_LEN > sj)).astype(f32)
    n_sel = min(SEL_TOPK, n_slc)

    q_rot = _rope_partial(q, cos, sin)
    ks = _rope_partial(ks, cos, sin)
    kw = _rope_partial(kw, cos, sin)
    n_qb = t // QBLK

    def to_qblocks(z):
        return z.reshape(bsz, n_qb, QBLK, C_KV_HEADS, C_GROUP, z.shape[-1]).transpose(1, 0, 3, 4, 2, 5)

    qr_b = to_qblocks(q_rot)
    qn_b = to_qblocks(q)
    g_b = to_qblocks(jax.nn.sigmoid(gl.reshape(bsz, t, C_HEADS, N_BRANCH)))
    ks_blk = ks.reshape(bsz, n_slc, SLC_BLK, C_KV_HEADS, C_HEAD_DIM).transpose(0, 3, 1, 2, 4)
    vs_blk = vs.reshape(bsz, n_slc, SLC_BLK, C_KV_HEADS, C_HEAD_DIM).transpose(0, 3, 1, 2, 4)
    pad = ((0, 0), (0, 0), (WIN, 0), (0, 0))
    kw_pad = jnp.pad(kw.transpose(0, 2, 1, 3), pad)
    vw_pad = jnp.pad(vw.transpose(0, 2, 1, 3), pad)
    b_ix = jnp.arange(bsz)[:, None, None, None]
    h_ix = jnp.arange(C_KV_HEADS)[None, :, None, None]
    jb = jnp.arange(n_slc)

    def body(args):
        qr, qn, gt, blk = args
        s0 = blk * QBLK
        t_pos = s0 + jnp.arange(QBLK)
        sc = jnp.einsum('bhgqd,bhnd->bhgqn', qn, k_cmp).astype(f32) * scale
        pc = _masked_softmax(sc, cmp_end[None, :] <= t_pos[:, None])
        o_c = jnp.einsum('bhgqn,bhnd->bhgqd', pc, v_cmp)
        imp = jnp.einsum('bhgqn,nj->bhqj', pc, overlap)
        cur = t_pos // SLC_BLK
        forced = (jb[None] == 0) | (jb[None] == cur[:, None]) | (jb[None] == cur[:, None] - 1)
        imp = jnp.where(jb[None] * SLC_BLK <= t_pos[:, None],
                        imp + jnp.where(forced, FORCE_BONUS, 0.0), NEG_INF)
        _, sel = lax.top_k(imp, n_sel)
        kg = ks_blk[b_ix, h_ix, sel]
        vg = vs_blk[b_ix, h_ix, sel]
        tok = sel[..., None] * SLC_BLK + jnp.arange(SLC_BLK)
        ms = (tok <= t_pos[:, None, None]).reshape(bsz, C_KV_HEADS, 1, QBLK, n_sel * SLC_BLK)
        ss = jnp.einsum('bhgqd,bhqnld->bhgqnl', qr, kg).astype(f32)
        ps = _masked_softmax(ss.reshape(bsz, C_KV_HEADS, C_GROUP, QBLK, n_sel * SLC_BLK) * scale, ms)
        o_s = jnp.einsum('bhgqm,bhqmd->bhgqd', ps,
                         vg.reshape(bsz, C_KV_HEADS, QBLK, n_sel * SLC_BLK, C_HEAD_DIM).astype(f32))
        kwb = lax.dynamic_slice_in_dim(kw_pad, s0, QBLK + WIN, axis=2)
        vwb = lax.dynamic_slice_in_dim(vw_pad, s0, QBLK + WIN, axis=2)
        key_pos = s0 - WIN + jnp.arange(QBLK + WIN)
        diff = t_pos[:, None] - key_pos[None, :]
        mw = (diff >= 0) & (diff < WIN) & (key_pos[None, :] >= 0)
        sw = jnp.einsum('bhgqd,bhkd->bhgqk', qr, kwb).astype(f32) * scale
        pw = _masked_softmax(sw, mw)
        o_w = jnp.einsum('bhgqk,bhkd->bhgqd', pw, vwb.astype(f32))
        gt = gt.astype(f32)
        return (gt[..., 0:1] * o_c + gt[..., 1:2] * o_s + gt[..., 2:3] * o_w).astype(qr.dtype)

    out = lax.map(body, (qr_b, qn_b, g_b, jnp.arange(n_qb)))
    return out.transpose(1, 0, 4, 2, 3, 5).reshape(bsz, t, C_WIDTH)

def _short_conv(bg, cg, hd, conv_w):
    z = cg * hd
    y = lax.conv_general_dilated(z, conv_w[:, None, :].astype(z.dtype), window_strides=(1,),
                                 padding=[(CONV_W - 1, 0)],
                                 dimension_numbers=('NWC', 'WIO', 'NWC'),
                                 feature_group_count=D_WIDTH)
    return bg * y

def _swiglu(h, w_gate, w_up, w_down):
    return (jax.nn.silu(h @ w_gate) * (h @ w_up)) @ w_down

def _moe_swiglu(h, w_router, b_router, w_gate, w_up, w_down):
    bsz, t, d = h.shape
    n = bsz * t
    nk = n * TOP_K
    xf = h.reshape(n, d)
    logits = (xf @ w_router).astype(jnp.float32) + b_router.astype(jnp.float32)
    top_val, top_idx = lax.top_k(logits, TOP_K)
    gates = jax.nn.softmax(top_val, axis=-1)
    e_flat = top_idx.reshape(-1)
    tok_flat = jnp.repeat(jnp.arange(n, dtype=jnp.int32), TOP_K)
    g_flat = gates.reshape(-1)
    order = jnp.argsort(e_flat)
    e_sorted = e_flat[order]
    counts = jax.ops.segment_sum(jnp.ones_like(e_flat), e_flat, num_segments=N_EXPERTS)
    padded = ((counts + MOE_BLK - 1) // MOE_BLK) * MOE_BLK
    p_end = jnp.cumsum(padded)
    p_start = p_end - padded
    u_start = jnp.cumsum(counts) - counts
    dest = p_start[e_sorted] + jnp.arange(nk) - u_start[e_sorted]
    n_blk = (nk + MOE_BLK - 1) // MOE_BLK + N_EXPERTS
    p_rows = n_blk * MOE_BLK
    row_tok = jnp.zeros((p_rows,), jnp.int32).at[dest].set(tok_flat[order])
    row_w = jnp.zeros((p_rows,), jnp.float32).at[dest].set(g_flat[order])
    blk_e = jnp.minimum(jnp.searchsorted(p_end, jnp.arange(n_blk) * MOE_BLK, side='right'), N_EXPERTS - 1)
    xs = xf[row_tok].reshape(n_blk, MOE_BLK, d)

    def expert_block(args):
        xb, e = args
        return (jax.nn.silu(xb @ w_gate[e]) * (xb @ w_up[e])) @ w_down[e]

    yb = lax.map(expert_block, (xs, blk_e)).reshape(p_rows, d)
    out = jnp.zeros((n, d), h.dtype).at[row_tok].add(yb * row_w[:, None].astype(yb.dtype))
    return out.reshape(bsz, t, d)

def second_inputs(seed: int = 0) -> dict:
    key = jax.random.key(seed)
    keys = iter(jax.random.split(key, 48))

    def nrm(shape, scale):
        return scale * jax.random.normal(next(keys), shape, jnp.float32)

    def gain(shape):
        return 1.0 + nrm(shape, 0.1)

    def unif(shape, lo, hi):
        return jax.random.uniform(next(keys), shape, jnp.float32, lo, hi)

    E, O, D = N_EVEN, N_ODD, D_MODEL
    return {
        "x": nrm((BATCH, SEQ, D), 1.0),
        "e_norm_mix": gain((E, D)),
        "e_w_in": nrm((E, D, IN0), D ** -0.5),
        "sgu_ln_g": gain((E, A_WIDTH)),
        "sgu_ln_b": nrm((E, A_WIDTH), 0.02),
        "sgu_w": nrm((E, A_GROUPS, CHUNK, CHUNK), CHUNK ** -0.5),
        "sgu_b": gain((E, A_GROUPS, CHUNK)),
        "rwkv_mu": unif((E, B_IN), 0.0, 1.0),
        "rwkv_w0": unif((E, B_WIDTH), -2.5, 0.5),
        "rwkv_w2": nrm((E, DECAY_LORA, B_WIDTH), 0.1 * DECAY_LORA ** -0.5),
        "rwkv_a0": nrm((E, B_WIDTH), 0.5),
        "rwkv_a2": nrm((E, ICLR_LORA, B_WIDTH), 0.5 * ICLR_LORA ** -0.5),
        "rwkv_g2": nrm((E, GATE_LORA, B_WIDTH), GATE_LORA ** -0.5),
        "rwkv_k_k": 0.85 + nrm((E, B_WIDTH), 0.1),
        "rwkv_k_a": gain((E, B_WIDTH)),
        "rwkv_r_k": nrm((E, B_HEADS, B_HEAD_DIM), 0.1),
        "rwkv_gn_g": gain((E, B_WIDTH)),
        "rwkv_gn_b": nrm((E, B_WIDTH), 0.02),
        "e_w_out": nrm((E, MIX_WIDTH, D), MIX_WIDTH ** -0.5),
        "e_norm_ffn": gain((E, D)),
        "ffn_w_gate": nrm((E, D, FFN_DIM), D ** -0.5),
        "ffn_w_up": nrm((E, D, FFN_DIM), D ** -0.5),
        "ffn_w_down": nrm((E, FFN_DIM, D), FFN_DIM ** -0.5),
        "o_norm_mix": gain((O, D)),
        "o_w_in": nrm((O, D, IN1), D ** -0.5),
        "nsa_cmp_pos_k": nrm((O, CMP_LEN, C_HEAD_DIM), 0.1),
        "nsa_cmp_pos_v": nrm((O, CMP_LEN, C_HEAD_DIM), 0.1),
        "nsa_cmp_k_w1": nrm((O, CMP_LEN * C_HEAD_DIM, CMP_HIDDEN), (CMP_LEN * C_HEAD_DIM) ** -0.5),
        "nsa_cmp_k_w2": nrm((O, CMP_HIDDEN, C_HEAD_DIM), CMP_HIDDEN ** -0.5),
        "nsa_cmp_v_w1": nrm((O, CMP_LEN * C_HEAD_DIM, CMP_HIDDEN), (CMP_LEN * C_HEAD_DIM) ** -0.5),
        "nsa_cmp_v_w2": nrm((O, CMP_HIDDEN, C_HEAD_DIM), CMP_HIDDEN ** -0.5),
        "conv_w": nrm((O, CONV_W, D_WIDTH), CONV_W ** -0.5),
        "o_w_out": nrm((O, MIX_WIDTH, D), MIX_WIDTH ** -0.5),
        "o_norm_ffn": gain((O, D)),
        "moe_router": nrm((O, D, N_EXPERTS), D ** -0.5),
        "moe_router_b": nrm((O, N_EXPERTS), 0.01),
        "moe_w_gate": nrm((O, N_EXPERTS, D, EXPERT_DIM), D ** -0.5),
        "moe_w_up": nrm((O, N_EXPERTS, D, EXPERT_DIM), D ** -0.5),
        "moe_w_down": nrm((O, N_EXPERTS, EXPERT_DIM, D), EXPERT_DIM ** -0.5),
        "final_norm": gain((D,)),
    }

def second_block(x, e_norm_mix, e_w_in, sgu_ln_g, sgu_ln_b, sgu_w, sgu_b, rwkv_mu, rwkv_w0, rwkv_w2,
              rwkv_a0, rwkv_a2, rwkv_g2, rwkv_k_k, rwkv_k_a, rwkv_r_k, rwkv_gn_g, rwkv_gn_b, e_w_out,
              e_norm_ffn, ffn_w_gate, ffn_w_up, ffn_w_down, o_norm_mix, o_w_in, nsa_cmp_pos_k,
              nsa_cmp_pos_v, nsa_cmp_k_w1, nsa_cmp_k_w2, nsa_cmp_v_w1, nsa_cmp_v_w2, conv_w, o_w_out,
              o_norm_ffn, moe_router, moe_router_b, moe_w_gate, moe_w_up, moe_w_down, final_norm):
    t = x.shape[1]
    pos = jnp.arange(t, dtype=jnp.float32)
    inv_freq = ROPE_THETA_2 ** (-jnp.arange(0, ROT_DIM, 2, dtype=jnp.float32) / ROT_DIM)
    ang = pos[:, None] * inv_freq[None, :]
    cos, sin = jnp.cos(ang), jnp.sin(ang)

    h = x
    for layer in range(DEPTH):
        i = layer // 2
        if layer % 2 == 0:
            hn = _rms_norm(h, e_norm_mix[i])
            p = hn @ e_w_in[i]
            pu, pv, pb = _split(p, [A_WIDTH, A_WIDTH, B_IN])
            ya = _chunked_sgu(jax.nn.gelu(pu), jax.nn.gelu(pv), sgu_ln_g[i], sgu_ln_b[i], sgu_w[i], sgu_b[i])
            yb = _rwkv7_time_mix(pb, rwkv_mu[i], rwkv_w0[i], rwkv_w2[i], rwkv_a0[i], rwkv_a2[i],
                                 rwkv_g2[i], rwkv_k_k[i], rwkv_k_a[i], rwkv_r_k[i],
                                 rwkv_gn_g[i], rwkv_gn_b[i])
            h = h + jnp.concatenate([ya.astype(h.dtype), yb.astype(h.dtype)], axis=-1) @ e_w_out[i]
            hn = _rms_norm(h, e_norm_ffn[i])
            h = h + _swiglu(hn, ffn_w_gate[i], ffn_w_up[i], ffn_w_down[i])
        else:
            hn = _rms_norm(h, o_norm_mix[i])
            p = hn @ o_w_in[i]
            q, kc, vc, ks, vs, kw, vw, gl, bg, cg, hd = _split(
                p, [C_WIDTH] + [KV_WIDTH] * 6 + [C_HEADS * N_BRANCH] + [D_WIDTH] * 3)
            yc = _nsa(q, kc, vc, ks, vs, kw, vw, gl, nsa_cmp_pos_k[i], nsa_cmp_pos_v[i],
                      nsa_cmp_k_w1[i], nsa_cmp_k_w2[i], nsa_cmp_v_w1[i], nsa_cmp_v_w2[i], cos, sin)
            yd = _short_conv(bg, cg, hd, conv_w[i])
            h = h + jnp.concatenate([yc.astype(h.dtype), yd.astype(h.dtype)], axis=-1) @ o_w_out[i]
            hn = _rms_norm(h, o_norm_ffn[i])
            h = h + _moe_swiglu(hn, moe_router[i], moe_router_b[i], moe_w_gate[i], moe_w_up[i], moe_w_down[i])
    return _rms_norm(h, final_norm)


def setup_inputs(seed=0):
    out = dict(first_inputs(seed))
    for name, value in second_inputs(seed + 1).items():
        if name != "x":
            out[name + "_2"] = value
    return out


def reference(
    x, l0_ffn1_norm, l0_ffn1_w_up, l0_ffn1_w_down, l0_mix_norm, l0_w_in, l0_conv_w, l0_a_log,
    l0_dt_bias, l0_gdn_norm, l0_w_out, l0_ffn2_norm, l0_ffn2_w_up, l0_ffn2_w_down, l1_ffn1_norm,
    l1_ffn1_w_up, l1_ffn1_w_down, l1_mix_norm, l1_w_in, l1_lambda_q1, l1_lambda_k1,
    l1_lambda_q2, l1_lambda_k2, l1_diff_norm, l1_w_out, l1_ffn2_norm, l1_ffn2_w_up,
    l1_ffn2_w_down, final_norm, e_norm_mix_2, e_w_in_2, sgu_ln_g_2, sgu_ln_b_2, sgu_w_2,
    sgu_b_2, rwkv_mu_2, rwkv_w0_2, rwkv_w2_2, rwkv_a0_2, rwkv_a2_2, rwkv_g2_2, rwkv_k_k_2,
    rwkv_k_a_2, rwkv_r_k_2, rwkv_gn_g_2, rwkv_gn_b_2, e_w_out_2, e_norm_ffn_2, ffn_w_gate_2,
    ffn_w_up_2, ffn_w_down_2, o_norm_mix_2, o_w_in_2, nsa_cmp_pos_k_2, nsa_cmp_pos_v_2,
    nsa_cmp_k_w1_2, nsa_cmp_k_w2_2, nsa_cmp_v_w1_2, nsa_cmp_v_w2_2, conv_w_2, o_w_out_2,
    o_norm_ffn_2, moe_router_2, moe_router_b_2, moe_w_gate_2, moe_w_up_2, moe_w_down_2,
    final_norm_2,
):
    x = first_block(
        x, l0_ffn1_norm, l0_ffn1_w_up, l0_ffn1_w_down, l0_mix_norm, l0_w_in, l0_conv_w,
        l0_a_log, l0_dt_bias, l0_gdn_norm, l0_w_out, l0_ffn2_norm, l0_ffn2_w_up, l0_ffn2_w_down,
        l1_ffn1_norm, l1_ffn1_w_up, l1_ffn1_w_down, l1_mix_norm, l1_w_in, l1_lambda_q1,
        l1_lambda_k1, l1_lambda_q2, l1_lambda_k2, l1_diff_norm, l1_w_out, l1_ffn2_norm,
        l1_ffn2_w_up, l1_ffn2_w_down, final_norm,
    )
    return second_block(
        x, e_norm_mix_2, e_w_in_2, sgu_ln_g_2, sgu_ln_b_2, sgu_w_2, sgu_b_2, rwkv_mu_2,
        rwkv_w0_2, rwkv_w2_2, rwkv_a0_2, rwkv_a2_2, rwkv_g2_2, rwkv_k_k_2, rwkv_k_a_2,
        rwkv_r_k_2, rwkv_gn_g_2, rwkv_gn_b_2, e_w_out_2, e_norm_ffn_2, ffn_w_gate_2, ffn_w_up_2,
        ffn_w_down_2, o_norm_mix_2, o_w_in_2, nsa_cmp_pos_k_2, nsa_cmp_pos_v_2, nsa_cmp_k_w1_2,
        nsa_cmp_k_w2_2, nsa_cmp_v_w1_2, nsa_cmp_v_w2_2, conv_w_2, o_w_out_2, o_norm_ffn_2,
        moe_router_2, moe_router_b_2, moe_w_gate_2, moe_w_up_2, moe_w_down_2, final_norm_2,
    )


_drawn_inputs = setup_inputs


def setup_inputs(seed=0):
    import zlib

    import numpy as np

    out = dict(_drawn_inputs(seed))
    spreads = {}
    factors = {'l1_lambda_k1': 8.271,
     'l1_lambda_k2': 7.46,
     'sgu_ln_b_2': 3.824,
     'rwkv_w2_2': 3.825,
     'nsa_cmp_pos_k_2': 8.0,
     'moe_router_b_2': 4.307,
     'l0_ffn2_norm': 2.779,
     'l1_ffn2_norm': 2.936,
     'rwkv_k_k_2': 2.763,
     'rwkv_gn_b_2': 3.156,
     'nsa_cmp_pos_v_2': 2.91,
     'l1_ffn1_norm': 4.294,
     'l1_mix_norm': 3.362,
     'l1_diff_norm': 3.317}
    for name, (base, spread) in spreads.items():
        noise = np.random.default_rng([zlib.crc32(name.encode()), seed]).standard_normal(out[name].shape)
        drawn = base * np.exp(spread * noise) if base else spread * noise
        out[name] = jnp.asarray(drawn.astype(out[name].dtype))
    for name, factor in factors.items():
        out[name] = (out[name] * factor).astype(out[name].dtype)
    return out
```

```python
import math
from contextlib import ExitStack, contextmanager

import numpy as np
import concourse.bass as bass
from concourse import mybir

F32 = mybir.dt.float32
ACT = mybir.ActivationFunctionType
ALU = mybir.AluOpType
AX = mybir.AxisListType

P = 128
SEQ, D_MODEL, D_FF = 256, 1024, 2816
TT = SEQ // P
KT = D_MODEL // P
EXPERTS, D_EXPERT = 8, 1408
EPS = 1e-6
STEP = 3 * D_MODEL
COLS = STEP // KT
SLOTS = 4
HEADS = 4
LEVELS = 7
LAMBDA_INIT = 0.8 - 0.6 * math.exp(-0.3)
CMP_N, CMP_PAD = 15, 16

NETWORK = [("ffn", 0), ("delta", 1), ("ffn", 2), ("ffn", 3), ("attention", 4), ("ffn", 5), ("final", 0),
           ("rwkv", 6), ("ffn", 7), ("sparse", 8), ("moe", 9), ("final", 1)]
FF_STEPS, MOE_STEPS = D_FF // P, EXPERTS * D_EXPERT // P
OUT_STEPS = -(-D_MODEL // COLS)
DELTA_T, DELTA_K = 4, 6
ATT_K = 8
RWKV_K, RWKV_T = 3, 5
SPARSE_K, SPARSE_T, SPARSE_C = 3, 6, 3
STEPS = {"ffn": FF_STEPS, "moe": MOE_STEPS, "final": 0, "delta": DELTA_T + DELTA_K + OUT_STEPS,
         "attention": ATT_K + OUT_STEPS, "rwkv": RWKV_K + RWKV_T + OUT_STEPS,
         "sparse": SPARSE_K + SPARSE_T + SPARSE_C + OUT_STEPS}


class Places:

    def __init__(self, sizes):
        self.at, self.width = {}, 0
        for name, n in sizes:
            self.at[name] = (self.width, self.width + n)
            self.width += n

    def __getitem__(self, name):
        return slice(*self.at[name])


COLUMN = Places([("gain", 10 * KT), ("conv", 4 * 12), ("mu", 14), ("w0", 4), ("a0", 4), ("k_k", 4), ("k_a", 4),
                 ("r_k", 4), ("sgu_b", 4), ("sgu_w", 4 * P), ("router", KT * EXPERTS), ("lora", 512), ("g2", 512),
                 ("cmp_k2", 2 * 64), ("cmp_v2", 2 * 64), ("pos_k", 16), ("pos_v", 16), ("conv3", 3 * 4)])
ROW = Places([("final0", D_MODEL), ("final1", D_MODEL), ("gdn_norm", P), ("diff_norm", P), ("ln_g", 512), ("ln_b", 512),
              ("gn_g", 512), ("gn_b", 512), ("a_log", 4), ("dt_bias", 4), ("router_b", 8), ("lq1", 64), ("lk1", 64),
              ("lq2", 64), ("lk2", 64)])
TABLE = Places([("eps", 4), ("ident", P), ("ones", P), ("incl_t", P), ("strict", P), ("upper", P), ("level", LEVELS * P),
                ("ret", HEADS * 3 * P), ("count", 3 * P), ("bias", 3 * P), ("bias_dil", 3 * P), ("cos32", TT * 32), ("sin32", TT * 32),
                ("cos64", TT * 64), ("sin64", TT * 64), ("cos8", TT * 8), ("sin8", TT * 8),
                ("cmp_bias", TT * CMP_PAD), ("cmp_mask", TT * CMP_PAD), ("pair_ones", P),
                ("pair_sel", 2), ("cmp_block", 8), ("expert_row", EXPERTS * P), ("lower8", EXPERTS * EXPERTS)])


class Progress:

    def __init__(self, marks, sem, name):
        self.marks, self.sem, self.name, self.n = marks, sem, name, 0

    def __call__(self, label=None):
        self.n += 1
        if label is not None:
            self.marks[label] = (self.name, self.n)
        return self.sem, 1

    def so_far(self):
        return self.sem, self.n


class Stage:

    def __init__(self, marks, sems, name):
        self.tensor, self.vector, self.scalar, self.pool = (
            sems.setdefault(f"{name}_{e}", Progress(marks, None, f"{name}_{e}"))
            for e in ("tensor", "vector", "scalar", "pool"))


STAGES = ("norm", "ffn", "delta", "attention", "rwkv", "sparse", "moe", "proj", "inverse")


def network_kernel(nc, x_in, stream, columns_in, rows_in, tables_in, out, marks):
    ctx = ExitStack()
    with ctx:
        def sb(name, shape):
            return ctx.enter_context(nc.sbuf_tensor(name, shape, F32))

        def sem(name):
            return ctx.enter_context(nc.semaphore(name))

        ring = sb("ring", [P, SLOTS, STEP])
        X = sb("X", [P, TT, D_MODEL])
        hT = sb("hT", [P, KT, SEQ])
        O = sb("O", [P, TT, D_MODEL])
        columns = sb("columns", [P, COLUMN.width])
        rows = sb("rows", [P, ROW.width])
        tables = sb("tables", [P, TABLE.width])
        squares = sb("squares", [P, TT])
        rms = sb("rms", [P, TT])
        rstd = sb("rstd", [P, TT])
        psum = ctx.enter_context(nc.psum_tensor("psum", [P, 8, 512], F32))

        @contextmanager
        def arena():
            with ExitStack() as own:
                yield lambda name, shape: own.enter_context(nc.sbuf_tensor(name, shape, F32))

        def col(name):
            return columns[:, COLUMN[name]]

        def row(name):
            return rows[:, ROW[name]]

        def table(name):
            return tables[:, TABLE[name]]

        def wide(ap, n):
            return ap.unsqueeze(len(ap.shape)).to_broadcast(list(ap.shape) + [n])

        def over(ap, n):
            return ap.unsqueeze(1).to_broadcast([ap.shape[0], n, ap.shape[1]])

        ident, ones = table("ident"), table("ones")
        eps, ln_eps, gn_eps, two_eps = (table("eps")[:, i:i + 1] for i in range(4))

        step_loaded = [sem(f"step_loaded_{s}") for s in range(SLOTS)]
        steps_used = sem("steps_used")
        ffn_up_ready = sem("ffn_up_ready")
        ffn_silu_ready = sem("ffn_silu_ready")
        ffn_gated = sem("ffn_gated")
        ffn_act_ready = sem("ffn_act_ready")
        stored = sem("out_stored")
        progress = {}
        stages = {name: Stage(marks, progress, name) for name in STAGES}
        progress["loaded"] = Progress(marks, None, "loaded")
        for name, one in progress.items():
            one.sem = sem(name)
        loaded = progress["loaded"].sem
        norm, ffn, delta, attn = (stages[n] for n in ("norm", "ffn", "delta", "attention"))
        rwkv, sparse, moe, proj, inverse = (stages[n] for n in ("rwkv", "sparse", "moe", "proj", "inverse"))

        def after(label):
            name, n = marks.get(label, ("norm_tensor", 1))
            return progress[name].sem, n

        bank_of, bank_order = {}, []

        def open_bank(pe, label):
            n = len(bank_order)
            bank_of[label] = n % 8
            bank_order.append(label)
            if n >= 8 and bank_order[n - 8] is not None:
                pe.wait_ge(*after(f"used {bank_order[n - 8]}"))
            return psum[:, n % 8, :]

        def reset_banks():
            bank_order[:] = [None] * 8

        def bank(label):
            return psum[:, bank_of[label], :]

        first_step, total = [], 0
        for kind, _ in NETWORK:
            first_step.append(total)
            total += STEPS[kind]

        def slot(g):
            return ring[:, g % SLOTS, :]

        def wait_step(pe, g):
            pe.wait_ge(step_loaded[g % SLOTS], 16 * (g // SLOTS + 1))

        block = ctx.enter_context(nc.Block())

        def norm_scalar(act, n):
            act.wait_ge(*after(f"x {n}"))
            for t in range(TT):
                act.activation(O[:, t, :], X[:, t, :], ACT.Square, scale=D_MODEL ** -0.5,
                               accum_out=squares[:, t:t + 1]).then_inc(*norm.scalar(f"norm {n} squares"))
            rstd_scalar(act, n)

        def rstd_scalar(act, n):
            act.wait_ge(*after(f"norm {n} squares"))
            act.activation(rms[:, :], squares[:, :], ACT.Sqrt, bias=eps).then_inc(*norm.scalar(f"norm {n} root"))

        def rstd_vector(dve, n):
            dve.wait_ge(*after(f"norm {n} root"))
            dve.reciprocal(rstd[:, :], rms[:, :]).then_inc(*norm.vector())
            dve.wait_ge(*norm.vector.so_far())

        def norm_vector(dve, n):
            rstd_vector(dve, n)
            for t in range(TT):
                dve.tensor_scalar(O[:, t, :], X[:, t, :], rstd[:, t:t + 1], None, ALU.mult) \
                   .then_inc(*norm.vector(f"norm {n} xn {t}"))
            turn_vector(dve, f"norm {n}", norm, KT, columns[:, KT * NETWORK[n][1]:KT * (NETWORK[n][1] + 1)])

        def norm_tensor(pe, n):
            turn_tensor(pe, f"norm {n}", norm, KT, [f"norm {n} xn {t}" for t in range(TT)])

        def turn_tensor(pe, name, stage, tiles, sources):
            for t in range(TT):
                pe.wait_ge(*after(sources[t]))
                for q in range(0, tiles, 4):
                    b = open_bank(pe, f"{name} turn {t} {q}")
                    for k in range(4):
                        last = pe.transpose(b[:, k * P:(k + 1) * P], O[:, t, (q + k) * P:(q + k + 1) * P], ident)
                    last.then_inc(*stage.tensor(f"{name} turn {t} {q}"))

        def turn_vector(dve, name, stage, tiles, gain=None):
            for t in range(TT):
                for q in range(0, tiles, 4):
                    dve.wait_ge(*after(f"{name} turn {t} {q}"))
                    dst = hT[:, q:q + 4, t * P:(t + 1) * P]
                    src = bank(f"{name} turn {t} {q}").rearrange("p (k c) -> p k c", k=4)
                    if gain is None:
                        ins = dve.tensor_copy(dst, src)
                    else:
                        ins = dve.tensor_tensor(dst, src, wide(gain[:, q:q + 4], P), ALU.mult)
                    ins.then_inc(*stage.vector(f"used {name} turn {t} {q}"))

        def wait_hT(eng, name, tiles=KT):
            eng.wait_ge(*after(f"used {name} turn {TT - 1} {tiles - 4}"))

        def proj_tiles(kinds):
            return [(s, kind, j) for s, kind in enumerate(kinds) for j in range({"k": TT, "t": 3, "v": 2, "u": 1}[kind])]

        def release(pe, name, s):
            pe.wait_ge(*after(f"{name} {s} last"))
            pe.nop().then_inc(steps_used, 1)

        def proj_tensor(pe, name, g0, kinds):
            for s, kind, j in proj_tiles(kinds):
                g = g0 + s
                w = slot(g).rearrange("p (k c) -> p k c", k=KT)
                if j == 0:
                    wait_step(pe, g)
                b = open_bank(pe, f"{name} {s} {j}")
                for k in range(KT):
                    if kind == "k":
                        ins = pe.matmul(b[:, 0:COLS], hT[:, k, j * P:(j + 1) * P], w[:, k, :],
                                        start=k == 0, stop=k == KT - 1)
                    else:
                        ins = pe.matmul(b[:, 0:SEQ], w[:, k, j * P:(j + 1) * P], hT[:, k, :],
                                        start=k == 0, stop=k == KT - 1)
                ins.then_inc(*proj.tensor(f"{name} {s} {j}"))
                marks[f"{name} {s} last"] = marks[f"{name} {s} {j}"]
                if j == 0 and s > 0:
                    release(pe, name, s - 1)
            release(pe, name, s)

        def proj_copies(eng, name, kinds, parity, place, steps=range(99)):
            for n, (s, kind, j) in enumerate(proj_tiles(kinds)):
                if n % 2 != parity or s not in steps:
                    continue
                eng.wait_ge(*after(f"{name} {s} {j}"))
                pairs = place(s, j, bank(f"{name} {s} {j}"))
                for i, (dst, src) in enumerate(pairs):
                    ins = eng.tensor_copy(dst, src) if parity else eng.activation(dst, src, ACT.Copy)
                    side = proj.vector if parity else proj.scalar
                    ins.then_inc(*side(f"used {name} {s} {j}" if i == len(pairs) - 1 else None))

        def wait_proj(eng, name, kinds, steps=range(99)):
            tiles = [x for x in proj_tiles(kinds) if x[0] in steps]
            for s, _, j in tiles[-2:]:
                eng.wait_ge(*after(f"used {name} {s} {j}"))

        def out_tensor(pe, name, g0, tiles=KT):
            wait_hT(pe, name, tiles)
            proj_tensor(pe, f"{name} out", g0, "k" * OUT_STEPS)

        def out_vector(dve, name, at):
            for s, kind, j in proj_tiles("k" * OUT_STEPS):
                c0, c1 = s * COLS, min((s + 1) * COLS, D_MODEL)
                dve.wait_ge(*after(f"{name} out {s} {j}"))
                dve.tensor_tensor(X[:, j, c0:c1], X[:, j, c0:c1], bank(f"{name} out {s} {j}")[:, 0:c1 - c0], ALU.add) \
                   .then_inc(*proj.vector(f"used {name} out {s} {j}"))
            marks[f"x {at + 1}"] = marks[f"used {name} out {OUT_STEPS - 1} {TT - 1}"]

        with arena() as take:
            silu, gated, act_t = (take(n, [P, 2, SEQ]) for n in ("silu", "gated", "act_t"))
            gate_rows = take("gate_rows", [P, EXPERTS, SEQ])
        ffn_steps_before, n_ff = [], 0
        for kind, _ in NETWORK:
            ffn_steps_before.append(n_ff)
            n_ff += STEPS[kind] if kind in ("ffn", "moe") else 0

        def ffn_loop(eng, n, step):
            turns = (n - 2) // SLOTS
            with eng.Fori(0, turns) as i:
                for u in range(SLOTS):
                    step(2 + u, SLOTS * i + 2 + u, i)
            for s in range(2 + turns * SLOTS, n):
                step(s, s, 0)

        def ffn_tensor(pe, at):
            n, g0, f0 = STEPS[NETWORK[at][0]], first_step[at], ffn_steps_before[at]

            def up(s, sv, turn, f_known):
                g = g0 + s
                w = slot(g)[:, 0:2 * D_MODEL].rearrange("p (o k c) -> p o k c", o=2, k=KT)
                pe.wait_ge(step_loaded[g % SLOTS], 16 * (g // SLOTS + 1) + 16 * turn)
                if f_known is None or f_known >= 2:
                    pe.wait_ge(ffn_act_ready, f0 + sv - 1)
                for o in range(2):
                    for k in range(KT):
                        ins = pe.matmul(psum[:, 4 + s % 2, o * SEQ:(o + 1) * SEQ], w[:, o, k, :], hT[:, k, :],
                                        start=k == 0, stop=k == KT - 1)
                ins.then_inc(ffn_up_ready, 1)

            def down(s, sv, first, last):
                w = slot(g0 + s)[:, 2 * D_MODEL:STEP]
                pe.wait_ge(ffn_act_ready, f0 + sv + 1)
                for t in range(TT):
                    for h in range(2):
                        ins = pe.matmul(psum[:, 2 * t + h, :], act_t[:, s % 2, t * P:(t + 1) * P],
                                        w[:, h * 512:(h + 1) * 512], start=first, stop=last, skip_group_check=True)
                ins.then_inc(steps_used, 1)

            up(0, 0, 0, f0)
            up(1, 1, 0, f0 + 1)
            down(0, 0, True, False)

            def step(s, sv, turn):
                up(s, sv, turn, None)
                down(s - 1, sv - 1, False, False)

            ffn_loop(pe, n, step)
            down(n - 1, n - 1, False, True)
            reset_banks()

        def ffn_scalar(act, at):
            n, f0 = STEPS[NETWORK[at][0]], ffn_steps_before[at]

            def step(s, sv, turn):
                act.wait_ge(ffn_up_ready, f0 + sv + 1)
                if s >= 2 or f0 > 0:
                    act.wait_ge(ffn_act_ready, f0 + sv - 1)
                act.activation(silu[:, s % 2, :], psum[:, 4 + s % 2, 0:SEQ], ACT.Silu).then_inc(ffn_silu_ready, 1)

            step(0, 0, 0)
            step(1, 1, 0)
            ffn_loop(act, n, step)

        def ffn_vector(dve, at, factor):
            kind = NETWORK[at][0]
            n, g0, f0 = STEPS[kind], first_step[at], ffn_steps_before[at]

            def step(s, sv, turn):
                dve.wait_ge(ffn_silu_ready, f0 + sv + 1)
                if kind == "ffn":
                    if s >= 2 or g0 > 0:
                        dve.wait_ge(steps_used, g0 + sv - 1)
                    dve.tensor_tensor(act_t[:, s % 2, :], silu[:, s % 2, :], psum[:, 4 + s % 2, SEQ:2 * SEQ],
                                      ALU.mult).then_inc(ffn_act_ready, 1)
                else:
                    dve.tensor_tensor(gated[:, s % 2, :], silu[:, s % 2, :], psum[:, 4 + s % 2, SEQ:2 * SEQ],
                                      ALU.mult).then_inc(ffn_gated, 1)
                    dve.wait_ge(ffn_gated, sv + 1)
                    dve.wait_ge(steps_used, g0 + sv - 1)
                    expert = sv // (D_EXPERT // P)
                    dve.tensor_tensor(act_t[:, s % 2, :], gated[:, s % 2, :], gate_rows[:, expert, :],
                                      ALU.mult).then_inc(ffn_act_ready, 1)

            step(0, 0, 0)
            step(1, 1, 0)
            ffn_loop(dve, n, step)
            dve.wait_ge(steps_used, g0 + n)
            for t in range(TT):
                for h in range(2):
                    c = slice(h * 512, (h + 1) * 512)
                    dve.scalar_tensor_tensor(X[:, t, c], psum[:, 2 * t + h, :], factor, X[:, t, c], ALU.mult, ALU.add) \
                       .then_inc(*ffn.vector(f"x {at + 1}"))

        def final_vector(dve, at):
            which = NETWORK[at][1]
            rstd_vector(dve, at)
            for t in range(TT):
                dve.scalar_tensor_tensor(X[:, t, :], X[:, t, :], rstd[:, t:t + 1], row(f"final{which}"),
                                         ALU.mult, ALU.mult).then_inc(*norm.vector(f"x {at + 1}"))
        def four(ap):
            return ap.rearrange("p (m c) -> p m c", m=4)

        def inverse_vector(dve, name, A, T, U, AM):
            dve.tensor_tensor(AM[:, :, :], A[:, :, :], over(table("level")[:, 0:P], 8), ALU.mult).then_inc(*inverse.vector())
            dve.wait_ge(*inverse.vector.so_far())
            dve.tensor_tensor(T[:, :, :], over(ident, 8), AM[:, :, :], ALU.subtract).then_inc(*inverse.vector(f"{name} T 0"))
            for l in range(1, LEVELS):
                for c in range(2):
                    m = slice(4 * c, 4 * c + 4)
                    dve.wait_ge(*after(f"{name} dU {l} {c}"))
                    dve.wait_ge(*after(f"{name} U 0 {c}" if l == 1 else f"{name} U {l - 1} {c}"))
                    dve.tensor_tensor(U[:, m, :], U[:, m, :], four(bank(f"{name} dU {l} {c}")), ALU.subtract) \
                       .then_inc(*inverse.vector(f"{name} U {l} {c}"))
                    marks[f"used {name} dU {l} {c}"] = marks[f"{name} U {l} {c}"]
                    if l < LEVELS - 1:
                        dve.wait_ge(*after(f"{name} dT {l} {c}"))
                        dve.tensor_tensor(T[:, m, :], T[:, m, :], four(bank(f"{name} dT {l} {c}")), ALU.subtract) \
                           .then_inc(*inverse.vector(f"{name} T {l} {c}"))
                        marks[f"used {name} dT {l} {c}"] = marks[f"{name} T {l} {c}"]

        def inverse_scalar(act, name, U, Y):
            for c in range(2):
                act.wait_ge(*after(f"{name} turn {c}"))
                act.activation(U[:, 4 * c:4 * c + 4, :], four(bank(f"{name} turn {c}")), ACT.Copy) \
                   .then_inc(*inverse.scalar(f"{name} U 0 {c}"))
                marks[f"used {name} turn {c}"] = marks[f"{name} U 0 {c}"]
            for l in range(1, LEVELS):
                for c in range(2):
                    act.wait_ge(*after(f"{name} Y {l} {c}"))
                    act.activation(Y[:, 4 * c:4 * c + 4, :], four(bank(f"{name} Y {l} {c}")), ACT.Copy) \
                       .then_inc(*inverse.scalar(f"used {name} Y {l} {c}"))

        def inverse_pool(pool, name, A, AM):
            for l in range(1, LEVELS):
                if l == 1:
                    pool.wait_ge(*after(f"{name} T 0"))
                else:
                    pool.wait_ge(*after(f"{name} Y {l - 1} 1"))
                pool.tensor_tensor(AM[:, :, :], A[:, :, :], over(table("level")[:, l * P:(l + 1) * P], 8), ALU.mult) \
                    .then_inc(*inverse.pool(f"{name} AM {l}"))

        def inverse_tensor(pe, name, T, U, Y, AM):
            pe.wait_ge(*after(f"{name} T 0"))
            for c in range(2):
                b = open_bank(pe, f"{name} turn {c}")
                for m in range(4):
                    ins = pe.transpose(b[:, m * P:(m + 1) * P], T[:, 4 * c + m, :], ident)
                ins.then_inc(*inverse.tensor(f"{name} turn {c}"))
            for l in range(1, LEVELS):
                pe.wait_ge(*after(f"{name} AM {l}"))
                for c in range(2):
                    pe.wait_ge(*after(f"{name} U {l - 1} {c}"))
                    b = open_bank(pe, f"{name} Y {l} {c}")
                    for m in range(4):
                        ins = pe.matmul(b[:, m * P:(m + 1) * P], AM[:, 4 * c + m, :], U[:, 4 * c + m, :], start=True, stop=True)
                    ins.then_inc(*inverse.tensor(f"{name} Y {l} {c}"))
                for c in range(2):
                    pe.wait_ge(*after(f"used {name} Y {l} {c}"))
                    if l >= 2:
                        pe.wait_ge(*after(f"{name} T {l - 1} {c}"))
                    b = open_bank(pe, f"{name} dU {l} {c}")
                    for m in range(4):
                        ins = pe.matmul(b[:, m * P:(m + 1) * P], T[:, 4 * c + m, :], Y[:, 4 * c + m, :], start=True, stop=True)
                    ins.then_inc(*inverse.tensor(f"{name} dU {l} {c}"))
                    if l < LEVELS - 1:
                        b = open_bank(pe, f"{name} dT {l} {c}")
                        for m in range(4):
                            ins = pe.matmul(b[:, m * P:(m + 1) * P], Y[:, 4 * c + m, :], T[:, 4 * c + m, :], start=True, stop=True)
                        ins.then_inc(*inverse.tensor(f"{name} dT {l} {c}"))

        def rope_vector(dve, stage, x, half, cos, sin, scratch):
            heads = x.shape[1]
            x1, x2 = x[:, :, 0:half], x[:, :, half:2 * half]
            c, s = over(cos, heads), over(sin, heads)
            for i, (a, b) in enumerate(((x1, c), (x2, s), (x1, s), (x2, c))):
                dve.tensor_tensor(scratch[:, i], a, b, ALU.mult).then_inc(*stage.vector())
            dve.wait_ge(*stage.vector.so_far())
            dve.tensor_tensor(x1, scratch[:, 0], scratch[:, 1], ALU.subtract).then_inc(*stage.vector())
            dve.tensor_tensor(x2, scratch[:, 2], scratch[:, 3], ALU.add).then_inc(*stage.vector())
            dve.wait_ge(*stage.vector.so_far())

        with arena() as take:
            d_pad = take("d_pad", [P, 12, SEQ + 3])
            d_qkv = take("d_qkv", [P, 12, SEQ])
            d_tok = take("d_tok", [P, TT, DELTA_K * COLS])
            d_A = take("d_A", [P, 8, P])
            d_qk = take("d_qk", [P, 8, P])
            d_Y = take("d_Y", [P, 8, P])
            d_AM = take("d_AM", [P, 8, P])
            d_T = take("d_T", [P, 8, P])
            d_U = take("d_U", [P, 8, P])
            d_k = take("d_k", [P, 8, P])
            d_v = take("d_v", [P, 8, P])
            d_rhs = take("d_rhs", [P, 4, P])
            d_vn = take("d_vn", [P, 4, P])
            d_s1 = take("d_s1", [P, 4, P])
            d_rope = take("d_rope", [P, 4, 8, 32])
            d_small = take("d_small", [P, 12, 8])
        d_beta, d_t, d_neg, d_pos, d_e, d_ln, d_ea, d_g, d_gc, d_egc, d_kdec = (d_small[:, i, :] for i in range(11))
        d_sum = take_sum = d_T.rearrange("p m c -> p (m c)")[:, 0:16]
        d_rms = d_T.rearrange("p m c -> p (m c)")[:, 16:32]
        pad_flat = d_pad.rearrange("p c t -> p (c t)")
        d_st = pad_flat[:, 0:4 * 384].rearrange("p (h c) -> p h c", h=4)
        d_rt = pad_flat[:, 1536:1536 + 1024].rearrange("p (i t) -> p i t", i=4)
        d_square = O.rearrange("p t d -> p (t d)").rearrange("p (c t) -> p c t", t=SEQ)
        d_out_square = d_qkv.rearrange("p c t -> p (c t)")[:, 0:TT * D_MODEL].rearrange("p (t d) -> p t d", t=TT)
        D_KINDS = "t" * DELTA_T + "k" * DELTA_K
        Z, B_, A_, RQ, RV, RG = 0, 512, 516, 520, 1032, 1544

        def d_place(s, j, b):
            if s < DELTA_T:
                return [(d_pad[:, 3 * s + j, 3:3 + SEQ], b[:, 0:SEQ])]
            return [(d_tok[:, j, (s - DELTA_T) * COLS:(s - DELTA_T + 1) * COLS], b[:, 0:COLS])]

        def d_chunk(i, c):
            return d_qkv[:, i, c * P:(c + 1) * P]

        def by_chunk(ap):
            return ap.rearrange("p (c h) -> p c h", c=2)

        def delta_tensor(pe, at):
            g0 = first_step[at]
            proj_tensor(pe, "delta", g0, D_KINDS)
            for q in range(4):
                if q == 0:
                    pe.wait_ge(*after("delta square"))
                b = open_bank(pe, f"delta ss {q}")
                pe.matmul(b, ones, d_square[:, 2 * q:2 * q + 2, :], start=True, stop=True) \
                  .then_inc(*delta.tensor(f"delta ss {q}"))
            pe.wait_ge(*after("delta g"))
            b = open_bank(pe, "delta gcum")
            pe.matmul(b[:, 0:8], table("incl_t"), d_g, start=True, stop=True).then_inc(*delta.tensor("delta gcum"))
            pe.wait_ge(*after("delta g wide"))
            for c in range(2):
                b = open_bank(pe, f"delta grow {c}")
                for h in range(4):
                    ins = pe.matmul(b[:, h * P:(h + 1) * P], d_AM[:, 4 * c + h, :], table("incl_t"), start=True, stop=True)
                ins.then_inc(*delta.tensor(f"delta grow {c}"))
            pe.wait_ge(*after("delta silu v"))
            pe.wait_ge(*after("delta norm 3"))
            for i, name in ((4, "k"), (8, "v")):
                for c in range(2):
                    b = open_bank(pe, f"delta tok {name} {c}")
                    for h in range(4):
                        ins = pe.transpose(b[:, h * P:(h + 1) * P], d_chunk(i + h, c), ident)
                    ins.then_inc(*delta.tensor(f"delta tok {name} {c}"))
            for i, name in ((4, "kk"), (0, "kq")):
                for c in range(2):
                    b = open_bank(pe, f"delta {name} {c}")
                    for h in range(4):
                        ins = pe.matmul(b[:, h * P:(h + 1) * P], d_chunk(4 + h, c), d_chunk(i + h, c), start=True, stop=True)
                    ins.then_inc(*delta.tensor(f"delta {name} {c}"))
            for t in range(TT):
                pe.wait_ge(*after(f"delta rope {t}"))
                b = open_bank(pe, f"delta rt {t}")
                for i in range(4):
                    ins = pe.transpose(b[:, i * P:(i + 1) * P], d_tok[:, t, RQ + i * P:RQ + (i + 1) * P], ident)
                ins.then_inc(*delta.tensor(f"delta rt {t}"))
            for t in range(TT):
                pe.wait_ge(*after(f"used delta rt {t}"))
            for h in range(HEADS):
                q, k = (d_rt[64 * (h % 2):64 * (h % 2) + 64, i + h // 2, :] for i in (0, 2))
                b = open_bank(pe, f"delta rs {h}")
                pe.matmul(b[:, 0:SEQ], k[:, 0:P], q, start=True, stop=True)
                pe.matmul(b[:, SEQ:3 * P], k[:, P:SEQ], q[:, P:SEQ], start=True, stop=True) \
                  .then_inc(*delta.tensor(f"delta rs {h}"))
            pe.wait_ge(*after(f"used delta rs {HEADS - 1}"))
            for t in range(TT):
                b = open_bank(pe, f"delta ro {t}")
                for h in range(HEADS):
                    for j in range(t + 1):
                        first = t * P if j == 0 else SEQ
                        ins = pe.matmul(b[:, h * P:(h + 1) * P], d_st[:, h, first:first + P],
                                        d_tok[:, j, RV + h * P:RV + (h + 1) * P], start=j == 0, stop=j == t)
                ins.then_inc(*delta.tensor(f"delta ro {t}"))
            inverse_tensor(pe, "delta", d_T, d_U, d_Y, d_AM)
            for c in range(2):
                if c == 1:
                    pe.wait_ge(*after("used delta s1"))
                    for i, name in ((4, "ks"), (0, "qs")):
                        b = open_bank(pe, f"delta {name}")
                        for h in range(4):
                            ins = pe.matmul(b[:, h * P:(h + 1) * P], d_chunk(i + h, 1), d_s1[:, h, :], start=True, stop=True)
                        ins.then_inc(*delta.tensor(f"delta {name}"))
                pe.wait_ge(*after(f"delta U {LEVELS - 1} {c}"))
                pe.wait_ge(*after(f"delta rhs {c}"))
                b = open_bank(pe, f"delta vn {c}")
                for h in range(4):
                    ins = pe.matmul(b[:, h * P:(h + 1) * P], d_U[:, 4 * c + h, :], d_rhs[:, h, :], start=True, stop=True)
                ins.then_inc(*delta.tensor(f"delta vn {c}"))
                pe.wait_ge(*after(f"used delta vn {c}"))
                if c == 0:
                    b = open_bank(pe, "delta s1")
                    for h in range(4):
                        ins = pe.matmul(b[:, h * P:(h + 1) * P], d_k[:, h, :], d_vn[:, h, :], start=True, stop=True)
                    ins.then_inc(*delta.tensor("delta s1"))
                b = open_bank(pe, f"delta o {c}")
                for h in range(4):
                    ins = pe.matmul(b[:, h * P:(h + 1) * P], d_qk[:, 4 * c + h, :], d_vn[:, h, :], start=True, stop=True)
                ins.then_inc(*delta.tensor(f"delta o {c}"))
            turn_tensor(pe, "delta", delta, KT, ["delta gated"] * TT)
            out_tensor(pe, "delta", g0 + DELTA_T + DELTA_K)

        def delta_scalar(act, at):
            def does(label, *args, **kw):
                act.activation(*args, **kw).then_inc(*delta.scalar(label))

            proj_copies(act, "delta", D_KINDS, 0, d_place, range(DELTA_T))
            act.wait_ge(*after("delta conv"))
            does("delta silu qk", d_qkv[:, 0:8, :], d_qkv[:, 0:8, :], ACT.Silu)
            does("delta silu v", d_qkv[:, 8:12, :], d_qkv[:, 8:12, :], ACT.Silu)
            act.wait_ge(*after("delta silu qk"))
            does("delta square", d_square, d_qkv[:, 0:8, :], ACT.Square)
            proj_copies(act, "delta", D_KINDS, 0, d_place, range(DELTA_T, DELTA_T + DELTA_K))
            wait_proj(act, "delta", D_KINDS)
            for q in range(4):
                act.wait_ge(*after(f"delta ss {q}"))
                scale, bias = (float(P), two_eps) if q < 2 else (1.0, eps)
                does(f"used delta ss {q}", d_square[:, 2 * q:2 * q + 2, :], bank(f"delta ss {q}").rearrange("p (c t) -> p c t", c=2),
                     ACT.Sqrt, bias=bias, scale=scale)
            does("delta z", d_tok[:, :, Z:Z + 512], d_tok[:, :, Z:Z + 512], ACT.Silu)
            does("delta rg", d_tok[:, :, RG:RG + 512], d_tok[:, :, RG:RG + 512], ACT.Silu)
            does("delta beta", by_chunk(d_beta), d_tok[:, :, B_:B_ + 4], ACT.Sigmoid)
            does("delta ea", d_ea[:, 0:4], row("a_log"), ACT.Exp)
            act.wait_ge(*after("delta neg"))
            does("delta e", d_e, d_neg, ACT.Exp)
            act.wait_ge(*after("delta e"))
            does("delta ln", d_ln, d_e, ACT.Ln, bias=1.0)
            for name, dst in (("k", d_k), ("v", d_v)):
                for c in range(2):
                    act.wait_ge(*after(f"delta tok {name} {c}"))
                    does(f"used delta tok {name} {c}", dst[:, 4 * c:4 * c + 4, :], four(bank(f"delta tok {name} {c}")), ACT.Copy)
            act.wait_ge(*after("delta diff"))
            does("delta D", d_A[:, :, :], d_A[:, :, :], ACT.Exp, scale=-1.0)
            does("delta DT", d_qk[:, :, :], d_qk[:, :, :], ACT.Exp)
            does("delta egc", d_egc, d_gc, ACT.Exp)
            does("delta kdec", d_kdec[:, 0:4], d_Y[:, 0:4, P - 1], ACT.Exp)
            for t in range(TT):
                act.wait_ge(*after(f"delta rt {t}"))
                does(f"used delta rt {t}", d_rt[:, :, t * P:(t + 1) * P], four(bank(f"delta rt {t}")), ACT.Copy)
            for t in range(TT):
                act.wait_ge(*after(f"delta ro {t}"))
                does(f"used delta ro {t}", O[:, t, 512:1024], bank(f"delta ro {t}"), ACT.Copy)
            inverse_scalar(act, "delta", d_U, d_Y)
            for c in range(2):
                act.wait_ge(*after(f"delta vn {c}"))
                does(f"used delta vn {c}", d_vn[:, :, :], four(bank(f"delta vn {c}")), ACT.Copy)
                if c == 0:
                    act.wait_ge(*after("delta s1"))
                    does("used delta s1", d_s1[:, :, :], four(bank("delta s1")), ACT.Copy)
            act.wait_ge(*after("delta o"))
            act.wait_ge(*after("used delta ro 1"))
            does("delta o square", d_out_square, O[:, :, :], ACT.Square)
            act.wait_ge(*after("delta o sum"))
            does("delta o root", d_rms, d_sum, ACT.Sqrt, scale=1.0 / P, bias=eps)

        def delta_pool(pool, at):
            inverse_pool(pool, "delta", d_A, d_AM)

        def delta_vector(dve, at):
            def does(label, op, *args, wait=None):
                op(*args).then_inc(*delta.vector(label))

            def settle():
                dve.wait_ge(*delta.vector.so_far())

            does("delta pad", dve.memset, d_pad[:, :, 0:3], 0.0)
            proj_copies(dve, "delta", D_KINDS, 1, d_place, range(DELTA_T))
            wait_proj(dve, "delta", D_KINDS, range(DELTA_T))
            settle()
            conv = col("conv")
            for j in range(4):
                for c in range(12):
                    w, x = conv[:, 12 * j + c:12 * j + c + 1], d_pad[:, c, j:j + SEQ]
                    if j == 0:
                        does(None, dve.tensor_scalar, d_qkv[:, c, :], x, w, None, ALU.mult)
                    else:
                        does("delta conv", dve.scalar_tensor_tensor, d_qkv[:, c, :], x, w, d_qkv[:, c, :], ALU.mult, ALU.add)
                settle()
            proj_copies(dve, "delta", D_KINDS, 1, d_place, range(DELTA_T, DELTA_T + DELTA_K))
            wait_proj(dve, "delta", D_KINDS)
            does(None, dve.tensor_tensor, by_chunk(d_t), d_tok[:, :, A_:A_ + 4], over(row("dt_bias"), 2), ALU.add)
            settle()
            does(None, dve.tensor_scalar, d_pos, d_t, 0.0, None, ALU.max)
            does(None, dve.tensor_scalar, d_neg, d_t, 0.0, None, ALU.min)
            settle()
            does("delta neg", dve.tensor_tensor, d_neg, d_neg, d_pos, ALU.subtract)
            for q in range(4):
                dve.wait_ge(*after(f"used delta ss {q}"))
                qk = d_qkv[:, 2 * q:2 * q + 2, :]
                does(None, dve.reciprocal, d_square[:, 2 * q:2 * q + 2, :], d_square[:, 2 * q:2 * q + 2, :])
                settle()
                does(f"delta norm {q}", dve.tensor_tensor, qk, qk, d_square[:, 2 * q:2 * q + 2, :], ALU.mult)
            dve.wait_ge(*after("delta ln"))
            does(None, dve.tensor_tensor, d_t, d_pos, d_ln, ALU.add)
            settle()
            does("delta g", dve.scalar_tensor_tensor, by_chunk(d_g), by_chunk(d_t), -1.0, over(d_ea[:, 0:4], 2), ALU.mult, ALU.mult)
            settle()
            does("delta g wide", dve.tensor_copy, d_AM[:, :, :], wide(d_g, P))
            dve.wait_ge(*after("delta gcum"))
            does("used delta gcum", dve.tensor_copy, d_gc, bank("delta gcum")[:, 0:8])
            settle()
            for c in range(2):
                dve.wait_ge(*after(f"delta grow {c}"))
                does(f"used delta grow {c}", dve.tensor_tensor, d_Y[:, 4 * c:4 * c + 4, :], four(bank(f"delta grow {c}")),
                     wide(d_gc[:, 4 * c:4 * c + 4], P), ALU.subtract)
            settle()
            does(None, dve.tensor_scalar, d_A[:, :, :], d_Y[:, :, :], 0.0, None, ALU.max)
            does("delta diff", dve.tensor_scalar, d_qk[:, :, :], d_Y[:, :, :], 0.0, None, ALU.min)
            for t in range(TT):
                rope_vector(dve, delta, d_tok[:, t, RQ:RQ + 512].rearrange("p (h d) -> p h d", d=64), 32,
                            table("cos32")[:, 32 * t:32 * t + 32], table("sin32")[:, 32 * t:32 * t + 32], d_rope)
                marks[f"delta rope {t}"] = (delta.vector.name, delta.vector.n)
            dve.wait_ge(*after("delta kdec"))
            does(None, dve.tensor_tensor, d_A[:, :, :], d_A[:, :, :], over(table("strict"), 8), ALU.mult)
            does(None, dve.tensor_tensor, d_qk[:, :, :], d_qk[:, :, :], over(table("incl_t"), 8), ALU.mult)
            settle()
            does(None, dve.tensor_tensor, d_A[:, :, :], d_A[:, :, :], wide(d_beta, P), ALU.mult)
            settle()
            for name, dst in (("kk", d_A), ("kq", d_qk)):
                for c in range(2):
                    dve.wait_ge(*after(f"delta {name} {c}"))
                    m = dst[:, 4 * c:4 * c + 4, :]
                    does(f"used delta {name} {c}", dve.tensor_tensor, m, m, four(bank(f"delta {name} {c}")), ALU.mult)
            for h in range(HEADS):
                dve.wait_ge(*after(f"delta rs {h}"))
                does(f"used delta rs {h}", dve.tensor_tensor, d_st[:, h, :], bank(f"delta rs {h}")[:, 0:3 * P],
                     table("ret")[:, 3 * P * h:3 * P * (h + 1)], ALU.mult)
            settle()
            dve.wait_ge(*after("used delta tok v 1"))
            does("delta rhs 0", dve.tensor_tensor, d_rhs[:, :, :], d_v[:, 0:4, :], wide(d_beta[:, 0:4], P), ALU.mult)
            does("delta k decayed", dve.tensor_tensor, d_k[:, 0:4, :], d_k[:, 0:4, :], wide(d_kdec[:, 0:4], P), ALU.mult)
            inverse_vector(dve, "delta", d_A, d_T, d_U, d_AM)
            dve.wait_ge(*after("delta ks"))
            does("used delta ks", dve.tensor_tensor, d_rhs[:, :, :], four(bank("delta ks")), wide(d_egc[:, 4:8], P), ALU.mult)
            settle()
            does(None, dve.tensor_tensor, d_rhs[:, :, :], d_v[:, 4:8, :], d_rhs[:, :, :], ALU.subtract)
            settle()
            does("delta rhs 1", dve.tensor_tensor, d_rhs[:, :, :], d_rhs[:, :, :], wide(d_beta[:, 4:8], P), ALU.mult)
            dve.wait_ge(*after("delta o 0"))
            does("used delta o 0", dve.tensor_copy, O[:, 0, 0:512], bank("delta o 0"))
            dve.wait_ge(*after("delta qs"))
            does("used delta qs", dve.tensor_tensor, four(O[:, 1, 0:512]), four(bank("delta qs")), wide(d_egc[:, 4:8], P), ALU.mult)
            settle()
            dve.wait_ge(*after("delta o 1"))
            does("delta o", dve.tensor_tensor, O[:, 1, 0:512], O[:, 1, 0:512], bank("delta o 1"), ALU.add)
            marks["used delta o 1"] = marks["delta o"]
            dve.wait_ge(*after("delta o square"))
            does("delta o sum", dve.tensor_reduce, d_sum, d_out_square.rearrange("p t (h d) -> p (t h) d", d=P), AX.X, ALU.add)
            dve.wait_ge(*after("delta o root"))
            does(None, dve.reciprocal, d_rms, d_rms)
            settle()
            heads = O.rearrange("p t (h d) -> p (t h) d", d=P)
            does(None, dve.tensor_tensor, heads, heads, wide(d_rms, P), ALU.mult)
            settle()
            for t in range(TT):
                does(None, dve.tensor_tensor, four(O[:, t, 0:512]), four(O[:, t, 0:512]), over(row("gdn_norm"), 4), ALU.mult)
            settle()
            dve.wait_ge(*after("delta rg"))
            does(None, dve.tensor_tensor, O[:, :, 0:512], O[:, :, 0:512], d_tok[:, :, Z:Z + 512], ALU.mult)
            does("delta gated", dve.tensor_tensor, O[:, :, 512:1024], O[:, :, 512:1024], d_tok[:, :, RG:RG + 512], ALU.mult)
            turn_vector(dve, "delta", delta, KT)
            out_vector(dve, "delta", at)

        UNIT = 3 * P

        def blocks(ap):
            return ap.rearrange("p u (b c) -> p (u b) c", c=P)

        def softmax_head_vector(dve, stage, name, S, units, scale, bias, small):
            for i, u in enumerate(units):
                dve.wait_ge(*after(f"{u}"))
                dve.scalar_tensor_tensor(S[:, i, :], bank(u)[:, 0:UNIT], scale, bias, ALU.mult, ALU.add) \
                   .then_inc(*stage.vector(f"used {u}"))
            dve.wait_ge(*stage.vector.so_far())
            dve.tensor_reduce(small.rearrange("p u b -> p (u b)"), blocks(S), AX.X, ALU.max).then_inc(*stage.vector())
            dve.wait_ge(*stage.vector.so_far())
            dve.tensor_tensor(small[:, :, 1], small[:, :, 1], small[:, :, 2], ALU.max).then_inc(*stage.vector())
            dve.wait_ge(*stage.vector.so_far())
            dve.tensor_copy(small[:, :, 2], small[:, :, 1]).then_inc(*stage.vector())
            dve.wait_ge(*stage.vector.so_far())
            dve.tensor_tensor(blocks(S), blocks(S), wide(small.rearrange("p u b -> p (u b)"), P), ALU.subtract) \
               .then_inc(*stage.vector(f"{name} less max"))

        def softmax_scalar(act, stage, name, S):
            act.wait_ge(*after(f"{name} less max"))
            act.activation(S, S, ACT.Exp).then_inc(*stage.scalar(f"{name} exp"))

        def softmax_tail_vector(dve, stage, name, S, small, count=None):
            dve.wait_ge(*after(f"{name} exp"))
            if count is not None:
                dve.tensor_tensor(S, S, over(count, 4), ALU.mult).then_inc(*stage.vector())
                dve.wait_ge(*stage.vector.so_far())
            dve.tensor_reduce(small.rearrange("p u b -> p (u b)"), blocks(S), AX.X, ALU.add).then_inc(*stage.vector())
            dve.wait_ge(*stage.vector.so_far())
            dve.tensor_tensor(small[:, :, 1], small[:, :, 1], small[:, :, 2], ALU.add).then_inc(*stage.vector())
            dve.wait_ge(*stage.vector.so_far())
            dve.tensor_copy(small[:, :, 2], small[:, :, 1]).then_inc(*stage.vector())
            dve.wait_ge(*stage.vector.so_far())
            dve.reciprocal(small, small).then_inc(*stage.vector())
            dve.wait_ge(*stage.vector.so_far())

        def scores_tensor(pe, stage, label, q, k):
            b = open_bank(pe, label)
            pe.matmul(b[:, 0:P], q[:, 0:P], k[:, 0:P], start=True, stop=True)
            pe.matmul(b[:, P:UNIT], q[:, P:SEQ], k, start=True, stop=True).then_inc(*stage.tensor(label))

        def turn_unit_tensor(pe, stage, label, s):
            b = open_bank(pe, label)
            for j in range(3):
                ins = pe.transpose(b[:, j * P:(j + 1) * P], s[:, j * P:(j + 1) * P], ident)
            ins.then_inc(*stage.tensor(label))

        def unit_blocks(s, t):
            return [s[:, 0:P]] if t == 0 else [s[:, P:2 * P], s[:, 2 * P:UNIT]]

        with arena() as take:
            a_tok = take("a_tok", [P, TT, ATT_K * COLS])
            a_T = take("a_T", [P, 16, SEQ])
            a_S = take("a_S", [P, 12, UNIT])
            a_rope = take("a_rope", [P, 4 * 8 * 64])
            a_max = take("a_max", [P, 12, 3])
            a_sum = take("a_sum", [P, 12, 3])
            a_lam = take("a_lam", [P, 2, 64])
            a_small = take("a_small", [P, 32])
        A_KINDS = "k" * ATT_K
        CV, DV = 1024, 2560
        GROUPS = {0: 0, 1: 512, 2: 1536, 3: 2048}
        A_GROUPS = [[f"attn s {u}" for u in range(4 * i, 4 * i + 4)] for i in range(3)]

        def a_place(s, j, b):
            return [(a_tok[:, j, s * COLS:(s + 1) * COLS], b[:, 0:COLS])]

        def attention_tensor(pe, at):
            g0 = first_step[at]
            proj_tensor(pe, "attn", g0, A_KINDS)
            for t in range(TT):
                for i, c0 in GROUPS.items():
                    pe.wait_ge(*after(f"attn rope {t} {i // 2}"))
                    b = open_bank(pe, f"attn turned {t} {i}")
                    for h in range(4):
                        ins = pe.transpose(b[:, h * P:(h + 1) * P], a_tok[:, t, c0 + h * P:c0 + (h + 1) * P], ident)
                    ins.then_inc(*attn.tensor(f"attn turned {t} {i}"))
            pe.wait_ge(*after(f"used attn turned {TT - 1} 3"))
            for h in range(HEADS):
                scores_tensor(pe, attn, f"attn s {h}", a_T[:, h, :], a_T[:, 4 + h, :])
            for h in range(HEADS):
                for half in range(2):
                    rows_ = slice(64 * half, 64 * half + 64)
                    scores_tensor(pe, attn, f"attn s {4 + 2 * h + half}", a_T[rows_, 8 + h, :], a_T[rows_, 12 + h, :])
            for i, u in enumerate([0, 1, 2, 3, 4, 6, 8, 10]):
                pe.wait_ge(*after("attn p dil" if u < 4 else f"attn p diff {(u - 4) // 4}"))
                turn_unit_tensor(pe, attn, f"attn pt {u}", a_S[:, u, :])
            for side, (units, v0) in enumerate((([0, 1, 2, 3], CV), ([4, 6, 8, 10], DV))):
                pe.wait_ge(*after(f"used attn pt {units[-1]}"))
                for t in range(TT):
                    b = open_bank(pe, f"attn o {side} {t}")
                    for h, u in enumerate(units):
                        for j, s in enumerate(unit_blocks(a_S[:, u, :], t)):
                            ins = pe.matmul(b[:, h * P:(h + 1) * P], s, a_tok[:, j, v0 + h * P:v0 + (h + 1) * P],
                                            start=j == 0, stop=j == t)
                    ins.then_inc(*attn.tensor(f"attn o {side} {t}"))
            turn_tensor(pe, "attn", attn, KT, ["attn normed"] * TT)
            out_tensor(pe, "attn", g0 + ATT_K)

        def attention_scalar(act, at):
            def does(label, *args, **kw):
                act.activation(*args, **kw).then_inc(*attn.scalar(label))

            proj_copies(act, "attn", A_KINDS, 0, a_place)
            act.wait_ge(*after("attn lam sums"))
            does("attn lam exp", a_small[:, 2:4], a_small[:, 0:2], ACT.Exp)
            for t in range(TT):
                for i in GROUPS:
                    act.wait_ge(*after(f"attn turned {t} {i}"))
                    does(f"used attn turned {t} {i}", a_T[:, 4 * i:4 * i + 4, t * P:(t + 1) * P], four(bank(f"attn turned {t} {i}")), ACT.Copy)
            for i in range(3):
                softmax_scalar(act, attn, f"attn {i}", a_S[:, 4 * i:4 * i + 4, :])
            for u in (0, 1, 2, 3, 4, 6, 8, 10):
                act.wait_ge(*after(f"attn pt {u}"))
                does(f"used attn pt {u}", a_S[:, u, :], bank(f"attn pt {u}")[:, 0:UNIT], ACT.Copy)
            for side in range(2):
                for t in range(TT):
                    act.wait_ge(*after(f"attn o {side} {t}"))
                    does(f"used attn o {side} {t}", O[:, t, 512 * side:512 * side + 512], bank(f"attn o {side} {t}"), ACT.Copy)
            act.wait_ge(*after("used attn o 1 1"))
            does("attn square", a_T[:, 0:4, :].rearrange("p h t -> p (h t)").rearrange("p (t d) -> p t d", t=TT), O[:, :, 512:1024], ACT.Square)
            act.wait_ge(*after("attn square sum"))
            does("attn root", a_small[:, 16:24], a_small[:, 8:16], ACT.Sqrt, scale=1.0 / P, bias=eps)

        def attention_pool(pool, at):
            pass

        def attention_vector(dve, at):
            def does(label, op, *args):
                op(*args).then_inc(*attn.vector(label))

            def settle():
                dve.wait_ge(*attn.vector.so_far())

            for i in range(2):
                does(None, dve.tensor_tensor, a_lam[:, i, :], row(f"lq{i + 1}"), row(f"lk{i + 1}"), ALU.mult)
            settle()
            does("attn lam sums", dve.tensor_reduce, a_small[:, 0:2], a_lam[:, :, :], AX.X, ALU.add)
            proj_copies(dve, "attn", A_KINDS, 1, a_place)
            wait_proj(dve, "attn", A_KINDS)
            for t in range(TT):
                for i, (c0, dim) in enumerate(((0, 128), (1536, 64))):
                    half = dim // 2
                    rope_vector(dve, attn, a_tok[:, t, c0:c0 + 1024].rearrange("p (h d) -> p h d", d=dim), half,
                                table(f"cos{half}")[:, half * t:half * t + half], table(f"sin{half}")[:, half * t:half * t + half],
                                a_rope.rearrange("p (i h c) -> p i h c", i=4, c=half))
                    marks[f"attn rope {t} {i}"] = (attn.vector.name, attn.vector.n)
            dve.wait_ge(*after("attn lam exp"))
            does(None, dve.tensor_tensor, a_small[:, 4:5], a_small[:, 3:4], a_small[:, 2:3], ALU.subtract)
            settle()
            does(None, dve.tensor_scalar, a_small[:, 5:6], a_small[:, 4:5], -LAMBDA_INIT, None, ALU.add)
            for i, units in enumerate(A_GROUPS):
                softmax_head_vector(dve, attn, f"attn {i}", a_S[:, 4 * i:4 * i + 4, :], units, (128 if i == 0 else 64) ** -0.5,
                                    table("bias_dil" if i == 0 else "bias"), a_max[:, 4 * i:4 * i + 4, :])
            for i in range(3):
                S, r = a_S[:, 4 * i:4 * i + 4, :], a_sum[:, 4 * i:4 * i + 4, :]
                softmax_tail_vector(dve, attn, f"attn {i}", S, r, table("count") if i == 0 else None)
                if i > 0:
                    pair = r.rearrange("p (h two) b -> p h two b", two=2)[:, :, 1, :]
                    does(None, dve.tensor_scalar, pair, pair, a_small[:, 5:6], None, ALU.mult)
                    settle()
                does("attn p dil" if i == 0 else None, dve.tensor_tensor, blocks(S), blocks(S), wide(r.rearrange("p u b -> p (u b)"), P), ALU.mult)
                if i > 0:
                    settle()
                    halves = S.rearrange("p (h two) c -> p h two c", two=2)
                    does(f"attn p diff {i - 1}", dve.tensor_tensor, halves[:, :, 0, :], halves[:, :, 0, :], halves[:, :, 1, :], ALU.add)
            dve.wait_ge(*after("attn square"))
            does("attn square sum", dve.tensor_reduce, a_small[:, 8:16], a_T[:, 0:4, :].rearrange("p h t -> p (h t)").rearrange("p (h d) -> p h d", d=P),
                 AX.X, ALU.add)
            dve.wait_ge(*after("attn root"))
            does(None, dve.reciprocal, a_small[:, 24:32], a_small[:, 16:24])
            settle()
            for t in range(TT):
                heads = four(O[:, t, 512:1024])
                does(None, dve.tensor_tensor, heads, heads, wide(a_small[:, 24 + 4 * t:28 + 4 * t], P), ALU.mult)
                settle()
                does("attn normed", dve.scalar_tensor_tensor, heads, heads, 1.0 - LAMBDA_INIT, over(row("diff_norm"), 4), ALU.mult, ALU.mult)
            turn_vector(dve, "attn", attn, KT)
            out_vector(dve, "attn", at)

        SLOTS8 = 8
        with arena() as take:
            n_tok = take("n_tok", [P, TT, SPARSE_K * COLS])
            n_z = [take(f"n_z{i}", [P, 2, SEQ]) for i in range(2)]
            n_bg, n_cg, n_hd = (take(f"n_{i}", [P, 4, SEQ]) for i in ("bg", "cg", "hd"))
            n_pad = take("n_pad", [P, 4, SEQ + 2])
            n_zb = [take(f"n_zb{i}", [P, 16, 2, CMP_PAD]) for i in range(2)]
            n_hid = [take(f"n_hid{i}", [P, 2, 2 * CMP_PAD]) for i in range(2)]
            n_hv = take("n_hv", [P, 2, 4, 2 * CMP_PAD])
            n_kcmp = take("n_kcmp", [P, CMP_PAD])
            n_vcmp = take("n_vcmp", [P, SLOTS8, 64])
            n_qn, n_qr = (take(f"n_{i}", [P, 4, SEQ]) for i in ("qn", "qr"))
            n_kt = take("n_kt", [P, 2, SEQ])
            n_S = take("n_S", [P, 16, UNIT])
            n_sc = take("n_sc", [P, TT, SLOTS8, CMP_PAD])
            n_pct = take("n_pct", [P, TT, P])
            n_gate = take("n_gate", [P, TT, 3, SLOTS8])
            n_max, n_sum = (take(f"n_{i}", [P, 16, 3]) for i in ("max", "sum"))
            n_cs = take("n_cs", [P, 2, 16])
            n_rope = take("n_rope", [P, 4, 8, 8])
        N_KINDS = "k" * SPARSE_K + "t" * (SPARSE_T - 1) + "u"
        KS, VS, KW, VW, GL = 512, 640, 768, 896, 1024
        N_GROUPS = [[f"sparse s {u}" for u in range(4 * i, 4 * i + 4)] for i in range(4)]

        def n_place(s, j, b):
            if s < SPARSE_K:
                return [(n_tok[:, j, s * COLS:(s + 1) * COLS], b[:, 0:COLS])]
            c = 3 * (s - SPARSE_K) + j
            if c < 4:
                z = n_z[c // 2]
                return [(z[0:64, c % 2, :], b[0:64, 0:SEQ]), (z[64:P, c % 2, 0:SEQ - 1], b[64:P, 1:SEQ])]
            return [((n_bg, n_cg, n_hd)[c // 4 - 1][:, c % 4, :], b[:, 0:SEQ])]

        def slot_rows(s):
            return slice(64 * (s % 2), 64 * (s % 2) + 64)

        def sparse_tensor(pe, at):
            g0 = first_step[at]
            proj_tensor(pe, "sparse", g0, N_KINDS)
            for t in range(TT):
                if t == 0:
                    for j in (0, 1):
                        pe.wait_ge(*after(f"used sparse 0 {j}"))
                        pe.wait_ge(*after(f"used sparse 1 {j}"))
                b = open_bank(pe, f"sparse qn {t}")
                for i in range(4):
                    ins = pe.transpose(b[:, i * P:(i + 1) * P], n_tok[:, t, i * P:(i + 1) * P], ident)
                ins.then_inc(*sparse.tensor(f"sparse qn {t}"))
            for t in range(TT):
                pe.wait_ge(*after(f"sparse rope {t}"))
                b = open_bank(pe, f"sparse qr {t}")
                for i in range(4):
                    ins = pe.transpose(b[:, i * P:(i + 1) * P], n_tok[:, t, i * P:(i + 1) * P], ident)
                ins.then_inc(*sparse.tensor(f"sparse qr {t}"))
                b = open_bank(pe, f"sparse kt {t}")
                for i, c0 in enumerate((KS, KW)):
                    ins = pe.transpose(b[:, i * P:(i + 1) * P], n_tok[:, t, c0:c0 + P], ident)
                ins.then_inc(*sparse.tensor(f"sparse kt {t}"))
            for s in range(SPARSE_C):
                g = g0 + SPARSE_K + SPARSE_T + s
                wait_step(pe, g)
                w = slot(g).rearrange("p (q c) -> p q c", q=12)
                for block_ in range(12 * s, min(12 * s + 12, 32)):
                    which, l = divmod(block_, 16)
                    if l == 0:
                        pe.wait_ge(*after(f"sparse zb {which}"))
                        hidden = [open_bank(pe, f"sparse hid {which} {i}") for i in range(2)]
                    for i in range(2):
                        ins = pe.matmul(hidden[i][:, 0:2 * CMP_PAD], w[:, block_ % 12, i * P:(i + 1) * P],
                                        n_zb[which][:, l, :, :], start=l == 0, stop=l == 15)
                        if l == 15 or (block_ % 12 == 11 and i == 1):
                            ins.then_inc(*sparse.tensor(f"sparse hid {which} {i}" if l == 15 else f"sparse c {s} last"))
                if s == SPARSE_C - 1:
                    marks[f"sparse c {s} last"] = marks["sparse hid 1 1"]
                release(pe, "sparse c", s)
            pe.wait_ge(*after("used sparse kt 1"))
            for br in range(2):
                for s in range(SLOTS8):
                    scores_tensor(pe, sparse, f"sparse s {8 * br + s}", n_qr[slot_rows(s), s // 2, :], n_kt[slot_rows(s), br, :])
            pe.wait_ge(*after("used sparse hid 0 1"))
            b = open_bank(pe, "sparse kcmp")
            for kv in range(2):
                for i in range(2):
                    ins = pe.matmul(b[64 * kv:64 * kv + 64, 0:CMP_PAD], col("cmp_k2")[:, 64 * i:64 * i + 64],
                                    n_hid[0][:, i, kv * CMP_PAD:(kv + 1) * CMP_PAD], start=i == 0, stop=i == 1)
            ins.then_inc(*sparse.tensor("sparse kcmp"))
            pe.wait_ge(*after("sparse hv"))
            b = open_bank(pe, "sparse vcmp")
            for i in range(2):
                ins = pe.matmul(b[:, 0:64], n_hv[:, i, :, :].rearrange("p j n -> p (j n)"), col("cmp_v2")[:, 64 * i:64 * i + 64],
                                start=i == 0, stop=i == 1)
            ins.then_inc(*sparse.tensor("sparse vcmp"))
            pe.wait_ge(*after("used sparse kcmp"))
            for par in range(2):
                b = open_bank(pe, f"sparse cs {par}")
                for t in range(TT):
                    for j in range(4):
                        c0 = (4 * t + j) * CMP_PAD
                        ins = pe.matmul(b[:, c0:c0 + CMP_PAD], n_qn[slot_rows(par), j, t * P:(t + 1) * P], n_kcmp[slot_rows(par), :],
                                        start=True, stop=True)
                ins.then_inc(*sparse.tensor(f"sparse cs {par}"))
            for i in range(4):
                pe.wait_ge(*after(f"sparse p {i}"))
                for u in range(4 * i, 4 * i + 4):
                    turn_unit_tensor(pe, sparse, f"sparse pt {u}", n_S[:, u, :])
            pe.wait_ge(*after("sparse pc"))
            for t in range(TT):
                b = open_bank(pe, f"sparse pct {t}")
                pe.transpose(b[:, 0:P], n_sc[:, t, :, :].rearrange("p s n -> p (s n)"), ident).then_inc(*sparse.tensor(f"sparse pct {t}"))
            pe.wait_ge(*after("used sparse vcmp"))
            pe.wait_ge(*after("used sparse pct 1"))
            for t in range(TT):
                b = open_bank(pe, f"sparse o {t}")
                pe.matmul(b, n_pct[:, t, :], n_vcmp.rearrange("p s d -> p (s d)"), start=True, stop=False)
                for br, v0 in enumerate((VS, VW)):
                    for s in range(SLOTS8):
                        for j, pt in enumerate(unit_blocks(n_S[:, 8 * br + s, :], t)):
                            v = n_tok[:, j, v0 + 64 * (s % 2):v0 + 64 * (s % 2) + 64]
                            ins = pe.matmul(b[:, 64 * s:64 * s + 64], pt, v, start=False,
                                            stop=br == 1 and s == SLOTS8 - 1 and j == t)
                ins.then_inc(*sparse.tensor(f"sparse o {t}"))
            turn_tensor(pe, "sparse", sparse, 4, [f"used sparse o {t}" for t in range(TT)])
            pe.wait_ge(*after("sparse conv"))
            out_tensor(pe, "sparse", g0 + SPARSE_K + SPARSE_T + SPARSE_C, 4)

        def sparse_scalar(act, at):
            def does(label, *args, **kw):
                act.activation(*args, **kw).then_inc(*sparse.scalar(label))

            proj_copies(act, "sparse", N_KINDS, 0, n_place)
            wait_proj(act, "sparse", N_KINDS, range(SPARSE_K))
            gl = n_tok[:, :, GL:GL + 24]
            does("sparse gate", n_gate.rearrange("p t b s -> p t (b s)"), gl, ACT.Sigmoid)
            for t in range(TT):
                act.wait_ge(*after(f"sparse qn {t}"))
                does(f"used sparse qn {t}", n_qn[:, :, t * P:(t + 1) * P], four(bank(f"sparse qn {t}")), ACT.Copy)
            for t in range(TT):
                act.wait_ge(*after(f"sparse qr {t}"))
                does(f"used sparse qr {t}", n_qr[:, :, t * P:(t + 1) * P], four(bank(f"sparse qr {t}")), ACT.Copy)
                act.wait_ge(*after(f"sparse kt {t}"))
                does(f"used sparse kt {t}", n_kt[:, :, t * P:(t + 1) * P],
                     bank(f"sparse kt {t}")[:, 0:2 * P].rearrange("p (i c) -> p i c", i=2), ACT.Copy)
            for which in range(2):
                for i in range(2):
                    act.wait_ge(*after(f"sparse hid {which} {i}"))
                    does(f"used sparse hid {which} {i}", n_hid[which][:, i, :], bank(f"sparse hid {which} {i}")[:, 0:2 * CMP_PAD],
                         ACT.Gelu_apprx_tanh)
            act.wait_ge(*after("sparse kcmp"))
            does("used sparse kcmp", n_kcmp[:, :], bank("sparse kcmp")[:, 0:CMP_PAD], ACT.Copy)
            for i in range(4):
                softmax_scalar(act, sparse, f"sparse {i}", n_S[:, 4 * i:4 * i + 4, :])
            act.wait_ge(*after("sparse c less max"))
            does("sparse c exp", n_sc[:, :, :, :], n_sc[:, :, :, :], ACT.Exp)
            for u in range(16):
                act.wait_ge(*after(f"sparse pt {u}"))
                does(f"used sparse pt {u}", n_S[:, u, :], bank(f"sparse pt {u}")[:, 0:UNIT], ACT.Copy)
            for t in range(TT):
                act.wait_ge(*after(f"sparse pct {t}"))
                does(f"used sparse pct {t}", n_pct[:, t, :], bank(f"sparse pct {t}")[:, 0:P], ACT.Copy)
            for t in range(TT):
                act.wait_ge(*after(f"sparse o {t}"))
                does(f"used sparse o {t}", O[:, t, 0:512], bank(f"sparse o {t}"), ACT.Copy)

        def sparse_pool(pool, at):
            pass

        def sparse_vector(dve, at):
            def does(label, op, *args):
                op(*args).then_inc(*sparse.vector(label))

            def settle():
                dve.wait_ge(*sparse.vector.so_far())

            does(None, dve.memset, n_pad[:, :, 0:2], 0.0)
            for which in range(2):
                does(None, dve.memset, n_zb[which][:, :, :, :], 0.0)
            proj_copies(dve, "sparse", N_KINDS, 1, n_place)
            wait_proj(dve, "sparse", N_KINDS)
            settle()
            for which, pos in enumerate(("pos_k", "pos_v")):
                for kv in range(2):
                    z = n_z[which][:, kv, :].rearrange("p (n b two) -> p b n two", b=8, two=2)
                    for a in range(2):
                        does(f"sparse zb {which}", dve.tensor_tensor, n_zb[which][:, 8 * a:8 * a + 8, kv, 0:CMP_N],
                             z[:, :, a:a + CMP_N, 0], wide(col(pos)[:, 8 * a:8 * a + 8], CMP_N), ALU.add)
            for t in range(TT):
                dve.wait_ge(*after(f"sparse qn {t}"))
                for c0, heads in ((0, 8), (KS, 2), (KW, 2)):
                    rope_vector(dve, sparse, n_tok[:, t, c0:c0 + 64 * heads].rearrange("p (h d) -> p h d", d=64), 8,
                                table("cos8")[:, 8 * t:8 * t + 8], table("sin8")[:, 8 * t:8 * t + 8], n_rope[:, :, 0:heads, :])
                marks[f"sparse rope {t}"] = (sparse.vector.name, sparse.vector.n)
            does(None, dve.tensor_tensor, n_pad[:, :, 2:2 + SEQ], n_cg[:, :, :], n_hd[:, :, :], ALU.mult)
            settle()
            for j in range(3):
                for c in range(4):
                    w, x = col("conv3")[:, 4 * j + c:4 * j + c + 1], n_pad[:, c, j:j + SEQ]
                    if j == 0:
                        does(None, dve.tensor_scalar, n_cg[:, c, :], x, w, None, ALU.mult)
                    else:
                        does(None, dve.scalar_tensor_tensor, n_cg[:, c, :], x, w, n_cg[:, c, :], ALU.mult, ALU.add)
                settle()
            does("sparse conv", dve.tensor_tensor, hT[:, 4:8, :], n_cg[:, :, :], n_bg[:, :, :], ALU.mult)
            for i, units in enumerate(N_GROUPS):
                softmax_head_vector(dve, sparse, f"sparse {i}", n_S[:, 4 * i:4 * i + 4, :], units, 64 ** -0.5, table("bias"),
                                    n_max[:, 4 * i:4 * i + 4, :])
            for i in range(2):
                dve.wait_ge(*after(f"used sparse hid 1 {i}"))
                does("sparse hv", dve.tensor_copy, n_hv[:, i, :, :], over(n_hid[1][:, i, :], 4))
            dve.wait_ge(*after("sparse vcmp"))
            does("used sparse vcmp", dve.tensor_tensor, n_vcmp[:, :, :], over(bank("sparse vcmp")[:, 0:64], 8), wide(table("cmp_block"), 64), ALU.mult)
            by_parity = n_sc.rearrange("p t (j two) n -> p t j two n", two=2)
            for par in range(2):
                dve.wait_ge(*after(f"sparse cs {par}"))
                for t in range(TT):
                    src = bank(f"sparse cs {par}")[:, 64 * t:64 * t + 64].rearrange("p (j n) -> p j n", j=4)
                    does(f"used sparse cs {par}", dve.scalar_tensor_tensor, by_parity[:, t, :, par, :], src, 64 ** -0.5,
                         over(table("cmp_bias")[:, CMP_PAD * t:CMP_PAD * (t + 1)], 4), ALU.mult, ALU.add)
            settle()
            sc = n_sc.rearrange("p t s n -> p (t s) n")
            does(None, dve.tensor_reduce, n_cs[:, 0, :], sc, AX.X, ALU.max)
            settle()
            does("sparse c less max", dve.tensor_tensor, sc, sc, wide(n_cs[:, 0, :], CMP_PAD), ALU.subtract)
            for i in range(4):
                S, r = n_S[:, 4 * i:4 * i + 4, :], n_sum[:, 4 * i:4 * i + 4, :]
                softmax_tail_vector(dve, sparse, f"sparse {i}", S, r)
                for b in range(3):
                    gate = n_gate[:, 0 if b == 0 else 1, 1 + i // 2, 4 * (i % 2):4 * (i % 2) + 4]
                    does(None, dve.tensor_tensor, r[:, :, b], r[:, :, b], gate, ALU.mult)
                settle()
                does(f"sparse p {i}", dve.tensor_tensor, blocks(S), blocks(S), wide(r.rearrange("p u b -> p (u b)"), P), ALU.mult)
            dve.wait_ge(*after("sparse c exp"))
            for t in range(TT):
                does(None, dve.tensor_tensor, n_sc[:, t, :, :], n_sc[:, t, :, :], over(table("cmp_mask")[:, CMP_PAD * t:CMP_PAD * (t + 1)], 8), ALU.mult)
            settle()
            does(None, dve.tensor_reduce, n_cs[:, 1, :], sc, AX.X, ALU.add)
            settle()
            does(None, dve.tensor_scalar, n_cs[:, 1, :], n_cs[:, 1, :], 1e-30, None, ALU.max)
            settle()
            does(None, dve.reciprocal, n_cs[:, 1, :], n_cs[:, 1, :])
            settle()
            by_token = n_cs[:, 1, :].rearrange("p (t s) -> p t s", t=TT)
            does(None, dve.tensor_tensor, by_token, by_token, n_gate[:, :, 0, :], ALU.mult)
            settle()
            does("sparse pc", dve.tensor_tensor, sc, sc, wide(n_cs[:, 1, :], CMP_PAD), ALU.mult)
            turn_vector(dve, "sparse", sparse, 4)
            out_vector(dve, "sparse", at)

        with arena() as take:
            r_tok = take("r_tok", [P, TT, RWKV_K * COLS])
            r_pb = take("r_pb", [P, 14, SEQ + 1])
            r_pm = take("r_pm", [P, 14, SEQ])
            r_a, r_kk = take("r_a", [P, 4, SEQ]), take("r_kk", [P, 4, SEQ])
            r_ld, r_c, r_e1, r_e1p, r_e2 = (take(f"r_{i}", [P, 4, SEQ]) for i in ("ld", "c", "e1", "e1p", "e2"))
            r_kt, r_bt = take("r_kt", [P, 512]), take("r_bt", [P, 512])
            r_rhs, r_sa = take("r_rhs", [P, 4, 64]), take("r_sa", [P, 4, 64])
            r_s1 = take("r_s1", [P, 2, P])
            r_mid = take("r_mid", [P, 4, 2])
            r_f = take("r_f", [P, 4])
            r_bonus = take("r_bonus", [P, TT, 8])
            r_stat = take("r_stat", [P, 6, 16])

        def matrices(ap, first=0):
            return ap[:, first:first + 8 * P].rearrange("p (m c) -> p m c", m=8)

        flat_pb, flat_tok = r_pb.rearrange("p c t -> p (c t)"), r_tok.rearrange("p t c -> p (t c)")
        r_A, r_T, r_L, r_R, r_B = (matrices(x.rearrange("p c t -> p (c t)")) for x in (r_ld, r_c, r_e1, r_e1p, r_e2))
        r_U, r_Y, r_AM = matrices(flat_pb), matrices(flat_tok), matrices(flat_tok, 8 * P)
        r_g, r_v = (flat_pb[:, c0:c0 + 2 * 512].rearrange("p (t c) -> p t c", t=2) for c0 in (1024, 2048))
        r_scratch = r_kk.rearrange("p c t -> p (c t)").rearrange("p (t c) -> p t c", t=TT)
        R_KINDS = "k" * RWKV_K + "t" * (RWKV_T - 1) + "v"
        NEG_ROOT_E = -math.exp(-0.5)
        R_MATRICES = ("A", "L", "R", "B")

        def r_place(s, j, b):
            if s < RWKV_K:
                return [(r_tok[:, j, s * COLS:(s + 1) * COLS], b[:, 0:COLS])]
            return [(r_pb[:, 3 * (s - RWKV_K) + j, 1:1 + SEQ], b[:, 0:SEQ])]

        def chunk_of(x, i, c, parity):
            return x[64 * parity:64 * parity + 64, i, c * P:(c + 1) * P]

        def rwkv_tensor(pe, at):
            g0 = first_step[at]
            proj_tensor(pe, "rwkv", g0, R_KINDS)
            lora = col("lora")
            for name, rows_, label in (("w", slice(0, 64), "rwkv tanh"), ("a", slice(64, P), "rwkv mixed")):
                pe.wait_ge(*after(label))
                for i in range(2):
                    b = open_bank(pe, f"rwkv {name} {i}")
                    for j in range(2):
                        c = 2 * i + j
                        ins = pe.matmul(b[:, j * SEQ:(j + 1) * SEQ], lora[rows_, c * P:(c + 1) * P], r_pm[rows_, 12, :], start=True, stop=True)
                    ins.then_inc(*rwkv.tensor(f"rwkv {name} {i}"))
            pe.wait_ge(*after("rwkv gate"))
            for t in range(TT):
                b = open_bank(pe, f"rwkv g {t}")
                pe.matmul(b, r_pm[:, 13, t * P:(t + 1) * P], col("g2"), start=True, stop=True).then_inc(*rwkv.tensor(f"rwkv g {t}"))
            pe.wait_ge(*after("rwkv sgu normed"))
            for t in range(TT):
                b = open_bank(pe, f"rwkv sgu {t}")
                for g in range(4):
                    ins = pe.matmul(b[:, g * P:(g + 1) * P], col("sgu_w")[:, g * P:(g + 1) * P], r_tok[:, t, 512 + g * P:512 + (g + 1) * P],
                                    start=True, stop=True)
                ins.then_inc(*rwkv.tensor(f"rwkv sgu {t}"))
            pe.wait_ge(*after("rwkv kk square"))
            for i in range(2):
                b = open_bank(pe, f"rwkv kn {i}")
                pe.matmul(b, table("pair_ones"), r_e2[:, 2 * i:2 * i + 2, :], start=True, stop=True).then_inc(*rwkv.tensor(f"rwkv kn {i}"))
            pe.wait_ge(*after("rwkv rk"))
            b = open_bank(pe, "rwkv bonus")
            for t in range(TT):
                for c in range(4):
                    ins = pe.matmul(b[:, 8 * t + 2 * c:8 * t + 2 * c + 2], r_e1[:, c, t * P:(t + 1) * P], table("pair_sel"), start=True, stop=True)
            ins.then_inc(*rwkv.tensor("rwkv bonus"))
            for t in range(TT):
                b = open_bank(pe, f"rwkv v {t}")
                for c in range(4):
                    ins = pe.transpose(b[:, c * P:(c + 1) * P], r_pm[:, 8 + c, t * P:(t + 1) * P], ident)
                ins.then_inc(*rwkv.tensor(f"rwkv v {t}"))
            pe.wait_ge(*after("rwkv decayed"))
            for name, x, c0 in (("kt", r_pm, 4), ("bt", r_a, 0)):
                b = open_bank(pe, f"rwkv {name}")
                for c in range(4):
                    ins = pe.transpose(b[:, c * P:(c + 1) * P], x[:, c0 + c, 0:P], ident)
                ins.then_inc(*rwkv.tensor(f"rwkv {name}"))
            for half in range(2):
                i0 = 2 * half
                operands = {"A": ((r_kk, 0), (r_a, 0)), "L": ((r_pm, 4), (r_kk, 0)), "R": ((r_pm, 4), (r_pm, 0)), "B": ((r_a, 0), (r_pm, 0))}
                for name in R_MATRICES:
                    (x, x0), (y, y0) = operands[name]
                    for par in range(2):
                        b = open_bank(pe, f"rwkv {name} {half} {par}")
                        for ti in range(2):
                            for c in range(2):
                                m = 2 * ti + c
                                ins = pe.matmul(b[:, m * P:(m + 1) * P], chunk_of(x, x0 + i0 + ti, c, par), chunk_of(y, y0 + i0 + ti, c, par),
                                                start=True, stop=True)
                        ins.then_inc(*rwkv.tensor(f"rwkv {name} {half} {par}"))
                inverse_tensor(pe, f"rwkv{half}", r_T, r_U, r_Y, r_AM)
                for par in range(2):
                    pe.wait_ge(*after(f"rwkv{half} U {LEVELS - 1} {par}"))
                pe.wait_ge(*after(f"rwkv masked {half}"))
                pe.wait_ge(*after("used rwkv bt"))
                for c in range(2):
                    tag = f"{half} {c}"
                    heads = [(ti, par, 2 * ti + par, 4 * par + 2 * ti + c, r_v[:, c, (i0 + ti) * P + 64 * par:(i0 + ti) * P + 64 * par + 64])
                             for ti in range(2) for par in range(2)]
                    if c == 1:
                        pe.wait_ge(*after(f"rwkv s1 {half} 1"))

                    def from_state(b, ti, x, x0):
                        if c == 1:
                            pe.matmul(b[:, ti * P:(ti + 1) * P], x[:, x0 + i0 + ti, P:SEQ], r_s1[:, ti, :], start=True, stop=False)

                    b = open_bank(pe, f"rwkv rhs {tag}")
                    for ti, par, hh, m, v in heads:
                        if par == 0:
                            from_state(b, ti, r_kk, 0)
                        ins = pe.matmul(b[:, hh * 64:hh * 64 + 64], r_L[:, m, :], v, start=c == 0, stop=c == 0 or par == 1)
                    ins.then_inc(*rwkv.tensor(f"rwkv rhs {tag}"))
                    pe.wait_ge(*after(f"used rwkv rhs {tag}"))
                    b = open_bank(pe, f"rwkv sa {tag}")
                    for ti, par, hh, m, v in heads:
                        ins = pe.matmul(b[:, hh * 64:hh * 64 + 64], r_U[:, m, :], r_rhs[:, hh, :], start=True, stop=True)
                    ins.then_inc(*rwkv.tensor(f"rwkv sa {tag}"))
                    pe.wait_ge(*after(f"used rwkv sa {tag}"))
                    b = open_bank(pe, f"rwkv y {tag}")
                    for ti in range(2):
                        from_state(b, ti, r_pm, 0)
                        for _, par, hh, m, v in heads[2 * ti:2 * ti + 2]:
                            pe.matmul(b[:, hh * 64:hh * 64 + 64], r_R[:, m, :], v, start=c == 0, stop=False)
                            ins = pe.matmul(b[:, hh * 64:hh * 64 + 64], r_B[:, m, :], r_sa[:, hh, :], start=False, stop=c == 0 or par == 1)
                    ins.then_inc(*rwkv.tensor(f"rwkv y {tag}"))
                    if c == 0:
                        b = open_bank(pe, f"rwkv ds {half}")
                        for ti in range(2):
                            tile = slice((i0 + ti) * P, (i0 + ti + 1) * P)
                            pe.matmul(b[:, ti * P:(ti + 1) * P], r_kt[:, tile], r_v[:, 0, tile], start=True, stop=False)
                            ins = pe.matmul(b[:, ti * P:(ti + 1) * P], r_bt[:, tile], r_sa[:, 2 * ti:2 * ti + 2, :], start=False, stop=True)
                        ins.then_inc(*rwkv.tensor(f"rwkv ds {half}"))
            turn_tensor(pe, "rwkv", rwkv, KT, ["rwkv gated"] * TT)
            out_tensor(pe, "rwkv", g0 + RWKV_K + RWKV_T)

        def rwkv_scalar(act, at):
            def does(label, *args, **kw):
                act.activation(*args, **kw).then_inc(*rwkv.scalar(label))

            proj_copies(act, "rwkv", R_KINDS, 0, r_place)
            wait_proj(act, "rwkv", R_KINDS, range(RWKV_K))
            does("rwkv gelu", r_tok[:, :, 0:1024], r_tok[:, :, 0:1024], ACT.Gelu_apprx_tanh)
            act.wait_ge(*after("rwkv mixed"))
            does("rwkv tanh", r_pm[0:64, 12, :], r_pm[0:64, 12, :], ACT.Tanh)
            does("rwkv gate", r_pm[:, 13, :], r_pm[:, 13, :], ACT.Sigmoid)
            for name, dst, bias in (("w", r_ld, "w0"), ("a", r_a, "a0")):
                for i in range(2):
                    act.wait_ge(*after(f"rwkv {name} {i}"))
                    for j in range(2):
                        c = 2 * i + j
                        does(f"used rwkv {name} {i}", dst[:, c, :], bank(f"rwkv {name} {i}")[:, j * SEQ:(j + 1) * SEQ], ACT.Sigmoid,
                             bias=col(bias)[:, c:c + 1])
            for t in range(TT):
                act.wait_ge(*after(f"rwkv g {t}"))
                does(f"used rwkv g {t}", r_g[:, t, :], bank(f"rwkv g {t}"), ACT.Copy)
            act.wait_ge(*after("rwkv kk"))
            does("rwkv kk square", r_e2[:, :, :], r_kk[:, :, :], ACT.Square)
            act.wait_ge(*after("rwkv sgu var"))
            does("rwkv sgu root", r_stat[:, 2, 0:8], r_stat[:, 1, 0:8], ACT.Sqrt, scale=1.0 / P, bias=ln_eps)
            act.wait_ge(*after("rwkv kk clipped"))
            does("rwkv kk root", r_e2[:, :, :], r_e2[:, :, :], ACT.Sqrt)
            for t in range(TT):
                act.wait_ge(*after(f"rwkv v {t}"))
                does(f"used rwkv v {t}", r_v[:, t, :], bank(f"rwkv v {t}"), ACT.Copy)
            act.wait_ge(*after("rwkv exponents"))
            act.wait_ge(*after("rwkv bonus"))
            act.wait_ge(*after("rwkv kk unit"))
            does(None, r_f[:, :], r_f[:, :], ACT.Exp)
            does(None, r_e1[:, :, :], r_c[:, :, :], ACT.Exp)
            does(None, r_e1p[:, :, :], r_e1p[:, :, :], ACT.Exp)
            does("rwkv exp", r_e2[:, :, :], r_c[:, :, :], ACT.Exp, scale=-1.0)
            for name, dst in (("kt", r_kt), ("bt", r_bt)):
                act.wait_ge(*after(f"rwkv {name}"))
                does(f"used rwkv {name}", dst[:, :], bank(f"rwkv {name}"), ACT.Copy)
            for half in range(2):
                inverse_scalar(act, f"rwkv{half}", r_U, r_Y)
                for c in range(2):
                    tag = f"{half} {c}"
                    act.wait_ge(*after(f"rwkv rhs {tag}"))
                    does(f"used rwkv rhs {tag}", r_rhs.rearrange("p h d -> p (h d)"), bank(f"rwkv rhs {tag}")[:, 0:SEQ], ACT.Copy)
                    act.wait_ge(*after(f"rwkv sa {tag}"))
                    does(f"used rwkv sa {tag}", r_sa.rearrange("p h d -> p (h d)"), bank(f"rwkv sa {tag}")[:, 0:SEQ], ACT.Copy, scale=-1.0)
            act.wait_ge(*after("rwkv centred"))
            does("rwkv y square", r_scratch[:, :, :], O[:, :, 512:1024], ACT.Square)
            act.wait_ge(*after("rwkv y var"))
            does("rwkv y root", r_stat[:, 4, :], r_stat[:, 3, :], ACT.Sqrt, scale=1.0 / 64, bias=gn_eps)

        def rwkv_pool(pool, at):
            for half in range(2):
                inverse_pool(pool, f"rwkv{half}", r_A, r_AM)

        def rwkv_vector(dve, at):
            def does(label, op, *args):
                op(*args).then_inc(*rwkv.vector(label))

            def settle():
                dve.wait_ge(*rwkv.vector.so_far())

            def groups(x, n):
                return x.rearrange("p (g c) -> p g c", c=n)

            def centre(x, stat, n, label):
                does(None, dve.tensor_reduce, stat, groups(x, n), AX.X, ALU.add)
                settle()
                does(None, dve.tensor_scalar, stat, stat, 1.0 / n, None, ALU.mult)
                settle()
                does(label, dve.tensor_tensor, groups(x, n), groups(x, n), wide(stat, n), ALU.subtract)

            does(None, dve.memset, r_pb[:, :, 0:1], 0.0)
            does(None, dve.tensor_tensor, col("sgu_w").rearrange("p (g c) -> p g c", g=4), col("sgu_w").rearrange("p (g c) -> p g c", g=4),
                 over(table("incl_t"), 4), ALU.mult)
            proj_copies(dve, "rwkv", R_KINDS, 1, r_place)
            wait_proj(dve, "rwkv", R_KINDS)
            settle()
            does(None, dve.tensor_tensor, r_pm[:, :, :], r_pb[:, :, 0:SEQ], r_pb[:, :, 1:1 + SEQ], ALU.subtract)
            settle()
            for c in [12, 13] + list(range(12)):
                does("rwkv mixed", dve.scalar_tensor_tensor, r_pm[:, c, :], r_pm[:, c, :], col("mu")[:, c:c + 1], r_pb[:, c, 1:1 + SEQ], ALU.mult, ALU.add)
            settle()
            for c in range(4):
                does("rwkv kk", dve.tensor_scalar, r_kk[:, c, :], r_pm[:, 4 + c, :], col("k_k")[:, c:c + 1], None, ALU.mult)
            dve.wait_ge(*after("rwkv gelu"))
            for t in range(TT):
                pv = r_tok[:, t, 512:1024]
                centre(pv, r_stat[:, 0, 4 * t:4 * t + 4], P, None)
                settle()
                does(None, dve.tensor_tensor, O[:, t, 512:1024], pv, pv, ALU.mult)
                settle()
                does("rwkv sgu var", dve.tensor_reduce, r_stat[:, 1, 4 * t:4 * t + 4], groups(O[:, t, 512:1024], P), AX.X, ALU.add)
            dve.wait_ge(*after("rwkv sgu root"))
            does(None, dve.reciprocal, r_stat[:, 2, 0:8], r_stat[:, 2, 0:8])
            settle()
            for t in range(TT):
                pv = r_tok[:, t, 512:1024]
                does(None, dve.tensor_tensor, groups(pv, P), groups(pv, P), wide(r_stat[:, 2, 4 * t:4 * t + 4], P), ALU.mult)
            settle()
            for t in range(TT):
                pv = r_tok[:, t, 512:1024]
                does(None, dve.tensor_tensor, pv, pv, row("ln_g"), ALU.mult)
            settle()
            for t in range(TT):
                pv = r_tok[:, t, 512:1024]
                does("rwkv sgu normed", dve.tensor_tensor, pv, pv, row("ln_b"), ALU.add)
            for i in range(2):
                dve.wait_ge(*after(f"rwkv kn {i}"))
                does("rwkv kk clipped", dve.tensor_scalar, r_e2[:, 2 * i:2 * i + 2, :], bank(f"rwkv kn {i}").rearrange("p (c t) -> p c t", c=2),
                     1e-24, None, ALU.max)
                marks[f"used rwkv kn {i}"] = marks["rwkv kk clipped"]
            for t in range(TT):
                dve.wait_ge(*after(f"rwkv sgu {t}"))
                does(f"used rwkv sgu {t}", dve.tensor_tensor, four(O[:, t, 0:512]), four(bank(f"rwkv sgu {t}")), wide(col("sgu_b"), P), ALU.add)
            settle()
            does(None, dve.tensor_tensor, O[:, :, 0:512], O[:, :, 0:512], r_tok[:, :, 0:512], ALU.mult)
            dve.wait_ge(*after("used rwkv g 1"))
            for c in range(4):
                does(None, dve.tensor_scalar, r_c[:, c, :], r_a[:, c, :], 1.0, col("k_a")[:, c:c + 1], ALU.subtract, ALU.mult)
            does(None, dve.tensor_scalar, r_ld[:, :, :], r_ld[:, :, :], NEG_ROOT_E, None, ALU.mult)
            settle()
            k = r_pm[:, 4:8, :]
            does(None, dve.scalar_tensor_tensor, k, r_c[:, :, :], 1.0, k, ALU.add, ALU.mult)
            settle()
            for c in range(4):
                does("rwkv rk", dve.scalar_tensor_tensor, r_e1[:, c, :], r_pm[:, c, :], col("r_k")[:, c:c + 1], r_pm[:, 4 + c, :], ALU.mult, ALU.mult)
            for c in range(4):
                for ch in range(2):
                    part = slice(ch * P, (ch + 1) * P)
                    does(None, dve.tensor_tensor_scan, r_c[:, c, part], ones, r_ld[:, c, part], 0.0, ALU.mult, ALU.add)
            settle()
            does(None, dve.tensor_scalar, r_mid[:, :, :], r_c.rearrange("p c (h t) -> p c h t", h=2)[:, :, :, P - 1], 0.5, None, ALU.mult)
            settle()
            does(None, dve.tensor_tensor, r_f[:, :], r_mid[:, :, 0], r_mid[:, :, 1], ALU.add)
            chunks = r_c.rearrange("p c (h t) -> p (c h) t", h=2)
            does(None, dve.tensor_tensor, chunks, chunks, wide(r_mid.rearrange("p c h -> p (c h)"), P), ALU.subtract)
            settle()
            does("rwkv exponents", dve.tensor_tensor, r_e1p[:, :, :], r_c[:, :, :], r_ld[:, :, :], ALU.subtract)
            dve.wait_ge(*after("rwkv kk root"))
            does(None, dve.reciprocal, r_e2[:, :, :], r_e2[:, :, :])
            settle()
            does("rwkv kk unit", dve.tensor_tensor, r_kk[:, :, :], r_kk[:, :, :], r_e2[:, :, :], ALU.mult)
            settle()
            does("rwkv b", dve.tensor_tensor, r_a[:, :, :], r_kk[:, :, :], r_a[:, :, :], ALU.mult)
            dve.wait_ge(*after("rwkv bonus"))
            does("used rwkv bonus", dve.tensor_copy, r_bonus.rearrange("p t h -> p (t h)"), bank("rwkv bonus")[:, 0:16])
            dve.wait_ge(*after("rwkv exp"))
            settle()
            for x, e in ((r_pm[:, 0:4, :], r_e1), (k, r_e2), (r_kk[:, :, :], r_e1p), (r_a[:, :, :], r_e2)):
                does("rwkv decayed", dve.tensor_tensor, x, x, e[:, :, :], ALU.mult)
            settle()
            for half in range(2):
                for name, dst, mask in (("A", r_A, "strict"), ("L", r_L, "upper"), ("R", r_R, "incl_t"), ("B", r_B, "incl_t")):
                    for par in range(2):
                        dve.wait_ge(*after(f"rwkv {name} {half} {par}"))
                        does(f"used rwkv {name} {half} {par}", dve.scalar_tensor_tensor, dst[:, 4 * par:4 * par + 4, :],
                             four(bank(f"rwkv {name} {half} {par}")), 1e30, over(table(mask), 4), ALU.min, ALU.mult)
                    if name == "A":
                        settle()
                marks[f"rwkv masked {half}"] = marks[f"used rwkv B {half} 1"]
                inverse_vector(dve, f"rwkv{half}", r_A, r_T, r_U, r_AM)
                for c in range(2):
                    if c == 1:
                        dve.wait_ge(*after(f"rwkv ds {half}"))
                        for ti in range(2):
                            does(f"rwkv s1 {half} {ti}", dve.scalar_tensor_tensor, r_s1[:, ti, :], bank(f"rwkv ds {half}")[:, ti * P:(ti + 1) * P],
                                 r_f[:, 2 * half + ti:2 * half + ti + 1], table("pair_ones"), ALU.mult, ALU.mult)
                        marks[f"used rwkv ds {half}"] = marks[f"rwkv s1 {half} 1"]
                    dve.wait_ge(*after(f"rwkv y {half} {c}"))
                    does(f"used rwkv y {half} {c}", dve.tensor_copy, O[:, c, 512 + 256 * half:768 + 256 * half], bank(f"rwkv y {half} {c}")[:, 0:SEQ])
            settle()
            for t in range(TT):
                centre(O[:, t, 512:1024], r_stat[:, 5, 8 * t:8 * t + 8], 64, "rwkv centred")
            dve.wait_ge(*after("rwkv y square"))
            does("rwkv y var", dve.tensor_reduce, r_stat[:, 3, :], r_scratch.rearrange("p t (h d) -> p (t h) d", d=64), AX.X, ALU.add)
            dve.wait_ge(*after("rwkv y root"))
            does(None, dve.reciprocal, r_stat[:, 4, :], r_stat[:, 4, :])
            for t in range(TT):
                does(None, dve.tensor_tensor, groups(r_scratch[:, t, :], 64), groups(r_v[:, t, :], 64), wide(r_bonus[:, t, :], 64), ALU.mult)
            settle()
            for t in range(TT):
                y = O[:, t, 512:1024]
                does(None, dve.tensor_tensor, groups(y, 64), groups(y, 64), wide(r_stat[:, 4, 8 * t:8 * t + 8], 64), ALU.mult)
                settle()
                does(None, dve.tensor_tensor, y, y, row("gn_g"), ALU.mult)
                settle()
                does(None, dve.tensor_tensor, y, y, row("gn_b"), ALU.add)
                settle()
                does(None, dve.tensor_tensor, y, y, r_scratch[:, t, :], ALU.add)
                settle()
                does("rwkv gated", dve.tensor_tensor, y, y, r_g[:, t, :], ALU.mult)
            turn_vector(dve, "rwkv", rwkv, KT)
            out_vector(dve, "rwkv", at)

        with arena() as take:
            for name in ("silu_kept", "gated_kept", "act_kept"):
                take(name, [P, 2, SEQ])
            take("gate_rows_kept", [P, EXPERTS, SEQ])
            m_logits = take("m_logits", [P, TT, EXPERTS])
            m_above = take("m_above", [P, TT, EXPERTS, EXPERTS])
            m_equal = take("m_equal", [P, TT, EXPERTS, EXPERTS])
            m_rank = take("m_rank", [P, TT, EXPERTS])
            m_one = take("m_one", [P, 2, TT])
            m_gt = take("m_gt", [EXPERTS, SEQ])

        def moe_tensor(pe):
            router = col("router").rearrange("p (k e) -> p k e", k=KT)
            b = open_bank(pe, "moe logits")
            for t in range(TT):
                for k in range(KT):
                    ins = pe.matmul(b[:, EXPERTS * t:EXPERTS * (t + 1)], hT[:, k, t * P:(t + 1) * P], router[:, k, :], start=k == 0, stop=k == KT - 1)
            ins.then_inc(*moe.tensor("moe logits"))
            pe.wait_ge(*after("moe gates"))
            b = open_bank(pe, "moe turned")
            for t in range(TT):
                ins = pe.transpose(b[0:EXPERTS, t * P:(t + 1) * P], m_logits[:, t, :], ident)
            ins.then_inc(*moe.tensor("moe turned"))
            pe.wait_ge(*after("used moe turned"))
            for q in range(EXPERTS // 2):
                b = open_bank(pe, f"moe row {q}")
                for i in range(2):
                    e = 2 * q + i
                    ins = pe.matmul(b[:, i * SEQ:(i + 1) * SEQ], table("expert_row")[0:EXPERTS, e * P:(e + 1) * P], m_gt[:, :], start=True, stop=True)
                ins.then_inc(*moe.tensor(f"moe row {q}"))
            pe.wait_ge(*after(f"used moe row {EXPERTS // 2 - 1}"))

        def moe_scalar(act):
            act.wait_ge(*after("moe less max"))
            act.activation(m_logits[:, :, :], m_logits[:, :, :], ACT.Exp).then_inc(*moe.scalar("moe exp"))
            act.wait_ge(*after("moe turned"))
            act.activation(m_gt[:, :], bank("moe turned")[0:EXPERTS, 0:SEQ], ACT.Copy).then_inc(*moe.scalar("used moe turned"))
            for q in range(EXPERTS // 2):
                act.wait_ge(*after(f"moe row {q}"))
                act.activation(gate_rows[:, 2 * q:2 * q + 2, :], bank(f"moe row {q}").rearrange("p (e t) -> p e t", e=2), ACT.Copy) \
                   .then_inc(*moe.scalar(f"used moe row {q}"))

        def moe_vector(dve):
            def does(label, op, *args):
                op(*args).then_inc(*moe.vector(label))

            def settle():
                dve.wait_ge(*moe.vector.so_far())

            dve.wait_ge(*after("moe logits"))
            does("used moe logits", dve.tensor_tensor, m_logits[:, :, :], bank("moe logits")[:, 0:TT * EXPERTS].rearrange("p (t e) -> p t e", t=TT),
                 over(row("router_b"), TT), ALU.add)
            settle()
            for t in range(TT):
                l = m_logits[:, t, :]
                does(None, dve.tensor_tensor, m_above[:, t, :, :], over(l, EXPERTS), wide(l, EXPERTS), ALU.is_gt)
                does(None, dve.tensor_tensor, m_equal[:, t, :, :], over(l, EXPERTS), wide(l, EXPERTS), ALU.is_equal)
            does(None, dve.tensor_reduce, m_one[:, 0, :], m_logits[:, :, :], AX.X, ALU.max)
            settle()
            for t in range(TT):
                does(None, dve.tensor_tensor, m_equal[:, t, :, :], m_equal[:, t, :, :], table("lower8").rearrange("p (e f) -> p e f", e=EXPERTS), ALU.mult)
            settle()
            does(None, dve.tensor_tensor, m_above[:, :, :, :], m_above[:, :, :, :], m_equal[:, :, :, :], ALU.add)
            does("moe less max", dve.tensor_tensor, m_logits[:, :, :], m_logits[:, :, :], wide(m_one[:, 0, :], EXPERTS), ALU.subtract)
            settle()
            does(None, dve.tensor_reduce, m_rank[:, :, :], m_above[:, :, :, :], AX.X, ALU.add)
            settle()
            does(None, dve.tensor_scalar, m_rank[:, :, :], m_rank[:, :, :], 1.5, None, ALU.is_lt)
            settle()
            dve.wait_ge(*after("moe exp"))
            does(None, dve.tensor_tensor, m_logits[:, :, :], m_logits[:, :, :], m_rank[:, :, :], ALU.mult)
            settle()
            does(None, dve.tensor_reduce, m_one[:, 1, :], m_logits[:, :, :], AX.X, ALU.add)
            settle()
            does(None, dve.reciprocal, m_one[:, 1, :], m_one[:, 1, :])
            settle()
            does("moe gates", dve.tensor_tensor, m_logits[:, :, :], m_logits[:, :, :], wide(m_one[:, 1, :], EXPERTS), ALU.mult)
            dve.wait_ge(*after(f"used moe row {EXPERTS // 2 - 1}"))

        MIXERS = {"delta": {"tensor": delta_tensor, "scalar": delta_scalar, "vector": delta_vector, "pool": delta_pool},
                  "attention": {"tensor": attention_tensor, "scalar": attention_scalar, "vector": attention_vector,
                                "pool": attention_pool},
                  "rwkv": {"tensor": rwkv_tensor, "scalar": rwkv_scalar, "vector": rwkv_vector, "pool": rwkv_pool},
                  "sparse": {"tensor": sparse_tensor, "scalar": sparse_scalar, "vector": sparse_vector, "pool": sparse_pool}}

        LOADS = 4
        marks["x 0"] = ("loaded", 16 * LOADS)

        @block.tensor
        def _(pe):
            pe.wait_ge(loaded, 16 * LOADS)
            for at, (kind, n) in enumerate(NETWORK):
                if kind == "final":
                    continue
                norm_tensor(pe, at)
                wait_hT(pe, f"norm {at}")
                if kind == "moe":
                    moe_tensor(pe)
                if kind in ("ffn", "moe"):
                    ffn_tensor(pe, at)
                else:
                    MIXERS[kind]["tensor"](pe, at)

        @block.scalar
        def _(act):
            act.dma_start(rows[:, :], rows_in.partition_broadcast(P)).then_inc(loaded, 16)
            act.dma_start(tables[:, :], tables_in).then_inc(loaded, 16)
            act.wait_ge(loaded, 16 * LOADS)
            for at, (kind, n) in enumerate(NETWORK):
                norm_scalar(act, at)
                if kind == "moe":
                    moe_scalar(act)
                if kind in ("ffn", "moe"):
                    ffn_scalar(act, at)
                elif kind != "final":
                    MIXERS[kind]["scalar"](act, at)

        @block.vector
        def _(dve):
            dve.wait_ge(loaded, 16 * LOADS)
            for at, (kind, n) in enumerate(NETWORK):
                if kind == "final":
                    final_vector(dve, at)
                    continue
                norm_vector(dve, at)
                if kind == "moe":
                    moe_vector(dve)
                if kind in ("ffn", "moe"):
                    ffn_vector(dve, at, 0.5 if n < 6 else 1.0)
                else:
                    MIXERS[kind]["vector"](dve, at)

        @block.gpsimd
        def _(pool):
            for at, (kind, n) in enumerate(NETWORK):
                if kind in MIXERS:
                    MIXERS[kind]["pool"](pool, at)

        @block.sync
        def _(sp):
            sp.dma_start(X[:, :, :], x_in.rearrange("o (t p) d -> p (o t) d", p=P)).then_inc(loaded, 16)
            sp.dma_start(columns[:, :], columns_in).then_inc(loaded, 16)
            for g in range(SLOTS):
                sp.dma_start(slot(g), stream[g]).then_inc(step_loaded[g], 16)
            turns = total // SLOTS - 1
            with sp.Fori(0, turns) as i:
                for s in range(SLOTS):
                    sp.wait_ge(steps_used, SLOTS * i + s + 1)
                    sp.dma_start(slot(s), stream[SLOTS * i + SLOTS + s]).then_inc(step_loaded[s], 16)
            for g in range(SLOTS * (turns + 1), total):
                sp.wait_ge(steps_used, g - SLOTS + 1)
                sp.dma_start(slot(g), stream[g]).then_inc(step_loaded[g % SLOTS], 16)
            sp.wait_ge(*after(f"x {len(NETWORK)}"))
            sp.dma_start(out.rearrange("o (t p) d -> p (o t) d", p=P), X[:, :, :]).then_inc(stored, 16)
            sp.wait_ge(stored, 16)


def by_row_tile(w):
    return np.ascontiguousarray(w).reshape(-1, P, w.shape[-1]).transpose(1, 0, 2)


def ffn_steps(gate, up, down):
    d = gate.shape[0]
    for j in range(0, down.shape[0], P):
        step = np.empty((P, STEP), np.float32)
        step[:, 0:d] = by_row_tile(gate[:, j:j + P]).reshape(P, -1)
        step[:, d:2 * d] = by_row_tile(up[:, j:j + P]).reshape(P, -1)
        step[:, 2 * d:] = down[j:j + P]
        yield step


def column_steps(parts, n):
    w = np.zeros((parts[0].shape[0], n * COLS), np.float32)
    at = 0
    for part in parts:
        w[:, at:at + part.shape[1]] = part
        at += part.shape[1]
    for s in range(n):
        yield by_row_tile(w[:, s * COLS:(s + 1) * COLS]).reshape(P, -1)


SLOT_HEADS = [0, 4, 1, 5, 2, 6, 3, 7]


def stream_steps(a):
    for kind, n in NETWORK:
        if kind == "ffn":
            if n < 6:
                name = {0: "l0_ffn1", 2: "l0_ffn2", 3: "l1_ffn1", 5: "l1_ffn2"}[n]
                up = a[name + "_w_up"]
                yield from ffn_steps(up[:, :D_FF], up[:, D_FF:], a[name + "_w_down"])
            else:
                yield from ffn_steps(a["ffn_w_gate_2"][0], a["ffn_w_up_2"][0], a["ffn_w_down_2"][0])
        elif kind == "moe":
            for e in range(EXPERTS):
                yield from ffn_steps(a["moe_w_gate_2"][0, e], a["moe_w_up_2"][0, e], a["moe_w_down_2"][0, e])
        elif kind == "delta":
            yield from column_steps([a["l0_w_in"][:, :1536]], DELTA_T)
            yield from column_steps([a["l0_w_in"][:, 1536:]], DELTA_K)
            yield from column_steps([a["l0_w_out"]], OUT_STEPS)
        elif kind == "attention":
            yield from column_steps([a["l1_w_in"]], ATT_K)
            yield from column_steps([a["l1_w_out"]], OUT_STEPS)
        elif kind == "rwkv":
            yield from column_steps([a["e_w_in_2"][0][:, :1024]], RWKV_K)
            yield from column_steps([a["e_w_in_2"][0][:, 1024:]], RWKV_T)
            yield from column_steps([a["e_w_out_2"][0]], OUT_STEPS)
        elif kind == "sparse":
            w = a["o_w_in_2"][0]
            q = w[:, :512].reshape(-1, 8, 64)[:, SLOT_HEADS].reshape(-1, 512)
            gl = w[:, 1280:1304].reshape(-1, 8, 3)[:, SLOT_HEADS].transpose(0, 2, 1).reshape(-1, 24)
            kc, vc = (w[:, c:c + 128].reshape(-1, 2, 1, 64).repeat(2, axis=2).reshape(-1, 256) for c in (512, 640))
            yield from column_steps([q, w[:, 768:1280], gl], SPARSE_K)
            yield from column_steps([kc, vc, w[:, 1304:]], SPARSE_T)
            tiles = np.concatenate([by_row_tile(a["nsa_cmp_k_w1_2"][0]), by_row_tile(a["nsa_cmp_v_w1_2"][0])], axis=1)
            padded = np.zeros((P, SPARSE_C * 12, 256), np.float32)
            padded[:, :32] = tiles
            for s in range(SPARSE_C):
                yield padded[:, 12 * s:12 * s + 12].reshape(P, -1)
            out = a["o_w_out_2"][0]
            yc = out[:512].reshape(8, 64, -1)[SLOT_HEADS].reshape(512, -1)
            yield from column_steps([np.concatenate([yc, out[512:]])], OUT_STEPS)


def pack_columns(a):
    c = np.zeros((P, COLUMN.width), np.float32)

    def per(v):
        return v.reshape(-1, P).T

    names = ["l0_ffn1_norm", "l0_mix_norm", "l0_ffn2_norm", "l1_ffn1_norm", "l1_mix_norm", "l1_ffn2_norm",
             "e_norm_mix_2", "e_norm_ffn_2", "o_norm_mix_2", "o_norm_ffn_2"]
    c[:, COLUMN["gain"]] = np.concatenate([per(a[n].reshape(-1)) for n in names], axis=1)
    c[:, COLUMN["conv"]] = np.concatenate([per(a["l0_conv_w"][j]) for j in range(4)], axis=1)
    c[:, COLUMN["conv3"]] = np.concatenate([per(a["conv_w_2"][0, j]) for j in range(3)], axis=1)
    for name, v in (("mu", "mu"), ("w0", "w0"), ("a0", "a0"), ("k_k", "k_k"), ("k_a", "k_a"), ("r_k", "r_k")):
        c[:, COLUMN[name]] = per(a[f"rwkv_{v}_2"][0].reshape(-1))
    c[:, COLUMN["sgu_b"]] = a["sgu_b_2"][0].T
    c[:, COLUMN["sgu_w"]] = a["sgu_w_2"][0].transpose(2, 0, 1).reshape(P, -1)
    c[:, COLUMN["router"]] = by_row_tile(a["moe_router_2"][0]).reshape(P, -1)
    c[0:64, COLUMN["lora"]], c[64:, COLUMN["lora"]] = a["rwkv_w2_2"][0], a["rwkv_a2_2"][0]
    c[:, COLUMN["g2"]] = a["rwkv_g2_2"][0]
    for s in "kv":
        c[:, COLUMN[f"cmp_{s}2"]] = by_row_tile(a[f"nsa_cmp_{s}_w2_2"][0]).reshape(P, -1)
        c[:, COLUMN[f"pos_{s}"]] = a[f"nsa_cmp_pos_{s}_2"][0].reshape(16, P).T
    return c


def pack_rows(a):
    r = np.empty(ROW.width, np.float32)
    for name, v in (("final0", "final_norm"), ("final1", "final_norm_2"), ("gdn_norm", "l0_gdn_norm"),
                    ("diff_norm", "l1_diff_norm"), ("ln_g", "sgu_ln_g_2"), ("ln_b", "sgu_ln_b_2"), ("gn_g", "rwkv_gn_g_2"),
                    ("gn_b", "rwkv_gn_b_2"), ("a_log", "l0_a_log"), ("dt_bias", "l0_dt_bias"), ("router_b", "moe_router_b_2"),
                    ("lq1", "l1_lambda_q1"), ("lk1", "l1_lambda_k1"), ("lq2", "l1_lambda_q2"), ("lk2", "l1_lambda_k2")):
        r[ROW[name]] = a[v].reshape(-1)
    return r


def shape_tables():
    t = np.zeros((P, TABLE.width), np.float32)
    t[:, TABLE["eps"]] = [EPS, 1e-5, 64e-5, 128 * EPS]
    p, f = np.arange(P)[:, None], np.arange(P)[None, :]
    t[:, TABLE["ident"]], t[:, TABLE["ones"]] = p == f, 1.0
    t[:, TABLE["incl_t"]], t[:, TABLE["upper"]], t[:, TABLE["strict"]] = f >= p, f > p, p > f
    t[:, TABLE["level"]] = np.concatenate([(p // (2 * b) == f // (2 * b)) & (p % (2 * b) >= b) & (f % (2 * b) < b)
                                           for b in (1 << n for n in range(LEVELS))], axis=1)
    token = np.arange(SEQ)[None, :]
    ret = []
    for h in range(HEADS):
        gamma, d = 1.0 - 2.0 ** (-5.0 - h), token - p
        m = np.where(d >= 0, gamma ** np.maximum(d, 0), 0.0) * 64 ** -0.5
        ret += [m, m[:, :P]]
    t[:, TABLE["ret"]] = np.concatenate(ret, axis=1)
    dist = np.concatenate([p - f, P + p - token], axis=1)
    count = (dist >= 0) * ((dist <= 128) * 1 + (dist % 4 == 0) + (dist % 16 == 0))
    t[:, TABLE["count"]], t[:, TABLE["bias_dil"]] = count, np.where(count > 0, 0.0, -1e30)
    t[:, TABLE["bias"]] = np.where(dist >= 0, 0.0, -1e30)
    for half, theta, dim in ((32, 10000.0, 64), (64, 10000.0, 128), (8, 500000.0, 16)):
        inv = np.float32(theta) ** (-np.arange(0, dim, 2, dtype=np.float32) / np.float32(dim))
        ang = (np.arange(SEQ, dtype=np.float32)[:, None] * inv[None, :]).reshape(TT, P, half).transpose(1, 0, 2)
        t[:, TABLE[f"cos{half}"]], t[:, TABLE[f"sin{half}"]] = (g(ang).reshape(P, -1) for g in (np.cos, np.sin))
    n = np.arange(CMP_PAD)[None, None, :]
    seen = (n < CMP_N) & (16 * n + 31 <= (p + P * np.arange(TT)[None, :])[:, :, None])
    t[:, TABLE["cmp_mask"]] = seen.reshape(P, -1)
    t[:, TABLE["cmp_bias"]] = np.where(seen, 0.0, -1e30).reshape(P, -1)
    t[:, TABLE["pair_ones"]] = p // 64 == f // 64
    t[:, TABLE["pair_sel"]] = p // 64 == np.arange(2)[None, :]
    t[:, TABLE["cmp_block"]] = p // CMP_PAD == np.arange(8)[None, :]
    t[:, TABLE["expert_row"]] = np.repeat(p == np.arange(EXPERTS)[None, :], P, axis=1)
    e = np.arange(EXPERTS)
    t[:, TABLE["lower8"]] = (e[None, :] < e[:, None]).reshape(1, -1)
    return t


def kernel(**inputs):
    import concourse.bacc as bacc
    from concourse.bass_utils import run_bass_kernel_spmd

    a = {name: np.asarray(v) for name, v in inputs.items()}
    steps = sum(STEPS[kind] for kind, _ in NETWORK)
    stream = np.empty((steps, P, STEP), np.float32)
    for g, step in enumerate(stream_steps(a)):
        stream[g] = step
    arrays = {"x": np.ascontiguousarray(a["x"]), "stream": stream, "columns": pack_columns(a), "rows": pack_rows(a),
              "tables": shape_tables()}
    marks = {}
    for _ in range(2):
        nc = bacc.Bacc("TRN2", target_bir_lowering=False, num_devices=1)
        args = [nc.dram_tensor(f"in_{n}", v.shape, F32, kind="ExternalInput").ap() for n, v in arrays.items()]
        out = nc.dram_tensor("result", a["x"].shape, F32, kind="ExternalOutput").ap()
        network_kernel(nc, *args, out, marks)
    r = run_bass_kernel_spmd(nc, [{f"in_{n}": v for n, v in arrays.items()}], core_ids=[0])
    return r.results[0]["result"]
```

```python
import math
from contextlib import ExitStack

import numpy as np
import concourse.bass as bass
from concourse import mybir

F32 = mybir.dt.float32
F32R = mybir.dt.float32r
ACT = mybir.ActivationFunctionType
ALU = mybir.AluOpType
AX = mybir.AxisListType

P = 128
SEQ, D_MODEL, D_FF = 256, 1024, 2816
TT = SEQ // P
KT = D_MODEL // P
EXPERTS, D_EXPERT = 8, 1408
EPS = 1e-6
STEP = 3 * D_MODEL
COLS = STEP // KT
SLOTS = 3
PART = STEP // 3
TURN = 6
HEADS = 4
LEVELS = 7
LAMBDA_INIT = 0.8 - 0.6 * math.exp(-0.3)
CMP_N, CMP_PAD = 15, 16

NETWORK = [("ffn", 0), ("delta", 1), ("ffn", 2), ("ffn", 3), ("attention", 4), ("ffn", 5), ("final", 0),
           ("rwkv", 6), ("ffn", 7), ("sparse", 8), ("moe", 9), ("final", 1)]
FF_STEPS, MOE_STEPS = D_FF // P, EXPERTS * D_EXPERT // P
OUT_STEPS = -(-D_MODEL // COLS)
DELTA_T, DELTA_K = 4, 6
ATT_K = 8
RWKV_K, RWKV_T = 3, 5
SPARSE_K, SPARSE_T, SPARSE_C = 3, 6, 3
STEPS = {"ffn": FF_STEPS, "moe": MOE_STEPS, "final": 0, "delta": DELTA_T + DELTA_K + OUT_STEPS,
         "attention": ATT_K + OUT_STEPS, "rwkv": RWKV_K + RWKV_T + OUT_STEPS,
         "sparse": SPARSE_K + SPARSE_T + SPARSE_C + OUT_STEPS}


class Places:

    def __init__(self, sizes):
        self.at, self.width = {}, 0
        for name, n in sizes:
            self.at[name] = (self.width, self.width + n)
            self.width += n

    def __getitem__(self, name):
        return slice(*self.at[name])


COLUMN = Places([("gain", 10 * KT), ("conv", 4 * 12), ("mu", 14), ("w0", 4), ("a0", 4), ("k_k", 4), ("k_a", 4),
                 ("r_k", 4), ("sgu_b", 4), ("sgu_w", 4 * P), ("router", KT * EXPERTS), ("lora", 512), ("g2", 512),
                 ("cmp_k2", 2 * 64), ("cmp_v2", 2 * 64), ("pos_k", 16), ("pos_v", 16), ("conv3", 3 * 4)])
ROW = Places([("gdn_norm", P), ("diff_norm", P), ("ln_g", 512), ("ln_b", 512),
              ("gn_g", 512), ("gn_b", 512), ("a_log", 4), ("dt_bias", 4), ("router_b", 8), ("lq1", 64), ("lk1", 64),
              ("lq2", 64), ("lk2", 64)])
TABLE = Places([("eps", 4), ("ident", P), ("ones", P), ("incl_t", P), ("strict", P), ("upper", P), ("level", LEVELS * P),
                ("ret", HEADS * 3 * P), ("count", 3 * P), ("bias", 3 * P), ("bias_dil", 3 * P), ("cos32", TT * 32), ("sin32", TT * 32),
                ("cos64", TT * 64), ("sin64", TT * 64), ("cos8", TT * 8), ("sin8", TT * 8),
                ("cmp_bias", TT * CMP_PAD), ("cmp_mask", TT * CMP_PAD), ("pair_ones", P),
                ("pair_sel", 2), ("cmp_block", 8), ("expert_row", EXPERTS * P), ("lower8", EXPERTS * EXPERTS)])


class Progress:

    def __init__(self, marks, sem, name):
        self.marks, self.sem, self.name, self.n = marks, sem, name, 0

    def __call__(self, label=None):
        self.n += 1
        if label is not None:
            self.marks[label] = (self.name, self.n)
        return self.sem, 1

    def so_far(self):
        return self.sem, self.n


class Stage:

    def __init__(self, marks, sems, name):
        self.tensor, self.vector, self.scalar, self.pool = (
            sems.setdefault(f"{name}_{e}", Progress(marks, None, f"{name}_{e}"))
            for e in ("tensor", "vector", "scalar", "pool"))


STAGES = ("norm", "ffn", "delta", "attention", "rwkv", "sparse", "moe", "proj", "inverse")


def network_kernel(nc, x_in, stream, columns_in, rows_in, tables_in, final_in, out, marks):
    ctx = ExitStack()
    with ctx:
        def sb(name, shape):
            return ctx.enter_context(nc.sbuf_tensor(name, shape, F32))

        def sem(name):
            return ctx.enter_context(nc.semaphore(name))

        ring = sb("ring", [P, SLOTS, STEP])
        X = sb("X", [P, TT, D_MODEL])
        hT_hi, hT_lo = (ctx.enter_context(nc.sbuf_tensor(n, [P, KT, SEQ], F32R)) for n in ("hT_hi", "hT_lo"))
        O = sb("O", [P, TT, D_MODEL])
        columns = sb("columns", [P, COLUMN.width])
        rows = sb("rows", [P, ROW.width])
        tables = sb("tables", [P, TABLE.width])
        squares = sb("squares", [P, TT])
        rms = sb("rms", [P, TT])
        rstd = sb("rstd", [P, TT])
        psum = ctx.enter_context(nc.psum_tensor("psum", [P, 8, 512], F32))

        class Arena:

            def __enter__(self):
                self.own, self.taken = ExitStack(), 0
                return self

            def __exit__(self, *error):
                self.own.close()

            def __call__(self, name, shape, dtype=F32):
                self.taken += 4 * math.prod(shape[1:])
                return self.own.enter_context(nc.sbuf_tensor(name, shape, dtype))

            def beyond_split(self, name):
                left = 4 * 4 * STEP - self.taken
                if left > 0:
                    self(name, [P, left // 4])

        with Arena() as take:
            w_hi, w_lo = (take(n, [P, 2, STEP], F32R) for n in ("w_hi", "w_lo"))
            silu, gated, gated_by = (take(n, [P, 2, SEQ]) for n in ("silu", "gated", "gated_by"))
            act_hi, act_lo = (take(n, [P, 2, SEQ], F32R) for n in ("act_hi", "act_lo"))
            gate_rows = take("gate_rows", [P, EXPERTS, SEQ])
            final_row = take("final_row", [P, D_MODEL])

        def col(name):
            return columns[:, COLUMN[name]]

        def row(name):
            return rows[:, ROW[name]]

        def table(name):
            return tables[:, TABLE[name]]

        def wide(ap, n):
            return ap.unsqueeze(len(ap.shape)).to_broadcast(list(ap.shape) + [n])

        def over(ap, n):
            return ap.unsqueeze(1).to_broadcast([ap.shape[0], n, ap.shape[1]])

        ident, ones = table("ident"), table("ones")
        eps, ln_eps, gn_eps, two_eps = (table("eps")[:, i:i + 1] for i in range(4))

        step_loaded = [sem(f"step_loaded_{s}") for s in range(SLOTS)]
        hi_ready = sem("hi_ready")
        lo_ready = sem("lo_ready")
        lo_last_ready = sem("lo_last_ready")
        early_used = sem("early_used")
        steps_used = sem("steps_used")
        ffn_up_ready = sem("ffn_up_ready")
        ffn_silu_ready = sem("ffn_silu_ready")
        ffn_gated = sem("ffn_gated")
        row_loaded = sem("final_row_loaded")
        ffn_act_ready = sem("ffn_act_ready")
        stored = sem("out_stored")
        progress = {}
        stages = {name: Stage(marks, progress, name) for name in STAGES}
        progress["loaded"] = Progress(marks, None, "loaded")
        for name, one in progress.items():
            one.sem = sem(name)
        loaded = progress["loaded"].sem
        norm, ffn, delta, attn = (stages[n] for n in ("norm", "ffn", "delta", "attention"))
        rwkv, sparse, moe, proj, inverse = (stages[n] for n in ("rwkv", "sparse", "moe", "proj", "inverse"))

        def after(label):
            name, n = marks.get(label, ("norm_tensor", 1))
            return progress[name].sem, n

        bank_of, bank_order = {}, []

        def open_bank(pe, label):
            n = len(bank_order)
            bank_of[label] = n % 8
            bank_order.append(label)
            if n >= 8 and bank_order[n - 8] is not None:
                pe.wait_ge(*after(f"used {bank_order[n - 8]}"))
            return psum[:, n % 8, :]

        def reset_banks():
            bank_order[:] = [None] * 8

        def bank(label):
            return psum[:, bank_of[label], :]

        first_step, total = [], 0
        for kind, _ in NETWORK:
            first_step.append(total)
            total += STEPS[kind]

        def slot(g):
            return ring[:, g % SLOTS, :]

        def part(x, g, i):
            return x[:, g % 2, i * PART:(i + 1) * PART]

        def split_hi(act, g, gv, parts=range(3)):
            for i in parts:
                if i == 0:
                    act.wait_ge(step_loaded[g % SLOTS], 16 * (gv // SLOTS) + 16)
                if g >= 2:
                    act.wait_ge(early_used if i < 2 else steps_used, gv - 1)
                act.activation(part(w_hi, g, i), slot(g)[:, i * PART:(i + 1) * PART], ACT.Copy).then_inc(hi_ready, 1)

        def split_lo(dve, g, gv):
            for i in range(2):
                dve.wait_ge(hi_ready, 3 * gv + i + 1)
                dve.tensor_tensor(part(w_lo, g, i), slot(g)[:, i * PART:(i + 1) * PART], part(w_hi, g, i).bitcast(F32), ALU.subtract) \
                   .then_inc(lo_ready, 1)

        def split_lo_last(pool, g, gv):
            pool.wait_ge(hi_ready, 3 * gv + 3)
            pool.tensor_tensor(part(w_lo, g, 2), slot(g)[:, 2 * PART:STEP], part(w_hi, g, 2).bitcast(F32), ALU.subtract) \
                .then_inc(lo_last_ready, 1)

        def wait_split(pe, g):
            pe.wait_ge(lo_ready, 2 * g + 2)
            pe.wait_ge(lo_last_ready, g + 1)

        def three_passes(pe, out_, w, x, first, last):
            pe.matmul(out_, w[0], x[0], start=first, stop=False, skip_group_check=True)
            pe.matmul(out_, w[0], x[1], start=False, stop=False, skip_group_check=True)
            return pe.matmul(out_, w[1], x[0], start=False, stop=last, skip_group_check=True)

        block = ctx.enter_context(nc.Block())

        def norm_scalar(act, n):
            act.wait_ge(*after(f"x {n}"))
            for t in range(TT):
                act.activation(O[:, t, :], X[:, t, :], ACT.Square, scale=D_MODEL ** -0.5,
                               accum_out=squares[:, t:t + 1]).then_inc(*norm.scalar(f"norm {n} squares"))
            rstd_scalar(act, n)

        def rstd_scalar(act, n):
            act.wait_ge(*after(f"norm {n} squares"))
            act.activation(rms[:, :], squares[:, :], ACT.Sqrt, bias=eps).then_inc(*norm.scalar(f"norm {n} root"))

        def rstd_vector(dve, n):
            dve.wait_ge(*after(f"norm {n} root"))
            dve.reciprocal(rstd[:, :], rms[:, :]).then_inc(*norm.vector())
            dve.wait_ge(*norm.vector.so_far())

        def norm_vector(dve, n):
            rstd_vector(dve, n)
            for t in range(TT):
                dve.tensor_scalar(O[:, t, :], X[:, t, :], rstd[:, t:t + 1], None, ALU.mult) \
                   .then_inc(*norm.vector(f"norm {n} xn {t}"))
            turn_vector(dve, f"norm {n}", norm, KT, columns[:, KT * NETWORK[n][1]:KT * (NETWORK[n][1] + 1)])

        def norm_turned_scalar(act, n):
            turn_scalar(act, f"norm {n}", norm, KT)

        def norm_tensor(pe, n):
            turn_tensor(pe, f"norm {n}", norm, KT, [f"norm {n} xn {t}" for t in range(TT)])

        def turn_tensor(pe, name, stage, tiles, sources):
            for t in range(TT):
                pe.wait_ge(*after(sources[t]))
                for q in range(0, tiles, 4):
                    b = open_bank(pe, f"{name} turn {t} {q}")
                    for k in range(4):
                        last = pe.transpose(b[:, k * P:(k + 1) * P], O[:, t, (q + k) * P:(q + k + 1) * P], ident)
                    last.then_inc(*stage.tensor(f"{name} turn {t} {q}"))

        def turned(t, q):
            return (slice(None), slice(q, q + 4), slice(t * P, (t + 1) * P)), four(O[:, t, q * P:(q + 4) * P])

        def turn_vector(dve, name, stage, tiles, gain=None):
            places = [(t, q) for t in range(TT) for q in range(0, tiles, 4)]
            for t, q in places:
                dve.wait_ge(*after(f"{name} turn {t} {q}"))
                src, (_, whole) = four(bank(f"{name} turn {t} {q}")), turned(t, q)
                if gain is None:
                    ins = dve.tensor_copy(whole, src)
                else:
                    ins = dve.tensor_tensor(whole, src, wide(gain[:, q:q + 4], P), ALU.mult)
                ins.then_inc(*stage.vector(f"used {name} turn {t} {q}"))
            for t, q in places:
                dve.wait_ge(*after(f"{name} hi {t} {q}"))
                at, whole = turned(t, q)
                dve.tensor_tensor(hT_lo[at], whole, hT_hi[at].bitcast(F32), ALU.subtract).then_inc(*stage.vector(f"{name} hT {t} {q}"))

        def turn_scalar(act, name, stage, tiles):
            for t in range(TT):
                for q in range(0, tiles, 4):
                    act.wait_ge(*after(f"used {name} turn {t} {q}"))
                    at, whole = turned(t, q)
                    act.activation(hT_hi[at], whole, ACT.Copy).then_inc(*stage.scalar(f"{name} hi {t} {q}"))

        def wait_hT(eng, name, tiles=KT):
            eng.wait_ge(*after(f"{name} hT {TT - 1} {tiles - 4}"))

        def four(ap):
            return ap.rearrange("p (m c) -> p m c", m=4)

        def proj_tiles(kinds):
            return [(s, kind, j) for s, kind in enumerate(kinds) for j in range({"k": TT, "t": 3, "v": 2, "u": 1}[kind])]

        def release(pe, name, s):
            pe.wait_ge(*after(f"{name} {s} last"))
            pe.nop().then_inc(early_used, 1)
            pe.nop().then_inc(steps_used, 1)

        def proj_tensor(pe, name, g0, kinds):
            for s, kind, j in proj_tiles(kinds):
                g = g0 + s
                w = [x[:, g % 2, :].rearrange("p (k c) -> p k c", k=KT) for x in (w_hi, w_lo)]
                if j == 0:
                    wait_split(pe, g)
                b = open_bank(pe, f"{name} {s} {j}")
                for k in range(KT):
                    if kind == "k":
                        ins = three_passes(pe, b[:, 0:COLS], [x[:, k, j * P:(j + 1) * P] for x in (hT_hi, hT_lo)],
                                           [x[:, k, :] for x in w], k == 0, k == KT - 1)
                    else:
                        ins = three_passes(pe, b[:, 0:SEQ], [x[:, k, j * P:(j + 1) * P] for x in w],
                                           [x[:, k, :] for x in (hT_hi, hT_lo)], k == 0, k == KT - 1)
                ins.then_inc(*proj.tensor(f"{name} {s} {j}"))
                marks[f"{name} {s} last"] = marks[f"{name} {s} {j}"]
                if j == 0 and s > 0:
                    release(pe, name, s - 1)
            release(pe, name, s)

        def proj_copies(eng, name, g0, kinds, parity, place, steps=range(99), ahead=False):
            n = -1
            for s, kind, j in proj_tiles(kinds):
                n += 1
                if s not in steps:
                    continue
                if j == 0 and (s + 1 < len(kinds) or ahead):
                    (split_lo if parity else split_hi)(eng, g0 + s + 1, g0 + s + 1)
                if n % 2 != parity:
                    continue
                eng.wait_ge(*after(f"{name} {s} {j}"))
                pairs = place(s, j, bank(f"{name} {s} {j}"))
                for i, (dst, src) in enumerate(pairs):
                    ins = eng.tensor_copy(dst, src) if parity else eng.activation(dst, src, ACT.Copy)
                    side = proj.vector if parity else proj.scalar
                    ins.then_inc(*side(f"used {name} {s} {j}" if i == len(pairs) - 1 else None))

        def proj_pool(pool, g0, n, ahead=False, first=False):
            for g in range(g0 + (not first), g0 + n + ahead):
                split_lo_last(pool, g, g)

        def wait_proj(eng, name, kinds, steps=range(99)):
            tiles = [x for x in proj_tiles(kinds) if x[0] in steps]
            for s, _, j in tiles[-2:]:
                eng.wait_ge(*after(f"used {name} {s} {j}"))

        def out_tensor(pe, name, g0, tiles=KT):
            wait_hT(pe, name, tiles)
            proj_tensor(pe, f"{name} out", g0, "k" * OUT_STEPS)

        def out_scalar(act, at, name, done, stage, tiles=KT):
            g0 = first_step[at] + STEPS[NETWORK[at][0]] - OUT_STEPS
            act.wait_ge(*after(done))
            split_hi(act, g0, g0)
            turn_scalar(act, name, stage, tiles)
            for g in range(g0 + 1, min(g0 + OUT_STEPS + 1, total)):
                split_hi(act, g, g)

        def out_pool(pool, at):
            g0 = first_step[at] + STEPS[NETWORK[at][0]] - OUT_STEPS
            for g in range(g0, min(g0 + OUT_STEPS + 1, total)):
                split_lo_last(pool, g, g)

        def out_vector(dve, name, at):
            g0 = first_step[at] + STEPS[NETWORK[at][0]] - OUT_STEPS
            for s, kind, j in proj_tiles("k" * OUT_STEPS):
                if j == 0 and g0 + s + 1 < total:
                    split_lo(dve, g0 + s + 1, g0 + s + 1)
                c0, c1 = s * COLS, min((s + 1) * COLS, D_MODEL)
                dve.wait_ge(*after(f"{name} out {s} {j}"))
                dve.tensor_tensor(X[:, j, c0:c1], X[:, j, c0:c1], bank(f"{name} out {s} {j}")[:, 0:c1 - c0], ALU.add) \
                   .then_inc(*proj.vector(f"used {name} out {s} {j}"))
            marks[f"x {at + 1}"] = marks[f"used {name} out {OUT_STEPS - 1} {TT - 1}"]

        def out_turn_vector(dve, name, at, stage, tiles=KT):
            g0 = first_step[at] + STEPS[NETWORK[at][0]] - OUT_STEPS
            split_lo(dve, g0, g0)
            turn_vector(dve, name, stage, tiles)
            out_vector(dve, name, at)

        ffn_steps_before, n_ff = [], 0
        for kind, _ in NETWORK:
            ffn_steps_before.append(n_ff)
            n_ff += STEPS[kind] if kind in ("ffn", "moe") else 0

        def ffn_loop(eng, n, step):
            turns = (n - 2) // TURN
            with eng.Fori(0, turns) as i:
                for u in range(TURN):
                    step(2 + u, TURN * i + 2 + u)
            for s in range(2 + turns * TURN, n):
                step(s, s)

        def ffn_tensor(pe, at):
            n, g0, f0 = STEPS[NETWORK[at][0]], first_step[at], ffn_steps_before[at]

            def up(s, sv, peeled=False):
                g = g0 + s
                w = [x[:, g % 2, 0:2 * D_MODEL].rearrange("p (o k c) -> p o k c", o=2, k=KT) for x in (w_hi, w_lo)]
                pe.wait_ge(lo_ready, 2 * (g0 + sv) + 2)
                if not (peeled and f0 == 0):
                    pe.wait_ge(ffn_act_ready, f0 + sv - 1)
                for o in range(2):
                    for k in range(KT):
                        ins = three_passes(pe, psum[:, 4 + s % 2, o * SEQ:(o + 1) * SEQ], [x[:, o, k, :] for x in w],
                                           [x[:, k, :] for x in (hT_hi, hT_lo)], k == 0, k == KT - 1)
                ins.then_inc(ffn_up_ready, 1)

            def down(s, sv, first, last):
                g = g0 + s
                pe.wait_ge(lo_last_ready, g0 + sv + 1)
                pe.wait_ge(ffn_act_ready, f0 + sv + 1)
                for t in range(TT):
                    for h in range(2):
                        c = slice(2 * D_MODEL + h * 512, 2 * D_MODEL + (h + 1) * 512)
                        ins = three_passes(pe, psum[:, 2 * t + h, :], [x[:, s % 2, t * P:(t + 1) * P] for x in (act_hi, act_lo)],
                                           [x[:, g % 2, c] for x in (w_hi, w_lo)], first, last)
                ins.then_inc(steps_used, 1)

            def early_done(sv):
                pe.wait_ge(ffn_up_ready, f0 + sv + 1)
                pe.nop().then_inc(early_used, 1)

            up(0, 0, True)
            up(1, 1, True)
            early_done(0)
            down(0, 0, True, False)
            early_done(1)

            def step(s, sv):
                up(s, sv)
                down(s - 1, sv - 1, False, False)
                early_done(sv)

            ffn_loop(pe, n, step)
            down(n - 1, n - 1, False, True)
            reset_banks()

        def ffn_scalar(act, at):
            n, g0, f0 = STEPS[NETWORK[at][0]], first_step[at], ffn_steps_before[at]

            def step(s, sv):
                more = g0 + s + 1 < total
                if more:
                    split_hi(act, g0 + s + 1, g0 + sv + 1, (0, 1))
                act.wait_ge(ffn_up_ready, f0 + sv + 1)
                if s >= 2 or f0 > 0:
                    act.wait_ge(ffn_act_ready, f0 + sv - 1)
                act.activation(silu[:, s % 2, :], psum[:, 4 + s % 2, 0:SEQ], ACT.Silu).then_inc(ffn_silu_ready, 1)
                if more:
                    split_hi(act, g0 + s + 1, g0 + sv + 1, (2,))

            step(0, 0)
            step(1, 1)
            ffn_loop(act, n, step)

        def ffn_pool(pool, at):
            n, g0 = STEPS[NETWORK[at][0]], first_step[at]

            def step(s, sv):
                if g0 + s + 1 < total:
                    split_lo_last(pool, g0 + s + 1, g0 + sv + 1)

            step(0, 0)
            step(1, 1)
            ffn_loop(pool, n, step)

        def ffn_vector(dve, at, factor):
            kind = NETWORK[at][0]
            n, g0, f0 = STEPS[kind], first_step[at], ffn_steps_before[at]
            made = 3 if kind == "moe" else 2

            def step(s, sv):
                if g0 + s + 1 < total:
                    split_lo(dve, g0 + s + 1, g0 + sv + 1)
                dve.wait_ge(ffn_silu_ready, f0 + sv + 1)
                if g0 + s >= 2:
                    dve.wait_ge(steps_used, g0 + sv - 1)
                dve.tensor_tensor(gated[:, s % 2, :], silu[:, s % 2, :], psum[:, 4 + s % 2, SEQ:2 * SEQ], ALU.mult).then_inc(ffn_gated, 1)
                whole = gated
                if kind == "moe":
                    dve.wait_ge(ffn_gated, 2 * f0 + made * sv + 1)
                    dve.tensor_tensor(gated_by[:, s % 2, :], gated[:, s % 2, :], gate_rows[:, sv // (D_EXPERT // P), :], ALU.mult) \
                       .then_inc(ffn_gated, 1)
                    whole = gated_by
                dve.wait_ge(ffn_gated, 2 * f0 + made * sv + made - 1)
                dve.tensor_copy(act_hi[:, s % 2, :], whole[:, s % 2, :]).then_inc(ffn_gated, 1)
                dve.wait_ge(ffn_gated, 2 * f0 + made * (sv + 1))
                dve.tensor_tensor(act_lo[:, s % 2, :], whole[:, s % 2, :], act_hi[:, s % 2, :].bitcast(F32), ALU.subtract) \
                   .then_inc(ffn_act_ready, 1)

            step(0, 0)
            step(1, 1)
            ffn_loop(dve, n, step)
            dve.wait_ge(steps_used, g0 + n)
            for t in range(TT):
                for h in range(2):
                    c = slice(h * 512, (h + 1) * 512)
                    dve.scalar_tensor_tensor(X[:, t, c], psum[:, 2 * t + h, :], factor, X[:, t, c], ALU.mult, ALU.add) \
                       .then_inc(*ffn.vector(f"x {at + 1}"))

        def final_scalar(act, at):
            which = NETWORK[at][1]
            act.dma_start(final_row[:, :], final_in[which].partition_broadcast(P)).then_inc(row_loaded, 16)

        def final_vector(dve, at):
            which = NETWORK[at][1]
            rstd_vector(dve, at)
            dve.wait_ge(row_loaded, 16 * sum(kind == "final" for kind, _ in NETWORK[:at + 1]))
            for t in range(TT):
                dve.scalar_tensor_tensor(X[:, t, :], X[:, t, :], rstd[:, t:t + 1], final_row[:, :],
                                         ALU.mult, ALU.mult).then_inc(*norm.vector(f"x {at + 1}"))
        def inverse_vector(dve, name, A, T, U, AM):
            dve.tensor_tensor(AM[:, :, :], A[:, :, :], over(table("level")[:, 0:P], 8), ALU.mult).then_inc(*inverse.vector())
            dve.wait_ge(*inverse.vector.so_far())
            dve.tensor_tensor(T[:, :, :], over(ident, 8), AM[:, :, :], ALU.subtract).then_inc(*inverse.vector(f"{name} T 0"))
            for l in range(1, LEVELS):
                for c in range(2):
                    m = slice(4 * c, 4 * c + 4)
                    dve.wait_ge(*after(f"{name} dU {l} {c}"))
                    dve.wait_ge(*after(f"{name} U 0 {c}" if l == 1 else f"{name} U {l - 1} {c}"))
                    dve.tensor_tensor(U[:, m, :], U[:, m, :], four(bank(f"{name} dU {l} {c}")), ALU.subtract) \
                       .then_inc(*inverse.vector(f"{name} U {l} {c}"))
                    marks[f"used {name} dU {l} {c}"] = marks[f"{name} U {l} {c}"]
                    if l < LEVELS - 1:
                        dve.wait_ge(*after(f"{name} dT {l} {c}"))
                        dve.tensor_tensor(T[:, m, :], T[:, m, :], four(bank(f"{name} dT {l} {c}")), ALU.subtract) \
                           .then_inc(*inverse.vector(f"{name} T {l} {c}"))
                        marks[f"used {name} dT {l} {c}"] = marks[f"{name} T {l} {c}"]

        def inverse_scalar(act, name, U, Y):
            for c in range(2):
                act.wait_ge(*after(f"{name} turn {c}"))
                act.activation(U[:, 4 * c:4 * c + 4, :], four(bank(f"{name} turn {c}")), ACT.Copy) \
                   .then_inc(*inverse.scalar(f"{name} U 0 {c}"))
                marks[f"used {name} turn {c}"] = marks[f"{name} U 0 {c}"]
            for l in range(1, LEVELS):
                for c in range(2):
                    act.wait_ge(*after(f"{name} Y {l} {c}"))
                    act.activation(Y[:, 4 * c:4 * c + 4, :], four(bank(f"{name} Y {l} {c}")), ACT.Copy) \
                       .then_inc(*inverse.scalar(f"used {name} Y {l} {c}"))

        def inverse_pool(pool, name, A, AM):
            for l in range(1, LEVELS):
                if l == 1:
                    pool.wait_ge(*after(f"{name} T 0"))
                else:
                    pool.wait_ge(*after(f"{name} Y {l - 1} 1"))
                pool.tensor_tensor(AM[:, :, :], A[:, :, :], over(table("level")[:, l * P:(l + 1) * P], 8), ALU.mult) \
                    .then_inc(*inverse.pool(f"{name} AM {l}"))

        def inverse_tensor(pe, name, T, U, Y, AM):
            pe.wait_ge(*after(f"{name} T 0"))
            for c in range(2):
                b = open_bank(pe, f"{name} turn {c}")
                for m in range(4):
                    ins = pe.transpose(b[:, m * P:(m + 1) * P], T[:, 4 * c + m, :], ident)
                ins.then_inc(*inverse.tensor(f"{name} turn {c}"))
            for l in range(1, LEVELS):
                pe.wait_ge(*after(f"{name} AM {l}"))
                for c in range(2):
                    pe.wait_ge(*after(f"{name} U {l - 1} {c}"))
                    b = open_bank(pe, f"{name} Y {l} {c}")
                    for m in range(4):
                        ins = pe.matmul(b[:, m * P:(m + 1) * P], AM[:, 4 * c + m, :], U[:, 4 * c + m, :], start=True, stop=True)
                    ins.then_inc(*inverse.tensor(f"{name} Y {l} {c}"))
                for c in range(2):
                    pe.wait_ge(*after(f"used {name} Y {l} {c}"))
                    if l >= 2:
                        pe.wait_ge(*after(f"{name} T {l - 1} {c}"))
                    b = open_bank(pe, f"{name} dU {l} {c}")
                    for m in range(4):
                        ins = pe.matmul(b[:, m * P:(m + 1) * P], T[:, 4 * c + m, :], Y[:, 4 * c + m, :], start=True, stop=True)
                    ins.then_inc(*inverse.tensor(f"{name} dU {l} {c}"))
                    if l < LEVELS - 1:
                        b = open_bank(pe, f"{name} dT {l} {c}")
                        for m in range(4):
                            ins = pe.matmul(b[:, m * P:(m + 1) * P], Y[:, 4 * c + m, :], T[:, 4 * c + m, :], start=True, stop=True)
                        ins.then_inc(*inverse.tensor(f"{name} dT {l} {c}"))

        def rope_vector(dve, stage, x, half, cos, sin, scratch):
            heads = x.shape[1]
            x1, x2 = x[:, :, 0:half], x[:, :, half:2 * half]
            c, s = over(cos, heads), over(sin, heads)
            for i, (a, b) in enumerate(((x1, c), (x2, s), (x1, s), (x2, c))):
                dve.tensor_tensor(scratch[:, i], a, b, ALU.mult).then_inc(*stage.vector())
            dve.wait_ge(*stage.vector.so_far())
            dve.tensor_tensor(x1, scratch[:, 0], scratch[:, 1], ALU.subtract).then_inc(*stage.vector())
            dve.tensor_tensor(x2, scratch[:, 2], scratch[:, 3], ALU.add).then_inc(*stage.vector())
            dve.wait_ge(*stage.vector.so_far())

        with Arena() as take:
            d_A = take("d_A", [P, 8, P])
            d_qk = take("d_qk", [P, 8, P])
            d_Y = take("d_Y", [P, 8, P])
            d_AM = take("d_AM", [P, 8, P])
            d_T = take("d_T", [P, 8, P])
            d_U = take("d_U", [P, 8, P])
            d_k = take("d_k", [P, 8, P])
            d_v = take("d_v", [P, 8, P])
            d_rhs = take("d_rhs", [P, 4, P])
            d_vn = take("d_vn", [P, 4, P])
            d_s1 = take("d_s1", [P, 4, P])
            d_rope = take("d_rope", [P, 4, 8, 32])
            d_small = take("d_small", [P, 12, 8])
            take.beyond_split("d_filler")
            d_pad = take("d_pad", [P, 12, SEQ + 3])
            d_qkv = take("d_qkv", [P, 12, SEQ])
            d_tok = take("d_tok", [P, TT, DELTA_K * COLS])
        d_beta, d_t, d_neg, d_pos, d_e, d_ln, d_ea, d_g, d_gc, d_egc, d_kdec = (d_small[:, i, :] for i in range(11))
        d_sum = d_T.rearrange("p m c -> p (m c)")[:, 0:16]
        d_rms = d_T.rearrange("p m c -> p (m c)")[:, 16:32]
        pad_flat = d_pad.rearrange("p c t -> p (c t)")
        d_st = pad_flat[:, 0:4 * 384].rearrange("p (h c) -> p h c", h=4)
        d_rt = pad_flat[:, 1536:1536 + 1024].rearrange("p (i t) -> p i t", i=4)
        d_square = O.rearrange("p t d -> p (t d)").rearrange("p (c t) -> p c t", t=SEQ)
        d_out_square = d_qkv.rearrange("p c t -> p (c t)")[:, 0:TT * D_MODEL].rearrange("p (t d) -> p t d", t=TT)
        D_KINDS = "t" * DELTA_T + "k" * DELTA_K
        Z, B_, A_, RQ, RV, RG = 0, 512, 516, 520, 1032, 1544

        def d_place(s, j, b):
            if s < DELTA_T:
                return [(d_pad[:, 3 * s + j, 3:3 + SEQ], b[:, 0:SEQ])]
            return [(d_tok[:, j, (s - DELTA_T) * COLS:(s - DELTA_T + 1) * COLS], b[:, 0:COLS])]

        def d_chunk(i, c):
            return d_qkv[:, i, c * P:(c + 1) * P]

        def by_chunk(ap):
            return ap.rearrange("p (c h) -> p c h", c=2)

        def delta_tensor(pe, at):
            g0 = first_step[at]
            proj_tensor(pe, "delta", g0, D_KINDS)
            for q in range(4):
                if q == 0:
                    pe.wait_ge(*after("delta square"))
                b = open_bank(pe, f"delta ss {q}")
                pe.matmul(b, ones, d_square[:, 2 * q:2 * q + 2, :], start=True, stop=True) \
                  .then_inc(*delta.tensor(f"delta ss {q}"))
            pe.wait_ge(*after("delta g"))
            b = open_bank(pe, "delta gcum")
            pe.matmul(b[:, 0:8], table("incl_t"), d_g, start=True, stop=True).then_inc(*delta.tensor("delta gcum"))
            pe.wait_ge(*after("delta g wide"))
            for c in range(2):
                b = open_bank(pe, f"delta grow {c}")
                for h in range(4):
                    ins = pe.matmul(b[:, h * P:(h + 1) * P], d_AM[:, 4 * c + h, :], table("incl_t"), start=True, stop=True)
                ins.then_inc(*delta.tensor(f"delta grow {c}"))
            pe.wait_ge(*after("delta silu v"))
            pe.wait_ge(*after("delta norm 3"))
            for i, name in ((4, "k"), (8, "v")):
                for c in range(2):
                    b = open_bank(pe, f"delta tok {name} {c}")
                    for h in range(4):
                        ins = pe.transpose(b[:, h * P:(h + 1) * P], d_chunk(i + h, c), ident)
                    ins.then_inc(*delta.tensor(f"delta tok {name} {c}"))
            for i, name in ((4, "kk"), (0, "kq")):
                for c in range(2):
                    b = open_bank(pe, f"delta {name} {c}")
                    for h in range(4):
                        ins = pe.matmul(b[:, h * P:(h + 1) * P], d_chunk(4 + h, c), d_chunk(i + h, c), start=True, stop=True)
                    ins.then_inc(*delta.tensor(f"delta {name} {c}"))
            for t in range(TT):
                pe.wait_ge(*after(f"delta rope {t}"))
                b = open_bank(pe, f"delta rt {t}")
                for i in range(4):
                    ins = pe.transpose(b[:, i * P:(i + 1) * P], d_tok[:, t, RQ + i * P:RQ + (i + 1) * P], ident)
                ins.then_inc(*delta.tensor(f"delta rt {t}"))
            for t in range(TT):
                pe.wait_ge(*after(f"used delta rt {t}"))
            for h in range(HEADS):
                q, k = (d_rt[64 * (h % 2):64 * (h % 2) + 64, i + h // 2, :] for i in (0, 2))
                b = open_bank(pe, f"delta rs {h}")
                pe.matmul(b[:, 0:SEQ], k[:, 0:P], q, start=True, stop=True)
                pe.matmul(b[:, SEQ:3 * P], k[:, P:SEQ], q[:, P:SEQ], start=True, stop=True) \
                  .then_inc(*delta.tensor(f"delta rs {h}"))
            pe.wait_ge(*after(f"used delta rs {HEADS - 1}"))
            for t in range(TT):
                b = open_bank(pe, f"delta ro {t}")
                for h in range(HEADS):
                    for j in range(t + 1):
                        first = t * P if j == 0 else SEQ
                        ins = pe.matmul(b[:, h * P:(h + 1) * P], d_st[:, h, first:first + P],
                                        d_tok[:, j, RV + h * P:RV + (h + 1) * P], start=j == 0, stop=j == t)
                ins.then_inc(*delta.tensor(f"delta ro {t}"))
            inverse_tensor(pe, "delta", d_T, d_U, d_Y, d_AM)
            for c in range(2):
                if c == 1:
                    pe.wait_ge(*after("used delta s1"))
                    for i, name in ((4, "ks"), (0, "qs")):
                        b = open_bank(pe, f"delta {name}")
                        for h in range(4):
                            ins = pe.matmul(b[:, h * P:(h + 1) * P], d_chunk(i + h, 1), d_s1[:, h, :], start=True, stop=True)
                        ins.then_inc(*delta.tensor(f"delta {name}"))
                pe.wait_ge(*after(f"delta U {LEVELS - 1} {c}"))
                pe.wait_ge(*after(f"delta rhs {c}"))
                b = open_bank(pe, f"delta vn {c}")
                for h in range(4):
                    ins = pe.matmul(b[:, h * P:(h + 1) * P], d_U[:, 4 * c + h, :], d_rhs[:, h, :], start=True, stop=True)
                ins.then_inc(*delta.tensor(f"delta vn {c}"))
                pe.wait_ge(*after(f"used delta vn {c}"))
                if c == 0:
                    b = open_bank(pe, "delta s1")
                    for h in range(4):
                        ins = pe.matmul(b[:, h * P:(h + 1) * P], d_k[:, h, :], d_vn[:, h, :], start=True, stop=True)
                    ins.then_inc(*delta.tensor("delta s1"))
                b = open_bank(pe, f"delta o {c}")
                for h in range(4):
                    ins = pe.matmul(b[:, h * P:(h + 1) * P], d_qk[:, 4 * c + h, :], d_vn[:, h, :], start=True, stop=True)
                ins.then_inc(*delta.tensor(f"delta o {c}"))
            turn_tensor(pe, "delta", delta, KT, ["delta gated"] * TT)
            out_tensor(pe, "delta", g0 + DELTA_T + DELTA_K)

        def delta_scalar(act, at):
            def does(label, *args, **kw):
                act.activation(*args, **kw).then_inc(*delta.scalar(label))

            proj_copies(act, "delta", first_step[at], D_KINDS, 0, d_place, range(DELTA_T))
            act.wait_ge(*after("delta conv"))
            does("delta silu qk", d_qkv[:, 0:8, :], d_qkv[:, 0:8, :], ACT.Silu)
            does("delta silu v", d_qkv[:, 8:12, :], d_qkv[:, 8:12, :], ACT.Silu)
            act.wait_ge(*after("delta silu qk"))
            does("delta square", d_square, d_qkv[:, 0:8, :], ACT.Square)
            proj_copies(act, "delta", first_step[at], D_KINDS, 0, d_place, range(DELTA_T, DELTA_T + DELTA_K))
            wait_proj(act, "delta", D_KINDS)
            for q in range(4):
                act.wait_ge(*after(f"delta ss {q}"))
                scale, bias = (float(P), two_eps) if q < 2 else (1.0, eps)
                does(f"used delta ss {q}", d_square[:, 2 * q:2 * q + 2, :], bank(f"delta ss {q}").rearrange("p (c t) -> p c t", c=2),
                     ACT.Sqrt, bias=bias, scale=scale)
            does("delta z", d_tok[:, :, Z:Z + 512], d_tok[:, :, Z:Z + 512], ACT.Silu)
            does("delta rg", d_tok[:, :, RG:RG + 512], d_tok[:, :, RG:RG + 512], ACT.Silu)
            does("delta beta", by_chunk(d_beta), d_tok[:, :, B_:B_ + 4], ACT.Sigmoid)
            does("delta ea", d_ea[:, 0:4], row("a_log"), ACT.Exp)
            act.wait_ge(*after("delta neg"))
            does("delta e", d_e, d_neg, ACT.Exp)
            act.wait_ge(*after("delta e"))
            does("delta ln", d_ln, d_e, ACT.Ln, bias=1.0)
            for name, dst in (("k", d_k), ("v", d_v)):
                for c in range(2):
                    act.wait_ge(*after(f"delta tok {name} {c}"))
                    does(f"used delta tok {name} {c}", dst[:, 4 * c:4 * c + 4, :], four(bank(f"delta tok {name} {c}")), ACT.Copy)
            act.wait_ge(*after("delta diff"))
            does("delta D", d_A[:, :, :], d_A[:, :, :], ACT.Exp, scale=-1.0)
            does("delta DT", d_qk[:, :, :], d_qk[:, :, :], ACT.Exp)
            does("delta egc", d_egc, d_gc, ACT.Exp)
            does("delta kdec", d_kdec[:, 0:4], d_Y[:, 0:4, P - 1], ACT.Exp)
            for t in range(TT):
                act.wait_ge(*after(f"delta rt {t}"))
                does(f"used delta rt {t}", d_rt[:, :, t * P:(t + 1) * P], four(bank(f"delta rt {t}")), ACT.Copy)
            for t in range(TT):
                act.wait_ge(*after(f"delta ro {t}"))
                does(f"used delta ro {t}", O[:, t, 512:1024], bank(f"delta ro {t}"), ACT.Copy)
            inverse_scalar(act, "delta", d_U, d_Y)
            for c in range(2):
                act.wait_ge(*after(f"delta vn {c}"))
                does(f"used delta vn {c}", d_vn[:, :, :], four(bank(f"delta vn {c}")), ACT.Copy)
                if c == 0:
                    act.wait_ge(*after("delta s1"))
                    does("used delta s1", d_s1[:, :, :], four(bank("delta s1")), ACT.Copy)
            act.wait_ge(*after("delta o"))
            act.wait_ge(*after("used delta ro 1"))
            does("delta o square", d_out_square, O[:, :, :], ACT.Square)
            act.wait_ge(*after("delta o sum"))
            does("delta o root", d_rms, d_sum, ACT.Sqrt, scale=1.0 / P, bias=eps)
            out_scalar(act, at, "delta", "delta gated", delta)

        def delta_pool(pool, at):
            proj_pool(pool, first_step[at], len(D_KINDS))
            inverse_pool(pool, "delta", d_A, d_AM)
            out_pool(pool, at)

        def delta_vector(dve, at):
            def does(label, op, *args, wait=None):
                op(*args).then_inc(*delta.vector(label))

            def settle():
                dve.wait_ge(*delta.vector.so_far())

            does("delta pad", dve.memset, d_pad[:, :, 0:3], 0.0)
            proj_copies(dve, "delta", first_step[at], D_KINDS, 1, d_place, range(DELTA_T))
            wait_proj(dve, "delta", D_KINDS, range(DELTA_T))
            settle()
            conv = col("conv")
            for j in range(4):
                for c in range(12):
                    w, x = conv[:, 12 * j + c:12 * j + c + 1], d_pad[:, c, j:j + SEQ]
                    if j == 0:
                        does(None, dve.tensor_scalar, d_qkv[:, c, :], x, w, None, ALU.mult)
                    else:
                        does("delta conv", dve.scalar_tensor_tensor, d_qkv[:, c, :], x, w, d_qkv[:, c, :], ALU.mult, ALU.add)
                settle()
            proj_copies(dve, "delta", first_step[at], D_KINDS, 1, d_place, range(DELTA_T, DELTA_T + DELTA_K))
            wait_proj(dve, "delta", D_KINDS)
            does(None, dve.tensor_tensor, by_chunk(d_t), d_tok[:, :, A_:A_ + 4], over(row("dt_bias"), 2), ALU.add)
            settle()
            does(None, dve.tensor_scalar, d_pos, d_t, 0.0, None, ALU.max)
            does(None, dve.tensor_scalar, d_neg, d_t, 0.0, None, ALU.min)
            settle()
            does("delta neg", dve.tensor_tensor, d_neg, d_neg, d_pos, ALU.subtract)
            for q in range(4):
                dve.wait_ge(*after(f"used delta ss {q}"))
                qk = d_qkv[:, 2 * q:2 * q + 2, :]
                does(None, dve.reciprocal, d_square[:, 2 * q:2 * q + 2, :], d_square[:, 2 * q:2 * q + 2, :])
                settle()
                does(f"delta norm {q}", dve.tensor_tensor, qk, qk, d_square[:, 2 * q:2 * q + 2, :], ALU.mult)
            dve.wait_ge(*after("delta ln"))
            does(None, dve.tensor_tensor, d_t, d_pos, d_ln, ALU.add)
            settle()
            does("delta g", dve.scalar_tensor_tensor, by_chunk(d_g), by_chunk(d_t), -1.0, over(d_ea[:, 0:4], 2), ALU.mult, ALU.mult)
            settle()
            does("delta g wide", dve.tensor_copy, d_AM[:, :, :], wide(d_g, P))
            dve.wait_ge(*after("delta gcum"))
            does("used delta gcum", dve.tensor_copy, d_gc, bank("delta gcum")[:, 0:8])
            settle()
            for c in range(2):
                dve.wait_ge(*after(f"delta grow {c}"))
                does(f"used delta grow {c}", dve.tensor_tensor, d_Y[:, 4 * c:4 * c + 4, :], four(bank(f"delta grow {c}")),
                     wide(d_gc[:, 4 * c:4 * c + 4], P), ALU.subtract)
            settle()
            does(None, dve.tensor_scalar, d_A[:, :, :], d_Y[:, :, :], 0.0, None, ALU.max)
            does("delta diff", dve.tensor_scalar, d_qk[:, :, :], d_Y[:, :, :], 0.0, None, ALU.min)
            for t in range(TT):
                rope_vector(dve, delta, d_tok[:, t, RQ:RQ + 512].rearrange("p (h d) -> p h d", d=64), 32,
                            table("cos32")[:, 32 * t:32 * t + 32], table("sin32")[:, 32 * t:32 * t + 32], d_rope)
                marks[f"delta rope {t}"] = (delta.vector.name, delta.vector.n)
            dve.wait_ge(*after("delta kdec"))
            does(None, dve.tensor_tensor, d_A[:, :, :], d_A[:, :, :], over(table("strict"), 8), ALU.mult)
            does(None, dve.tensor_tensor, d_qk[:, :, :], d_qk[:, :, :], over(table("incl_t"), 8), ALU.mult)
            settle()
            does(None, dve.tensor_tensor, d_A[:, :, :], d_A[:, :, :], wide(d_beta, P), ALU.mult)
            settle()
            for name, dst in (("kk", d_A), ("kq", d_qk)):
                for c in range(2):
                    dve.wait_ge(*after(f"delta {name} {c}"))
                    m = dst[:, 4 * c:4 * c + 4, :]
                    does(f"used delta {name} {c}", dve.tensor_tensor, m, m, four(bank(f"delta {name} {c}")), ALU.mult)
            for h in range(HEADS):
                dve.wait_ge(*after(f"delta rs {h}"))
                does(f"used delta rs {h}", dve.tensor_tensor, d_st[:, h, :], bank(f"delta rs {h}")[:, 0:3 * P],
                     table("ret")[:, 3 * P * h:3 * P * (h + 1)], ALU.mult)
            settle()
            dve.wait_ge(*after("used delta tok v 1"))
            does("delta rhs 0", dve.tensor_tensor, d_rhs[:, :, :], d_v[:, 0:4, :], wide(d_beta[:, 0:4], P), ALU.mult)
            does("delta k decayed", dve.tensor_tensor, d_k[:, 0:4, :], d_k[:, 0:4, :], wide(d_kdec[:, 0:4], P), ALU.mult)
            inverse_vector(dve, "delta", d_A, d_T, d_U, d_AM)
            dve.wait_ge(*after("delta ks"))
            does("used delta ks", dve.tensor_tensor, d_rhs[:, :, :], four(bank("delta ks")), wide(d_egc[:, 4:8], P), ALU.mult)
            settle()
            does(None, dve.tensor_tensor, d_rhs[:, :, :], d_v[:, 4:8, :], d_rhs[:, :, :], ALU.subtract)
            settle()
            does("delta rhs 1", dve.tensor_tensor, d_rhs[:, :, :], d_rhs[:, :, :], wide(d_beta[:, 4:8], P), ALU.mult)
            dve.wait_ge(*after("delta o 0"))
            does("used delta o 0", dve.tensor_copy, O[:, 0, 0:512], bank("delta o 0"))
            dve.wait_ge(*after("delta qs"))
            does("used delta qs", dve.tensor_tensor, four(O[:, 1, 0:512]), four(bank("delta qs")), wide(d_egc[:, 4:8], P), ALU.mult)
            settle()
            dve.wait_ge(*after("delta o 1"))
            does("delta o", dve.tensor_tensor, O[:, 1, 0:512], O[:, 1, 0:512], bank("delta o 1"), ALU.add)
            marks["used delta o 1"] = marks["delta o"]
            dve.wait_ge(*after("delta o square"))
            does("delta o sum", dve.tensor_reduce, d_sum, d_out_square.rearrange("p t (h d) -> p (t h) d", d=P), AX.X, ALU.add)
            dve.wait_ge(*after("delta o root"))
            does(None, dve.reciprocal, d_rms, d_rms)
            settle()
            heads = O.rearrange("p t (h d) -> p (t h) d", d=P)
            does(None, dve.tensor_tensor, heads, heads, wide(d_rms, P), ALU.mult)
            settle()
            for t in range(TT):
                does(None, dve.tensor_tensor, four(O[:, t, 0:512]), four(O[:, t, 0:512]), over(row("gdn_norm"), 4), ALU.mult)
            settle()
            dve.wait_ge(*after("delta rg"))
            does(None, dve.tensor_tensor, O[:, :, 0:512], O[:, :, 0:512], d_tok[:, :, Z:Z + 512], ALU.mult)
            does("delta gated", dve.tensor_tensor, O[:, :, 512:1024], O[:, :, 512:1024], d_tok[:, :, RG:RG + 512], ALU.mult)
            out_turn_vector(dve, "delta", at, delta)

        UNIT = 3 * P

        def blocks(ap):
            return ap.rearrange("p u (b c) -> p (u b) c", c=P)

        def softmax_head_vector(dve, stage, name, S, units, scale, bias, small):
            for i, u in enumerate(units):
                dve.wait_ge(*after(f"{u}"))
                dve.scalar_tensor_tensor(S[:, i, :], bank(u)[:, 0:UNIT], scale, bias, ALU.mult, ALU.add) \
                   .then_inc(*stage.vector(f"used {u}"))
            dve.wait_ge(*stage.vector.so_far())
            dve.tensor_reduce(small.rearrange("p u b -> p (u b)"), blocks(S), AX.X, ALU.max).then_inc(*stage.vector())
            dve.wait_ge(*stage.vector.so_far())
            dve.tensor_tensor(small[:, :, 1], small[:, :, 1], small[:, :, 2], ALU.max).then_inc(*stage.vector())
            dve.wait_ge(*stage.vector.so_far())
            dve.tensor_copy(small[:, :, 2], small[:, :, 1]).then_inc(*stage.vector())
            dve.wait_ge(*stage.vector.so_far())
            dve.tensor_tensor(blocks(S), blocks(S), wide(small.rearrange("p u b -> p (u b)"), P), ALU.subtract) \
               .then_inc(*stage.vector(f"{name} less max"))

        def softmax_scalar(act, stage, name, S):
            act.wait_ge(*after(f"{name} less max"))
            act.activation(S, S, ACT.Exp).then_inc(*stage.scalar(f"{name} exp"))

        def softmax_tail_vector(dve, stage, name, S, small, count=None):
            dve.wait_ge(*after(f"{name} exp"))
            if count is not None:
                dve.tensor_tensor(S, S, over(count, 4), ALU.mult).then_inc(*stage.vector())
                dve.wait_ge(*stage.vector.so_far())
            dve.tensor_reduce(small.rearrange("p u b -> p (u b)"), blocks(S), AX.X, ALU.add).then_inc(*stage.vector())
            dve.wait_ge(*stage.vector.so_far())
            dve.tensor_tensor(small[:, :, 1], small[:, :, 1], small[:, :, 2], ALU.add).then_inc(*stage.vector())
            dve.wait_ge(*stage.vector.so_far())
            dve.tensor_copy(small[:, :, 2], small[:, :, 1]).then_inc(*stage.vector())
            dve.wait_ge(*stage.vector.so_far())
            dve.reciprocal(small, small).then_inc(*stage.vector())
            dve.wait_ge(*stage.vector.so_far())

        def scores_tensor(pe, stage, label, q, k):
            b = open_bank(pe, label)
            pe.matmul(b[:, 0:P], q[:, 0:P], k[:, 0:P], start=True, stop=True)
            pe.matmul(b[:, P:UNIT], q[:, P:SEQ], k, start=True, stop=True).then_inc(*stage.tensor(label))

        def turn_unit_tensor(pe, stage, label, s):
            b = open_bank(pe, label)
            for j in range(3):
                ins = pe.transpose(b[:, j * P:(j + 1) * P], s[:, j * P:(j + 1) * P], ident)
            ins.then_inc(*stage.tensor(label))

        def unit_blocks(s, t):
            return [s[:, 0:P]] if t == 0 else [s[:, P:2 * P], s[:, 2 * P:UNIT]]

        with Arena() as take:
            a_T = take("a_T", [P, 16, SEQ])
            a_S = take("a_S", [P, 12, UNIT])
            a_rope = take("a_rope", [P, 4 * 8 * 64])
            a_max = take("a_max", [P, 12, 3])
            a_sum = take("a_sum", [P, 12, 3])
            take.beyond_split("a_filler")
            a_tok = take("a_tok", [P, TT, ATT_K * COLS])
            a_lam = take("a_lam", [P, 2, 64])
            a_small = take("a_small", [P, 32])
        A_KINDS = "k" * ATT_K
        CV, DV = 1024, 2560
        GROUPS = {0: 0, 1: 512, 2: 1536, 3: 2048}
        A_GROUPS = [[f"attn s {u}" for u in range(4 * i, 4 * i + 4)] for i in range(3)]

        def a_place(s, j, b):
            return [(a_tok[:, j, s * COLS:(s + 1) * COLS], b[:, 0:COLS])]

        def attention_tensor(pe, at):
            g0 = first_step[at]
            proj_tensor(pe, "attn", g0, A_KINDS)
            for t in range(TT):
                for i, c0 in GROUPS.items():
                    pe.wait_ge(*after(f"attn rope {t} {i // 2}"))
                    b = open_bank(pe, f"attn turned {t} {i}")
                    for h in range(4):
                        ins = pe.transpose(b[:, h * P:(h + 1) * P], a_tok[:, t, c0 + h * P:c0 + (h + 1) * P], ident)
                    ins.then_inc(*attn.tensor(f"attn turned {t} {i}"))
            pe.wait_ge(*after(f"used attn turned {TT - 1} 3"))
            for h in range(HEADS):
                scores_tensor(pe, attn, f"attn s {h}", a_T[:, h, :], a_T[:, 4 + h, :])
            for h in range(HEADS):
                for half in range(2):
                    rows_ = slice(64 * half, 64 * half + 64)
                    scores_tensor(pe, attn, f"attn s {4 + 2 * h + half}", a_T[rows_, 8 + h, :], a_T[rows_, 12 + h, :])
            for i, u in enumerate([0, 1, 2, 3, 4, 6, 8, 10]):
                pe.wait_ge(*after("attn p dil" if u < 4 else f"attn p diff {(u - 4) // 4}"))
                turn_unit_tensor(pe, attn, f"attn pt {u}", a_S[:, u, :])
            for side, (units, v0) in enumerate((([0, 1, 2, 3], CV), ([4, 6, 8, 10], DV))):
                pe.wait_ge(*after(f"used attn pt {units[-1]}"))
                for t in range(TT):
                    b = open_bank(pe, f"attn o {side} {t}")
                    for h, u in enumerate(units):
                        for j, s in enumerate(unit_blocks(a_S[:, u, :], t)):
                            ins = pe.matmul(b[:, h * P:(h + 1) * P], s, a_tok[:, j, v0 + h * P:v0 + (h + 1) * P],
                                            start=j == 0, stop=j == t)
                    ins.then_inc(*attn.tensor(f"attn o {side} {t}"))
            turn_tensor(pe, "attn", attn, KT, ["attn normed"] * TT)
            out_tensor(pe, "attn", g0 + ATT_K)

        def attention_scalar(act, at):
            def does(label, *args, **kw):
                act.activation(*args, **kw).then_inc(*attn.scalar(label))

            proj_copies(act, "attn", first_step[at], A_KINDS, 0, a_place)
            act.wait_ge(*after("attn lam sums"))
            does("attn lam exp", a_small[:, 2:4], a_small[:, 0:2], ACT.Exp)
            for t in range(TT):
                for i in GROUPS:
                    act.wait_ge(*after(f"attn turned {t} {i}"))
                    does(f"used attn turned {t} {i}", a_T[:, 4 * i:4 * i + 4, t * P:(t + 1) * P], four(bank(f"attn turned {t} {i}")), ACT.Copy)
            for i in range(3):
                softmax_scalar(act, attn, f"attn {i}", a_S[:, 4 * i:4 * i + 4, :])
            for u in (0, 1, 2, 3, 4, 6, 8, 10):
                act.wait_ge(*after(f"attn pt {u}"))
                does(f"used attn pt {u}", a_S[:, u, :], bank(f"attn pt {u}")[:, 0:UNIT], ACT.Copy)
            for side in range(2):
                for t in range(TT):
                    act.wait_ge(*after(f"attn o {side} {t}"))
                    does(f"used attn o {side} {t}", O[:, t, 512 * side:512 * side + 512], bank(f"attn o {side} {t}"), ACT.Copy)
            act.wait_ge(*after("used attn o 1 1"))
            does("attn square", a_T[:, 0:4, :].rearrange("p h t -> p (h t)").rearrange("p (t d) -> p t d", t=TT), O[:, :, 512:1024], ACT.Square)
            act.wait_ge(*after("attn square sum"))
            does("attn root", a_small[:, 16:24], a_small[:, 8:16], ACT.Sqrt, scale=1.0 / P, bias=eps)
            out_scalar(act, at, "attn", "attn normed", attn)

        def attention_pool(pool, at):
            proj_pool(pool, first_step[at], ATT_K)
            out_pool(pool, at)

        def attention_vector(dve, at):
            def does(label, op, *args):
                op(*args).then_inc(*attn.vector(label))

            def settle():
                dve.wait_ge(*attn.vector.so_far())

            for i in range(2):
                does(None, dve.tensor_tensor, a_lam[:, i, :], row(f"lq{i + 1}"), row(f"lk{i + 1}"), ALU.mult)
            settle()
            does("attn lam sums", dve.tensor_reduce, a_small[:, 0:2], a_lam[:, :, :], AX.X, ALU.add)
            proj_copies(dve, "attn", first_step[at], A_KINDS, 1, a_place)
            wait_proj(dve, "attn", A_KINDS)
            for t in range(TT):
                for i, (c0, dim) in enumerate(((0, 128), (1536, 64))):
                    half = dim // 2
                    rope_vector(dve, attn, a_tok[:, t, c0:c0 + 1024].rearrange("p (h d) -> p h d", d=dim), half,
                                table(f"cos{half}")[:, half * t:half * t + half], table(f"sin{half}")[:, half * t:half * t + half],
                                a_rope.rearrange("p (i h c) -> p i h c", i=4, c=half))
                    marks[f"attn rope {t} {i}"] = (attn.vector.name, attn.vector.n)
            dve.wait_ge(*after("attn lam exp"))
            does(None, dve.tensor_tensor, a_small[:, 4:5], a_small[:, 3:4], a_small[:, 2:3], ALU.subtract)
            settle()
            does(None, dve.tensor_scalar, a_small[:, 5:6], a_small[:, 4:5], -LAMBDA_INIT, None, ALU.add)
            for i, units in enumerate(A_GROUPS):
                softmax_head_vector(dve, attn, f"attn {i}", a_S[:, 4 * i:4 * i + 4, :], units, (128 if i == 0 else 64) ** -0.5,
                                    table("bias_dil" if i == 0 else "bias"), a_max[:, 4 * i:4 * i + 4, :])
            for i in range(3):
                S, r = a_S[:, 4 * i:4 * i + 4, :], a_sum[:, 4 * i:4 * i + 4, :]
                softmax_tail_vector(dve, attn, f"attn {i}", S, r, table("count") if i == 0 else None)
                if i > 0:
                    pair = r.rearrange("p (h two) b -> p h two b", two=2)[:, :, 1, :]
                    does(None, dve.tensor_scalar, pair, pair, a_small[:, 5:6], None, ALU.mult)
                    settle()
                does("attn p dil" if i == 0 else None, dve.tensor_tensor, blocks(S), blocks(S), wide(r.rearrange("p u b -> p (u b)"), P), ALU.mult)
                if i > 0:
                    settle()
                    halves = S.rearrange("p (h two) c -> p h two c", two=2)
                    does(f"attn p diff {i - 1}", dve.tensor_tensor, halves[:, :, 0, :], halves[:, :, 0, :], halves[:, :, 1, :], ALU.add)
            dve.wait_ge(*after("attn square"))
            does("attn square sum", dve.tensor_reduce, a_small[:, 8:16], a_T[:, 0:4, :].rearrange("p h t -> p (h t)").rearrange("p (h d) -> p h d", d=P),
                 AX.X, ALU.add)
            dve.wait_ge(*after("attn root"))
            does(None, dve.reciprocal, a_small[:, 24:32], a_small[:, 16:24])
            settle()
            for t in range(TT):
                heads = four(O[:, t, 512:1024])
                does(None, dve.tensor_tensor, heads, heads, wide(a_small[:, 24 + 4 * t:28 + 4 * t], P), ALU.mult)
                settle()
                does("attn normed", dve.scalar_tensor_tensor, heads, heads, 1.0 - LAMBDA_INIT, over(row("diff_norm"), 4), ALU.mult, ALU.mult)
            out_turn_vector(dve, "attn", at, attn)

        SLOTS8 = 8
        with Arena() as take:
            n_S = take("n_S", [P, 16, UNIT])
            n_qn, n_qr = (take(f"n_{i}", [P, 4, SEQ]) for i in ("qn", "qr"))
            n_kt = take("n_kt", [P, 2, SEQ])
            n_vcmp = take("n_vcmp", [P, SLOTS8, 64])
            n_sc = take("n_sc", [P, TT, SLOTS8, CMP_PAD])
            n_pct = take("n_pct", [P, TT, P])
            n_max, n_sum = (take(f"n_{i}", [P, 16, 3]) for i in ("max", "sum"))
            n_cs = take("n_cs", [P, 2, 16])
            n_kcmp = take("n_kcmp", [P, CMP_PAD])
            take.beyond_split("n_filler")
            n_tok = take("n_tok", [P, TT, SPARSE_K * COLS])
            n_z = [take(f"n_z{i}", [P, 2, SEQ]) for i in range(2)]
            n_bg, n_cg, n_hd = (take(f"n_{i}", [P, 4, SEQ]) for i in ("bg", "cg", "hd"))
            n_pad = take("n_pad", [P, 4, SEQ + 2])
            n_zb = [take(f"n_zb{i}", [P, 16, 2, CMP_PAD]) for i in range(2)]
            n_zb_hi, n_zb_lo = ([take(f"n_zb_{n}{i}", [P, 16, 2, CMP_PAD], F32R) for i in range(2)] for n in ("hi", "lo"))
            n_hid = [take(f"n_hid{i}", [P, 2, 2 * CMP_PAD]) for i in range(2)]
            n_hv = take("n_hv", [P, 2, 4, 2 * CMP_PAD])
            n_gate = take("n_gate", [P, TT, 3, SLOTS8])
            n_rope = take("n_rope", [P, 4, 8, 8])
        N_KINDS = "k" * SPARSE_K + "t" * (SPARSE_T - 1) + "u"
        KS, VS, KW, VW, GL = 512, 640, 768, 896, 1024
        N_GROUPS = [[f"sparse s {u}" for u in range(4 * i, 4 * i + 4)] for i in range(4)]

        def n_place(s, j, b):
            if s < SPARSE_K:
                return [(n_tok[:, j, s * COLS:(s + 1) * COLS], b[:, 0:COLS])]
            c = 3 * (s - SPARSE_K) + j
            if c < 4:
                z = n_z[c // 2]
                return [(z[0:64, c % 2, :], b[0:64, 0:SEQ]), (z[64:P, c % 2, 0:SEQ - 1], b[64:P, 1:SEQ])]
            return [((n_bg, n_cg, n_hd)[c // 4 - 1][:, c % 4, :], b[:, 0:SEQ])]

        def slot_rows(s):
            return slice(64 * (s % 2), 64 * (s % 2) + 64)

        def sparse_tensor(pe, at):
            g0 = first_step[at]
            proj_tensor(pe, "sparse", g0, N_KINDS)
            for s in range(SPARSE_C):
                g = g0 + SPARSE_K + SPARSE_T + s
                wait_split(pe, g)
                w = [x[:, g % 2, :].rearrange("p (q c) -> p q c", q=12) for x in (w_hi, w_lo)]
                for block_ in range(12 * s, min(12 * s + 12, 32)):
                    which, l = divmod(block_, 16)
                    if l == 0:
                        pe.wait_ge(*after(f"sparse zb {which}"))
                        hidden = [open_bank(pe, f"sparse hid {which} {i}") for i in range(2)]
                    for i in range(2):
                        ins = three_passes(pe, hidden[i][:, 0:2 * CMP_PAD], [x[:, block_ % 12, i * P:(i + 1) * P] for x in w],
                                           [x[which][:, l, :, :].rearrange("p h n -> p (h n)") for x in (n_zb_hi, n_zb_lo)], l == 0, l == 15)
                        if l == 15 or (block_ % 12 == 11 and i == 1):
                            ins.then_inc(*sparse.tensor(f"sparse hid {which} {i}" if l == 15 else f"sparse c {s} last"))
                if s == SPARSE_C - 1:
                    marks[f"sparse c {s} last"] = marks["sparse hid 1 1"]
                release(pe, "sparse c", s)
            for t in range(TT):
                if t == 0:
                    for j in (0, 1):
                        pe.wait_ge(*after(f"used sparse 0 {j}"))
                        pe.wait_ge(*after(f"used sparse 1 {j}"))
                b = open_bank(pe, f"sparse qn {t}")
                for i in range(4):
                    ins = pe.transpose(b[:, i * P:(i + 1) * P], n_tok[:, t, i * P:(i + 1) * P], ident)
                ins.then_inc(*sparse.tensor(f"sparse qn {t}"))
            for t in range(TT):
                pe.wait_ge(*after(f"sparse rope {t}"))
                b = open_bank(pe, f"sparse qr {t}")
                for i in range(4):
                    ins = pe.transpose(b[:, i * P:(i + 1) * P], n_tok[:, t, i * P:(i + 1) * P], ident)
                ins.then_inc(*sparse.tensor(f"sparse qr {t}"))
                b = open_bank(pe, f"sparse kt {t}")
                for i, c0 in enumerate((KS, KW)):
                    ins = pe.transpose(b[:, i * P:(i + 1) * P], n_tok[:, t, c0:c0 + P], ident)
                ins.then_inc(*sparse.tensor(f"sparse kt {t}"))
            pe.wait_ge(*after("used sparse kt 1"))
            for br in range(2):
                for s in range(SLOTS8):
                    scores_tensor(pe, sparse, f"sparse s {8 * br + s}", n_qr[slot_rows(s), s // 2, :], n_kt[slot_rows(s), br, :])
            pe.wait_ge(*after("used sparse hid 0 1"))
            b = open_bank(pe, "sparse kcmp")
            for kv in range(2):
                for i in range(2):
                    ins = pe.matmul(b[64 * kv:64 * kv + 64, 0:CMP_PAD], col("cmp_k2")[:, 64 * i:64 * i + 64],
                                    n_hid[0][:, i, kv * CMP_PAD:(kv + 1) * CMP_PAD], start=i == 0, stop=i == 1)
            ins.then_inc(*sparse.tensor("sparse kcmp"))
            pe.wait_ge(*after("sparse hv"))
            b = open_bank(pe, "sparse vcmp")
            for i in range(2):
                ins = pe.matmul(b[:, 0:64], n_hv[:, i, :, :].rearrange("p j n -> p (j n)"), col("cmp_v2")[:, 64 * i:64 * i + 64],
                                start=i == 0, stop=i == 1)
            ins.then_inc(*sparse.tensor("sparse vcmp"))
            pe.wait_ge(*after("used sparse kcmp"))
            for par in range(2):
                b = open_bank(pe, f"sparse cs {par}")
                for t in range(TT):
                    for j in range(4):
                        c0 = (4 * t + j) * CMP_PAD
                        ins = pe.matmul(b[:, c0:c0 + CMP_PAD], n_qn[slot_rows(par), j, t * P:(t + 1) * P], n_kcmp[slot_rows(par), :],
                                        start=True, stop=True)
                ins.then_inc(*sparse.tensor(f"sparse cs {par}"))
            for i in range(4):
                pe.wait_ge(*after(f"sparse p {i}"))
                for u in range(4 * i, 4 * i + 4):
                    turn_unit_tensor(pe, sparse, f"sparse pt {u}", n_S[:, u, :])
            pe.wait_ge(*after("sparse pc"))
            for t in range(TT):
                b = open_bank(pe, f"sparse pct {t}")
                pe.transpose(b[:, 0:P], n_sc[:, t, :, :].rearrange("p s n -> p (s n)"), ident).then_inc(*sparse.tensor(f"sparse pct {t}"))
            pe.wait_ge(*after("used sparse vcmp"))
            pe.wait_ge(*after("used sparse pct 1"))
            for t in range(TT):
                b = open_bank(pe, f"sparse o {t}")
                pe.matmul(b, n_pct[:, t, :], n_vcmp.rearrange("p s d -> p (s d)"), start=True, stop=False)
                for br, v0 in enumerate((VS, VW)):
                    for s in range(SLOTS8):
                        for j, pt in enumerate(unit_blocks(n_S[:, 8 * br + s, :], t)):
                            v = n_tok[:, j, v0 + 64 * (s % 2):v0 + 64 * (s % 2) + 64]
                            ins = pe.matmul(b[:, 64 * s:64 * s + 64], pt, v, start=False,
                                            stop=br == 1 and s == SLOTS8 - 1 and j == t)
                ins.then_inc(*sparse.tensor(f"sparse o {t}"))
            turn_tensor(pe, "sparse", sparse, 4, [f"used sparse o {t}" for t in range(TT)])
            pe.wait_ge(*after("sparse conv"))
            out_tensor(pe, "sparse", g0 + SPARSE_K + SPARSE_T + SPARSE_C, 4)

        def sparse_scalar(act, at):
            def does(label, *args, **kw):
                act.activation(*args, **kw).then_inc(*sparse.scalar(label))

            proj_copies(act, "sparse", first_step[at], N_KINDS, 0, n_place, ahead=True)
            c0 = first_step[at] + len(N_KINDS)
            for g in range(c0 + 1, c0 + SPARSE_C):
                split_hi(act, g, g)
            for which in range(2):
                for i in range(2):
                    act.wait_ge(*after(f"sparse hid {which} {i}"))
                    does(f"used sparse hid {which} {i}", n_hid[which][:, i, :], bank(f"sparse hid {which} {i}")[:, 0:2 * CMP_PAD],
                         ACT.Gelu_apprx_tanh)
            wait_proj(act, "sparse", N_KINDS, range(SPARSE_K))
            gl = n_tok[:, :, GL:GL + 24]
            does("sparse gate", n_gate.rearrange("p t b s -> p t (b s)"), gl, ACT.Sigmoid)
            for t in range(TT):
                act.wait_ge(*after(f"sparse qn {t}"))
                does(f"used sparse qn {t}", n_qn[:, :, t * P:(t + 1) * P], four(bank(f"sparse qn {t}")), ACT.Copy)
            for t in range(TT):
                act.wait_ge(*after(f"sparse qr {t}"))
                does(f"used sparse qr {t}", n_qr[:, :, t * P:(t + 1) * P], four(bank(f"sparse qr {t}")), ACT.Copy)
                act.wait_ge(*after(f"sparse kt {t}"))
                does(f"used sparse kt {t}", n_kt[:, :, t * P:(t + 1) * P],
                     bank(f"sparse kt {t}")[:, 0:2 * P].rearrange("p (i c) -> p i c", i=2), ACT.Copy)
            act.wait_ge(*after("sparse kcmp"))
            does("used sparse kcmp", n_kcmp[:, :], bank("sparse kcmp")[:, 0:CMP_PAD], ACT.Copy)
            for i in range(4):
                softmax_scalar(act, sparse, f"sparse {i}", n_S[:, 4 * i:4 * i + 4, :])
            act.wait_ge(*after("sparse c less max"))
            does("sparse c exp", n_sc[:, :, :, :], n_sc[:, :, :, :], ACT.Exp)
            for u in range(16):
                act.wait_ge(*after(f"sparse pt {u}"))
                does(f"used sparse pt {u}", n_S[:, u, :], bank(f"sparse pt {u}")[:, 0:UNIT], ACT.Copy)
            for t in range(TT):
                act.wait_ge(*after(f"sparse pct {t}"))
                does(f"used sparse pct {t}", n_pct[:, t, :], bank(f"sparse pct {t}")[:, 0:P], ACT.Copy)
            for t in range(TT):
                act.wait_ge(*after(f"sparse o {t}"))
                does(f"used sparse o {t}", O[:, t, 0:512], bank(f"sparse o {t}"), ACT.Copy)
            out_scalar(act, at, "sparse", "used sparse o 1", sparse, 4)

        def sparse_pool(pool, at):
            proj_pool(pool, first_step[at], len(N_KINDS) + SPARSE_C)
            out_pool(pool, at)

        def sparse_vector(dve, at):
            def does(label, op, *args):
                op(*args).then_inc(*sparse.vector(label))

            def settle():
                dve.wait_ge(*sparse.vector.so_far())

            does(None, dve.memset, n_pad[:, :, 0:2], 0.0)
            for which in range(2):
                does(None, dve.memset, n_zb[which][:, :, :, :], 0.0)
            proj_copies(dve, "sparse", first_step[at], N_KINDS, 1, n_place, ahead=True)
            wait_proj(dve, "sparse", N_KINDS)
            settle()
            for which, pos in enumerate(("pos_k", "pos_v")):
                for kv in range(2):
                    z = n_z[which][:, kv, :].rearrange("p (n b two) -> p b n two", b=8, two=2)
                    for a in range(2):
                        does(None, dve.tensor_tensor, n_zb[which][:, 8 * a:8 * a + 8, kv, 0:CMP_N],
                             z[:, :, a:a + CMP_N, 0], wide(col(pos)[:, 8 * a:8 * a + 8], CMP_N), ALU.add)
            settle()
            for which in range(2):
                does(None, dve.tensor_copy, n_zb_hi[which][:, :, :, :], n_zb[which][:, :, :, :])
            settle()
            for which in range(2):
                does(f"sparse zb {which}", dve.tensor_tensor, n_zb_lo[which][:, :, :, :], n_zb[which][:, :, :, :],
                     n_zb_hi[which][:, :, :, :].bitcast(F32), ALU.subtract)
            c0 = first_step[at] + len(N_KINDS)
            for g in range(c0 + 1, c0 + SPARSE_C):
                split_lo(dve, g, g)
            for t in range(TT):
                dve.wait_ge(*after(f"sparse qn {t}"))
                for c0, heads in ((0, 8), (KS, 2), (KW, 2)):
                    rope_vector(dve, sparse, n_tok[:, t, c0:c0 + 64 * heads].rearrange("p (h d) -> p h d", d=64), 8,
                                table("cos8")[:, 8 * t:8 * t + 8], table("sin8")[:, 8 * t:8 * t + 8], n_rope[:, :, 0:heads, :])
                marks[f"sparse rope {t}"] = (sparse.vector.name, sparse.vector.n)
            does(None, dve.tensor_tensor, n_pad[:, :, 2:2 + SEQ], n_cg[:, :, :], n_hd[:, :, :], ALU.mult)
            settle()
            for j in range(3):
                for c in range(4):
                    w, x = col("conv3")[:, 4 * j + c:4 * j + c + 1], n_pad[:, c, j:j + SEQ]
                    if j == 0:
                        does(None, dve.tensor_scalar, n_cg[:, c, :], x, w, None, ALU.mult)
                    else:
                        does(None, dve.scalar_tensor_tensor, n_cg[:, c, :], x, w, n_cg[:, c, :], ALU.mult, ALU.add)
                settle()
            does(None, dve.tensor_tensor, n_cg[:, :, :], n_cg[:, :, :], n_bg[:, :, :], ALU.mult)
            settle()
            does(None, dve.tensor_copy, hT_hi[:, 4:8, :], n_cg[:, :, :])
            settle()
            does("sparse conv", dve.tensor_tensor, hT_lo[:, 4:8, :], n_cg[:, :, :], hT_hi[:, 4:8, :].bitcast(F32), ALU.subtract)
            for i, units in enumerate(N_GROUPS):
                softmax_head_vector(dve, sparse, f"sparse {i}", n_S[:, 4 * i:4 * i + 4, :], units, 64 ** -0.5, table("bias"),
                                    n_max[:, 4 * i:4 * i + 4, :])
            for i in range(2):
                dve.wait_ge(*after(f"used sparse hid 1 {i}"))
                does("sparse hv", dve.tensor_copy, n_hv[:, i, :, :], over(n_hid[1][:, i, :], 4))
            dve.wait_ge(*after("sparse vcmp"))
            does("used sparse vcmp", dve.tensor_tensor, n_vcmp[:, :, :], over(bank("sparse vcmp")[:, 0:64], 8), wide(table("cmp_block"), 64), ALU.mult)
            by_parity = n_sc.rearrange("p t (j two) n -> p t j two n", two=2)
            for par in range(2):
                dve.wait_ge(*after(f"sparse cs {par}"))
                for t in range(TT):
                    src = bank(f"sparse cs {par}")[:, 64 * t:64 * t + 64].rearrange("p (j n) -> p j n", j=4)
                    does(f"used sparse cs {par}", dve.scalar_tensor_tensor, by_parity[:, t, :, par, :], src, 64 ** -0.5,
                         over(table("cmp_bias")[:, CMP_PAD * t:CMP_PAD * (t + 1)], 4), ALU.mult, ALU.add)
            settle()
            sc = n_sc.rearrange("p t s n -> p (t s) n")
            does(None, dve.tensor_reduce, n_cs[:, 0, :], sc, AX.X, ALU.max)
            settle()
            does("sparse c less max", dve.tensor_tensor, sc, sc, wide(n_cs[:, 0, :], CMP_PAD), ALU.subtract)
            for i in range(4):
                S, r = n_S[:, 4 * i:4 * i + 4, :], n_sum[:, 4 * i:4 * i + 4, :]
                softmax_tail_vector(dve, sparse, f"sparse {i}", S, r)
                for b in range(3):
                    gate = n_gate[:, 0 if b == 0 else 1, 1 + i // 2, 4 * (i % 2):4 * (i % 2) + 4]
                    does(None, dve.tensor_tensor, r[:, :, b], r[:, :, b], gate, ALU.mult)
                settle()
                does(f"sparse p {i}", dve.tensor_tensor, blocks(S), blocks(S), wide(r.rearrange("p u b -> p (u b)"), P), ALU.mult)
            dve.wait_ge(*after("sparse c exp"))
            for t in range(TT):
                does(None, dve.tensor_tensor, n_sc[:, t, :, :], n_sc[:, t, :, :], over(table("cmp_mask")[:, CMP_PAD * t:CMP_PAD * (t + 1)], 8), ALU.mult)
            settle()
            does(None, dve.tensor_reduce, n_cs[:, 1, :], sc, AX.X, ALU.add)
            settle()
            does(None, dve.tensor_scalar, n_cs[:, 1, :], n_cs[:, 1, :], 1e-30, None, ALU.max)
            settle()
            does(None, dve.reciprocal, n_cs[:, 1, :], n_cs[:, 1, :])
            settle()
            by_token = n_cs[:, 1, :].rearrange("p (t s) -> p t s", t=TT)
            does(None, dve.tensor_tensor, by_token, by_token, n_gate[:, :, 0, :], ALU.mult)
            settle()
            does("sparse pc", dve.tensor_tensor, sc, sc, wide(n_cs[:, 1, :], CMP_PAD), ALU.mult)
            out_turn_vector(dve, "sparse", at, sparse, 4)

        with Arena() as take:
            r_pm = take("r_pm", [P, 14, SEQ])
            r_a, r_kk = take("r_a", [P, 4, SEQ]), take("r_kk", [P, 4, SEQ])
            r_ld, r_c, r_e1, r_e1p, r_e2 = (take(f"r_{i}", [P, 4, SEQ]) for i in ("ld", "c", "e1", "e1p", "e2"))
            r_kt, r_bt = take("r_kt", [P, 512]), take("r_bt", [P, 512])
            r_rhs, r_sa = take("r_rhs", [P, 4, 64]), take("r_sa", [P, 4, 64])
            r_s1 = take("r_s1", [P, 2, P])
            r_mid = take("r_mid", [P, 4, 2])
            r_f = take("r_f", [P, 4])
            r_bonus = take("r_bonus", [P, TT, 8])
            r_stat = take("r_stat", [P, 6, 16])
            take.beyond_split("r_filler")
            r_tok = take("r_tok", [P, TT, RWKV_K * COLS])
            r_pb = take("r_pb", [P, 14, SEQ + 1])

        def matrices(ap, first=0):
            return ap[:, first:first + 8 * P].rearrange("p (m c) -> p m c", m=8)

        flat_pb, flat_tok = r_pb.rearrange("p c t -> p (c t)"), r_tok.rearrange("p t c -> p (t c)")
        r_A, r_T, r_L, r_R, r_B = (matrices(x.rearrange("p c t -> p (c t)")) for x in (r_ld, r_c, r_e1, r_e1p, r_e2))
        r_U, r_Y, r_AM = matrices(flat_pb), matrices(flat_tok), matrices(flat_tok, 8 * P)
        r_g, r_v = (flat_pb[:, c0:c0 + 2 * 512].rearrange("p (t c) -> p t c", t=2) for c0 in (1024, 2048))
        r_scratch = r_kk.rearrange("p c t -> p (c t)").rearrange("p (t c) -> p t c", t=TT)
        R_KINDS = "k" * RWKV_K + "t" * (RWKV_T - 1) + "v"
        NEG_ROOT_E = -math.exp(-0.5)
        R_MATRICES = ("A", "L", "R", "B")

        def r_place(s, j, b):
            if s < RWKV_K:
                return [(r_tok[:, j, s * COLS:(s + 1) * COLS], b[:, 0:COLS])]
            return [(r_pb[:, 3 * (s - RWKV_K) + j, 1:1 + SEQ], b[:, 0:SEQ])]

        def chunk_of(x, i, c, parity):
            return x[64 * parity:64 * parity + 64, i, c * P:(c + 1) * P]

        def rwkv_tensor(pe, at):
            g0 = first_step[at]
            proj_tensor(pe, "rwkv", g0, R_KINDS)
            lora = col("lora")
            for name, rows_, label in (("w", slice(0, 64), "rwkv tanh"), ("a", slice(64, P), "rwkv mixed")):
                pe.wait_ge(*after(label))
                for i in range(2):
                    b = open_bank(pe, f"rwkv {name} {i}")
                    for j in range(2):
                        c = 2 * i + j
                        ins = pe.matmul(b[:, j * SEQ:(j + 1) * SEQ], lora[rows_, c * P:(c + 1) * P], r_pm[rows_, 12, :], start=True, stop=True)
                    ins.then_inc(*rwkv.tensor(f"rwkv {name} {i}"))
            pe.wait_ge(*after("rwkv gate"))
            for t in range(TT):
                b = open_bank(pe, f"rwkv g {t}")
                pe.matmul(b, r_pm[:, 13, t * P:(t + 1) * P], col("g2"), start=True, stop=True).then_inc(*rwkv.tensor(f"rwkv g {t}"))
            pe.wait_ge(*after("rwkv sgu normed"))
            for t in range(TT):
                b = open_bank(pe, f"rwkv sgu {t}")
                for g in range(4):
                    ins = pe.matmul(b[:, g * P:(g + 1) * P], col("sgu_w")[:, g * P:(g + 1) * P], r_tok[:, t, 512 + g * P:512 + (g + 1) * P],
                                    start=True, stop=True)
                ins.then_inc(*rwkv.tensor(f"rwkv sgu {t}"))
            pe.wait_ge(*after("rwkv kk square"))
            for i in range(2):
                b = open_bank(pe, f"rwkv kn {i}")
                pe.matmul(b, table("pair_ones"), r_e2[:, 2 * i:2 * i + 2, :], start=True, stop=True).then_inc(*rwkv.tensor(f"rwkv kn {i}"))
            pe.wait_ge(*after("rwkv rk"))
            b = open_bank(pe, "rwkv bonus")
            for t in range(TT):
                for c in range(4):
                    ins = pe.matmul(b[:, 8 * t + 2 * c:8 * t + 2 * c + 2], r_e1[:, c, t * P:(t + 1) * P], table("pair_sel"), start=True, stop=True)
            ins.then_inc(*rwkv.tensor("rwkv bonus"))
            for t in range(TT):
                b = open_bank(pe, f"rwkv v {t}")
                for c in range(4):
                    ins = pe.transpose(b[:, c * P:(c + 1) * P], r_pm[:, 8 + c, t * P:(t + 1) * P], ident)
                ins.then_inc(*rwkv.tensor(f"rwkv v {t}"))
            pe.wait_ge(*after("rwkv decayed"))
            for name, x, c0 in (("kt", r_pm, 4), ("bt", r_a, 0)):
                b = open_bank(pe, f"rwkv {name}")
                for c in range(4):
                    ins = pe.transpose(b[:, c * P:(c + 1) * P], x[:, c0 + c, 0:P], ident)
                ins.then_inc(*rwkv.tensor(f"rwkv {name}"))
            for half in range(2):
                i0 = 2 * half
                operands = {"A": ((r_kk, 0), (r_a, 0)), "L": ((r_pm, 4), (r_kk, 0)), "R": ((r_pm, 4), (r_pm, 0)), "B": ((r_a, 0), (r_pm, 0))}
                for name in R_MATRICES:
                    (x, x0), (y, y0) = operands[name]
                    for par in range(2):
                        b = open_bank(pe, f"rwkv {name} {half} {par}")
                        for ti in range(2):
                            for c in range(2):
                                m = 2 * ti + c
                                ins = pe.matmul(b[:, m * P:(m + 1) * P], chunk_of(x, x0 + i0 + ti, c, par), chunk_of(y, y0 + i0 + ti, c, par),
                                                start=True, stop=True)
                        ins.then_inc(*rwkv.tensor(f"rwkv {name} {half} {par}"))
                inverse_tensor(pe, f"rwkv{half}", r_T, r_U, r_Y, r_AM)
                for par in range(2):
                    pe.wait_ge(*after(f"rwkv{half} U {LEVELS - 1} {par}"))
                pe.wait_ge(*after(f"rwkv masked {half}"))
                pe.wait_ge(*after("used rwkv bt"))
                for c in range(2):
                    tag = f"{half} {c}"
                    heads = [(ti, par, 2 * ti + par, 4 * par + 2 * ti + c, r_v[:, c, (i0 + ti) * P + 64 * par:(i0 + ti) * P + 64 * par + 64])
                             for ti in range(2) for par in range(2)]
                    if c == 1:
                        pe.wait_ge(*after(f"rwkv s1 {half} 1"))

                    def from_state(b, ti, x, x0):
                        if c == 1:
                            pe.matmul(b[:, ti * P:(ti + 1) * P], x[:, x0 + i0 + ti, P:SEQ], r_s1[:, ti, :], start=True, stop=False)

                    b = open_bank(pe, f"rwkv rhs {tag}")
                    for ti, par, hh, m, v in heads:
                        if par == 0:
                            from_state(b, ti, r_kk, 0)
                        ins = pe.matmul(b[:, hh * 64:hh * 64 + 64], r_L[:, m, :], v, start=c == 0, stop=c == 0 or par == 1)
                    ins.then_inc(*rwkv.tensor(f"rwkv rhs {tag}"))
                    pe.wait_ge(*after(f"used rwkv rhs {tag}"))
                    b = open_bank(pe, f"rwkv sa {tag}")
                    for ti, par, hh, m, v in heads:
                        ins = pe.matmul(b[:, hh * 64:hh * 64 + 64], r_U[:, m, :], r_rhs[:, hh, :], start=True, stop=True)
                    ins.then_inc(*rwkv.tensor(f"rwkv sa {tag}"))
                    pe.wait_ge(*after(f"used rwkv sa {tag}"))
                    b = open_bank(pe, f"rwkv y {tag}")
                    for ti in range(2):
                        from_state(b, ti, r_pm, 0)
                        for _, par, hh, m, v in heads[2 * ti:2 * ti + 2]:
                            pe.matmul(b[:, hh * 64:hh * 64 + 64], r_R[:, m, :], v, start=c == 0, stop=False)
                            ins = pe.matmul(b[:, hh * 64:hh * 64 + 64], r_B[:, m, :], r_sa[:, hh, :], start=False, stop=c == 0 or par == 1)
                    ins.then_inc(*rwkv.tensor(f"rwkv y {tag}"))
                    if c == 0:
                        b = open_bank(pe, f"rwkv ds {half}")
                        for ti in range(2):
                            tile = slice((i0 + ti) * P, (i0 + ti + 1) * P)
                            pe.matmul(b[:, ti * P:(ti + 1) * P], r_kt[:, tile], r_v[:, 0, tile], start=True, stop=False)
                            ins = pe.matmul(b[:, ti * P:(ti + 1) * P], r_bt[:, tile], r_sa[:, 2 * ti:2 * ti + 2, :], start=False, stop=True)
                        ins.then_inc(*rwkv.tensor(f"rwkv ds {half}"))
            turn_tensor(pe, "rwkv", rwkv, KT, ["rwkv gated"] * TT)
            out_tensor(pe, "rwkv", g0 + RWKV_K + RWKV_T)

        def rwkv_scalar(act, at):
            def does(label, *args, **kw):
                act.activation(*args, **kw).then_inc(*rwkv.scalar(label))

            proj_copies(act, "rwkv", first_step[at], R_KINDS, 0, r_place)
            wait_proj(act, "rwkv", R_KINDS, range(RWKV_K))
            does("rwkv gelu", r_tok[:, :, 0:1024], r_tok[:, :, 0:1024], ACT.Gelu_apprx_tanh)
            act.wait_ge(*after("rwkv mixed"))
            does("rwkv tanh", r_pm[0:64, 12, :], r_pm[0:64, 12, :], ACT.Tanh)
            does("rwkv gate", r_pm[:, 13, :], r_pm[:, 13, :], ACT.Sigmoid)
            for name, dst, bias in (("w", r_ld, "w0"), ("a", r_a, "a0")):
                for i in range(2):
                    act.wait_ge(*after(f"rwkv {name} {i}"))
                    for j in range(2):
                        c = 2 * i + j
                        does(f"used rwkv {name} {i}", dst[:, c, :], bank(f"rwkv {name} {i}")[:, j * SEQ:(j + 1) * SEQ], ACT.Sigmoid,
                             bias=col(bias)[:, c:c + 1])
            for t in range(TT):
                act.wait_ge(*after(f"rwkv g {t}"))
                does(f"used rwkv g {t}", r_g[:, t, :], bank(f"rwkv g {t}"), ACT.Copy)
            act.wait_ge(*after("rwkv kk"))
            does("rwkv kk square", r_e2[:, :, :], r_kk[:, :, :], ACT.Square)
            act.wait_ge(*after("rwkv sgu var"))
            does("rwkv sgu root", r_stat[:, 2, 0:8], r_stat[:, 1, 0:8], ACT.Sqrt, scale=1.0 / P, bias=ln_eps)
            act.wait_ge(*after("rwkv kk clipped"))
            does("rwkv kk root", r_e2[:, :, :], r_e2[:, :, :], ACT.Sqrt)
            for t in range(TT):
                act.wait_ge(*after(f"rwkv v {t}"))
                does(f"used rwkv v {t}", r_v[:, t, :], bank(f"rwkv v {t}"), ACT.Copy)
            act.wait_ge(*after("rwkv exponents"))
            act.wait_ge(*after("rwkv bonus"))
            act.wait_ge(*after("rwkv kk unit"))
            does(None, r_f[:, :], r_f[:, :], ACT.Exp)
            does(None, r_e1[:, :, :], r_c[:, :, :], ACT.Exp)
            does(None, r_e1p[:, :, :], r_e1p[:, :, :], ACT.Exp)
            does("rwkv exp", r_e2[:, :, :], r_c[:, :, :], ACT.Exp, scale=-1.0)
            for name, dst in (("kt", r_kt), ("bt", r_bt)):
                act.wait_ge(*after(f"rwkv {name}"))
                does(f"used rwkv {name}", dst[:, :], bank(f"rwkv {name}"), ACT.Copy)
            for half in range(2):
                inverse_scalar(act, f"rwkv{half}", r_U, r_Y)
                for c in range(2):
                    tag = f"{half} {c}"
                    act.wait_ge(*after(f"rwkv rhs {tag}"))
                    does(f"used rwkv rhs {tag}", r_rhs.rearrange("p h d -> p (h d)"), bank(f"rwkv rhs {tag}")[:, 0:SEQ], ACT.Copy)
                    act.wait_ge(*after(f"rwkv sa {tag}"))
                    does(f"used rwkv sa {tag}", r_sa.rearrange("p h d -> p (h d)"), bank(f"rwkv sa {tag}")[:, 0:SEQ], ACT.Copy, scale=-1.0)
            act.wait_ge(*after("rwkv centred"))
            does("rwkv y square", r_scratch[:, :, :], O[:, :, 512:1024], ACT.Square)
            act.wait_ge(*after("rwkv y var"))
            does("rwkv y root", r_stat[:, 4, :], r_stat[:, 3, :], ACT.Sqrt, scale=1.0 / 64, bias=gn_eps)
            out_scalar(act, at, "rwkv", "rwkv gated", rwkv)

        def rwkv_pool(pool, at):
            proj_pool(pool, first_step[at], len(R_KINDS))
            for half in range(2):
                inverse_pool(pool, f"rwkv{half}", r_A, r_AM)
            out_pool(pool, at)

        def rwkv_vector(dve, at):
            def does(label, op, *args):
                op(*args).then_inc(*rwkv.vector(label))

            def settle():
                dve.wait_ge(*rwkv.vector.so_far())

            def groups(x, n):
                return x.rearrange("p (g c) -> p g c", c=n)

            def centre(x, stat, n, label):
                does(None, dve.tensor_reduce, stat, groups(x, n), AX.X, ALU.add)
                settle()
                does(None, dve.tensor_scalar, stat, stat, 1.0 / n, None, ALU.mult)
                settle()
                does(label, dve.tensor_tensor, groups(x, n), groups(x, n), wide(stat, n), ALU.subtract)

            does(None, dve.memset, r_pb[:, :, 0:1], 0.0)
            does(None, dve.tensor_tensor, col("sgu_w").rearrange("p (g c) -> p g c", g=4), col("sgu_w").rearrange("p (g c) -> p g c", g=4),
                 over(table("incl_t"), 4), ALU.mult)
            proj_copies(dve, "rwkv", first_step[at], R_KINDS, 1, r_place)
            wait_proj(dve, "rwkv", R_KINDS)
            settle()
            does(None, dve.tensor_tensor, r_pm[:, :, :], r_pb[:, :, 0:SEQ], r_pb[:, :, 1:1 + SEQ], ALU.subtract)
            settle()
            for c in [12, 13] + list(range(12)):
                does("rwkv mixed", dve.scalar_tensor_tensor, r_pm[:, c, :], r_pm[:, c, :], col("mu")[:, c:c + 1], r_pb[:, c, 1:1 + SEQ], ALU.mult, ALU.add)
            settle()
            for c in range(4):
                does("rwkv kk", dve.tensor_scalar, r_kk[:, c, :], r_pm[:, 4 + c, :], col("k_k")[:, c:c + 1], None, ALU.mult)
            dve.wait_ge(*after("rwkv gelu"))
            for t in range(TT):
                pv = r_tok[:, t, 512:1024]
                centre(pv, r_stat[:, 0, 4 * t:4 * t + 4], P, None)
                settle()
                does(None, dve.tensor_tensor, O[:, t, 512:1024], pv, pv, ALU.mult)
                settle()
                does("rwkv sgu var", dve.tensor_reduce, r_stat[:, 1, 4 * t:4 * t + 4], groups(O[:, t, 512:1024], P), AX.X, ALU.add)
            dve.wait_ge(*after("rwkv sgu root"))
            does(None, dve.reciprocal, r_stat[:, 2, 0:8], r_stat[:, 2, 0:8])
            settle()
            for t in range(TT):
                pv = r_tok[:, t, 512:1024]
                does(None, dve.tensor_tensor, groups(pv, P), groups(pv, P), wide(r_stat[:, 2, 4 * t:4 * t + 4], P), ALU.mult)
            settle()
            for t in range(TT):
                pv = r_tok[:, t, 512:1024]
                does(None, dve.tensor_tensor, pv, pv, row("ln_g"), ALU.mult)
            settle()
            for t in range(TT):
                pv = r_tok[:, t, 512:1024]
                does("rwkv sgu normed", dve.tensor_tensor, pv, pv, row("ln_b"), ALU.add)
            for i in range(2):
                dve.wait_ge(*after(f"rwkv kn {i}"))
                does("rwkv kk clipped", dve.tensor_scalar, r_e2[:, 2 * i:2 * i + 2, :], bank(f"rwkv kn {i}").rearrange("p (c t) -> p c t", c=2),
                     1e-24, None, ALU.max)
                marks[f"used rwkv kn {i}"] = marks["rwkv kk clipped"]
            for t in range(TT):
                dve.wait_ge(*after(f"rwkv sgu {t}"))
                does(f"used rwkv sgu {t}", dve.tensor_tensor, four(O[:, t, 0:512]), four(bank(f"rwkv sgu {t}")), wide(col("sgu_b"), P), ALU.add)
            settle()
            does(None, dve.tensor_tensor, O[:, :, 0:512], O[:, :, 0:512], r_tok[:, :, 0:512], ALU.mult)
            dve.wait_ge(*after("used rwkv g 1"))
            for c in range(4):
                does(None, dve.tensor_scalar, r_c[:, c, :], r_a[:, c, :], 1.0, col("k_a")[:, c:c + 1], ALU.subtract, ALU.mult)
            does(None, dve.tensor_scalar, r_ld[:, :, :], r_ld[:, :, :], NEG_ROOT_E, None, ALU.mult)
            settle()
            k = r_pm[:, 4:8, :]
            does(None, dve.scalar_tensor_tensor, k, r_c[:, :, :], 1.0, k, ALU.add, ALU.mult)
            settle()
            for c in range(4):
                does("rwkv rk", dve.scalar_tensor_tensor, r_e1[:, c, :], r_pm[:, c, :], col("r_k")[:, c:c + 1], r_pm[:, 4 + c, :], ALU.mult, ALU.mult)
            for c in range(4):
                for ch in range(2):
                    part = slice(ch * P, (ch + 1) * P)
                    does(None, dve.tensor_tensor_scan, r_c[:, c, part], ones, r_ld[:, c, part], 0.0, ALU.mult, ALU.add)
            settle()
            does(None, dve.tensor_scalar, r_mid[:, :, :], r_c.rearrange("p c (h t) -> p c h t", h=2)[:, :, :, P - 1], 0.5, None, ALU.mult)
            settle()
            does(None, dve.tensor_tensor, r_f[:, :], r_mid[:, :, 0], r_mid[:, :, 1], ALU.add)
            chunks = r_c.rearrange("p c (h t) -> p (c h) t", h=2)
            does(None, dve.tensor_tensor, chunks, chunks, wide(r_mid.rearrange("p c h -> p (c h)"), P), ALU.subtract)
            settle()
            does("rwkv exponents", dve.tensor_tensor, r_e1p[:, :, :], r_c[:, :, :], r_ld[:, :, :], ALU.subtract)
            dve.wait_ge(*after("rwkv kk root"))
            does(None, dve.reciprocal, r_e2[:, :, :], r_e2[:, :, :])
            settle()
            does("rwkv kk unit", dve.tensor_tensor, r_kk[:, :, :], r_kk[:, :, :], r_e2[:, :, :], ALU.mult)
            settle()
            does("rwkv b", dve.tensor_tensor, r_a[:, :, :], r_kk[:, :, :], r_a[:, :, :], ALU.mult)
            dve.wait_ge(*after("rwkv bonus"))
            does("used rwkv bonus", dve.tensor_copy, r_bonus.rearrange("p t h -> p (t h)"), bank("rwkv bonus")[:, 0:16])
            dve.wait_ge(*after("rwkv exp"))
            settle()
            for x, e in ((r_pm[:, 0:4, :], r_e1), (k, r_e2), (r_kk[:, :, :], r_e1p), (r_a[:, :, :], r_e2)):
                does("rwkv decayed", dve.tensor_tensor, x, x, e[:, :, :], ALU.mult)
            settle()
            for half in range(2):
                for name, dst, mask in (("A", r_A, "strict"), ("L", r_L, "upper"), ("R", r_R, "incl_t"), ("B", r_B, "incl_t")):
                    for par in range(2):
                        dve.wait_ge(*after(f"rwkv {name} {half} {par}"))
                        does(f"used rwkv {name} {half} {par}", dve.scalar_tensor_tensor, dst[:, 4 * par:4 * par + 4, :],
                             four(bank(f"rwkv {name} {half} {par}")), 1e30, over(table(mask), 4), ALU.min, ALU.mult)
                    if name == "A":
                        settle()
                marks[f"rwkv masked {half}"] = marks[f"used rwkv B {half} 1"]
                inverse_vector(dve, f"rwkv{half}", r_A, r_T, r_U, r_AM)
                for c in range(2):
                    if c == 1:
                        dve.wait_ge(*after(f"rwkv ds {half}"))
                        for ti in range(2):
                            does(f"rwkv s1 {half} {ti}", dve.scalar_tensor_tensor, r_s1[:, ti, :], bank(f"rwkv ds {half}")[:, ti * P:(ti + 1) * P],
                                 r_f[:, 2 * half + ti:2 * half + ti + 1], table("pair_ones"), ALU.mult, ALU.mult)
                        marks[f"used rwkv ds {half}"] = marks[f"rwkv s1 {half} 1"]
                    dve.wait_ge(*after(f"rwkv y {half} {c}"))
                    does(f"used rwkv y {half} {c}", dve.tensor_copy, O[:, c, 512 + 256 * half:768 + 256 * half], bank(f"rwkv y {half} {c}")[:, 0:SEQ])
            settle()
            for t in range(TT):
                centre(O[:, t, 512:1024], r_stat[:, 5, 8 * t:8 * t + 8], 64, "rwkv centred")
            dve.wait_ge(*after("rwkv y square"))
            does("rwkv y var", dve.tensor_reduce, r_stat[:, 3, :], r_scratch.rearrange("p t (h d) -> p (t h) d", d=64), AX.X, ALU.add)
            dve.wait_ge(*after("rwkv y root"))
            does(None, dve.reciprocal, r_stat[:, 4, :], r_stat[:, 4, :])
            for t in range(TT):
                does(None, dve.tensor_tensor, groups(r_scratch[:, t, :], 64), groups(r_v[:, t, :], 64), wide(r_bonus[:, t, :], 64), ALU.mult)
            settle()
            for t in range(TT):
                y = O[:, t, 512:1024]
                does(None, dve.tensor_tensor, groups(y, 64), groups(y, 64), wide(r_stat[:, 4, 8 * t:8 * t + 8], 64), ALU.mult)
                settle()
                does(None, dve.tensor_tensor, y, y, row("gn_g"), ALU.mult)
                settle()
                does(None, dve.tensor_tensor, y, y, row("gn_b"), ALU.add)
                settle()
                does(None, dve.tensor_tensor, y, y, r_scratch[:, t, :], ALU.add)
                settle()
                does("rwkv gated", dve.tensor_tensor, y, y, r_g[:, t, :], ALU.mult)
            out_turn_vector(dve, "rwkv", at, rwkv)

        with Arena() as take:
            take.beyond_split("m_filler")
            take("m_kept", [P, 10 * SEQ + EXPERTS * SEQ + D_MODEL])
            m_logits = take("m_logits", [P, TT, EXPERTS])
            m_above = take("m_above", [P, TT, EXPERTS, EXPERTS])
            m_equal = take("m_equal", [P, TT, EXPERTS, EXPERTS])
            m_rank = take("m_rank", [P, TT, EXPERTS])
            m_one = take("m_one", [P, 2, TT])
            m_gt = take("m_gt", [EXPERTS, SEQ])
            m_router_hi, m_router_lo = (take(n, [P, KT, EXPERTS], F32R) for n in ("m_router_hi", "m_router_lo"))

        def moe_tensor(pe):
            pe.wait_ge(*after("moe router"))
            b = open_bank(pe, "moe logits")
            for t in range(TT):
                for k in range(KT):
                    ins = three_passes(pe, b[:, EXPERTS * t:EXPERTS * (t + 1)], [x[:, k, t * P:(t + 1) * P] for x in (hT_hi, hT_lo)],
                                       [x[:, k, :] for x in (m_router_hi, m_router_lo)], k == 0, k == KT - 1)
            ins.then_inc(*moe.tensor("moe logits"))
            pe.wait_ge(*after("moe gates"))
            b = open_bank(pe, "moe turned")
            for t in range(TT):
                ins = pe.transpose(b[0:EXPERTS, t * P:(t + 1) * P], m_logits[:, t, :], ident)
            ins.then_inc(*moe.tensor("moe turned"))
            pe.wait_ge(*after("used moe turned"))
            for q in range(EXPERTS // 2):
                b = open_bank(pe, f"moe row {q}")
                for i in range(2):
                    e = 2 * q + i
                    ins = pe.matmul(b[:, i * SEQ:(i + 1) * SEQ], table("expert_row")[0:EXPERTS, e * P:(e + 1) * P], m_gt[:, :], start=True, stop=True)
                ins.then_inc(*moe.tensor(f"moe row {q}"))
            pe.wait_ge(*after(f"used moe row {EXPERTS // 2 - 1}"))

        def moe_scalar(act):
            act.wait_ge(*after("moe less max"))
            act.activation(m_logits[:, :, :], m_logits[:, :, :], ACT.Exp).then_inc(*moe.scalar("moe exp"))
            act.wait_ge(*after("moe turned"))
            act.activation(m_gt[:, :], bank("moe turned")[0:EXPERTS, 0:SEQ], ACT.Copy).then_inc(*moe.scalar("used moe turned"))
            for q in range(EXPERTS // 2):
                act.wait_ge(*after(f"moe row {q}"))
                act.activation(gate_rows[:, 2 * q:2 * q + 2, :], bank(f"moe row {q}").rearrange("p (e t) -> p e t", e=2), ACT.Copy) \
                   .then_inc(*moe.scalar(f"used moe row {q}"))

        def moe_vector(dve):
            def does(label, op, *args):
                op(*args).then_inc(*moe.vector(label))

            def settle():
                dve.wait_ge(*moe.vector.so_far())

            router = col("router").rearrange("p (k e) -> p k e", k=KT)
            does(None, dve.tensor_copy, m_router_hi[:, :, :], router)
            settle()
            does("moe router", dve.tensor_tensor, m_router_lo[:, :, :], router, m_router_hi[:, :, :].bitcast(F32), ALU.subtract)
            dve.wait_ge(*after("moe logits"))
            does("used moe logits", dve.tensor_tensor, m_logits[:, :, :], bank("moe logits")[:, 0:TT * EXPERTS].rearrange("p (t e) -> p t e", t=TT),
                 over(row("router_b"), TT), ALU.add)
            settle()
            for t in range(TT):
                l = m_logits[:, t, :]
                does(None, dve.tensor_tensor, m_above[:, t, :, :], over(l, EXPERTS), wide(l, EXPERTS), ALU.is_gt)
                does(None, dve.tensor_tensor, m_equal[:, t, :, :], over(l, EXPERTS), wide(l, EXPERTS), ALU.is_equal)
            does(None, dve.tensor_reduce, m_one[:, 0, :], m_logits[:, :, :], AX.X, ALU.max)
            settle()
            for t in range(TT):
                does(None, dve.tensor_tensor, m_equal[:, t, :, :], m_equal[:, t, :, :], table("lower8").rearrange("p (e f) -> p e f", e=EXPERTS), ALU.mult)
            settle()
            does(None, dve.tensor_tensor, m_above[:, :, :, :], m_above[:, :, :, :], m_equal[:, :, :, :], ALU.add)
            does("moe less max", dve.tensor_tensor, m_logits[:, :, :], m_logits[:, :, :], wide(m_one[:, 0, :], EXPERTS), ALU.subtract)
            settle()
            does(None, dve.tensor_reduce, m_rank[:, :, :], m_above[:, :, :, :], AX.X, ALU.add)
            settle()
            does(None, dve.tensor_scalar, m_rank[:, :, :], m_rank[:, :, :], 1.5, None, ALU.is_lt)
            settle()
            dve.wait_ge(*after("moe exp"))
            does(None, dve.tensor_tensor, m_logits[:, :, :], m_logits[:, :, :], m_rank[:, :, :], ALU.mult)
            settle()
            does(None, dve.tensor_reduce, m_one[:, 1, :], m_logits[:, :, :], AX.X, ALU.add)
            settle()
            does(None, dve.reciprocal, m_one[:, 1, :], m_one[:, 1, :])
            settle()
            does("moe gates", dve.tensor_tensor, m_logits[:, :, :], m_logits[:, :, :], wide(m_one[:, 1, :], EXPERTS), ALU.mult)
            dve.wait_ge(*after(f"used moe row {EXPERTS // 2 - 1}"))

        MIXERS = {"delta": {"tensor": delta_tensor, "scalar": delta_scalar, "vector": delta_vector, "pool": delta_pool},
                  "attention": {"tensor": attention_tensor, "scalar": attention_scalar, "vector": attention_vector,
                                "pool": attention_pool},
                  "rwkv": {"tensor": rwkv_tensor, "scalar": rwkv_scalar, "vector": rwkv_vector, "pool": rwkv_pool},
                  "sparse": {"tensor": sparse_tensor, "scalar": sparse_scalar, "vector": sparse_vector, "pool": sparse_pool}}

        LOADS = 4
        marks["x 0"] = ("loaded", 16 * LOADS)

        @block.tensor
        def _(pe):
            pe.wait_ge(loaded, 16 * LOADS)
            for at, (kind, n) in enumerate(NETWORK):
                if kind == "final":
                    continue
                norm_tensor(pe, at)
                wait_hT(pe, f"norm {at}")
                if kind == "moe":
                    moe_tensor(pe)
                if kind in ("ffn", "moe"):
                    ffn_tensor(pe, at)
                else:
                    MIXERS[kind]["tensor"](pe, at)

        @block.scalar
        def _(act):
            act.dma_start(rows[:, :], rows_in.partition_broadcast(P)).then_inc(loaded, 16)
            act.dma_start(tables[:, :], tables_in).then_inc(loaded, 16)
            act.wait_ge(loaded, 16 * LOADS)
            split_hi(act, 0, 0)
            for at, (kind, n) in enumerate(NETWORK):
                if kind == "final":
                    final_scalar(act, at)
                norm_scalar(act, at)
                if kind != "final":
                    norm_turned_scalar(act, at)
                if kind == "moe":
                    moe_scalar(act)
                if kind in ("ffn", "moe"):
                    ffn_scalar(act, at)
                elif kind != "final":
                    MIXERS[kind]["scalar"](act, at)

        @block.vector
        def _(dve):
            dve.wait_ge(loaded, 16 * LOADS)
            split_lo(dve, 0, 0)
            for at, (kind, n) in enumerate(NETWORK):
                if kind == "final":
                    final_vector(dve, at)
                    continue
                norm_vector(dve, at)
                if kind == "moe":
                    moe_vector(dve)
                if kind in ("ffn", "moe"):
                    ffn_vector(dve, at, 0.5 if n < 6 else 1.0)
                else:
                    MIXERS[kind]["vector"](dve, at)

        @block.gpsimd
        def _(pool):
            split_lo_last(pool, 0, 0)
            for at, (kind, n) in enumerate(NETWORK):
                if kind in MIXERS:
                    MIXERS[kind]["pool"](pool, at)
                elif kind != "final":
                    ffn_pool(pool, at)

        @block.sync
        def _(sp):
            sp.dma_start(X[:, :, :], x_in.rearrange("o (t p) d -> p (o t) d", p=P)).then_inc(loaded, 16)
            sp.dma_start(columns[:, :], columns_in).then_inc(loaded, 16)
            for g in range(SLOTS):
                sp.dma_start(slot(g), stream[g]).then_inc(step_loaded[g], 16)
            turns = total // SLOTS - 1
            with sp.Fori(0, turns) as i:
                for s in range(SLOTS):
                    sp.wait_ge(lo_ready, 2 * (SLOTS * i + s + 1))
                    sp.wait_ge(lo_last_ready, SLOTS * i + s + 1)
                    sp.dma_start(slot(s), stream[SLOTS * i + SLOTS + s]).then_inc(step_loaded[s], 16)
            for g in range(SLOTS * (turns + 1), total):
                sp.wait_ge(lo_ready, 2 * (g - SLOTS + 1))
                sp.wait_ge(lo_last_ready, g - SLOTS + 1)
                sp.dma_start(slot(g), stream[g]).then_inc(step_loaded[g % SLOTS], 16)
            sp.wait_ge(*after(f"x {len(NETWORK)}"))
            sp.dma_start(out.rearrange("o (t p) d -> p (o t) d", p=P), X[:, :, :]).then_inc(stored, 16)
            sp.wait_ge(stored, 16)


def by_row_tile(w):
    return np.ascontiguousarray(w).reshape(-1, P, w.shape[-1]).transpose(1, 0, 2)


def ffn_steps(gate, up, down):
    d = gate.shape[0]
    for j in range(0, down.shape[0], P):
        step = np.empty((P, STEP), np.float32)
        step[:, 0:d] = by_row_tile(gate[:, j:j + P]).reshape(P, -1)
        step[:, d:2 * d] = by_row_tile(up[:, j:j + P]).reshape(P, -1)
        step[:, 2 * d:] = down[j:j + P]
        yield step


def column_steps(parts, n):
    w = np.zeros((parts[0].shape[0], n * COLS), np.float32)
    at = 0
    for part in parts:
        w[:, at:at + part.shape[1]] = part
        at += part.shape[1]
    for s in range(n):
        yield by_row_tile(w[:, s * COLS:(s + 1) * COLS]).reshape(P, -1)


SLOT_HEADS = [0, 4, 1, 5, 2, 6, 3, 7]


def stream_steps(a):
    for kind, n in NETWORK:
        if kind == "ffn":
            if n < 6:
                name = {0: "l0_ffn1", 2: "l0_ffn2", 3: "l1_ffn1", 5: "l1_ffn2"}[n]
                up = a[name + "_w_up"]
                yield from ffn_steps(up[:, :D_FF], up[:, D_FF:], a[name + "_w_down"])
            else:
                yield from ffn_steps(a["ffn_w_gate_2"][0], a["ffn_w_up_2"][0], a["ffn_w_down_2"][0])
        elif kind == "moe":
            for e in range(EXPERTS):
                yield from ffn_steps(a["moe_w_gate_2"][0, e], a["moe_w_up_2"][0, e], a["moe_w_down_2"][0, e])
        elif kind == "delta":
            yield from column_steps([a["l0_w_in"][:, :1536]], DELTA_T)
            yield from column_steps([a["l0_w_in"][:, 1536:]], DELTA_K)
            yield from column_steps([a["l0_w_out"]], OUT_STEPS)
        elif kind == "attention":
            yield from column_steps([a["l1_w_in"]], ATT_K)
            yield from column_steps([a["l1_w_out"]], OUT_STEPS)
        elif kind == "rwkv":
            yield from column_steps([a["e_w_in_2"][0][:, :1024]], RWKV_K)
            yield from column_steps([a["e_w_in_2"][0][:, 1024:]], RWKV_T)
            yield from column_steps([a["e_w_out_2"][0]], OUT_STEPS)
        elif kind == "sparse":
            w = a["o_w_in_2"][0]
            q = w[:, :512].reshape(-1, 8, 64)[:, SLOT_HEADS].reshape(-1, 512)
            gl = w[:, 1280:1304].reshape(-1, 8, 3)[:, SLOT_HEADS].transpose(0, 2, 1).reshape(-1, 24)
            kc, vc = (w[:, c:c + 128].reshape(-1, 2, 1, 64).repeat(2, axis=2).reshape(-1, 256) for c in (512, 640))
            yield from column_steps([q, w[:, 768:1280], gl], SPARSE_K)
            yield from column_steps([kc, vc, w[:, 1304:]], SPARSE_T)
            tiles = np.concatenate([by_row_tile(a["nsa_cmp_k_w1_2"][0]), by_row_tile(a["nsa_cmp_v_w1_2"][0])], axis=1)
            padded = np.zeros((P, SPARSE_C * 12, 256), np.float32)
            padded[:, :32] = tiles
            for s in range(SPARSE_C):
                yield padded[:, 12 * s:12 * s + 12].reshape(P, -1)
            out = a["o_w_out_2"][0]
            yc = out[:512].reshape(8, 64, -1)[SLOT_HEADS].reshape(512, -1)
            yield from column_steps([np.concatenate([yc, out[512:]])], OUT_STEPS)


def pack_columns(a):
    c = np.zeros((P, COLUMN.width), np.float32)

    def per(v):
        return v.reshape(-1, P).T

    names = ["l0_ffn1_norm", "l0_mix_norm", "l0_ffn2_norm", "l1_ffn1_norm", "l1_mix_norm", "l1_ffn2_norm",
             "e_norm_mix_2", "e_norm_ffn_2", "o_norm_mix_2", "o_norm_ffn_2"]
    c[:, COLUMN["gain"]] = np.concatenate([per(a[n].reshape(-1)) for n in names], axis=1)
    c[:, COLUMN["conv"]] = np.concatenate([per(a["l0_conv_w"][j]) for j in range(4)], axis=1)
    c[:, COLUMN["conv3"]] = np.concatenate([per(a["conv_w_2"][0, j]) for j in range(3)], axis=1)
    for name, v in (("mu", "mu"), ("w0", "w0"), ("a0", "a0"), ("k_k", "k_k"), ("k_a", "k_a"), ("r_k", "r_k")):
        c[:, COLUMN[name]] = per(a[f"rwkv_{v}_2"][0].reshape(-1))
    c[:, COLUMN["sgu_b"]] = a["sgu_b_2"][0].T
    c[:, COLUMN["sgu_w"]] = a["sgu_w_2"][0].transpose(2, 0, 1).reshape(P, -1)
    c[:, COLUMN["router"]] = by_row_tile(a["moe_router_2"][0]).reshape(P, -1)
    c[0:64, COLUMN["lora"]], c[64:, COLUMN["lora"]] = a["rwkv_w2_2"][0], a["rwkv_a2_2"][0]
    c[:, COLUMN["g2"]] = a["rwkv_g2_2"][0]
    for s in "kv":
        c[:, COLUMN[f"cmp_{s}2"]] = by_row_tile(a[f"nsa_cmp_{s}_w2_2"][0]).reshape(P, -1)
        c[:, COLUMN[f"pos_{s}"]] = a[f"nsa_cmp_pos_{s}_2"][0].reshape(16, P).T
    return c


def pack_rows(a):
    r = np.empty(ROW.width, np.float32)
    for name, v in (("gdn_norm", "l0_gdn_norm"),
                    ("diff_norm", "l1_diff_norm"), ("ln_g", "sgu_ln_g_2"), ("ln_b", "sgu_ln_b_2"), ("gn_g", "rwkv_gn_g_2"),
                    ("gn_b", "rwkv_gn_b_2"), ("a_log", "l0_a_log"), ("dt_bias", "l0_dt_bias"), ("router_b", "moe_router_b_2"),
                    ("lq1", "l1_lambda_q1"), ("lk1", "l1_lambda_k1"), ("lq2", "l1_lambda_q2"), ("lk2", "l1_lambda_k2")):
        r[ROW[name]] = a[v].reshape(-1)
    return r


def shape_tables():
    t = np.zeros((P, TABLE.width), np.float32)
    t[:, TABLE["eps"]] = [EPS, 1e-5, 64e-5, 128 * EPS]
    p, f = np.arange(P)[:, None], np.arange(P)[None, :]
    t[:, TABLE["ident"]], t[:, TABLE["ones"]] = p == f, 1.0
    t[:, TABLE["incl_t"]], t[:, TABLE["upper"]], t[:, TABLE["strict"]] = f >= p, f > p, p > f
    t[:, TABLE["level"]] = np.concatenate([(p // (2 * b) == f // (2 * b)) & (p % (2 * b) >= b) & (f % (2 * b) < b)
                                           for b in (1 << n for n in range(LEVELS))], axis=1)
    token = np.arange(SEQ)[None, :]
    ret = []
    for h in range(HEADS):
        gamma, d = 1.0 - 2.0 ** (-5.0 - h), token - p
        m = np.where(d >= 0, gamma ** np.maximum(d, 0), 0.0) * 64 ** -0.5
        ret += [m, m[:, :P]]
    t[:, TABLE["ret"]] = np.concatenate(ret, axis=1)
    dist = np.concatenate([p - f, P + p - token], axis=1)
    count = (dist >= 0) * ((dist <= 128) * 1 + (dist % 4 == 0) + (dist % 16 == 0))
    t[:, TABLE["count"]], t[:, TABLE["bias_dil"]] = count, np.where(count > 0, 0.0, -1e30)
    t[:, TABLE["bias"]] = np.where(dist >= 0, 0.0, -1e30)
    for half, theta, dim in ((32, 10000.0, 64), (64, 10000.0, 128), (8, 500000.0, 16)):
        inv = np.float32(theta) ** (-np.arange(0, dim, 2, dtype=np.float32) / np.float32(dim))
        ang = (np.arange(SEQ, dtype=np.float32)[:, None] * inv[None, :]).reshape(TT, P, half).transpose(1, 0, 2)
        t[:, TABLE[f"cos{half}"]], t[:, TABLE[f"sin{half}"]] = (g(ang).reshape(P, -1) for g in (np.cos, np.sin))
    n = np.arange(CMP_PAD)[None, None, :]
    seen = (n < CMP_N) & (16 * n + 31 <= (p + P * np.arange(TT)[None, :])[:, :, None])
    t[:, TABLE["cmp_mask"]] = seen.reshape(P, -1)
    t[:, TABLE["cmp_bias"]] = np.where(seen, 0.0, -1e30).reshape(P, -1)
    t[:, TABLE["pair_ones"]] = p // 64 == f // 64
    t[:, TABLE["pair_sel"]] = p // 64 == np.arange(2)[None, :]
    t[:, TABLE["cmp_block"]] = p // CMP_PAD == np.arange(8)[None, :]
    t[:, TABLE["expert_row"]] = np.repeat(p == np.arange(EXPERTS)[None, :], P, axis=1)
    e = np.arange(EXPERTS)
    t[:, TABLE["lower8"]] = (e[None, :] < e[:, None]).reshape(1, -1)
    return t


def kernel(**inputs):
    import concourse.bacc as bacc
    from concourse.bass_utils import run_bass_kernel_spmd

    a = {name: np.asarray(v) for name, v in inputs.items()}
    steps = sum(STEPS[kind] for kind, _ in NETWORK)
    stream = np.empty((steps, P, STEP), np.float32)
    for g, step in enumerate(stream_steps(a)):
        stream[g] = step
    arrays = {"x": np.ascontiguousarray(a["x"]), "stream": stream, "columns": pack_columns(a), "rows": pack_rows(a),
              "tables": shape_tables(), "final": np.stack([a["final_norm"], a["final_norm_2"]])}
    marks = {}
    for _ in range(2):
        nc = bacc.Bacc("TRN2", target_bir_lowering=False, num_devices=1)
        args = [nc.dram_tensor(f"in_{n}", v.shape, F32, kind="ExternalInput").ap() for n, v in arrays.items()]
        out = nc.dram_tensor("result", a["x"].shape, F32, kind="ExternalOutput").ap()
        network_kernel(nc, *args, out, marks)
    r = run_bass_kernel_spmd(nc, [{f"in_{n}": v for n, v in arrays.items()}], core_ids=[0])
    return r.results[0]["result"]
```

```python
import math
from contextlib import ExitStack

import numpy as np
import concourse.bass as bass
from concourse import mybir

F32 = mybir.dt.float32
F32R = mybir.dt.float32r
ACT = mybir.ActivationFunctionType
ALU = mybir.AluOpType
AX = mybir.AxisListType

P = 128
SEQ, D_MODEL, D_FF = 256, 1024, 2816
TT = SEQ // P
KT = D_MODEL // P
EXPERTS, D_EXPERT = 8, 1408
EPS = 1e-6
STEP = 3 * D_MODEL
COLS = STEP // KT
SLOTS = 3
PART = STEP // 3
TURN = 6
HEADS = 4
LEVELS = 7
LAMBDA_INIT = 0.8 - 0.6 * math.exp(-0.3)
CMP_N, CMP_PAD = 15, 16

NETWORK = [("ffn", 0), ("delta", 1), ("ffn", 2), ("ffn", 3), ("attention", 4), ("ffn", 5), ("final", 0),
           ("rwkv", 6), ("ffn", 7), ("sparse", 8), ("moe", 9), ("final", 1)]
FF_STEPS, EXPERT_STEPS = D_FF // P, D_EXPERT // P
OUT_STEPS = -(-D_MODEL // COLS)
DELTA_T, DELTA_K = 4, 6
ATT_K = 8
RWKV_K, RWKV_T = 3, 5
SPARSE_K, SPARSE_T, SPARSE_C = 3, 6, 3
STEPS = {"ffn": FF_STEPS, "moe": EXPERTS * EXPERT_STEPS, "final": 0, "delta": DELTA_T + DELTA_K + OUT_STEPS,
         "attention": ATT_K + OUT_STEPS, "rwkv": RWKV_K + RWKV_T + OUT_STEPS,
         "sparse": SPARSE_K + SPARSE_T + SPARSE_C + OUT_STEPS}


class Places:

    def __init__(self, sizes):
        self.at, self.width = {}, 0
        for name, n in sizes:
            self.at[name] = (self.width, self.width + n)
            self.width += n

    def __getitem__(self, name):
        return slice(*self.at[name])


COLUMN = Places([("gain", 10 * KT), ("conv", 4 * 12), ("mu", 14), ("w0", 4), ("a0", 4), ("k_k", 4), ("k_a", 4),
                 ("r_k", 4), ("sgu_b", 4), ("sgu_w", 4 * P), ("router", KT * EXPERTS), ("lora", 512), ("g2", 512),
                 ("cmp_k2", 2 * 64), ("cmp_v2", 2 * 64), ("pos_k", 16), ("pos_v", 16), ("conv3", 3 * 4)])
ROW = Places([("gdn_norm", P), ("diff_norm", P), ("ln_g", 512), ("ln_b", 512),
              ("gn_g", 512), ("gn_b", 512), ("a_log", 4), ("dt_bias", 4), ("router_b", 8), ("lq1", 64), ("lk1", 64),
              ("lq2", 64), ("lk2", 64)])
TABLE = Places([("eps", 4), ("ident", P), ("ones", P), ("incl_t", P), ("strict", P), ("upper", P), ("level", LEVELS * P),
                ("ret", HEADS * 3 * P), ("count", 3 * P), ("bias", 3 * P), ("bias_dil", 3 * P), ("cos32", TT * 32), ("sin32", TT * 32),
                ("cos64", TT * 64), ("sin64", TT * 64), ("cos8", TT * 8), ("sin8", TT * 8),
                ("cmp_bias", TT * CMP_PAD), ("cmp_mask", TT * CMP_PAD), ("pair_ones", P),
                ("pair_sel", 2), ("cmp_block", 8), ("lower8", EXPERTS * EXPERTS), ("slots", SEQ)])


class Progress:

    def __init__(self, marks, sem, name):
        self.marks, self.sem, self.name, self.n = marks, sem, name, 0

    def __call__(self, label=None):
        self.n += 1
        if label is not None:
            self.marks[label] = (self.name, self.n)
        return self.sem, 1

    def so_far(self):
        return self.sem, self.n


class Stage:

    def __init__(self, marks, sems, name):
        self.tensor, self.vector, self.scalar, self.pool = (
            sems.setdefault(f"{name}_{e}", Progress(marks, None, f"{name}_{e}"))
            for e in ("tensor", "vector", "scalar", "pool"))


STAGES = ("norm", "ffn", "delta", "attention", "rwkv", "sparse", "moe", "proj", "inverse")


def network_kernel(nc, x_in, stream, columns_in, rows_in, tables_in, gains_in, out, marks):
    ctx = ExitStack()
    with ctx:
        def sb(name, shape):
            return ctx.enter_context(nc.sbuf_tensor(name, shape, F32))

        def sem(name):
            return ctx.enter_context(nc.semaphore(name))

        ring = sb("ring", [P, SLOTS, STEP])
        X = sb("X", [P, TT, D_MODEL])
        hT_hi, hT_lo = (ctx.enter_context(nc.sbuf_tensor(n, [P, KT, SEQ], F32R)) for n in ("hT_hi", "hT_lo"))
        O = sb("O", [P, TT, D_MODEL])
        columns = sb("columns", [P, COLUMN.width])
        rows = sb("rows", [P, ROW.width])
        tables = sb("tables", [P, TABLE.width])
        squares = sb("squares", [P, TT])
        rms = sb("rms", [P, TT])
        rstd = sb("rstd", [P, TT])
        warm = sb("warm", [P, 1])
        psum = ctx.enter_context(nc.psum_tensor("psum", [P, 8, 512], F32))

        class Arena:

            def __enter__(self):
                self.own, self.taken = ExitStack(), 0
                return self

            def __exit__(self, *error):
                self.own.close()

            def __call__(self, name, shape, dtype=F32):
                self.taken += 4 * math.prod(shape[1:])
                return self.own.enter_context(nc.sbuf_tensor(name, shape, dtype))

            def beyond_split(self, name):
                left = 4 * 4 * STEP - self.taken
                if left > 0:
                    self(name, [P, left // 4])

        with Arena() as take:
            w_hi, w_lo = (take(n, [P, 2, STEP], F32R) for n in ("w_hi", "w_lo"))
            silu, gated = (take(n, [P, 2, SEQ]) for n in ("silu", "gated"))
            act_hi, act_lo = (take(n, [P, 2, SEQ], F32R) for n in ("act_hi", "act_lo"))
            gain_row = take("gain_row", [P, D_MODEL])

        def col(name):
            return columns[:, COLUMN[name]]

        def row(name):
            return rows[:, ROW[name]]

        def table(name):
            return tables[:, TABLE[name]]

        def wide(ap, n):
            return ap.unsqueeze(len(ap.shape)).to_broadcast(list(ap.shape) + [n])

        def over(ap, n):
            return ap.unsqueeze(1).to_broadcast([ap.shape[0], n, ap.shape[1]])

        ident, ones = table("ident"), table("ones")
        eps, ln_eps, gn_eps, two_eps = (table("eps")[:, i:i + 1] for i in range(4))

        early_loaded = [sem(f"early_loaded_{s}") for s in range(SLOTS)]
        late_loaded = [sem(f"late_loaded_{s}") for s in range(SLOTS)]
        hi_ready = sem("hi_ready")
        hi_last_ready = sem("hi_last_ready")
        lo_ready = sem("lo_ready")
        lo_last_ready = sem("lo_last_ready")
        early_used = sem("early_used")
        steps_used = sem("steps_used")
        ffn_up_ready = sem("ffn_up_ready")
        ffn_silu_ready = sem("ffn_silu_ready")
        ffn_gated = sem("ffn_gated")
        row_loaded = sem("gain_row_loaded")
        ffn_act_ready = sem("ffn_act_ready")
        stored = sem("out_stored")
        progress = {}
        stages = {name: Stage(marks, progress, name) for name in STAGES}
        for name in ("loaded", "first_loaded"):
            progress[name] = Progress(marks, None, name)
        for name, one in progress.items():
            one.sem = sem(name)
        first_loaded, loaded = progress["first_loaded"].sem, progress["loaded"].sem
        norm, ffn, delta, attn = (stages[n] for n in ("norm", "ffn", "delta", "attention"))
        rwkv, sparse, moe, proj, inverse = (stages[n] for n in ("rwkv", "sparse", "moe", "proj", "inverse"))

        def after(label):
            name, n = marks.get(label, ("norm_tensor", 1))
            return progress[name].sem, n

        bank_of, bank_order = {}, []

        def open_bank(pe, label):
            n = len(bank_order)
            bank_of[label] = n % 8
            bank_order.append(label)
            if n >= 8 and bank_order[n - 8] is not None:
                pe.wait_ge(*after(f"used {bank_order[n - 8]}"))
            return psum[:, n % 8, :]

        def reset_banks():
            bank_order[:] = [None] * 8

        def bank(label):
            return psum[:, bank_of[label], :]

        first_step, total = [], 0
        for kind, _ in NETWORK:
            first_step.append(total)
            total += STEPS[kind]
        moe_first = total - sum(STEPS[kind] for kind, _ in NETWORK if kind == "moe")

        def part(x, g, i):
            return x[:, g % 2, i * PART:(i + 1) * PART]

        def in_ring(g, gv, e=0):
            if g < moe_first:
                return g % SLOTS, gv // SLOTS + 1
            s = (g - moe_first) % EXPERT_STEPS
            k = (moe_first + s) % SLOTS
            earlier, each = (len(range((k - at) % SLOTS, n, SLOTS)) for at, n in ((0, moe_first), (moe_first, EXPERT_STEPS)))
            return k, earlier + each * e + s // SLOTS + 1

        def split_hi(act, g, gv, parts=range(3), e=0):
            k, n = in_ring(g, gv, e)
            for i in parts:
                if i != 1:
                    act.wait_ge((early_loaded if i == 0 else late_loaded)[k], 16 * n)
                if g >= 2:
                    act.wait_ge(early_used if i < 2 else steps_used, gv - 1)
                act.activation(part(w_hi, g, i), ring[:, k, i * PART:(i + 1) * PART], ACT.Copy) \
                   .then_inc(hi_ready if i < 2 else hi_last_ready, 1)

        def split_lo(dve, g, gv, parts=range(2)):
            k = in_ring(g, g)[0]
            for i in parts:
                dve.wait_ge(hi_ready, 2 * gv + i + 1)
                dve.tensor_tensor(part(w_lo, g, i), ring[:, k, i * PART:(i + 1) * PART], part(w_hi, g, i).bitcast(F32), ALU.subtract) \
                   .then_inc(lo_ready, 1)

        def split_lo_last(pool, g, gv):
            k = in_ring(g, g)[0]
            pool.wait_ge(hi_last_ready, gv + 1)
            pool.tensor_tensor(part(w_lo, g, 2), ring[:, k, 2 * PART:STEP], part(w_hi, g, 2).bitcast(F32), ALU.subtract) \
                .then_inc(lo_last_ready, 1)

        def wait_split(pe, g):
            pe.wait_ge(lo_ready, 2 * g + 2)
            pe.wait_ge(lo_last_ready, g + 1)

        def three_passes(pe, out_, w, x, first, last):
            pe.matmul(out_, w[0], x[0], start=first, stop=False, skip_group_check=True)
            pe.matmul(out_, w[0], x[1], start=False, stop=False, skip_group_check=True)
            return pe.matmul(out_, w[1], x[0], start=False, stop=last, skip_group_check=True)

        block = ctx.enter_context(nc.Block())

        def norm_scalar(act, n):
            if n > 0:
                act.activation(warm[:, :], eps, ACT.Sqrt)
            for t in range(TT):
                act.wait_ge(*after(f"x {n} {t}"))
                act.activation(O[:, t, :], X[:, t, :], ACT.Square, scale=D_MODEL ** -0.5,
                               accum_out=squares[:, t:t + 1]).then_inc(*norm.scalar(f"norm {n} squares {t}"))
                act.wait_ge(*after(f"norm {n} squares {t}"))
                act.activation(rms[:, t:t + 1], squares[:, t:t + 1], ACT.Sqrt, bias=eps).then_inc(*norm.scalar(f"norm {n} root {t}"))

        def rstd_vector(dve, n, t):
            dve.wait_ge(*after(f"norm {n} root {t}"))
            dve.reciprocal(rstd[:, t:t + 1], rms[:, t:t + 1]).then_inc(*norm.vector())
            dve.wait_ge(*norm.vector.so_far())

        def norm_vector(dve, n):
            for t in range(TT):
                rstd_vector(dve, n, t)
                dve.tensor_scalar(O[:, t, :], X[:, t, :], rstd[:, t:t + 1], None, ALU.mult) \
                   .then_inc(*norm.vector(f"norm {n} xn {t}"))
            turn_vector(dve, f"norm {n}", norm, KT, columns[:, KT * NETWORK[n][1]:KT * (NETWORK[n][1] + 1)])

        def norm_turned_scalar(act, n):
            turn_scalar(act, f"norm {n}", norm, KT, gained_=True)

        def norm_tensor(pe, n):
            turn_tensor(pe, f"norm {n}", norm, KT, [f"norm {n} xn {t}" for t in range(TT)])

        def turn_tensor(pe, name, stage, tiles, sources, ts=range(TT)):
            for t in ts:
                pe.wait_ge(*after(sources[t]))
                for q in range(0, tiles, 4):
                    b = open_bank(pe, f"{name} turn {t} {q}")
                    for k in range(4):
                        last = pe.transpose(b[:, k * P:(k + 1) * P], O[:, t, (q + k) * P:(q + k + 1) * P], ident)
                    last.then_inc(*stage.tensor(f"{name} turn {t} {q}"))

        def turned(t, q):
            return (slice(None), slice(q, q + 4), slice(t * P, (t + 1) * P)), four(O[:, t, q * P:(q + 4) * P])

        def places(tiles, ts):
            return [(t, q) for t in ts for q in range(0, tiles, 4)]

        def turn_vector(dve, name, stage, tiles, gain=None, ts=range(TT)):
            if gain is not None:
                for t, q in places(tiles, ts):
                    dve.wait_ge(*after(f"{name} turn {t} {q}"))
                    src, (_, whole) = four(bank(f"{name} turn {t} {q}")), turned(t, q)
                    dve.tensor_tensor(whole, src, wide(gain[:, q:q + 4], P), ALU.mult).then_inc(*stage.vector(f"used {name} turn {t} {q}"))
            for t, q in places(tiles, ts):
                dve.wait_ge(*after(f"{name} hi {t} {q}"))
                at, whole = turned(t, q)
                src = four(bank(f"{name} turn {t} {q}")) if gain is None else whole
                dve.tensor_tensor(hT_lo[at], src, hT_hi[at].bitcast(F32), ALU.subtract).then_inc(*stage.vector(f"{name} hT {t} {q}"))
                if gain is None:
                    marks[f"used {name} turn {t} {q}"] = marks[f"{name} hT {t} {q}"]

        def turn_scalar(act, name, stage, tiles, ts=range(TT), gained_=False):
            for t, q in places(tiles, ts):
                at, whole = turned(t, q)
                if gained_:
                    act.wait_ge(*after(f"used {name} turn {t} {q}"))
                else:
                    act.wait_ge(*after(f"{name} turn {t} {q}"))
                src = whole if gained_ else four(bank(f"{name} turn {t} {q}"))
                act.activation(hT_hi[at], src, ACT.Copy).then_inc(*stage.scalar(f"{name} hi {t} {q}"))

        def wait_hT(eng, name, t=TT - 1, k=KT - 1):
            eng.wait_ge(*after(f"{name} hT {t} {k - k % 4}"))

        def four(ap):
            return ap.rearrange("p (m c) -> p m c", m=4)

        def proj_tiles(kinds):
            return [(s, kind, j) for s, kind in enumerate(kinds) for j in range({"k": TT, "t": 3, "v": 2, "u": 1}[kind])]

        def release(pe, name, s):
            pe.wait_ge(*after(f"{name} {s} last"))
            pe.nop().then_inc(early_used, 1)
            pe.nop().then_inc(steps_used, 1)

        def proj_tensor(pe, name, g0, kinds, source, tiles=KT, between={}, after_first=None):
            for s, kind, j in proj_tiles(kinds):
                g = g0 + s
                w = [x[:, g % 2, :].rearrange("p (k c) -> p k c", k=KT) for x in (w_hi, w_lo)]
                if j == 0:
                    wait_split(pe, g)
                b = open_bank(pe, f"{name} {s} {j}")
                for k in range(KT):
                    if s == 0 and k % 4 == 0 and k < tiles and (kind == "k" or j == 0):
                        wait_hT(pe, source, j if kind == "k" else TT - 1, k)
                    if kind == "k":
                        ins = three_passes(pe, b[:, 0:COLS], [x[:, k, j * P:(j + 1) * P] for x in (hT_hi, hT_lo)],
                                           [x[:, k, :] for x in w], k == 0, k == KT - 1)
                    else:
                        ins = three_passes(pe, b[:, 0:SEQ], [x[:, k, j * P:(j + 1) * P] for x in w],
                                           [x[:, k, :] for x in (hT_hi, hT_lo)], k == 0, k == KT - 1)
                ins.then_inc(*proj.tensor(f"{name} {s} {j}"))
                marks[f"{name} {s} last"] = marks[f"{name} {s} {j}"]
                if j == 0 and s > 0:
                    release(pe, name, s - 1)
                if (s, j) == (0, 0) and after_first is not None:
                    after_first()
                if s in between and (s, kind, j) == [x for x in proj_tiles(kinds) if x[0] == s][-1]:
                    between[s]()
            release(pe, name, s)

        def proj_copies(eng, name, g0, kinds, parity, place, between={}, ahead=False):
            tiles = proj_tiles(kinds)
            for n, (s, kind, j) in enumerate(tiles):
                if j == 0 and s > 0 and s - 1 in between:
                    between[s - 1]()
                if j == 0 and s + 1 < len(kinds) + ahead:
                    (split_lo if parity else split_hi)(eng, g0 + s + 1, g0 + s + 1)
                if n % 2 != parity:
                    continue
                eng.wait_ge(*after(f"{name} {s} {j}"))
                pairs = place(s, j, bank(f"{name} {s} {j}"))
                for i, (dst, src) in enumerate(pairs):
                    ins = eng.tensor_copy(dst, src) if parity else eng.activation(dst, src, ACT.Copy)
                    side = proj.vector if parity else proj.scalar
                    ins.then_inc(*side(f"used {name} {s} {j}" if i == len(pairs) - 1 else None))

        def proj_pool(pool, g0, n):
            for g in range(g0 + 1, g0 + n):
                split_lo_last(pool, g, g)

        def wait_proj(eng, name, kinds, steps=range(99)):
            tiles = [x for x in proj_tiles(kinds) if x[0] in steps]
            for s, _, j in tiles[-2:]:
                eng.wait_ge(*after(f"used {name} {s} {j}"))

        def out_tensor(pe, name, g0, tiles=KT, after_first=None):
            proj_tensor(pe, f"{name} out", g0, "k" * OUT_STEPS, name, tiles, after_first=after_first)

        def out_scalar(act, at, name, done, stage, tiles=KT, meanwhile=None):
            g0 = first_step[at] + STEPS[NETWORK[at][0]] - OUT_STEPS
            if meanwhile is None:
                turn_scalar(act, name, stage, tiles, range(TT - 1))
            act.wait_ge(*after(done))
            split_hi(act, g0, g0)
            if meanwhile is not None:
                turn_scalar(act, name, stage, tiles, range(TT - 1))
                meanwhile()
            turn_scalar(act, name, stage, tiles, range(TT - 1, TT))
            for g in range(g0 + 1, min(g0 + OUT_STEPS + 1, moe_first)):
                split_hi(act, g, g)

        def out_pool(pool, at):
            g0 = first_step[at] + STEPS[NETWORK[at][0]] - OUT_STEPS
            for g in range(g0, min(g0 + OUT_STEPS + 1, moe_first)):
                split_lo_last(pool, g, g)

        def out_vector(dve, name, at):
            g0 = first_step[at] + STEPS[NETWORK[at][0]] - OUT_STEPS
            for s, kind, j in proj_tiles("k" * OUT_STEPS):
                if j == 0 and g0 + s + 1 < moe_first:
                    split_lo(dve, g0 + s + 1, g0 + s + 1)
                c0, c1 = s * COLS, min((s + 1) * COLS, D_MODEL)
                dve.wait_ge(*after(f"{name} out {s} {j}"))
                dve.tensor_tensor(X[:, j, c0:c1], X[:, j, c0:c1], bank(f"{name} out {s} {j}")[:, 0:c1 - c0], ALU.add) \
                   .then_inc(*proj.vector(f"used {name} out {s} {j}"))
            for t in range(TT):
                marks[f"x {at + 1} {t}"] = marks[f"used {name} out {OUT_STEPS - 1} {t}"]

        def out_turn_vector(dve, name, at, stage, tiles=KT, meanwhile=None):
            g0 = first_step[at] + STEPS[NETWORK[at][0]] - OUT_STEPS
            if meanwhile is not None:
                split_lo(dve, g0, g0)
            turn_vector(dve, name, stage, tiles, ts=range(TT - 1))
            if meanwhile is None:
                split_lo(dve, g0, g0)
            else:
                meanwhile()
            turn_vector(dve, name, stage, tiles, ts=range(TT - 1, TT))
            out_vector(dve, name, at)

        ffn_steps_before, n_ff = [], 0
        for kind, _ in NETWORK:
            ffn_steps_before.append(n_ff)
            n_ff += STEPS[kind] if kind in ("ffn", "moe") else 0

        def ffn_loop(eng, n, step):
            turns = (n - 2) // TURN
            with eng.Fori(0, turns) as i:
                for u in range(TURN):
                    step(2 + u, TURN * i + 2 + u)
            for s in range(2 + turns * TURN, n):
                step(s, s)

        def ffn_tensor(pe, at):
            n, g0, f0 = STEPS[NETWORK[at][0]], first_step[at], ffn_steps_before[at]

            def up(s, sv, peeled=False):
                g = g0 + s
                w = [x[:, g % 2, 0:2 * D_MODEL].rearrange("p (o k c) -> p o k c", o=2, k=KT) for x in (w_hi, w_lo)]
                pe.wait_ge(lo_ready, 2 * (g0 + sv) + 2)
                if not (peeled and f0 == 0):
                    pe.wait_ge(ffn_act_ready, f0 + sv - 1)
                for k in range(KT):
                    if s == 0 and k % 4 == 0:
                        wait_hT(pe, f"norm {at}", k=k)
                    for o in range(2):
                        ins = three_passes(pe, psum[:, 4 + s % 2, o * SEQ:(o + 1) * SEQ], [x[:, o, k, :] for x in w],
                                           [x[:, k, :] for x in (hT_hi, hT_lo)], k == 0 and o == 0, k == KT - 1)
                ins.then_inc(ffn_up_ready, 1)

            def down(s, sv, first, last):
                g = g0 + s
                pe.wait_ge(lo_last_ready, g0 + sv + 1)
                pe.wait_ge(ffn_act_ready, f0 + sv + 1)
                for t in range(TT):
                    for h in range(2):
                        c = slice(2 * D_MODEL + h * 512, 2 * D_MODEL + (h + 1) * 512)
                        ins = three_passes(pe, psum[:, 2 * t + h, :], [x[:, s % 2, t * P:(t + 1) * P] for x in (act_hi, act_lo)],
                                           [x[:, g % 2, c] for x in (w_hi, w_lo)], first, last)
                    if last and t == 0:
                        ins.then_inc(*ffn.tensor(f"ffn {at} down 0"))
                ins.then_inc(steps_used, 1)

            def early_done(sv):
                pe.wait_ge(ffn_up_ready, f0 + sv + 1)
                pe.nop().then_inc(early_used, 1)

            up(0, 0, True)
            up(1, 1, True)
            early_done(0)
            down(0, 0, True, False)
            early_done(1)

            def step(s, sv):
                up(s, sv)
                down(s - 1, sv - 1, False, False)
                early_done(sv)

            ffn_loop(pe, n, step)
            down(n - 1, n - 1, False, True)
            reset_banks()

        def ffn_scalar(act, at):
            n, g0, f0 = STEPS[NETWORK[at][0]], first_step[at], ffn_steps_before[at]

            def step(s, sv):
                more = g0 + s + 1 < moe_first
                if more:
                    split_hi(act, g0 + s + 1, g0 + sv + 1, (0, 1))
                act.wait_ge(ffn_up_ready, f0 + sv + 1)
                if s >= 2 or f0 > 0:
                    act.wait_ge(ffn_act_ready, f0 + sv - 1)
                act.activation(silu[:, s % 2, :], psum[:, 4 + s % 2, 0:SEQ], ACT.Silu).then_inc(ffn_silu_ready, 1)
                if more:
                    split_hi(act, g0 + s + 1, g0 + sv + 1, (2,))

            step(0, 0)
            step(1, 1)
            ffn_loop(act, n, step)

        def ffn_pool(pool, at):
            n, g0 = STEPS[NETWORK[at][0]], first_step[at]

            def step(s, sv):
                if g0 + s + 1 < moe_first:
                    split_lo_last(pool, g0 + s + 1, g0 + sv + 1)

            step(0, 0)
            step(1, 1)
            ffn_loop(pool, n, step)

        def ffn_vector(dve, at, factor):
            n, g0, f0 = STEPS[NETWORK[at][0]], first_step[at], ffn_steps_before[at]

            def step(s, sv):
                if g0 + s + 1 < moe_first:
                    split_lo(dve, g0 + s + 1, g0 + sv + 1)
                dve.wait_ge(ffn_silu_ready, f0 + sv + 1)
                if g0 + s >= 2:
                    dve.wait_ge(steps_used, g0 + sv - 1)
                dve.tensor_tensor(gated[:, s % 2, :], silu[:, s % 2, :], psum[:, 4 + s % 2, SEQ:2 * SEQ], ALU.mult).then_inc(ffn_gated, 1)
                dve.wait_ge(ffn_gated, 2 * (f0 + sv) + 1)
                dve.tensor_copy(act_hi[:, s % 2, :], gated[:, s % 2, :]).then_inc(ffn_gated, 1)
                dve.wait_ge(ffn_gated, 2 * (f0 + sv) + 2)
                dve.tensor_tensor(act_lo[:, s % 2, :], gated[:, s % 2, :], act_hi[:, s % 2, :].bitcast(F32), ALU.subtract) \
                   .then_inc(ffn_act_ready, 1)

            step(0, 0)
            step(1, 1)
            ffn_loop(dve, n, step)
            for t in range(TT):
                if t == 0:
                    dve.wait_ge(*after(f"ffn {at} down 0"))
                else:
                    dve.wait_ge(steps_used, g0 + n)
                for h in range(2):
                    c = slice(h * 512, (h + 1) * 512)
                    dve.scalar_tensor_tensor(X[:, t, c], psum[:, 2 * t + h, :], factor, X[:, t, c], ALU.mult, ALU.add) \
                       .then_inc(*ffn.vector(f"x {at + 1} {t}"))

        def load_gain_row(act, which):
            act.dma_start(gain_row[:, :], gains_in[which].partition_broadcast(P)).then_inc(row_loaded, 16)

        def gained(dve, at, to):
            dve.wait_ge(row_loaded, 16 * sum(kind in ("final", "moe") for kind, _ in NETWORK[:at + 1]))
            for t in range(TT):
                yield dve.scalar_tensor_tensor(to[:, t, :], X[:, t, :], rstd[:, t:t + 1], gain_row[:, :], ALU.mult, ALU.mult)

        def final_vector(dve, at):
            for t in range(TT):
                rstd_vector(dve, at, t)
            for t, ins in enumerate(gained(dve, at, X)):
                ins.then_inc(*norm.vector(f"x {at + 1} {t}"))
        def inverse_vector(dve, name, A, T, U, AM):
            dve.tensor_tensor(AM[:, :, :], A[:, :, :], over(table("level")[:, 0:P], 8), ALU.mult).then_inc(*inverse.vector())
            dve.wait_ge(*inverse.vector.so_far())
            dve.tensor_tensor(T[:, :, :], over(ident, 8), AM[:, :, :], ALU.subtract).then_inc(*inverse.vector(f"{name} T 0"))
            for l in range(1, LEVELS):
                for c in range(2):
                    m = slice(4 * c, 4 * c + 4)
                    dve.wait_ge(*after(f"{name} dU {l} {c}"))
                    dve.wait_ge(*after(f"{name} U 0 {c}" if l == 1 else f"{name} U {l - 1} {c}"))
                    dve.tensor_tensor(U[:, m, :], U[:, m, :], four(bank(f"{name} dU {l} {c}")), ALU.subtract) \
                       .then_inc(*inverse.vector(f"{name} U {l} {c}"))
                    marks[f"used {name} dU {l} {c}"] = marks[f"{name} U {l} {c}"]
                    if l < LEVELS - 1:
                        dve.wait_ge(*after(f"{name} dT {l} {c}"))
                        dve.tensor_tensor(T[:, m, :], T[:, m, :], four(bank(f"{name} dT {l} {c}")), ALU.subtract) \
                           .then_inc(*inverse.vector(f"{name} T {l} {c}"))
                        marks[f"used {name} dT {l} {c}"] = marks[f"{name} T {l} {c}"]

        def inverse_scalar(act, name, U, Y):
            for c in range(2):
                act.wait_ge(*after(f"{name} turn {c}"))
                act.activation(U[:, 4 * c:4 * c + 4, :], four(bank(f"{name} turn {c}")), ACT.Copy) \
                   .then_inc(*inverse.scalar(f"{name} U 0 {c}"))
                marks[f"used {name} turn {c}"] = marks[f"{name} U 0 {c}"]
            for l in range(1, LEVELS):
                for c in range(2):
                    act.wait_ge(*after(f"{name} Y {l} {c}"))
                    act.activation(Y[:, 4 * c:4 * c + 4, :], four(bank(f"{name} Y {l} {c}")), ACT.Copy) \
                       .then_inc(*inverse.scalar(f"used {name} Y {l} {c}"))

        def inverse_pool(pool, name, A, AM):
            for l in range(1, LEVELS):
                if l == 1:
                    pool.wait_ge(*after(f"{name} T 0"))
                else:
                    pool.wait_ge(*after(f"{name} Y {l - 1} 1"))
                pool.tensor_tensor(AM[:, :, :], A[:, :, :], over(table("level")[:, l * P:(l + 1) * P], 8), ALU.mult) \
                    .then_inc(*inverse.pool(f"{name} AM {l}"))

        def inverse_tensor(pe, name, T, U, Y, AM):
            pe.wait_ge(*after(f"{name} T 0"))
            for c in range(2):
                b = open_bank(pe, f"{name} turn {c}")
                for m in range(4):
                    ins = pe.transpose(b[:, m * P:(m + 1) * P], T[:, 4 * c + m, :], ident)
                ins.then_inc(*inverse.tensor(f"{name} turn {c}"))
            for l in range(1, LEVELS):
                pe.wait_ge(*after(f"{name} AM {l}"))
                for c in range(2):
                    pe.wait_ge(*after(f"{name} U {l - 1} {c}"))
                    b = open_bank(pe, f"{name} Y {l} {c}")
                    for m in range(4):
                        ins = pe.matmul(b[:, m * P:(m + 1) * P], AM[:, 4 * c + m, :], U[:, 4 * c + m, :], start=True, stop=True)
                    ins.then_inc(*inverse.tensor(f"{name} Y {l} {c}"))
                for c in range(2):
                    pe.wait_ge(*after(f"used {name} Y {l} {c}"))
                    if l >= 2:
                        pe.wait_ge(*after(f"{name} T {l - 1} {c}"))
                    b = open_bank(pe, f"{name} dU {l} {c}")
                    for m in range(4):
                        ins = pe.matmul(b[:, m * P:(m + 1) * P], T[:, 4 * c + m, :], Y[:, 4 * c + m, :], start=True, stop=True)
                    ins.then_inc(*inverse.tensor(f"{name} dU {l} {c}"))
                    if l < LEVELS - 1:
                        b = open_bank(pe, f"{name} dT {l} {c}")
                        for m in range(4):
                            ins = pe.matmul(b[:, m * P:(m + 1) * P], Y[:, 4 * c + m, :], T[:, 4 * c + m, :], start=True, stop=True)
                        ins.then_inc(*inverse.tensor(f"{name} dT {l} {c}"))

        def rope_vector(dve, stage, x, half, cos, sin, scratch):
            heads = x.shape[1]
            x1, x2 = x[:, :, 0:half], x[:, :, half:2 * half]
            c, s = over(cos, heads), over(sin, heads)
            for i, (a, b) in enumerate(((x1, c), (x2, s), (x1, s), (x2, c))):
                dve.tensor_tensor(scratch[:, i], a, b, ALU.mult).then_inc(*stage.vector())
            dve.wait_ge(*stage.vector.so_far())
            dve.tensor_tensor(x1, scratch[:, 0], scratch[:, 1], ALU.subtract).then_inc(*stage.vector())
            dve.tensor_tensor(x2, scratch[:, 2], scratch[:, 3], ALU.add).then_inc(*stage.vector())
            dve.wait_ge(*stage.vector.so_far())

        with Arena() as take:
            d_A = take("d_A", [P, 8, P])
            d_qk = take("d_qk", [P, 8, P])
            d_Y = take("d_Y", [P, 8, P])
            d_AM = take("d_AM", [P, 8, P])
            d_T = take("d_T", [P, 8, P])
            d_U = take("d_U", [P, 8, P])
            d_k = take("d_k", [P, 8, P])
            d_v = take("d_v", [P, 8, P])
            d_rhs = take("d_rhs", [P, 4, P])
            d_vn = take("d_vn", [P, 4, P])
            d_s1 = take("d_s1", [P, 4, P])
            d_rope = take("d_rope", [P, 4, 8, 32])
            take.beyond_split("d_filler")
            d_small = take("d_small", [P, 12, 8])
            d_pad = take("d_pad", [P, 12, SEQ + 3])
            d_qkv = take("d_qkv", [P, 12, SEQ])
            d_tok = take("d_tok", [P, TT, DELTA_K * COLS])
        d_beta, d_t, d_neg, d_pos, d_e, d_ln, d_ea, d_g, d_gc, d_egc, d_kdec = (d_small[:, i, :] for i in range(11))
        d_sum = d_pad.rearrange("p c t -> p (c t)")[:, TT * D_MODEL:TT * D_MODEL + 16]
        d_rms = d_pad.rearrange("p c t -> p (c t)")[:, TT * D_MODEL + 16:TT * D_MODEL + 32]
        pad_flat = d_pad.rearrange("p c t -> p (c t)")
        d_st = pad_flat[:, 0:4 * 384].rearrange("p (h c) -> p h c", h=4)
        d_rt = pad_flat[:, 1536:1536 + 1024].rearrange("p (i t) -> p i t", i=4)
        d_square = O.rearrange("p t d -> p (t d)").rearrange("p (c t) -> p c t", t=SEQ)
        d_out_square = d_pad.rearrange("p c t -> p (c t)")[:, 0:TT * D_MODEL].rearrange("p (t d) -> p t d", t=TT)
        D_KINDS = "t" * DELTA_T + "k" * DELTA_K
        Z, B_, A_, RQ, RV, RG = 0, 512, 516, 520, 1032, 1544

        def d_place(s, j, b):
            if s < DELTA_T:
                return [(d_pad[:, 3 * s + j, 3:3 + SEQ], b[:, 0:SEQ])]
            return [(d_tok[:, j, (s - DELTA_T) * COLS:(s - DELTA_T + 1) * COLS], b[:, 0:COLS])]

        def d_chunk(i, c):
            return d_qkv[:, i, c * P:(c + 1) * P]

        def by_chunk(ap):
            return ap.rearrange("p (c h) -> p c h", c=2)

        def delta_tensor(pe, at):
            g0 = first_step[at]

            def squared_norms(which, s):
                pe.wait_ge(*after(f"delta square {s}"))
                for q in which:
                    b = open_bank(pe, f"delta ss {q}")
                    pe.matmul(b, ones, d_square[:, 2 * q:2 * q + 2, :], start=True, stop=True) \
                      .then_inc(*delta.tensor(f"delta ss {q}"))

            proj_tensor(pe, "delta", g0, D_KINDS, f"norm {at}", 
                        between={DELTA_T: lambda: squared_norms((0, 1, 2), 1), DELTA_T + 1: lambda: squared_norms((3,), 2)})
            pe.wait_ge(*after("delta g"))
            b = open_bank(pe, "delta gcum")
            pe.matmul(b[:, 0:8], table("incl_t"), d_g, start=True, stop=True).then_inc(*delta.tensor("delta gcum"))
            pe.wait_ge(*after("delta g wide"))
            for c in range(2):
                b = open_bank(pe, f"delta grow {c}")
                for h in range(4):
                    ins = pe.matmul(b[:, h * P:(h + 1) * P], d_AM[:, 4 * c + h, :], table("incl_t"), start=True, stop=True)
                ins.then_inc(*delta.tensor(f"delta grow {c}"))
            pe.wait_ge(*after(f"delta silu {DELTA_T - 1}"))
            pe.wait_ge(*after("delta norm 3"))
            for i, name in ((4, "k"), (8, "v")):
                for c in range(2):
                    b = open_bank(pe, f"delta tok {name} {c}")
                    for h in range(4):
                        ins = pe.transpose(b[:, h * P:(h + 1) * P], d_chunk(i + h, c), ident)
                    ins.then_inc(*delta.tensor(f"delta tok {name} {c}"))
            for i, name in ((4, "kk"), (0, "kq")):
                for c in range(2):
                    b = open_bank(pe, f"delta {name} {c}")
                    for h in range(4):
                        ins = pe.matmul(b[:, h * P:(h + 1) * P], d_chunk(4 + h, c), d_chunk(i + h, c), start=True, stop=True)
                    ins.then_inc(*delta.tensor(f"delta {name} {c}"))
            for t in range(TT):
                pe.wait_ge(*after(f"delta rope {t}"))
                b = open_bank(pe, f"delta rt {t}")
                for i in range(4):
                    ins = pe.transpose(b[:, i * P:(i + 1) * P], d_tok[:, t, RQ + i * P:RQ + (i + 1) * P], ident)
                ins.then_inc(*delta.tensor(f"delta rt {t}"))
            for t in range(TT):
                pe.wait_ge(*after(f"used delta rt {t}"))
            for h in range(HEADS):
                q, k = (d_rt[64 * (h % 2):64 * (h % 2) + 64, i + h // 2, :] for i in (0, 2))
                b = open_bank(pe, f"delta rs {h}")
                pe.matmul(b[:, 0:SEQ], k[:, 0:P], q, start=True, stop=True)
                pe.matmul(b[:, SEQ:3 * P], k[:, P:SEQ], q[:, P:SEQ], start=True, stop=True) \
                  .then_inc(*delta.tensor(f"delta rs {h}"))
            pe.wait_ge(*after(f"used delta rs {HEADS - 1}"))
            for t in range(TT):
                b = open_bank(pe, f"delta ro {t}")
                for h in range(HEADS):
                    for j in range(t + 1):
                        first = t * P if j == 0 else SEQ
                        ins = pe.matmul(b[:, h * P:(h + 1) * P], d_st[:, h, first:first + P],
                                        d_tok[:, j, RV + h * P:RV + (h + 1) * P], start=j == 0, stop=j == t)
                ins.then_inc(*delta.tensor(f"delta ro {t}"))
            inverse_tensor(pe, "delta", d_T, d_U, d_Y, d_AM)
            for c in range(2):
                if c == 1:
                    pe.wait_ge(*after("used delta s1"))
                    for i, name in ((4, "ks"), (0, "qs")):
                        b = open_bank(pe, f"delta {name}")
                        for h in range(4):
                            ins = pe.matmul(b[:, h * P:(h + 1) * P], d_chunk(i + h, 1), d_s1[:, h, :], start=True, stop=True)
                        ins.then_inc(*delta.tensor(f"delta {name}"))
                pe.wait_ge(*after(f"delta U {LEVELS - 1} {c}"))
                pe.wait_ge(*after(f"delta rhs {c}"))
                b = open_bank(pe, f"delta vn {c}")
                for h in range(4):
                    ins = pe.matmul(b[:, h * P:(h + 1) * P], d_U[:, 4 * c + h, :], d_rhs[:, h, :], start=True, stop=True)
                ins.then_inc(*delta.tensor(f"delta vn {c}"))
                pe.wait_ge(*after(f"used delta vn {c}"))
                if c == 0:
                    b = open_bank(pe, "delta s1")
                    for h in range(4):
                        ins = pe.matmul(b[:, h * P:(h + 1) * P], d_k[:, h, :], d_vn[:, h, :], start=True, stop=True)
                    ins.then_inc(*delta.tensor("delta s1"))
                b = open_bank(pe, f"delta o {c}")
                for h in range(4):
                    ins = pe.matmul(b[:, h * P:(h + 1) * P], d_qk[:, 4 * c + h, :], d_vn[:, h, :], start=True, stop=True)
                ins.then_inc(*delta.tensor(f"delta o {c}"))
            gated = [f"delta gated {t}" for t in range(TT)]
            turn_tensor(pe, "delta", delta, KT, gated, range(TT - 1))
            out_tensor(pe, "delta", g0 + DELTA_T + DELTA_K,
                       after_first=lambda: turn_tensor(pe, "delta", delta, KT, gated, range(TT - 1, TT)))

        def delta_scalar(act, at):
            def does(label, *args, **kw):
                act.activation(*args, **kw).then_inc(*delta.scalar(label))

            def activate(s):
                mine = slice(3 * s, 3 * s + 3)
                act.wait_ge(*after(f"delta conv {s}"))
                does(f"delta silu {s}", d_qkv[:, mine, :], d_qkv[:, mine, :], ACT.Silu)
                if 3 * s < 8:
                    mine = slice(3 * s, min(3 * s + 3, 8))
                    act.wait_ge(*after(f"delta silu {s}"))
                    does(f"delta square {s}", d_square[:, mine, :], d_qkv[:, mine, :], ACT.Square)

            def roots(which):
                for q in which:
                    act.wait_ge(*after(f"delta ss {q}"))
                    scale, bias = (float(P), two_eps) if q < 2 else (1.0, eps)
                    does(f"used delta ss {q}", d_square[:, 2 * q:2 * q + 2, :], bank(f"delta ss {q}").rearrange("p (c t) -> p c t", c=2),
                         ACT.Sqrt, bias=bias, scale=scale)

            def decays():
                does("delta ea", d_ea[:, 0:4], row("a_log"), ACT.Exp)
                act.wait_ge(*after("delta neg"))
                does("delta e", d_e, d_neg, ACT.Exp)
                act.wait_ge(*after("delta e"))
                does("delta ln", d_ln, d_e, ACT.Ln, bias=1.0)

            between = {s + 2: lambda s=s: activate(s) for s in range(DELTA_T)}
            between[DELTA_T + 1] = lambda: (activate(DELTA_T - 1), roots((0, 1, 2)))
            between[DELTA_T + 2], between[DELTA_T + 3] = lambda: roots((3,)), decays
            proj_copies(act, "delta", first_step[at], D_KINDS, 0, d_place, between)
            wait_proj(act, "delta", D_KINDS)
            does("delta beta", by_chunk(d_beta), d_tok[:, :, B_:B_ + 4], ACT.Sigmoid)
            does("delta z", d_tok[:, :, Z:Z + 512], d_tok[:, :, Z:Z + 512], ACT.Silu)
            does("delta rg", d_tok[:, :, RG:RG + 512], d_tok[:, :, RG:RG + 512], ACT.Silu)
            for name, dst in (("k", d_k), ("v", d_v)):
                for c in range(2):
                    act.wait_ge(*after(f"delta tok {name} {c}"))
                    does(f"used delta tok {name} {c}", dst[:, 4 * c:4 * c + 4, :], four(bank(f"delta tok {name} {c}")), ACT.Copy)
            act.wait_ge(*after("delta diff"))
            does("delta D", d_A[:, :, :], d_A[:, :, :], ACT.Exp, scale=-1.0)
            does("delta DT", d_qk[:, :, :], d_qk[:, :, :], ACT.Exp)
            does("delta egc", d_egc, d_gc, ACT.Exp)
            does("delta kdec", d_kdec[:, 0:4], d_Y[:, 0:4, P - 1], ACT.Exp)
            for t in range(TT):
                act.wait_ge(*after(f"delta rt {t}"))
                does(f"used delta rt {t}", d_rt[:, :, t * P:(t + 1) * P], four(bank(f"delta rt {t}")), ACT.Copy)
            for t in range(TT):
                act.wait_ge(*after(f"delta ro {t}"))
                does(f"used delta ro {t}", O[:, t, 512:1024], bank(f"delta ro {t}"), ACT.Copy)
            inverse_scalar(act, "delta", d_U, d_Y)
            for c in range(2):
                act.wait_ge(*after(f"delta vn {c}"))
                does(f"used delta vn {c}", d_vn[:, :, :], four(bank(f"delta vn {c}")), ACT.Copy)
                if c == 0:
                    act.wait_ge(*after("delta s1"))
                    does("used delta s1", d_s1[:, :, :], four(bank("delta s1")), ACT.Copy)

            def root(t, label):
                mine = slice(8 * t, 8 * t + 8)
                act.wait_ge(*after(label))
                act.wait_ge(*after(f"used delta ro {t}"))
                does(f"delta o square {t}", d_out_square[:, t, :], O[:, t, :], ACT.Square)
                act.wait_ge(*after(f"delta o sum {t}"))
                does(f"delta o root {t}", d_rms[:, mine], d_sum[:, mine], ACT.Sqrt, scale=1.0 / P, bias=eps)

            root(0, "used delta o 0")
            out_scalar(act, at, "delta", "delta o", delta, meanwhile=lambda: root(1, "delta o"))

        def delta_pool(pool, at):
            proj_pool(pool, first_step[at], len(D_KINDS))
            inverse_pool(pool, "delta", d_A, d_AM)
            out_pool(pool, at)

        def delta_vector(dve, at):
            def does(label, op, *args, wait=None):
                op(*args).then_inc(*delta.vector(label))

            def settle():
                dve.wait_ge(*delta.vector.so_far())

            def square_sums(t):
                dve.wait_ge(*after(f"delta o square {t}"))
                does(f"delta o sum {t}", dve.tensor_reduce, d_sum[:, 8 * t:8 * t + 8], d_out_square[:, t, :].rearrange("p (h d) -> p h d", d=P), AX.X, ALU.add)

            def normalise(t):
                mine, y = slice(8 * t, 8 * t + 8), O[:, t, :].rearrange("p (h d) -> p h d", d=P)
                dve.wait_ge(*after(f"delta o root {t}"))
                does(None, dve.reciprocal, d_rms[:, mine], d_rms[:, mine])
                dve.wait_ge(*after("delta rg"))
                settle()
                does(None, dve.tensor_tensor, y, y, wide(d_rms[:, mine], P), ALU.mult)
                settle()
                does(None, dve.tensor_tensor, four(O[:, t, 0:512]), four(O[:, t, 0:512]), over(row("gdn_norm"), 4), ALU.mult)
                settle()
                does(None, dve.tensor_tensor, O[:, t, 0:512], O[:, t, 0:512], d_tok[:, t, Z:Z + 512], ALU.mult)
                does(f"delta gated {t}", dve.tensor_tensor, O[:, t, 512:1024], O[:, t, 512:1024], d_tok[:, t, RG:RG + 512], ALU.mult)

            does("delta pad", dve.memset, d_pad[:, :, 0:3], 0.0)
            def convolve(s):
                wait_proj(dve, "delta", D_KINDS, [s])
                settle()
                for j in range(4):
                    for c in range(3 * s, 3 * s + 3):
                        w, x = col("conv")[:, 12 * j + c:12 * j + c + 1], d_pad[:, c, j:j + SEQ]
                        if j == 0:
                            does(None, dve.tensor_scalar, d_qkv[:, c, :], x, w, None, ALU.mult)
                        else:
                            does(f"delta conv {s}", dve.scalar_tensor_tensor, d_qkv[:, c, :], x, w, d_qkv[:, c, :], ALU.mult, ALU.add)
                    settle()

            def biased():
                wait_proj(dve, "delta", D_KINDS, [DELTA_T + A_ // COLS])
                does(None, dve.tensor_tensor, by_chunk(d_t), d_tok[:, :, A_:A_ + 4], over(row("dt_bias"), 2), ALU.add)
                settle()
                does(None, dve.tensor_scalar, d_pos, d_t, 0.0, None, ALU.max)
                does(None, dve.tensor_scalar, d_neg, d_t, 0.0, None, ALU.min)
                settle()
                does("delta neg", dve.tensor_tensor, d_neg, d_neg, d_pos, ALU.subtract)

            def unit(q):
                dve.wait_ge(*after(f"used delta ss {q}"))
                qk = d_qkv[:, 2 * q:2 * q + 2, :]
                does(None, dve.reciprocal, d_square[:, 2 * q:2 * q + 2, :], d_square[:, 2 * q:2 * q + 2, :])
                settle()
                does(f"delta norm {q}", dve.tensor_tensor, qk, qk, d_square[:, 2 * q:2 * q + 2, :], ALU.mult)

            def log_decays():
                dve.wait_ge(*after("delta ln"))
                does(None, dve.tensor_tensor, d_t, d_pos, d_ln, ALU.add)
                settle()
                does("delta g", dve.scalar_tensor_tensor, by_chunk(d_g), by_chunk(d_t), -1.0, over(d_ea[:, 0:4], 2), ALU.mult, ALU.mult)

            between = {s + 1: lambda s=s: convolve(s) for s in range(DELTA_T)}
            between[DELTA_T + 1] = biased
            for q in range(3):
                between[DELTA_T + 2 + q] = lambda q=q: unit(q)
            proj_copies(dve, "delta", first_step[at], D_KINDS, 1, d_place, between)
            log_decays()
            unit(3)
            wait_proj(dve, "delta", D_KINDS)
            settle()
            does("delta g wide", dve.tensor_copy, d_AM[:, :, :], wide(d_g, P))
            dve.wait_ge(*after("delta gcum"))
            does("used delta gcum", dve.tensor_copy, d_gc, bank("delta gcum")[:, 0:8])
            settle()
            for c in range(2):
                dve.wait_ge(*after(f"delta grow {c}"))
                does(f"used delta grow {c}", dve.tensor_tensor, d_Y[:, 4 * c:4 * c + 4, :], four(bank(f"delta grow {c}")),
                     wide(d_gc[:, 4 * c:4 * c + 4], P), ALU.subtract)
            settle()
            does(None, dve.tensor_scalar, d_A[:, :, :], d_Y[:, :, :], 0.0, None, ALU.max)
            does("delta diff", dve.tensor_scalar, d_qk[:, :, :], d_Y[:, :, :], 0.0, None, ALU.min)
            for t in range(TT):
                rope_vector(dve, delta, d_tok[:, t, RQ:RQ + 512].rearrange("p (h d) -> p h d", d=64), 32,
                            table("cos32")[:, 32 * t:32 * t + 32], table("sin32")[:, 32 * t:32 * t + 32], d_rope)
                marks[f"delta rope {t}"] = (delta.vector.name, delta.vector.n)
            dve.wait_ge(*after("delta kdec"))
            does(None, dve.tensor_tensor, d_A[:, :, :], d_A[:, :, :], over(table("strict"), 8), ALU.mult)
            does(None, dve.tensor_tensor, d_qk[:, :, :], d_qk[:, :, :], over(table("incl_t"), 8), ALU.mult)
            settle()
            does(None, dve.tensor_tensor, d_A[:, :, :], d_A[:, :, :], wide(d_beta, P), ALU.mult)
            settle()
            for name, dst in (("kk", d_A), ("kq", d_qk)):
                for c in range(2):
                    dve.wait_ge(*after(f"delta {name} {c}"))
                    m = dst[:, 4 * c:4 * c + 4, :]
                    does(f"used delta {name} {c}", dve.tensor_tensor, m, m, four(bank(f"delta {name} {c}")), ALU.mult)
            for h in range(HEADS):
                dve.wait_ge(*after(f"delta rs {h}"))
                does(f"used delta rs {h}", dve.tensor_tensor, d_st[:, h, :], bank(f"delta rs {h}")[:, 0:3 * P],
                     table("ret")[:, 3 * P * h:3 * P * (h + 1)], ALU.mult)
            settle()
            dve.wait_ge(*after("used delta tok v 1"))
            does("delta rhs 0", dve.tensor_tensor, d_rhs[:, :, :], d_v[:, 0:4, :], wide(d_beta[:, 0:4], P), ALU.mult)
            does("delta k decayed", dve.tensor_tensor, d_k[:, 0:4, :], d_k[:, 0:4, :], wide(d_kdec[:, 0:4], P), ALU.mult)
            inverse_vector(dve, "delta", d_A, d_T, d_U, d_AM)
            dve.wait_ge(*after("delta ks"))
            does("used delta ks", dve.tensor_tensor, d_rhs[:, :, :], four(bank("delta ks")), wide(d_egc[:, 4:8], P), ALU.mult)
            settle()
            does(None, dve.tensor_tensor, d_rhs[:, :, :], d_v[:, 4:8, :], d_rhs[:, :, :], ALU.subtract)
            settle()
            does("delta rhs 1", dve.tensor_tensor, d_rhs[:, :, :], d_rhs[:, :, :], wide(d_beta[:, 4:8], P), ALU.mult)
            dve.wait_ge(*after("delta o 0"))
            does("used delta o 0", dve.tensor_copy, O[:, 0, 0:512], bank("delta o 0"))
            dve.wait_ge(*after("delta qs"))
            does("used delta qs", dve.tensor_tensor, four(O[:, 1, 0:512]), four(bank("delta qs")), wide(d_egc[:, 4:8], P), ALU.mult)
            settle()
            square_sums(0)
            dve.wait_ge(*after("delta o 1"))
            does("delta o", dve.tensor_tensor, O[:, 1, 0:512], O[:, 1, 0:512], bank("delta o 1"), ALU.add)
            marks["used delta o 1"] = marks["delta o"]
            normalise(0)
            out_turn_vector(dve, "delta", at, delta, meanwhile=lambda: (square_sums(1), normalise(1)))

        UNIT = 3 * P

        def blocks(ap):
            return ap.rearrange("p u (b c) -> p (u b) c", c=P)

        def softmax_head_vector(dve, stage, name, S, units, scale, bias, small):
            for i, u in enumerate(units):
                dve.wait_ge(*after(f"{u}"))
                dve.scalar_tensor_tensor(S[:, i, :], bank(u)[:, 0:UNIT], scale, bias, ALU.mult, ALU.add) \
                   .then_inc(*stage.vector(f"used {u}"))
            dve.wait_ge(*stage.vector.so_far())
            dve.tensor_reduce(small.rearrange("p u b -> p (u b)"), blocks(S), AX.X, ALU.max).then_inc(*stage.vector())
            dve.wait_ge(*stage.vector.so_far())
            dve.tensor_tensor(small[:, :, 1], small[:, :, 1], small[:, :, 2], ALU.max).then_inc(*stage.vector())
            dve.wait_ge(*stage.vector.so_far())
            dve.tensor_scalar(small[:, :, 0:2], small[:, :, 0:2], -1.0, None, ALU.mult).then_inc(*stage.vector(f"{name} max"))

        def softmax_scalar(act, stage, name, S, less, sums):
            act.wait_ge(*after(f"{name} max"))
            for u in range(4):
                for t, cols in enumerate((slice(0, P), slice(P, UNIT))):
                    act.activation(S[:, u, cols], S[:, u, cols], ACT.Exp, bias=less[:, u, t:t + 1], accum_out=sums[:, u, t:t + 1]) \
                       .then_inc(*stage.scalar(f"{name} exp"))

        def softmax_tail_vector(dve, stage, name, S, small, count=None):
            dve.wait_ge(*after(f"{name} exp"))
            if count is not None:
                dve.tensor_tensor(S, S, over(count, 4), ALU.mult).then_inc(*stage.vector())
                dve.wait_ge(*stage.vector.so_far())
                dve.tensor_reduce(small.rearrange("p u b -> p (u b)"), blocks(S), AX.X, ALU.add).then_inc(*stage.vector())
                dve.wait_ge(*stage.vector.so_far())
                dve.tensor_tensor(small[:, :, 1], small[:, :, 1], small[:, :, 2], ALU.add).then_inc(*stage.vector())
                dve.wait_ge(*stage.vector.so_far())
            dve.tensor_copy(small[:, :, 2], small[:, :, 1]).then_inc(*stage.vector())
            dve.wait_ge(*stage.vector.so_far())
            dve.reciprocal(small, small).then_inc(*stage.vector())
            dve.wait_ge(*stage.vector.so_far())

        def scores_tensor(pe, stage, label, q, k):
            b = open_bank(pe, label)
            pe.matmul(b[:, 0:P], q[:, 0:P], k[:, 0:P], start=True, stop=True)
            pe.matmul(b[:, P:UNIT], q[:, P:SEQ], k, start=True, stop=True).then_inc(*stage.tensor(label))

        def turn_unit_tensor(pe, stage, label, s):
            b = open_bank(pe, label)
            for j in range(3):
                ins = pe.transpose(b[:, j * P:(j + 1) * P], s[:, j * P:(j + 1) * P], ident)
            ins.then_inc(*stage.tensor(label))

        def unit_blocks(s, t):
            return [s[:, 0:P]] if t == 0 else [s[:, P:2 * P], s[:, 2 * P:UNIT]]

        with Arena() as take:
            a_S = take("a_S", [P, 12, UNIT])
            a_max = take("a_max", [P, 12, 3])
            a_sum = take("a_sum", [P, 12, 3])
            take.beyond_split("a_filler")
            a_T = take("a_T", [P, 16, SEQ])
            a_rope = take("a_rope", [P, 4 * 8 * 64])
            a_tok = take("a_tok", [P, TT, ATT_K * COLS])
            a_lam = take("a_lam", [P, 2, 64])
            a_small = take("a_small", [P, 32])
        A_KINDS = "k" * ATT_K
        CV, DV = 1024, 2560
        GROUPS = {0: 0, 1: 512, 2: 1536, 3: 2048}
        A_EARLY, A_LATE = ([(t, i) for t in range(TT) for i in pair] for pair in ((0, 1), (2, 3)))
        A_GROUPS = [[f"attn s {u}" for u in range(4 * i, 4 * i + 4)] for i in range(3)]

        def a_place(s, j, b):
            return [(a_tok[:, j, s * COLS:(s + 1) * COLS], b[:, 0:COLS])]

        def attention_tensor(pe, at):
            g0 = first_step[at]

            def turn_groups(which):
                for t, i in which:
                    pe.wait_ge(*after(f"attn rope {t} {i // 2}"))
                    b = open_bank(pe, f"attn turned {t} {i}")
                    for h in range(4):
                        c = GROUPS[i] + h * P
                        ins = pe.transpose(b[:, h * P:(h + 1) * P], a_tok[:, t, c:c + P], ident)
                    ins.then_inc(*attn.tensor(f"attn turned {t} {i}"))

            proj_tensor(pe, "attn", g0, A_KINDS, f"norm {at}", between={5: lambda: turn_groups(A_EARLY)})
            turn_groups(A_LATE)
            pe.wait_ge(*after(f"used attn turned {TT - 1} 3"))
            for h in range(HEADS):
                scores_tensor(pe, attn, f"attn s {h}", a_T[:, h, :], a_T[:, 4 + h, :])
            for h in range(HEADS):
                for half in range(2):
                    rows_ = slice(64 * half, 64 * half + 64)
                    scores_tensor(pe, attn, f"attn s {4 + 2 * h + half}", a_T[rows_, 8 + h, :], a_T[rows_, 12 + h, :])
            for i, u in enumerate([0, 1, 2, 3, 4, 6, 8, 10]):
                pe.wait_ge(*after("attn p dil" if u < 4 else f"attn p diff {(u - 4) // 4}"))
                turn_unit_tensor(pe, attn, f"attn pt {u}", a_S[:, u, :])
            for side, (units, v0) in enumerate((([0, 1, 2, 3], CV), ([4, 6, 8, 10], DV))):
                pe.wait_ge(*after(f"used attn pt {units[-1]}"))
                for t in range(TT):
                    b = open_bank(pe, f"attn o {side} {t}")
                    for h, u in enumerate(units):
                        for j, s in enumerate(unit_blocks(a_S[:, u, :], t)):
                            ins = pe.matmul(b[:, h * P:(h + 1) * P], s, a_tok[:, j, v0 + h * P:v0 + (h + 1) * P],
                                            start=j == 0, stop=j == t)
                    ins.then_inc(*attn.tensor(f"attn o {side} {t}"))
            turn_tensor(pe, "attn", attn, KT, [f"attn normed {t}" for t in range(TT)])
            out_tensor(pe, "attn", g0 + ATT_K)

        def attention_scalar(act, at):
            def does(label, *args, **kw):
                act.activation(*args, **kw).then_inc(*attn.scalar(label))

            def by_channel(which):
                for t, i in which:
                    act.wait_ge(*after(f"attn turned {t} {i}"))
                    does(f"used attn turned {t} {i}", a_T[:, 4 * i:4 * i + 4, t * P:(t + 1) * P], four(bank(f"attn turned {t} {i}")), ACT.Copy)

            proj_copies(act, "attn", first_step[at], A_KINDS, 0, a_place, {5: lambda: by_channel(A_EARLY)})
            act.wait_ge(*after("attn lam sums"))
            does("attn lam exp", a_small[:, 2:4], a_small[:, 0:2], ACT.Exp)
            by_channel(A_LATE)
            for i in range(3):
                softmax_scalar(act, attn, f"attn {i}", *(x[:, 4 * i:4 * i + 4, :] for x in (a_S, a_max, a_sum)))
            for u in (0, 1, 2, 3, 4, 6, 8, 10):
                act.wait_ge(*after(f"attn pt {u}"))
                does(f"used attn pt {u}", a_S[:, u, :], bank(f"attn pt {u}")[:, 0:UNIT], ACT.Copy)
            for side in range(2):
                for t in range(TT):
                    act.wait_ge(*after(f"attn o {side} {t}"))
                    does(f"used attn o {side} {t}", O[:, t, 512 * side:512 * side + 512], bank(f"attn o {side} {t}"), ACT.Copy)
            act.wait_ge(*after("used attn o 1 1"))
            does("attn square", a_T[:, 0:4, :].rearrange("p h t -> p (h t)").rearrange("p (t d) -> p t d", t=TT), O[:, :, 512:1024], ACT.Square)
            act.wait_ge(*after("attn square sum"))
            does("attn root", a_small[:, 16:24], a_small[:, 8:16], ACT.Sqrt, scale=1.0 / P, bias=eps)
            out_scalar(act, at, "attn", "attn normed 1", attn)

        def attention_pool(pool, at):
            proj_pool(pool, first_step[at], ATT_K)
            out_pool(pool, at)

        def attention_vector(dve, at):
            def does(label, op, *args):
                op(*args).then_inc(*attn.vector(label))

            def settle():
                dve.wait_ge(*attn.vector.so_far())

            for i in range(2):
                does(None, dve.tensor_tensor, a_lam[:, i, :], row(f"lq{i + 1}"), row(f"lk{i + 1}"), ALU.mult)
            settle()
            does("attn lam sums", dve.tensor_reduce, a_small[:, 0:2], a_lam[:, :, :], AX.X, ALU.add)

            def rotate(t, i):
                c0, dim = ((0, 128), (1536, 64))[i]
                half = dim // 2
                wait_proj(dve, "attn", A_KINDS, [(c0 + 1024 - 1) // COLS])
                rope_vector(dve, attn, a_tok[:, t, c0:c0 + 1024].rearrange("p (h d) -> p h d", d=dim), half,
                            table(f"cos{half}")[:, half * t:half * t + half], table(f"sin{half}")[:, half * t:half * t + half],
                            a_rope.rearrange("p (i h c) -> p i h c", i=4, c=half))
                marks[f"attn rope {t} {i}"] = (attn.vector.name, attn.vector.n)

            proj_copies(dve, "attn", first_step[at], A_KINDS, 1, a_place,
                        {3: lambda: rotate(0, 0), 4: lambda: rotate(1, 0), 6: lambda: rotate(0, 1)})
            rotate(1, 1)
            wait_proj(dve, "attn", A_KINDS)
            dve.wait_ge(*after("attn lam exp"))
            does(None, dve.tensor_tensor, a_small[:, 4:5], a_small[:, 3:4], a_small[:, 2:3], ALU.subtract)
            settle()
            does(None, dve.tensor_scalar, a_small[:, 5:6], a_small[:, 4:5], -LAMBDA_INIT, None, ALU.add)
            def scores(i):
                softmax_head_vector(dve, attn, f"attn {i}", a_S[:, 4 * i:4 * i + 4, :], A_GROUPS[i], (128 if i == 0 else 64) ** -0.5,
                                    table("bias_dil" if i == 0 else "bias"), a_max[:, 4 * i:4 * i + 4, :])

            def weights(i):
                S, r = a_S[:, 4 * i:4 * i + 4, :], a_sum[:, 4 * i:4 * i + 4, :]
                softmax_tail_vector(dve, attn, f"attn {i}", S, r, table("count") if i == 0 else None)
                if i > 0:
                    pair = r.rearrange("p (h two) b -> p h two b", two=2)[:, :, 1, :]
                    does(None, dve.tensor_scalar, pair, pair, a_small[:, 5:6], None, ALU.mult)
                    settle()
                does("attn p dil" if i == 0 else None, dve.tensor_tensor, blocks(S), blocks(S), wide(r.rearrange("p u b -> p (u b)"), P), ALU.mult)
                if i > 0:
                    settle()
                    halves = S.rearrange("p (h two) c -> p h two c", two=2)
                    does(f"attn p diff {i - 1}", dve.tensor_tensor, halves[:, :, 0, :], halves[:, :, 0, :], halves[:, :, 1, :], ALU.add)

            scores(0)
            scores(1)
            weights(0)
            scores(2)
            weights(1)
            weights(2)
            dve.wait_ge(*after("attn square"))
            does("attn square sum", dve.tensor_reduce, a_small[:, 8:16], a_T[:, 0:4, :].rearrange("p h t -> p (h t)").rearrange("p (h d) -> p h d", d=P),
                 AX.X, ALU.add)
            dve.wait_ge(*after("attn root"))
            does(None, dve.reciprocal, a_small[:, 24:32], a_small[:, 16:24])
            settle()
            for t in range(TT):
                heads = four(O[:, t, 512:1024])
                does(None, dve.tensor_tensor, heads, heads, wide(a_small[:, 24 + 4 * t:28 + 4 * t], P), ALU.mult)
                settle()
                does(f"attn normed {t}", dve.scalar_tensor_tensor, heads, heads, 1.0 - LAMBDA_INIT, over(row("diff_norm"), 4), ALU.mult, ALU.mult)
            out_turn_vector(dve, "attn", at, attn)

        SLOTS8 = 8
        with Arena() as take:
            n_S = take("n_S", [P, 16, UNIT])
            n_qr = take("n_qr", [P, 4, SEQ])
            n_kt = take("n_kt", [P, 2, SEQ])
            n_vcmp = take("n_vcmp", [P, SLOTS8, 64])
            n_sc = take("n_sc", [P, TT, SLOTS8, CMP_PAD])
            n_pct = take("n_pct", [P, TT, P])
            n_max, n_sum = (take(f"n_{i}", [P, 16, 3]) for i in ("max", "sum"))
            n_cs = take("n_cs", [P, 2, 16])
            n_kcmp = take("n_kcmp", [P, CMP_PAD])
            take.beyond_split("n_filler")
            n_rows = take("n_rows", [2 * CMP_PAD, 2, 2 * P])
            n_qn = take("n_qn", [P, 4, SEQ])
            n_tok = take("n_tok", [P, TT, SPARSE_K * COLS])
            n_z = [take(f"n_z{i}", [P, 2, SEQ]) for i in range(2)]
            n_bg, n_cg, n_hd = (take(f"n_{i}", [P, 4, SEQ]) for i in ("bg", "cg", "hd"))
            n_pad = take("n_pad", [P, 4, SEQ + 2])
            n_zb = [take(f"n_zb{i}", [P, 16, 2, CMP_PAD]) for i in range(2)]
            n_zb_hi, n_zb_lo = ([take(f"n_zb_{n}{i}", [P, 16 + 3, 2, CMP_PAD], F32R) for i in range(2)] for n in ("hi", "lo"))
            n_hid = [take(f"n_hid{i}", [P, 2, 2 * CMP_PAD]) for i in range(2)]
            n_hv = take("n_hv", [P, 2, 4, 2 * CMP_PAD])
            n_gate = take("n_gate", [P, TT, 3, SLOTS8])
            n_rope = take("n_rope", [P, 4, 8, 8])
        N_KINDS = "k" * SPARSE_K + "t" * (SPARSE_T - 1) + "u"
        KS, VS, KW, VW, GL = 512, 640, 768, 896, 1024
        N_GROUPS = [[f"sparse s {u}" for u in range(4 * i, 4 * i + 4)] for i in range(4)]

        def n_place(s, j, b):
            if s < SPARSE_K:
                return [(n_tok[:, j, s * COLS:(s + 1) * COLS], b[:, 0:COLS])]
            c = 3 * (s - SPARSE_K) + j
            if c < 4:
                z = n_z[c // 2]
                return [(z[0:64, c % 2, :], b[0:64, 0:SEQ]), (z[64:P, c % 2, 0:SEQ - 1], b[64:P, 1:SEQ])]
            return [((n_bg, n_cg, n_hd)[c // 4 - 1][:, c % 4, :], b[:, 0:SEQ])]

        def slot_rows(s):
            return slice(64 * (s % 2), 64 * (s % 2) + 64)

        def sparse_tensor(pe, at):
            g0 = first_step[at]

            def turn_plain():
                for t in range(TT):
                    for s in (0, 1):
                        for j in (0, 1):
                            pe.wait_ge(*after(f"used sparse {s} {j}"))
                    b = open_bank(pe, f"sparse qn {t}")
                    for i in range(4):
                        ins = pe.transpose(b[:, i * P:(i + 1) * P], n_tok[:, t, i * P:(i + 1) * P], ident)
                    ins.then_inc(*sparse.tensor(f"sparse qn {t}"))

            proj_tensor(pe, "sparse", g0, N_KINDS, f"norm {at}", between={2: turn_plain})
            for s in range(SPARSE_C):
                g = g0 + SPARSE_K + SPARSE_T + s
                wait_split(pe, g)
                w = [x[:, g % 2, :].rearrange("p (q c) -> p q c", q=12) for x in (w_hi, w_lo)]
                for block_ in range(12 * s, min(12 * s + 12, 32)):
                    which, l = divmod(block_, 16)
                    if l == 0:
                        pe.wait_ge(*after(f"sparse zb {which}"))
                        b = open_bank(pe, f"sparse hid {which}")
                    windows = [x[which].rearrange("p l h n -> p (l h n)")[:, 2 * CMP_PAD * l:2 * CMP_PAD * l + P] for x in (n_zb_hi, n_zb_lo)]
                    ins = three_passes(pe, b[:, 0:2 * P], windows, [x[:, block_ % 12, :] for x in w], l == 0, l == 15)
                    if l == 15 or block_ % 12 == 11:
                        ins.then_inc(*sparse.tensor(f"sparse hid {which}" if l == 15 else f"sparse c {s} last"))
                if s == SPARSE_C - 1:
                    marks[f"sparse c {s} last"] = marks["sparse hid 1"]
                release(pe, "sparse c", s)
            for t in range(TT):
                pe.wait_ge(*after(f"sparse rope {t}"))
                b = open_bank(pe, f"sparse qr {t}")
                for i in range(4):
                    ins = pe.transpose(b[:, i * P:(i + 1) * P], n_tok[:, t, i * P:(i + 1) * P], ident)
                ins.then_inc(*sparse.tensor(f"sparse qr {t}"))
                b = open_bank(pe, f"sparse kt {t}")
                for i, c0 in enumerate((KS, KW)):
                    ins = pe.transpose(b[:, i * P:(i + 1) * P], n_tok[:, t, c0:c0 + P], ident)
                ins.then_inc(*sparse.tensor(f"sparse kt {t}"))
            for which in range(2):
                pe.wait_ge(*after(f"used sparse hid {which}"))
                b = open_bank(pe, f"sparse hid turned {which}")
                for i in range(2):
                    ins = pe.transpose(b[:, 2 * CMP_PAD * i:2 * CMP_PAD * (i + 1)], n_rows[:, which, i * P:(i + 1) * P], ident[0:2 * CMP_PAD, 0:2 * CMP_PAD])
                ins.then_inc(*sparse.tensor(f"sparse hid turned {which}"))
            pe.wait_ge(*after("used sparse kt 1"))

            def scores(units):
                for u in units:
                    s = u % SLOTS8
                    scores_tensor(pe, sparse, f"sparse s {u}", n_qr[slot_rows(s), s // 2, :], n_kt[slot_rows(s), u // SLOTS8, :])

            scores(range(0, 4))
            pe.wait_ge(*after("used sparse hid turned 1"))
            b = open_bank(pe, "sparse kcmp")
            for kv in range(2):
                for i in range(2):
                    ins = pe.matmul(b[64 * kv:64 * kv + 64, 0:CMP_PAD], col("cmp_k2")[:, 64 * i:64 * i + 64],
                                    n_hid[0][:, i, kv * CMP_PAD:(kv + 1) * CMP_PAD], start=i == 0, stop=i == 1)
            ins.then_inc(*sparse.tensor("sparse kcmp"))
            pe.wait_ge(*after("sparse hv"))
            b = open_bank(pe, "sparse vcmp")
            for i in range(2):
                ins = pe.matmul(b[:, 0:64], n_hv[:, i, :, :].rearrange("p j n -> p (j n)"), col("cmp_v2")[:, 64 * i:64 * i + 64],
                                start=i == 0, stop=i == 1)
            ins.then_inc(*sparse.tensor("sparse vcmp"))
            scores(range(4, 8))
            pe.wait_ge(*after("used sparse kcmp"))
            for par in range(2):
                b = open_bank(pe, f"sparse cs {par}")
                for t in range(TT):
                    for j in range(4):
                        c0 = (4 * t + j) * CMP_PAD
                        ins = pe.matmul(b[:, c0:c0 + CMP_PAD], n_qn[slot_rows(par), j, t * P:(t + 1) * P], n_kcmp[slot_rows(par), :],
                                        start=True, stop=True)
                ins.then_inc(*sparse.tensor(f"sparse cs {par}"))
            scores(range(8, 16))

            def turn_units(i):
                pe.wait_ge(*after(f"sparse p {i}"))
                for u in range(4 * i, 4 * i + 4):
                    turn_unit_tensor(pe, sparse, f"sparse pt {u}", n_S[:, u, :])

            for i in range(4):
                turn_units(i)
            pe.wait_ge(*after("sparse pc"))
            for t in range(TT):
                b = open_bank(pe, f"sparse pct {t}")
                pe.transpose(b[:, 0:P], n_sc[:, t, :, :].rearrange("p s n -> p (s n)"), ident).then_inc(*sparse.tensor(f"sparse pct {t}"))
            pe.wait_ge(*after("used sparse vcmp"))
            pe.wait_ge(*after("used sparse pct 1"))
            for t in range(TT):
                b = open_bank(pe, f"sparse o {t}")
                pe.matmul(b, n_pct[:, t, :], n_vcmp.rearrange("p s d -> p (s d)"), start=True, stop=False)
                for br, v0 in enumerate((VS, VW)):
                    for s in range(SLOTS8):
                        for j, pt in enumerate(unit_blocks(n_S[:, 8 * br + s, :], t)):
                            v = n_tok[:, j, v0 + 64 * (s % 2):v0 + 64 * (s % 2) + 64]
                            ins = pe.matmul(b[:, 64 * s:64 * s + 64], pt, v, start=False,
                                            stop=br == 1 and s == SLOTS8 - 1 and j == t)
                ins.then_inc(*sparse.tensor(f"sparse o {t}"))
            turn_tensor(pe, "sparse", sparse, 4, [f"used sparse o {t}" for t in range(TT)])
            pe.wait_ge(*after("sparse conv"))
            out_tensor(pe, "sparse", g0 + SPARSE_K + SPARSE_T + SPARSE_C, 4)

        def sparse_scalar(act, at):
            def does(label, *args, **kw):
                act.activation(*args, **kw).then_inc(*sparse.scalar(label))

            def plain():
                for t in range(TT):
                    act.wait_ge(*after(f"sparse qn {t}"))
                    does(f"used sparse qn {t}", n_qn[:, :, t * P:(t + 1) * P], four(bank(f"sparse qn {t}")), ACT.Copy)

            proj_copies(act, "sparse", first_step[at], N_KINDS, 0, n_place, {2: plain}, ahead=True)
            c0 = first_step[at] + len(N_KINDS)
            for g in range(c0 + 1, c0 + SPARSE_C):
                split_hi(act, g, g)
            for which in range(2):
                act.wait_ge(*after(f"sparse hid {which}"))
                does(f"used sparse hid {which}", n_rows[:, which, :], bank(f"sparse hid {which}")[0:2 * CMP_PAD, 0:2 * P], ACT.Gelu_apprx_tanh)
            for t in range(TT):
                act.wait_ge(*after(f"sparse qr {t}"))
                does(f"used sparse qr {t}", n_qr[:, :, t * P:(t + 1) * P], four(bank(f"sparse qr {t}")), ACT.Copy)
                act.wait_ge(*after(f"sparse kt {t}"))
                does(f"used sparse kt {t}", n_kt[:, :, t * P:(t + 1) * P],
                     bank(f"sparse kt {t}")[:, 0:2 * P].rearrange("p (i c) -> p i c", i=2), ACT.Copy)
            wait_proj(act, "sparse", N_KINDS, range(SPARSE_K))
            does("sparse gate", n_gate.rearrange("p t b s -> p t (b s)"), n_tok[:, :, GL:GL + 24], ACT.Sigmoid)
            for which in range(2):
                act.wait_ge(*after(f"sparse hid turned {which}"))
                does(f"used sparse hid turned {which}", n_hid[which].rearrange("p i c -> p (i c)"),
                     bank(f"sparse hid turned {which}")[:, 0:4 * CMP_PAD], ACT.Copy)
            act.wait_ge(*after("sparse kcmp"))
            does("used sparse kcmp", n_kcmp[:, :], bank("sparse kcmp")[:, 0:CMP_PAD], ACT.Copy)
            for i in range(4):
                if i == 2:
                    act.wait_ge(*after("sparse c less max"))
                    does("sparse c exp", n_sc[:, :, :, :], n_sc[:, :, :, :], ACT.Exp)
                softmax_scalar(act, sparse, f"sparse {i}", *(x[:, 4 * i:4 * i + 4, :] for x in (n_S, n_max, n_sum)))
            for u in range(16):
                act.wait_ge(*after(f"sparse pt {u}"))
                does(f"used sparse pt {u}", n_S[:, u, :], bank(f"sparse pt {u}")[:, 0:UNIT], ACT.Copy)
            for t in range(TT):
                act.wait_ge(*after(f"sparse pct {t}"))
                does(f"used sparse pct {t}", n_pct[:, t, :], bank(f"sparse pct {t}")[:, 0:P], ACT.Copy)
            for t in range(TT):
                act.wait_ge(*after(f"sparse o {t}"))
                does(f"used sparse o {t}", O[:, t, 0:512], bank(f"sparse o {t}"), ACT.Copy)
            out_scalar(act, at, "sparse", "used sparse o 1", sparse, 4)

        def sparse_pool(pool, at):
            proj_pool(pool, first_step[at], len(N_KINDS) + SPARSE_C)
            out_pool(pool, at)

        def sparse_vector(dve, at):
            def does(label, op, *args):
                op(*args).then_inc(*sparse.vector(label))

            def settle():
                dve.wait_ge(*sparse.vector.so_far())

            does(None, dve.memset, n_pad[:, :, 0:2], 0.0)
            for which in range(2):
                does(None, dve.memset, n_zb[which][:, :, :, :], 0.0)
                for x in (n_zb_hi, n_zb_lo):
                    does(None, dve.memset, x[which][:, 16:, :, :].bitcast(F32), 0.0)

            def rotate(t):
                dve.wait_ge(*after(f"sparse qn {t}"))
                wait_proj(dve, "sparse", N_KINDS, range(SPARSE_K))
                for c0, heads in ((0, 8), (KS, 2), (KW, 2)):
                    rope_vector(dve, sparse, n_tok[:, t, c0:c0 + 64 * heads].rearrange("p (h d) -> p h d", d=64), 8,
                                table("cos8")[:, 8 * t:8 * t + 8], table("sin8")[:, 8 * t:8 * t + 8], n_rope[:, :, 0:heads, :])
                marks[f"sparse rope {t}"] = (sparse.vector.name, sparse.vector.n)

            def windows():
                wait_proj(dve, "sparse", N_KINDS, range(SPARSE_K, SPARSE_K + 2))
                settle()
                for which, pos in enumerate(("pos_k", "pos_v")):
                    for kv in range(2):
                        z = n_z[which][:, kv, :].rearrange("p (n b two) -> p b n two", b=8, two=2)
                        for a in range(2):
                            does(None, dve.tensor_tensor, n_zb[which][:, 8 * a:8 * a + 8, kv, 0:CMP_N],
                                 z[:, :, a:a + CMP_N, 0], wide(col(pos)[:, 8 * a:8 * a + 8], CMP_N), ALU.add)
                settle()
                for which in range(2):
                    does(None, dve.tensor_copy, n_zb_hi[which][:, 0:16, :, :], n_zb[which][:, :, :, :])
                settle()
                for which in range(2):
                    does(f"sparse zb {which}", dve.tensor_tensor, n_zb_lo[which][:, 0:16, :, :], n_zb[which][:, :, :, :],
                         n_zb_hi[which][:, 0:16, :, :].bitcast(F32), ALU.subtract)

            proj_copies(dve, "sparse", first_step[at], N_KINDS, 1, n_place,
                        {3: lambda: rotate(0), 4: lambda: rotate(1), 6: windows}, ahead=True)
            wait_proj(dve, "sparse", N_KINDS)
            settle()
            c0 = first_step[at] + len(N_KINDS)
            for g in range(c0 + 1, c0 + SPARSE_C):
                split_lo(dve, g, g)
            does(None, dve.tensor_tensor, n_pad[:, :, 2:2 + SEQ], n_cg[:, :, :], n_hd[:, :, :], ALU.mult)
            settle()
            for j in range(3):
                for c in range(4):
                    w, x = col("conv3")[:, 4 * j + c:4 * j + c + 1], n_pad[:, c, j:j + SEQ]
                    if j == 0:
                        does(None, dve.tensor_scalar, n_cg[:, c, :], x, w, None, ALU.mult)
                    else:
                        does(None, dve.scalar_tensor_tensor, n_cg[:, c, :], x, w, n_cg[:, c, :], ALU.mult, ALU.add)
                settle()
            does(None, dve.tensor_tensor, n_cg[:, :, :], n_cg[:, :, :], n_bg[:, :, :], ALU.mult)
            settle()
            does(None, dve.tensor_copy, hT_hi[:, 4:8, :], n_cg[:, :, :])
            settle()
            does("sparse conv", dve.tensor_tensor, hT_lo[:, 4:8, :], n_cg[:, :, :], hT_hi[:, 4:8, :].bitcast(F32), ALU.subtract)

            def scores(i):
                softmax_head_vector(dve, sparse, f"sparse {i}", n_S[:, 4 * i:4 * i + 4, :], N_GROUPS[i], 64 ** -0.5, table("bias"),
                                    n_max[:, 4 * i:4 * i + 4, :])

            def weights(i):
                S, r = n_S[:, 4 * i:4 * i + 4, :], n_sum[:, 4 * i:4 * i + 4, :]
                softmax_tail_vector(dve, sparse, f"sparse {i}", S, r)
                for b in range(3):
                    gate = n_gate[:, 0 if b == 0 else 1, 1 + i // 2, 4 * (i % 2):4 * (i % 2) + 4]
                    does(None, dve.tensor_tensor, r[:, :, b], r[:, :, b], gate, ALU.mult)
                settle()
                does(f"sparse p {i}", dve.tensor_tensor, blocks(S), blocks(S), wide(r.rearrange("p u b -> p (u b)"), P), ALU.mult)

            dve.wait_ge(*after("used sparse hid turned 1"))
            for i in range(2):
                does("sparse hv", dve.tensor_copy, n_hv[:, i, :, :], over(n_hid[1][:, i, :], 4))
            scores(0)
            scores(1)
            dve.wait_ge(*after("sparse vcmp"))
            does("used sparse vcmp", dve.tensor_tensor, n_vcmp[:, :, :], over(bank("sparse vcmp")[:, 0:64], 8), wide(table("cmp_block"), 64), ALU.mult)
            by_parity = n_sc.rearrange("p t (j two) n -> p t j two n", two=2)
            for par in range(2):
                dve.wait_ge(*after(f"sparse cs {par}"))
                for t in range(TT):
                    src = bank(f"sparse cs {par}")[:, 64 * t:64 * t + 64].rearrange("p (j n) -> p j n", j=4)
                    does(f"used sparse cs {par}", dve.scalar_tensor_tensor, by_parity[:, t, :, par, :], src, 64 ** -0.5,
                         over(table("cmp_bias")[:, CMP_PAD * t:CMP_PAD * (t + 1)], 4), ALU.mult, ALU.add)
            settle()
            sc = n_sc.rearrange("p t s n -> p (t s) n")
            does(None, dve.tensor_reduce, n_cs[:, 0, :], sc, AX.X, ALU.max)
            settle()
            does("sparse c less max", dve.tensor_tensor, sc, sc, wide(n_cs[:, 0, :], CMP_PAD), ALU.subtract)
            weights(0)
            scores(2)
            weights(1)
            scores(3)
            weights(2)
            weights(3)
            dve.wait_ge(*after("sparse c exp"))
            for t in range(TT):
                does(None, dve.tensor_tensor, n_sc[:, t, :, :], n_sc[:, t, :, :], over(table("cmp_mask")[:, CMP_PAD * t:CMP_PAD * (t + 1)], 8), ALU.mult)
            settle()
            does(None, dve.tensor_reduce, n_cs[:, 1, :], sc, AX.X, ALU.add)
            settle()
            does(None, dve.tensor_scalar, n_cs[:, 1, :], n_cs[:, 1, :], 1e-30, None, ALU.max)
            settle()
            does(None, dve.reciprocal, n_cs[:, 1, :], n_cs[:, 1, :])
            settle()
            by_token = n_cs[:, 1, :].rearrange("p (t s) -> p t s", t=TT)
            does(None, dve.tensor_tensor, by_token, by_token, n_gate[:, :, 0, :], ALU.mult)
            settle()
            does("sparse pc", dve.tensor_tensor, sc, sc, wide(n_cs[:, 1, :], CMP_PAD), ALU.mult)
            out_turn_vector(dve, "sparse", at, sparse, 4)

        with Arena() as take:
            r_late = take("r_late", [P, 3 * 1024])
            r_a, r_kk = take("r_a", [P, 4, SEQ]), take("r_kk", [P, 4, SEQ])
            r_ld, r_c, r_e1, r_e1p, r_e2 = (take(f"r_{i}", [P, 4, SEQ]) for i in ("ld", "c", "e1", "e1p", "e2"))
            r_kt, r_bt = take("r_kt", [P, 512]), take("r_bt", [P, 512])
            r_rhs, r_sa = take("r_rhs", [P, 4, 64]), take("r_sa", [P, 4, 64])
            r_s1 = take("r_s1", [P, 2, P])
            r_mid = take("r_mid", [P, 4, 2])
            r_f = take("r_f", [P, 4])
            r_bonus = take("r_bonus", [P, TT, 8])
            take.beyond_split("r_filler")
            r_stat = take("r_stat", [P, 6, 16])
            r_diff = take("r_diff", [P, 3, SEQ])
            r_tok = take("r_tok", [P, TT, RWKV_K * COLS])
            r_pb = take("r_pb", [P, 14, SEQ + 1])

        def matrices(ap, first=0):
            return ap[:, first:first + 8 * P].rearrange("p (m c) -> p m c", m=8)

        r_pm, flat_tok = r_pb[:, :, 1:1 + SEQ], r_tok.rearrange("p t c -> p (t c)")
        r_A, r_T, r_L, r_R, r_B = (matrices(x.rearrange("p c t -> p (c t)")) for x in (r_ld, r_c, r_e1, r_e1p, r_e2))
        r_U, r_Y, r_AM = matrices(r_late), matrices(flat_tok), matrices(flat_tok, 8 * P)
        r_g, r_v = (r_late[:, c0:c0 + 2 * 512].rearrange("p (t c) -> p t c", t=2) for c0 in (1024, 2048))
        r_add, r_gate = (flat_tok[:, c0:c0 + TT * 512].rearrange("p (t c) -> p t c", t=TT) for c0 in (0, TT * 512))
        r_square = r_diff.rearrange("p c t -> p (c t)")[:, 0:512]
        R_KINDS = "k" * RWKV_K + "t" * (RWKV_T - 1) + "v"
        NEG_ROOT_E = -math.exp(-0.5)
        R_MATRICES = ("A", "L", "R", "B")

        def r_place(s, j, b):
            if s < RWKV_K:
                return [(r_tok[:, j, s * COLS:(s + 1) * COLS], b[:, 0:COLS])]
            return [(r_pb[:, 3 * (s - RWKV_K) + j, 1:1 + SEQ], b[:, 0:SEQ])]

        def chunk_of(x, i, c, parity):
            return x[64 * parity:64 * parity + 64, i, c * P:(c + 1) * P]

        def rwkv_tensor(pe, at):
            g0 = first_step[at]
            proj_tensor(pe, "rwkv", g0, R_KINDS, f"norm {at}")
            pe.wait_ge(*after("rwkv kk square"))
            for i in range(2):
                b = open_bank(pe, f"rwkv kn {i}")
                pe.matmul(b, table("pair_ones"), r_e2[:, 2 * i:2 * i + 2, :], start=True, stop=True).then_inc(*rwkv.tensor(f"rwkv kn {i}"))
            lora = col("lora")
            for name, rows_, label in (("w", slice(0, 64), "rwkv tanh"), ("a", slice(64, P), "rwkv mixed")):
                pe.wait_ge(*after(label))
                for i in range(2):
                    b = open_bank(pe, f"rwkv {name} {i}")
                    for j in range(2):
                        c = 2 * i + j
                        ins = pe.matmul(b[:, j * SEQ:(j + 1) * SEQ], lora[rows_, c * P:(c + 1) * P], r_pm[rows_, 12, :], start=True, stop=True)
                    ins.then_inc(*rwkv.tensor(f"rwkv {name} {i}"))
            pe.wait_ge(*after("rwkv gate"))
            for t in range(TT):
                b = open_bank(pe, f"rwkv g {t}")
                pe.matmul(b, r_pm[:, 13, t * P:(t + 1) * P], col("g2"), start=True, stop=True).then_inc(*rwkv.tensor(f"rwkv g {t}"))
            pe.wait_ge(*after("rwkv sgu normed"))
            for t in range(TT):
                b = open_bank(pe, f"rwkv sgu {t}")
                for g in range(4):
                    ins = pe.matmul(b[:, g * P:(g + 1) * P], col("sgu_w")[:, g * P:(g + 1) * P], r_tok[:, t, 512 + g * P:512 + (g + 1) * P],
                                    start=True, stop=True)
                ins.then_inc(*rwkv.tensor(f"rwkv sgu {t}"))
            pe.wait_ge(*after("rwkv rk"))
            b = open_bank(pe, "rwkv bonus")
            for t in range(TT):
                for c in range(4):
                    ins = pe.matmul(b[:, 8 * t + 2 * c:8 * t + 2 * c + 2], r_e1[:, c, t * P:(t + 1) * P], table("pair_sel"), start=True, stop=True)
            ins.then_inc(*rwkv.tensor("rwkv bonus"))
            for t in range(TT):
                b = open_bank(pe, f"rwkv v {t}")
                for c in range(4):
                    ins = pe.transpose(b[:, c * P:(c + 1) * P], r_pm[:, 8 + c, t * P:(t + 1) * P], ident)
                ins.then_inc(*rwkv.tensor(f"rwkv v {t}"))
            pe.wait_ge(*after("rwkv decayed"))
            for name, x, c0 in (("kt", r_pm, 4), ("bt", r_a, 0)):
                b = open_bank(pe, f"rwkv {name}")
                for c in range(4):
                    ins = pe.transpose(b[:, c * P:(c + 1) * P], x[:, c0 + c, 0:P], ident)
                ins.then_inc(*rwkv.tensor(f"rwkv {name}"))
            for half in range(2):
                i0 = 2 * half
                operands = {"A": ((r_kk, 0), (r_a, 0)), "L": ((r_pm, 4), (r_kk, 0)), "R": ((r_pm, 4), (r_pm, 0)), "B": ((r_a, 0), (r_pm, 0))}
                for name in R_MATRICES:
                    (x, x0), (y, y0) = operands[name]
                    for par in range(2):
                        b = open_bank(pe, f"rwkv {name} {half} {par}")
                        for ti in range(2):
                            for c in range(2):
                                m = 2 * ti + c
                                ins = pe.matmul(b[:, m * P:(m + 1) * P], chunk_of(x, x0 + i0 + ti, c, par), chunk_of(y, y0 + i0 + ti, c, par),
                                                start=True, stop=True)
                        ins.then_inc(*rwkv.tensor(f"rwkv {name} {half} {par}"))
                inverse_tensor(pe, f"rwkv{half}", r_T, r_U, r_Y, r_AM)
                for par in range(2):
                    pe.wait_ge(*after(f"rwkv{half} U {LEVELS - 1} {par}"))
                pe.wait_ge(*after(f"rwkv masked {half}"))
                pe.wait_ge(*after("used rwkv bt"))
                for c in range(2):
                    tag = f"{half} {c}"
                    heads = [(ti, par, 2 * ti + par, 4 * par + 2 * ti + c, r_v[:, c, (i0 + ti) * P + 64 * par:(i0 + ti) * P + 64 * par + 64])
                             for ti in range(2) for par in range(2)]
                    if c == 1:
                        pe.wait_ge(*after(f"rwkv s1 {half} 1"))

                    def from_state(b, ti, x, x0):
                        if c == 1:
                            pe.matmul(b[:, ti * P:(ti + 1) * P], x[:, x0 + i0 + ti, P:SEQ], r_s1[:, ti, :], start=True, stop=False)

                    b = open_bank(pe, f"rwkv rhs {tag}")
                    for ti, par, hh, m, v in heads:
                        if par == 0:
                            from_state(b, ti, r_kk, 0)
                        ins = pe.matmul(b[:, hh * 64:hh * 64 + 64], r_L[:, m, :], v, start=c == 0, stop=c == 0 or par == 1)
                    ins.then_inc(*rwkv.tensor(f"rwkv rhs {tag}"))
                    pe.wait_ge(*after(f"used rwkv rhs {tag}"))
                    b = open_bank(pe, f"rwkv sa {tag}")
                    for ti, par, hh, m, v in heads:
                        ins = pe.matmul(b[:, hh * 64:hh * 64 + 64], r_U[:, m, :], r_rhs[:, hh, :], start=True, stop=True)
                    ins.then_inc(*rwkv.tensor(f"rwkv sa {tag}"))
                    pe.wait_ge(*after(f"used rwkv sa {tag}"))
                    b = open_bank(pe, f"rwkv y {tag}")
                    for ti in range(2):
                        from_state(b, ti, r_pm, 0)
                        for _, par, hh, m, v in heads[2 * ti:2 * ti + 2]:
                            pe.matmul(b[:, hh * 64:hh * 64 + 64], r_R[:, m, :], v, start=c == 0, stop=False)
                            ins = pe.matmul(b[:, hh * 64:hh * 64 + 64], r_B[:, m, :], r_sa[:, hh, :], start=False, stop=c == 0 or par == 1)
                    ins.then_inc(*rwkv.tensor(f"rwkv y {tag}"))
                    if c == 0:
                        b = open_bank(pe, f"rwkv ds {half}")
                        for ti in range(2):
                            tile = slice((i0 + ti) * P, (i0 + ti + 1) * P)
                            pe.matmul(b[:, ti * P:(ti + 1) * P], r_kt[:, tile], r_v[:, 0, tile], start=True, stop=False)
                            ins = pe.matmul(b[:, ti * P:(ti + 1) * P], r_bt[:, tile], r_sa[:, 2 * ti:2 * ti + 2, :], start=False, stop=True)
                        ins.then_inc(*rwkv.tensor(f"rwkv ds {half}"))
            gated = [f"rwkv gated {t}" for t in range(TT)]
            turn_tensor(pe, "rwkv", rwkv, KT, gated, range(TT - 1))
            out_tensor(pe, "rwkv", g0 + RWKV_K + RWKV_T,
                       after_first=lambda: turn_tensor(pe, "rwkv", rwkv, KT, gated, range(TT - 1, TT)))

        def rwkv_scalar(act, at):
            def does(label, *args, **kw):
                act.activation(*args, **kw).then_inc(*rwkv.scalar(label))

            def gelu():
                wait_proj(act, "rwkv", R_KINDS, range(RWKV_K))
                does("rwkv gelu", r_tok[:, :, 0:1024], r_tok[:, :, 0:1024], ACT.Gelu_apprx_tanh)

            def group_roots():
                act.wait_ge(*after("rwkv sgu var"))
                does("rwkv sgu root", r_stat[:, 2, 0:8], r_stat[:, 1, 0:8], ACT.Sqrt, scale=1.0 / P, bias=ln_eps)

            proj_copies(act, "rwkv", first_step[at], R_KINDS, 0, r_place, {RWKV_K - 1: gelu, RWKV_K + 1: group_roots})
            act.wait_ge(*after("rwkv kk"))
            does("rwkv kk square", r_e2[:, :, :], r_kk[:, :, :], ACT.Square)
            act.wait_ge(*after("rwkv kk clipped"))
            does("rwkv kk root", r_e2[:, :, :], r_e2[:, :, :], ACT.Sqrt)
            act.wait_ge(*after("rwkv mixed"))
            does("rwkv tanh", r_pm[0:64, 12, :], r_pm[0:64, 12, :], ACT.Tanh)
            does("rwkv gate", r_pm[:, 13, :], r_pm[:, 13, :], ACT.Sigmoid)
            for name, dst, bias in (("w", r_ld, "w0"), ("a", r_a, "a0")):
                for i in range(2):
                    act.wait_ge(*after(f"rwkv {name} {i}"))
                    for j in range(2):
                        c = 2 * i + j
                        does(f"used rwkv {name} {i}", dst[:, c, :], bank(f"rwkv {name} {i}")[:, j * SEQ:(j + 1) * SEQ], ACT.Sigmoid,
                             bias=col(bias)[:, c:c + 1])
            for t in range(TT):
                act.wait_ge(*after(f"rwkv g {t}"))
                does(f"used rwkv g {t}", r_g[:, t, :], bank(f"rwkv g {t}"), ACT.Copy)
            for t in range(TT):
                act.wait_ge(*after(f"rwkv v {t}"))
                does(f"used rwkv v {t}", r_v[:, t, :], bank(f"rwkv v {t}"), ACT.Copy)
            act.wait_ge(*after("rwkv exponents"))
            act.wait_ge(*after("rwkv bonus"))
            act.wait_ge(*after("rwkv kk unit"))
            does(None, r_f[:, :], r_f[:, :], ACT.Exp)
            does(None, r_e1[:, :, :], r_c[:, :, :], ACT.Exp)
            does(None, r_e1p[:, :, :], r_e1p[:, :, :], ACT.Exp)
            does("rwkv exp", r_e2[:, :, :], r_c[:, :, :], ACT.Exp, scale=-1.0)
            for name, dst in (("kt", r_kt), ("bt", r_bt)):
                act.wait_ge(*after(f"rwkv {name}"))
                does(f"used rwkv {name}", dst[:, :], bank(f"rwkv {name}"), ACT.Copy)
            for half in range(2):
                inverse_scalar(act, f"rwkv{half}", r_U, r_Y)
                for c in range(2):
                    tag = f"{half} {c}"
                    act.wait_ge(*after(f"rwkv rhs {tag}"))
                    does(f"used rwkv rhs {tag}", r_rhs.rearrange("p h d -> p (h d)"), bank(f"rwkv rhs {tag}")[:, 0:SEQ], ACT.Copy)
                    act.wait_ge(*after(f"rwkv sa {tag}"))
                    does(f"used rwkv sa {tag}", r_sa.rearrange("p h d -> p (h d)"), bank(f"rwkv sa {tag}")[:, 0:SEQ], ACT.Copy, scale=-1.0)

            def root(t):
                act.wait_ge(*after(f"rwkv y var {t}"))
                does(f"rwkv y root {t}", r_stat[:, 4, 8 * t:8 * t + 8], r_stat[:, 3, 8 * t:8 * t + 8], ACT.Sqrt, scale=1.0 / 64, bias=gn_eps)

            root(0)
            out_scalar(act, at, "rwkv", "used rwkv y 1 1", rwkv, meanwhile=lambda: root(1))

        def rwkv_pool(pool, at):
            proj_pool(pool, first_step[at], len(R_KINDS))
            for half in range(2):
                inverse_pool(pool, f"rwkv{half}", r_A, r_AM)
            pool.wait_ge(*after(f"rwkv1 U {LEVELS - 1} 1"))
            for t in range(TT):
                pool.tensor_tensor(r_add[:, t, :].rearrange("p (g c) -> p g c", c=64), r_v[:, t, :].rearrange("p (g c) -> p g c", c=64),
                                   wide(r_bonus[:, t, :], 64), ALU.mult).then_inc(*rwkv.pool(f"rwkv bonus v {t}"))
            for t in range(TT):
                pool.wait_ge(*after(f"rwkv bonus v {t}"))
                pool.tensor_tensor(r_add[:, t, :], r_add[:, t, :], row("gn_b"), ALU.add).then_inc(*rwkv.pool(f"rwkv add {t}"))
            pool.tensor_copy(r_gate[:, :, :], r_g[:, :, :]).then_inc(*rwkv.pool("rwkv gate kept"))
            out_pool(pool, at)

        def rwkv_vector(dve, at):
            def does(label, op, *args):
                op(*args).then_inc(*rwkv.vector(label))

            def settle():
                dve.wait_ge(*rwkv.vector.so_far())

            def groups(x, n):
                return x.rearrange("p (g c) -> p g c", c=n)

            def centre(x, stat, n, label):
                does(None, dve.tensor_reduce, stat, groups(x, n), AX.X, ALU.add)
                settle()
                does(None, dve.tensor_scalar, stat, stat, 1.0 / n, None, ALU.mult)
                settle()
                does(label, dve.tensor_tensor, groups(x, n), groups(x, n), wide(stat, n), ALU.subtract)

            def variances(t):
                y = O[:, t, 512:1024]
                settle()
                centre(y, r_stat[:, 5, 8 * t:8 * t + 8], 64, None)
                settle()
                does(None, dve.tensor_tensor, r_square, y, y, ALU.mult)
                settle()
                does(f"rwkv y var {t}", dve.tensor_reduce, r_stat[:, 3, 8 * t:8 * t + 8], groups(r_square, 64), AX.X, ALU.add)

            def normalise(t):
                y, r = O[:, t, 512:1024], r_stat[:, 4, 8 * t:8 * t + 8]
                dve.wait_ge(*after(f"rwkv y root {t}"))
                does(None, dve.reciprocal, r, r)
                settle()
                does(None, dve.tensor_tensor, groups(y, 64), groups(y, 64), wide(r, 64), ALU.mult)
                settle()
                does(None, dve.tensor_tensor, y, y, row("gn_g"), ALU.mult)
                settle()
                does(None, dve.tensor_tensor, y, y, r_add[:, t, :], ALU.add)
                settle()
                does(f"rwkv gated {t}", dve.tensor_tensor, y, y, r_gate[:, t, :], ALU.mult)

            does(None, dve.memset, r_pb[:, :, 0:1], 0.0)
            does(None, dve.tensor_tensor, col("sgu_w").rearrange("p (g c) -> p g c", g=4), col("sgu_w").rearrange("p (g c) -> p g c", g=4),
                 over(table("incl_t"), 4), ALU.mult)
            def mix(s):
                wait_proj(dve, "rwkv", R_KINDS, [s])
                settle()
                c0 = 3 * (s - RWKV_K)
                n = min(3, 14 - c0)
                does(None, dve.tensor_tensor, r_diff[:, 0:n, :], r_pb[:, c0:c0 + n, 0:SEQ], r_pb[:, c0:c0 + n, 1:1 + SEQ], ALU.subtract)
                settle()
                for c in range(n):
                    does("rwkv mixed", dve.scalar_tensor_tensor, r_pm[:, c0 + c, :], r_diff[:, c, :], col("mu")[:, c0 + c:c0 + c + 1], r_pm[:, c0 + c, :], ALU.mult, ALU.add)

            def group_var(t):
                dve.wait_ge(*after("rwkv gelu"))
                pv = r_tok[:, t, 512:1024]
                centre(pv, r_stat[:, 0, 4 * t:4 * t + 4], P, None)
                settle()
                does(None, dve.tensor_tensor, O[:, t, 512:1024], pv, pv, ALU.mult)
                settle()
                does("rwkv sgu var", dve.tensor_reduce, r_stat[:, 1, 4 * t:4 * t + 4], groups(O[:, t, 512:1024], P), AX.X, ALU.add)

            def group_norm(t):
                if t == 0:
                    dve.wait_ge(*after("rwkv sgu root"))
                    does(None, dve.reciprocal, r_stat[:, 2, 0:8], r_stat[:, 2, 0:8])
                    settle()
                pv = r_tok[:, t, 512:1024]
                does(None, dve.tensor_tensor, groups(pv, P), groups(pv, P), wide(r_stat[:, 2, 4 * t:4 * t + 4], P), ALU.mult)
                settle()
                does(None, dve.tensor_tensor, pv, pv, row("ln_g"), ALU.mult)
                settle()
                does("rwkv sgu normed", dve.tensor_tensor, pv, pv, row("ln_b"), ALU.add)

            def after_step(s):
                if s == RWKV_K:
                    group_var(0)
                elif s == RWKV_K + 1:
                    mix(s - 1)
                    group_var(1)
                elif s > RWKV_K + 1:
                    mix(s - 1)
                    group_norm(s - RWKV_K - 2)

            proj_copies(dve, "rwkv", first_step[at], R_KINDS, 1, r_place, {s: lambda s=s: after_step(s) for s in range(RWKV_K, RWKV_K + 4)})
            for s in (RWKV_K + RWKV_T - 1, RWKV_K + RWKV_T - 2):
                mix(s)
            settle()
            for c in range(4):
                does("rwkv kk", dve.tensor_scalar, r_kk[:, c, :], r_pm[:, 4 + c, :], col("k_k")[:, c:c + 1], None, ALU.mult)
            for i in range(2):
                dve.wait_ge(*after(f"rwkv kn {i}"))
                does("rwkv kk clipped", dve.tensor_scalar, r_e2[:, 2 * i:2 * i + 2, :], bank(f"rwkv kn {i}").rearrange("p (c t) -> p c t", c=2),
                     1e-24, None, ALU.max)
                marks[f"used rwkv kn {i}"] = marks["rwkv kk clipped"]
            dve.wait_ge(*after("rwkv kk root"))
            does(None, dve.reciprocal, r_e2[:, :, :], r_e2[:, :, :])
            settle()
            does("rwkv kk unit", dve.tensor_tensor, r_kk[:, :, :], r_kk[:, :, :], r_e2[:, :, :], ALU.mult)
            settle()
            for t in range(TT):
                dve.wait_ge(*after(f"rwkv sgu {t}"))
                does(f"used rwkv sgu {t}", dve.tensor_tensor, four(O[:, t, 0:512]), four(bank(f"rwkv sgu {t}")), wide(col("sgu_b"), P), ALU.add)
            settle()
            does(None, dve.tensor_tensor, O[:, :, 0:512], O[:, :, 0:512], r_tok[:, :, 0:512], ALU.mult)
            dve.wait_ge(*after("used rwkv g 1"))
            for c in range(4):
                does(None, dve.tensor_scalar, r_c[:, c, :], r_a[:, c, :], 1.0, col("k_a")[:, c:c + 1], ALU.subtract, ALU.mult)
            does(None, dve.tensor_scalar, r_ld[:, :, :], r_ld[:, :, :], NEG_ROOT_E, None, ALU.mult)
            settle()
            k = r_pm[:, 4:8, :]
            does(None, dve.scalar_tensor_tensor, k, r_c[:, :, :], 1.0, k, ALU.add, ALU.mult)
            settle()
            for c in range(4):
                does("rwkv rk", dve.scalar_tensor_tensor, r_e1[:, c, :], r_pm[:, c, :], col("r_k")[:, c:c + 1], r_pm[:, 4 + c, :], ALU.mult, ALU.mult)
            for c in range(4):
                for ch in range(2):
                    part = slice(ch * P, (ch + 1) * P)
                    does(None, dve.tensor_tensor_scan, r_c[:, c, part], ones, r_ld[:, c, part], 0.0, ALU.mult, ALU.add)
            settle()
            does(None, dve.tensor_scalar, r_mid[:, :, :], r_c.rearrange("p c (h t) -> p c h t", h=2)[:, :, :, P - 1], 0.5, None, ALU.mult)
            settle()
            does(None, dve.tensor_tensor, r_f[:, :], r_mid[:, :, 0], r_mid[:, :, 1], ALU.add)
            chunks = r_c.rearrange("p c (h t) -> p (c h) t", h=2)
            does(None, dve.tensor_tensor, chunks, chunks, wide(r_mid.rearrange("p c h -> p (c h)"), P), ALU.subtract)
            settle()
            does("rwkv exponents", dve.tensor_tensor, r_e1p[:, :, :], r_c[:, :, :], r_ld[:, :, :], ALU.subtract)
            does("rwkv b", dve.tensor_tensor, r_a[:, :, :], r_kk[:, :, :], r_a[:, :, :], ALU.mult)
            dve.wait_ge(*after("rwkv bonus"))
            does("used rwkv bonus", dve.tensor_copy, r_bonus.rearrange("p t h -> p (t h)"), bank("rwkv bonus")[:, 0:16])
            dve.wait_ge(*after("rwkv exp"))
            settle()
            for x, e in ((r_pm[:, 0:4, :], r_e1), (k, r_e2), (r_kk[:, :, :], r_e1p), (r_a[:, :, :], r_e2)):
                does("rwkv decayed", dve.tensor_tensor, x, x, e[:, :, :], ALU.mult)
            settle()
            for half in range(2):
                for name, dst, mask in (("A", r_A, "strict"), ("L", r_L, "upper"), ("R", r_R, "incl_t"), ("B", r_B, "incl_t")):
                    for par in range(2):
                        dve.wait_ge(*after(f"rwkv {name} {half} {par}"))
                        does(f"used rwkv {name} {half} {par}", dve.scalar_tensor_tensor, dst[:, 4 * par:4 * par + 4, :],
                             four(bank(f"rwkv {name} {half} {par}")), 1e30, over(table(mask), 4), ALU.min, ALU.mult)
                    if name == "A":
                        settle()
                marks[f"rwkv masked {half}"] = marks[f"used rwkv B {half} 1"]
                inverse_vector(dve, f"rwkv{half}", r_A, r_T, r_U, r_AM)
                for c in range(2):
                    if c == 1:
                        dve.wait_ge(*after(f"rwkv ds {half}"))
                        for ti in range(2):
                            does(f"rwkv s1 {half} {ti}", dve.scalar_tensor_tensor, r_s1[:, ti, :], bank(f"rwkv ds {half}")[:, ti * P:(ti + 1) * P],
                                 r_f[:, 2 * half + ti:2 * half + ti + 1], table("pair_ones"), ALU.mult, ALU.mult)
                        marks[f"used rwkv ds {half}"] = marks[f"rwkv s1 {half} 1"]
                        if half == 1:
                            variances(0)
                            dve.wait_ge(*after("rwkv gate kept"))
                    dve.wait_ge(*after(f"rwkv y {half} {c}"))
                    does(f"used rwkv y {half} {c}", dve.tensor_copy, O[:, c, 512 + 256 * half:768 + 256 * half], bank(f"rwkv y {half} {c}")[:, 0:SEQ])
            normalise(0)
            out_turn_vector(dve, "rwkv", at, rwkv, meanwhile=lambda: (variances(1), normalise(1)))

        PAIR = 2 * EXPERT_STEPS
        UP_BANK, AUX_BANK = 4, 6
        CHUNKS = [(t, h) for t in range(TT) for h in range(2)]

        with Arena() as take:
            take.beyond_split("m_filler")
            take("m_kept", [P, 8 * SEQ + D_MODEL])
            hn_hi, hn_lo = (take(n, [P, TT, D_MODEL], F32R) for n in ("hn_hi", "hn_lo"))
            y_hi, y_lo = (take(n, [P, TT, D_MODEL], F32R) for n in ("y_hi", "y_lo"))
            m_pick = take("m_pick", [P, TT, SEQ], F32R)
            m_back = take("m_back", [P, 2, TT, SEQ], F32R)
            m_now = take("m_now", [P, 2, TT])
            m_gate = take("m_gate", [P, 2, TT])
            m_route = take("m_route", [P, EXPERTS + 1, 2, TT])
            m_logits, m_rank = (take(n, [P, TT, EXPERTS]) for n in ("m_logits", "m_rank"))
            m_above, m_equal = (take(n, [P, TT, EXPERTS, EXPERTS]) for n in ("m_above", "m_equal"))
            m_one = take("m_one", [P, 2, TT])
            m_most = take("m_most", [P, 1])
            m_most_int = take("m_most_int", [P, 1], mybir.dt.int32)
            m_router_hi, m_router_lo = (take(n, [P, KT, EXPERTS], F32R) for n in ("m_router_hi", "m_router_lo"))

        turned_ready = sem("moe_turned_ready")
        pick_ready = sem("moe_pick_ready")
        piece_ready = sem("moe_piece_ready")
        even_taken = sem("moe_even_taken")
        odd_taken = sem("moe_odd_taken")
        y_hi_ready = sem("moe_y_hi_ready")
        y_ready = sem("moe_y_ready")
        chunk_ready = sem("moe_chunk_ready")
        chunk_added = sem("moe_chunk_added")

        def pieces(tiles):
            per = 512 // (tiles * P)
            return ["back", "gate"] + [(part_, k) for k in range(0, KT, per) for part_ in range(2)]

        def jobs(tiles):
            n = len(pieces(tiles))
            if tiles == 1:
                plan = [(2 + p, 1, ("piece", p)) for p in range(n)]
                plan += [(EXPERT_STEPS + 5 + min(p, 5), 2, ("piece", p)) for p in range(n)]
            else:
                plan = [(EXPERT_STEPS * x - 1, x, ("piece", p)) for x in (1, 2) for p in range(n)]
            plan += [(EXPERT_STEPS + 1 + c, 0, ("chunk", c)) for c in range(len(CHUNKS))]
            plan += [(0, 1, ("pick", 0)), (EXPERT_STEPS + 1, 2, ("pick", 0)), (EXPERT_STEPS, 0, ("result", 0))]
            return [[job[1:] for job in plan if job[0] == n] for n in range(PAIR)]

        def gathered(x, tiles, parity, k):
            return x[:, k, 0:2 * P] if tiles == 2 else x[:, k, parity * P:(parity + 1) * P]

        def up_products(f, tiles):
            return psum[:, UP_BANK + f % 2, 0:tiles * 2 * P].rearrange("p (j o c) -> p j o c", j=tiles, o=2)

        def by_tile(x, f, tiles):
            return x[:, f % 2, 0:tiles * P].rearrange("p (j c) -> p j c", j=tiles)

        def each_pair(eng, at, tiles, step, end):
            f0, g0 = ffn_steps_before[at], moe_first
            with eng.Fori(0, EXPERTS // 2) as i:
                for n in range(PAIR):
                    step(n, i, f0 + n, PAIR * i + f0 + n, g0 + n, PAIR * i + g0 + n)
                end(i)

        def by_load(eng, at, run):
            eng.wait_ge(*after("moe most"))
            most = eng.value_load(m_most_int[0:1, 0:1], min_val=0, max_val=SEQ)
            with eng.If(most > P):
                run(eng, at, 2)
            with eng.Else():
                run(eng, at, 1)

        def moe_tensor(pe, at):
            pe.wait_ge(*after("moe router"))
            b = open_bank(pe, "moe logits")
            for t in range(TT):
                for k in range(KT):
                    ins = three_passes(pe, b[:, EXPERTS * t:EXPERTS * (t + 1)], [x[:, k, t * P:(t + 1) * P] for x in (hT_hi, hT_lo)],
                                       [x[:, k, :] for x in (m_router_hi, m_router_lo)], k == 0, k == KT - 1)
            ins.then_inc(*moe.tensor("moe logits"))
            pe.wait_ge(*after("moe chosen"))
            b = open_bank(pe, "moe before")
            for c, (w0, w1) in enumerate((("upper", None), ("ones", "upper"), ("ones", "ones"))):
                o = b[:, c * EXPERTS:(c + 1) * EXPERTS]
                ins = pe.matmul(o, table(w0), m_rank[:, 0, :], start=True, stop=w1 is None, skip_group_check=True)
                if w1:
                    ins = pe.matmul(o, table(w1), m_rank[:, 1, :], start=False, stop=True, skip_group_check=True)
            ins.then_inc(*moe.tensor("moe before"))
            by_load(pe, at, experts_tensor)

        def experts_tensor(pe, at, tiles):
            slots, n_pieces, half = tiles * P, len(pieces(tiles)), len(pieces(tiles)) // 2

            def piece(x, p, first=False):
                if p == 0:
                    pe.wait_ge(pick_ready, 3 * x + 3)
                if p >= 2 or not first:
                    pe.wait_ge(odd_taken if p % 2 else even_taken, half * x + p // 2)
                b, what = psum[:, AUX_BANK + p % 2, :], pieces(tiles)[p]
                if what == "back":
                    for j in range(tiles):
                        for t in range(TT):
                            ins = pe.transpose(b[:, (j * TT + t) * P:(j * TT + t + 1) * P], m_pick[:, t, j * P:(j + 1) * P].bitcast(F32), ident)
                elif what == "gate":
                    for j in range(tiles):
                        for t in range(TT):
                            ins = pe.matmul(b[:, j:j + 1], m_pick[:, t, j * P:(j + 1) * P].bitcast(F32), m_now[:, 1, t:t + 1],
                                            start=t == 0, stop=t == TT - 1, skip_group_check=True)
                else:
                    source = (hn_hi, hn_lo)[what[0]]
                    for k in range(512 // slots):
                        m = (what[1] + k) * P
                        for t in range(TT):
                            ins = pe.matmul(b[:, k * slots:(k + 1) * slots], source[:, t, m:m + P], m_pick[:, t, 0:slots],
                                            start=t == 0, stop=t == TT - 1, skip_group_check=True)
                ins.then_inc(piece_ready, 1)

            def chunk(e, parity, c):
                t, h = CHUNKS[c]
                if c == 0:
                    pe.wait_ge(y_ready, 2 * tiles * e + 2 * tiles)
                if c >= 2:
                    pe.wait_ge(chunk_added, len(CHUNKS) * e + c - 1)
                terms = [(j, y) for j in range(tiles) for y in (y_hi, y_lo)]
                for n, (j, y) in enumerate(terms):
                    ins = pe.matmul(psum[:, AUX_BANK + c % 2, :], m_back[:, parity, j, t * P:(t + 1) * P], y[:, j, h * 512:(h + 1) * 512],
                                    start=n == 0, stop=n == len(terms) - 1, skip_group_check=True)
                ins.then_inc(chunk_ready, 1)

            def up(n, e, f, fv, g, gv, halves):
                w = [x[:, g % 2, 0:2 * D_MODEL].rearrange("p (o k c) -> p o k c", o=2, k=KT) for x in (w_hi, w_lo)]
                for half_ in halves:
                    if half_ == 0:
                        if n % EXPERT_STEPS == 0:
                            pe.wait_ge(even_taken, half * e + half)
                            pe.wait_ge(odd_taken, half * e + half)
                        pe.wait_ge(lo_ready, 2 * gv + 2)
                        pe.wait_ge(ffn_act_ready, fv - 1)
                    for k in range(half_ * KT // 2, (half_ + 1) * KT // 2):
                        for j in range(tiles):
                            rows_ = [gathered(x, tiles, n // EXPERT_STEPS, k)[:, j * P:(j + 1) * P] for x in (hT_hi, hT_lo)]
                            ins = three_passes(pe, up_products(f, tiles)[:, j, :, :], rows_, [x[:, :, k, :] for x in w],
                                               k == 0 and j == 0, k == KT - 1)
                    if half_ == 1:
                        ins.then_inc(ffn_up_ready, 1)

            def turn(f, fv):
                pe.wait_ge(ffn_gated, 2 * fv + 1)
                for j in range(tiles):
                    ins = pe.transpose(psum[:, UP_BANK + f % 2, j * P:(j + 1) * P], by_tile(gated, f, tiles)[:, j, :], ident)
                ins.then_inc(turned_ready, 1)

            def down(n, e, f, fv, g, gv):
                s = n % EXPERT_STEPS
                pe.wait_ge(lo_last_ready, gv + 1)
                pe.wait_ge(ffn_act_ready, fv + 1)
                if n == EXPERT_STEPS:
                    pe.wait_ge(y_ready, 2 * tiles * e)
                for j in range(tiles):
                    for h in range(2):
                        c = slice(2 * D_MODEL + h * 512, 2 * D_MODEL + (h + 1) * 512)
                        ins = three_passes(pe, psum[:, 2 * j + h, :], [x[:, f % 2, j * P:(j + 1) * P] for x in (act_hi, act_lo)],
                                           [x[:, g % 2, c] for x in (w_hi, w_lo)], s == 0, s == EXPERT_STEPS - 1)
                ins.then_inc(steps_used, 1)

            def step(n, i, f, fv, g, gv):
                up(n, 2 * i + n // EXPERT_STEPS, f, fv, g, gv, (0,))
                if n > 0:
                    turn(f - 1, fv - 1)
                up(n, 2 * i + n // EXPERT_STEPS, f, fv, g, gv, (1,))
                if n > 0:
                    down(n - 1, 2 * i + (n - 1) // EXPERT_STEPS, f - 1, fv - 1, g - 1, gv - 1)
                pe.wait_ge(ffn_up_ready, fv + 1)
                pe.nop().then_inc(early_used, 1)
                for x, (what, p) in jobs(tiles)[n]:
                    if what == "piece":
                        if (x, p) == (2, 0):
                            pe.wait_ge(chunk_added, len(CHUNKS) * 2 * i + len(CHUNKS))
                        piece(2 * i + x, p)
                    elif what == "chunk":
                        chunk(2 * i + x, x % 2, p)

            def end(i):
                n, f0 = PAIR - 1, ffn_steps_before[at]
                turn(f0 + n, PAIR * i + f0 + n)
                down(n, 2 * i + 1, f0 + n, PAIR * i + f0 + n, moe_first + n, PAIR * i + moe_first + n)
                pe.wait_ge(even_taken, half * (2 * i + 2) + half)
                pe.wait_ge(odd_taken, half * (2 * i + 2) + half)
                for c in range(len(CHUNKS)):
                    chunk(2 * i + 1, 1, c)
                pe.wait_ge(chunk_added, len(CHUNKS) * (2 * i + 2))

            for p in range(n_pieces):
                piece(0, p, True)
            each_pair(pe, at, tiles, step, end)

        def moe_scalar(act, at):
            act.wait_ge(*after("moe normed"))
            act.activation(hn_hi[:, :, :], O[:, :, :], ACT.Copy).then_inc(*moe.scalar("moe normed hi"))
            split_hi(act, moe_first, moe_first)
            split_hi(act, moe_first + 1, moe_first + 1, (0, 1))
            act.wait_ge(*after("moe less max"))
            act.activation(m_logits[:, :, :], m_logits[:, :, :], ACT.Exp).then_inc(*moe.scalar("moe exp"))
            by_load(act, at, experts_scalar)

        def experts_scalar(act, at, tiles):
            slots, n_pieces, half = tiles * P, len(pieces(tiles)), len(pieces(tiles)) // 2

            def piece(x, parity, p):
                act.wait_ge(piece_ready, n_pieces * x + p + 1)
                b, what = psum[:, AUX_BANK, :], pieces(tiles)[p]
                if what == "back":
                    ins = act.activation(m_back[:, parity, 0:tiles, :], b[:, 0:tiles * SEQ].rearrange("p (j t) -> p j t", j=tiles), ACT.Copy)
                else:
                    n = 512 // slots
                    ins = act.activation(gathered(hT_hi, tiles, parity, slice(what[1], what[1] + n)), b.rearrange("p (k s) -> p k s", k=n), ACT.Copy)
                ins.then_inc(even_taken, 1)

            def result(e, parity, gv):
                act.wait_ge(steps_used, gv + 1)
                act.wait_ge(odd_taken, half * e + 1)
                for j in range(tiles):
                    for h in range(2):
                        act.activation(y_hi[:, j, h * 512:(h + 1) * 512], psum[:, 2 * j + h, :], ACT.Copy, scale=m_gate[:, parity, j:j + 1]) \
                           .then_inc(y_hi_ready, 1)

            def step(n, i, f, fv, g, gv):
                def split_later(ahead, parts):
                    e = 2 * i + (n + ahead) // EXPERT_STEPS
                    with ExitStack() as if_there:
                        if n + ahead >= PAIR:
                            if_there.enter_context(act.If(i < EXPERTS // 2 - 1))
                        split_hi(act, g + ahead, gv + ahead, parts, e)

                act.wait_ge(ffn_up_ready, fv + 1)
                act.wait_ge(ffn_act_ready, fv - 1)
                act.activation(by_tile(silu, f, tiles), up_products(f, tiles)[:, :, 0, :], ACT.Silu).then_inc(ffn_silu_ready, 1)
                split_later(2, (0, 1))
                for x, (what, p) in jobs(tiles)[n]:
                    if what == "piece" and p % 2 == 0:
                        piece(2 * i + x, x % 2, p)
                    elif what == "result":
                        result(2 * i + x, x % 2, gv - 1)
                split_later(1, (2,))

            def end(i):
                result(2 * i + 1, 1, PAIR * i + moe_first + PAIR - 1)

            for p in range(0, n_pieces, 2):
                piece(0, 0, p)
            each_pair(act, at, tiles, step, end)

        def moe_pool(pool, at):
            def step(n, i, f, fv, g, gv):
                split_lo_last(pool, g, gv)

            each_pair(pool, at, None, step, lambda i: None)

        def moe_vector(dve, at):
            def does(label, op, *args):
                op(*args).then_inc(*moe.vector(label))

            def settle():
                dve.wait_ge(*moe.vector.so_far())

            router = col("router").rearrange("p (k e) -> p k e", k=KT)
            does(None, dve.tensor_copy, m_router_hi[:, :, :], router)
            settle()
            does("moe router", dve.tensor_tensor, m_router_lo[:, :, :], router, m_router_hi[:, :, :].bitcast(F32), ALU.subtract)
            for ins in gained(dve, at, O):
                ins.then_inc(*moe.vector("moe normed"))
            dve.wait_ge(*after("moe normed hi"))
            does(None, dve.tensor_tensor, hn_lo[:, :, :], O[:, :, :], hn_hi[:, :, :].bitcast(F32), ALU.subtract)
            dve.wait_ge(*after("moe logits"))
            does("used moe logits", dve.tensor_tensor, m_logits[:, :, :], bank("moe logits")[:, 0:TT * EXPERTS].rearrange("p (t e) -> p t e", t=TT),
                 over(row("router_b"), TT), ALU.add)
            settle()
            for t in range(TT):
                l = m_logits[:, t, :]
                does(None, dve.tensor_tensor, m_above[:, t, :, :], over(l, EXPERTS), wide(l, EXPERTS), ALU.is_gt)
                does(None, dve.tensor_tensor, m_equal[:, t, :, :], over(l, EXPERTS), wide(l, EXPERTS), ALU.is_equal)
            does(None, dve.tensor_reduce, m_one[:, 0, :], m_logits[:, :, :], AX.X, ALU.max)
            settle()
            for t in range(TT):
                does(None, dve.tensor_tensor, m_equal[:, t, :, :], m_equal[:, t, :, :], table("lower8").rearrange("p (e f) -> p e f", e=EXPERTS), ALU.mult)
            settle()
            does(None, dve.tensor_tensor, m_above[:, :, :, :], m_above[:, :, :, :], m_equal[:, :, :, :], ALU.add)
            does("moe less max", dve.tensor_tensor, m_logits[:, :, :], m_logits[:, :, :], wide(m_one[:, 0, :], EXPERTS), ALU.subtract)
            settle()
            does(None, dve.tensor_reduce, m_rank[:, :, :], m_above[:, :, :, :], AX.X, ALU.add)
            settle()
            does("moe chosen", dve.tensor_scalar, m_rank[:, :, :], m_rank[:, :, :], 1.5, None, ALU.is_lt)
            settle()
            dve.wait_ge(*after("moe exp"))
            does(None, dve.tensor_tensor, m_logits[:, :, :], m_logits[:, :, :], m_rank[:, :, :], ALU.mult)
            settle()
            does(None, dve.tensor_reduce, m_one[:, 1, :], m_logits[:, :, :], AX.X, ALU.add)
            settle()
            does(None, dve.reciprocal, m_one[:, 1, :], m_one[:, 1, :])
            settle()
            does(None, dve.tensor_tensor, m_route[:, 0:EXPERTS, 1, :].rearrange("p e t -> p t e"), m_logits[:, :, :],
                 wide(m_one[:, 1, :], EXPERTS), ALU.mult)
            does(None, dve.memset, m_route[:, EXPERTS, 0, :], -1.0)
            does(None, dve.memset, m_route[:, EXPERTS, 1, :], 0.0)
            dve.wait_ge(*after("moe before"))
            b = bank("moe before")
            does(None, dve.scalar_tensor_tensor, m_rank[:, :, :], b[:, 0:TT * EXPERTS].rearrange("p (t e) -> p t e", t=TT), 1.0,
                 m_rank[:, :, :], ALU.add, ALU.mult)
            does("used moe before", dve.tensor_reduce, m_most[:, :], b[:, TT * EXPERTS:(TT + 1) * EXPERTS], AX.X, ALU.max)
            settle()
            does(None, dve.tensor_scalar, m_route[:, 0:EXPERTS, 0, :].rearrange("p e t -> p t e"), m_rank[:, :, :], -1.0, None, ALU.add)
            does("moe most", dve.tensor_copy, m_most_int[:, :], m_most[:, :])
            for g in range(moe_first, moe_first + 2):
                split_lo(dve, g, g)
            settle()
            by_load(dve, at, experts_vector)
            for t in range(TT):
                dve.nop().then_inc(*ffn.vector(f"x {at + 1} {t}"))

        def experts_vector(dve, at, tiles):
            slots, n_pieces, half = tiles * P, len(pieces(tiles)), len(pieces(tiles)) // 2

            def pick(x, first=False):
                if not first:
                    dve.wait_ge(piece_ready, n_pieces * x)
                dve.tensor_copy(m_now[:, :, :], m_route[:, x, :, :]).then_inc(pick_ready, 1)
                dve.wait_ge(pick_ready, 3 * x + 1)
                for t in range(TT):
                    dve.tensor_scalar(m_pick[:, t, 0:slots], table("slots")[:, 0:slots], m_now[:, 0, t:t + 1], None, ALU.is_equal) \
                       .then_inc(pick_ready, 1)

            def piece(x, parity, p):
                dve.wait_ge(piece_ready, n_pieces * x + p + 1)
                b, what = psum[:, AUX_BANK + 1, :], pieces(tiles)[p]
                if what == "gate":
                    ins = dve.tensor_copy(m_gate[:, parity, 0:tiles], b[:, 0:tiles])
                else:
                    n = 512 // slots
                    ins = dve.tensor_copy(gathered(hT_lo, tiles, parity, slice(what[1], what[1] + n)), b.rearrange("p (k s) -> p k s", k=n))
                ins.then_inc(odd_taken, 1)

            def result(e, parity):
                for j in range(tiles):
                    for h in range(2):
                        dve.wait_ge(y_hi_ready, 2 * tiles * e + 2 * j + h + 1)
                        c = slice(h * 512, (h + 1) * 512)
                        dve.scalar_tensor_tensor(y_lo[:, j, c], psum[:, 2 * j + h, :], m_gate[:, parity, j:j + 1], y_hi[:, j, c].bitcast(F32),
                                                 ALU.mult, ALU.subtract).then_inc(y_ready, 1)

            def chunk(e, c):
                t, h = CHUNKS[c]
                dve.wait_ge(chunk_ready, len(CHUNKS) * e + c + 1)
                x = X[:, t, h * 512:(h + 1) * 512]
                dve.tensor_tensor(x, x, psum[:, AUX_BANK + c % 2, :], ALU.add).then_inc(chunk_added, 1)

            def step(n, i, f, fv, g, gv):
                def split_later(ahead, parts):
                    with ExitStack() as if_there:
                        if n + ahead >= PAIR:
                            if_there.enter_context(dve.If(i < EXPERTS // 2 - 1))
                        split_lo(dve, g + ahead, gv + ahead, parts)

                dve.wait_ge(ffn_silu_ready, fv + 1)
                dve.tensor_tensor(by_tile(gated, f, tiles), by_tile(silu, f, tiles), up_products(f, tiles)[:, :, 1, :], ALU.mult) \
                   .then_inc(ffn_gated, 1)
                split_later(2, (0,))
                for x, (what, p) in jobs(tiles)[n]:
                    if what == "piece" and p % 2:
                        piece(2 * i + x, x % 2, p)
                    elif what == "pick":
                        pick(2 * i + x)
                    elif what == "result":
                        result(2 * i + x, x % 2)
                    elif what == "chunk":
                        chunk(2 * i + x, p)
                dve.wait_ge(turned_ready, PAIR * i + n + 1)
                dve.wait_ge(steps_used, gv - 1)
                operand = psum[:, UP_BANK + f % 2, 0:slots]
                dve.tensor_copy(act_hi[:, f % 2, 0:slots], operand).then_inc(ffn_gated, 1)
                dve.wait_ge(ffn_gated, 2 * fv + 2)
                dve.tensor_tensor(act_lo[:, f % 2, 0:slots], operand, act_hi[:, f % 2, 0:slots].bitcast(F32), ALU.subtract) \
                   .then_inc(ffn_act_ready, 1)
                split_later(2, (1,))

            def end(i):
                result(2 * i + 1, 1)
                for c in range(len(CHUNKS)):
                    chunk(2 * i + 1, c)

            pick(0, True)
            for p in range(1, n_pieces, 2):
                piece(0, 0, p)
            each_pair(dve, at, tiles, step, end)
            dve.wait_ge(chunk_added, len(CHUNKS) * EXPERTS)

        MIXERS = {"delta": {"tensor": delta_tensor, "scalar": delta_scalar, "vector": delta_vector, "pool": delta_pool},
                  "attention": {"tensor": attention_tensor, "scalar": attention_scalar, "vector": attention_vector,
                                "pool": attention_pool},
                  "rwkv": {"tensor": rwkv_tensor, "scalar": rwkv_scalar, "vector": rwkv_vector, "pool": rwkv_pool},
                  "sparse": {"tensor": sparse_tensor, "scalar": sparse_scalar, "vector": sparse_vector, "pool": sparse_pool}}

        FIRST_LOADS, LOADS = 3, 3
        for t in range(TT):
            marks[f"x 0 {t}"] = ("first_loaded", 16 * FIRST_LOADS)
        first_mixer = min([at for at, (kind, _) in enumerate(NETWORK) if kind not in ("ffn", "final")], default=None)

        @block.tensor
        def _(pe):
            pe.wait_ge(first_loaded, 16 * FIRST_LOADS)
            for at, (kind, n) in enumerate(NETWORK):
                if at == first_mixer:
                    pe.wait_ge(loaded, 16 * LOADS)
                if kind == "final":
                    continue
                norm_tensor(pe, at)
                if kind == "moe":
                    wait_hT(pe, f"norm {at}")
                    moe_tensor(pe, at)
                elif kind == "ffn":
                    ffn_tensor(pe, at)
                else:
                    MIXERS[kind]["tensor"](pe, at)

        @block.scalar
        def _(act):
            act.wait_ge(first_loaded, 16 * FIRST_LOADS)
            split_hi(act, 0, 0)
            for at, (kind, n) in enumerate(NETWORK):
                if at == first_mixer:
                    act.wait_ge(loaded, 16 * LOADS)
                if kind in ("final", "moe"):
                    load_gain_row(act, n if kind == "final" else 2)
                norm_scalar(act, at)
                if kind != "final":
                    norm_turned_scalar(act, at)
                if kind == "moe":
                    moe_scalar(act, at)
                elif kind == "ffn":
                    ffn_scalar(act, at)
                elif kind != "final":
                    MIXERS[kind]["scalar"](act, at)

        @block.vector
        def _(dve):
            dve.wait_ge(first_loaded, 16 * FIRST_LOADS)
            split_lo(dve, 0, 0)
            for at, (kind, n) in enumerate(NETWORK):
                if at == first_mixer:
                    dve.wait_ge(loaded, 16 * LOADS)
                if kind == "final":
                    final_vector(dve, at)
                    continue
                norm_vector(dve, at)
                if kind == "moe":
                    moe_vector(dve, at)
                elif kind == "ffn":
                    ffn_vector(dve, at, 0.5 if n < 6 else 1.0)
                else:
                    MIXERS[kind]["vector"](dve, at)

        @block.gpsimd
        def _(pool):
            split_lo_last(pool, 0, 0)
            for at, (kind, n) in enumerate(NETWORK):
                if at == first_mixer:
                    pool.wait_ge(loaded, 16 * LOADS)
                if kind in MIXERS:
                    MIXERS[kind]["pool"](pool, at)
                elif kind == "moe":
                    moe_pool(pool, at)
                elif kind == "ffn":
                    ffn_pool(pool, at)

        @block.sync
        def _(sp):
            sp.dma_start(X[:, :, :], x_in.rearrange("o (t p) d -> p (o t) d", p=P)).then_inc(first_loaded, 16)
            head_c, head_t = COLUMN.at["gain"][1], TABLE.at["ident"][1]
            sp.dma_start(columns[:, 0:head_c], columns_in[:, 0:head_c]).then_inc(first_loaded, 16)
            sp.dma_start(tables[:, 0:head_t], tables_in[:, 0:head_t]).then_inc(first_loaded, 16)
            def load_early(g, gv, before):
                k = in_ring(g, g)[0]
                if before is not None:
                    sp.wait_ge(lo_ready, 2 * (before + 1))
                sp.dma_start(ring[:, k, 0:2 * PART], stream[gv, :, 0:2 * PART]).then_inc(early_loaded[k], 16)

            def load_late(g, gv, before):
                k = in_ring(g, g)[0]
                if before is not None:
                    sp.wait_ge(lo_last_ready, before + 1)
                sp.dma_start(ring[:, k, 2 * PART:STEP], stream[gv, :, 2 * PART:STEP]).then_inc(late_loaded[k], 16)

            def load(*step):
                load_early(*step)
                load_late(*step)

            for g in range(SLOTS):
                load(g, g, None)
            sp.dma_start(columns[:, head_c:], columns_in[:, head_c:]).then_inc(loaded, 16)
            sp.dma_start(tables[:, head_t:], tables_in[:, head_t:]).then_inc(loaded, 16)
            sp.dma_start(rows[:, :], rows_in.partition_broadcast(P)).then_inc(loaded, 16)
            turns = max(moe_first // SLOTS - 1, 0)
            with sp.Fori(0, turns) as i:
                for s in range(SLOTS):
                    load(SLOTS + s, SLOTS * i + SLOTS + s, SLOTS * i + s)
            for g in range(SLOTS * (turns + 1), moe_first):
                load(g, g, g - SLOTS)
            if moe_first < total:
                last_in = {in_ring(moe_first + s, 0)[0]: s for s in range(EXPERT_STEPS)}
                last = EXPERT_STEPS - 1
                for s in range(EXPERT_STEPS):
                    g = moe_first + s
                    load_early(g, g, g - SLOTS)
                    if s > 0:
                        load_late(g - 1, g - 1, g - 1 - SLOTS)
                with sp.Fori(0, EXPERTS - 1) as i:
                    for s in range(EXPERT_STEPS):
                        g = moe_first + EXPERT_STEPS * i + EXPERT_STEPS + s
                        before = [g - SLOTS if r >= SLOTS else g - s + last_in[in_ring(moe_first + r, 0)[0]] - EXPERT_STEPS for r in (s, s - 1)]
                        load_early(moe_first + s, g, before[0])
                        if s == 0:
                            load_late(moe_first + last, g - 1, g - 1 - SLOTS)
                        else:
                            load_late(moe_first + s - 1, g - 1, before[1] - (s - 1 >= SLOTS))
                load_late(moe_first + last, total - 1, total - 1 - SLOTS)
            for t in range(TT):
                sp.wait_ge(*after(f"x {len(NETWORK)} {t}"))
                sp.dma_start(out.rearrange("o (t p) d -> p (o t) d", p=P)[:, t, :], X[:, t, :]).then_inc(stored, 16)
            sp.wait_ge(stored, 16 * TT)


def by_row_tile(w):
    return np.ascontiguousarray(w).reshape(-1, P, w.shape[-1]).transpose(1, 0, 2)


def ffn_steps(gate, up, down):
    d = gate.shape[0]
    for j in range(0, down.shape[0], P):
        step = np.empty((P, STEP), np.float32)
        step[:, 0:d] = by_row_tile(gate[:, j:j + P]).reshape(P, -1)
        step[:, d:2 * d] = by_row_tile(up[:, j:j + P]).reshape(P, -1)
        step[:, 2 * d:] = down[j:j + P]
        yield step


def column_steps(parts, n):
    w = np.zeros((parts[0].shape[0], n * COLS), np.float32)
    at = 0
    for part in parts:
        w[:, at:at + part.shape[1]] = part
        at += part.shape[1]
    for s in range(n):
        yield by_row_tile(w[:, s * COLS:(s + 1) * COLS]).reshape(P, -1)


SLOT_HEADS = [0, 4, 1, 5, 2, 6, 3, 7]


def stream_steps(a):
    for kind, n in NETWORK:
        if kind == "ffn":
            if n < 6:
                name = {0: "l0_ffn1", 2: "l0_ffn2", 3: "l1_ffn1", 5: "l1_ffn2"}[n]
                up = a[name + "_w_up"]
                yield from ffn_steps(up[:, :D_FF], up[:, D_FF:], a[name + "_w_down"])
            else:
                yield from ffn_steps(a["ffn_w_gate_2"][0], a["ffn_w_up_2"][0], a["ffn_w_down_2"][0])
        elif kind == "moe":
            for e in range(EXPERTS):
                yield from ffn_steps(a["moe_w_gate_2"][0, e], a["moe_w_up_2"][0, e], a["moe_w_down_2"][0, e])
        elif kind == "delta":
            yield from column_steps([a["l0_w_in"][:, :1536]], DELTA_T)
            yield from column_steps([a["l0_w_in"][:, 1536:]], DELTA_K)
            yield from column_steps([a["l0_w_out"]], OUT_STEPS)
        elif kind == "attention":
            yield from column_steps([a["l1_w_in"]], ATT_K)
            yield from column_steps([a["l1_w_out"]], OUT_STEPS)
        elif kind == "rwkv":
            yield from column_steps([a["e_w_in_2"][0][:, :1024]], RWKV_K)
            yield from column_steps([a["e_w_in_2"][0][:, 1024:]], RWKV_T)
            yield from column_steps([a["e_w_out_2"][0]], OUT_STEPS)
        elif kind == "sparse":
            w = a["o_w_in_2"][0]
            q = w[:, :512].reshape(-1, 8, 64)[:, SLOT_HEADS].reshape(-1, 512)
            gl = w[:, 1280:1304].reshape(-1, 8, 3)[:, SLOT_HEADS].transpose(0, 2, 1).reshape(-1, 24)
            kc, vc = (w[:, c:c + 128].reshape(-1, 2, 1, 64).repeat(2, axis=2).reshape(-1, 256) for c in (512, 640))
            yield from column_steps([q, w[:, 768:1280], gl], SPARSE_K)
            yield from column_steps([kc, vc, w[:, 1304:]], SPARSE_T)
            tiles = np.concatenate([by_row_tile(a["nsa_cmp_k_w1_2"][0]), by_row_tile(a["nsa_cmp_v_w1_2"][0])], axis=1)
            padded = np.zeros((P, SPARSE_C * 12, 256), np.float32)
            padded[:, :32] = tiles
            for s in range(SPARSE_C):
                yield padded[:, 12 * s:12 * s + 12].reshape(P, -1)
            out = a["o_w_out_2"][0]
            yc = out[:512].reshape(8, 64, -1)[SLOT_HEADS].reshape(512, -1)
            yield from column_steps([np.concatenate([yc, out[512:]])], OUT_STEPS)


def pack_columns(a):
    c = np.zeros((P, COLUMN.width), np.float32)

    def per(v):
        return v.reshape(-1, P).T

    names = ["l0_ffn1_norm", "l0_mix_norm", "l0_ffn2_norm", "l1_ffn1_norm", "l1_mix_norm", "l1_ffn2_norm",
             "e_norm_mix_2", "e_norm_ffn_2", "o_norm_mix_2", "o_norm_ffn_2"]
    c[:, COLUMN["gain"]] = np.concatenate([per(a[n].reshape(-1)) for n in names], axis=1)
    c[:, COLUMN["conv"]] = np.concatenate([per(a["l0_conv_w"][j]) for j in range(4)], axis=1)
    c[:, COLUMN["conv3"]] = np.concatenate([per(a["conv_w_2"][0, j]) for j in range(3)], axis=1)
    for name, v in (("mu", "mu"), ("w0", "w0"), ("a0", "a0"), ("k_k", "k_k"), ("k_a", "k_a"), ("r_k", "r_k")):
        c[:, COLUMN[name]] = per(a[f"rwkv_{v}_2"][0].reshape(-1))
    c[:, COLUMN["sgu_b"]] = a["sgu_b_2"][0].T
    c[:, COLUMN["sgu_w"]] = a["sgu_w_2"][0].transpose(2, 0, 1).reshape(P, -1)
    c[:, COLUMN["router"]] = by_row_tile(a["moe_router_2"][0]).reshape(P, -1)
    c[0:64, COLUMN["lora"]], c[64:, COLUMN["lora"]] = a["rwkv_w2_2"][0], a["rwkv_a2_2"][0]
    c[:, COLUMN["g2"]] = a["rwkv_g2_2"][0]
    for s in "kv":
        c[:, COLUMN[f"cmp_{s}2"]] = by_row_tile(a[f"nsa_cmp_{s}_w2_2"][0]).reshape(P, -1)
        c[:, COLUMN[f"pos_{s}"]] = a[f"nsa_cmp_pos_{s}_2"][0].reshape(16, P).T
    return c


def pack_rows(a):
    r = np.empty(ROW.width, np.float32)
    for name, v in (("gdn_norm", "l0_gdn_norm"),
                    ("diff_norm", "l1_diff_norm"), ("ln_g", "sgu_ln_g_2"), ("ln_b", "sgu_ln_b_2"), ("gn_g", "rwkv_gn_g_2"),
                    ("gn_b", "rwkv_gn_b_2"), ("a_log", "l0_a_log"), ("dt_bias", "l0_dt_bias"), ("router_b", "moe_router_b_2"),
                    ("lq1", "l1_lambda_q1"), ("lk1", "l1_lambda_k1"), ("lq2", "l1_lambda_q2"), ("lk2", "l1_lambda_k2")):
        r[ROW[name]] = a[v].reshape(-1)
    return r


def shape_tables():
    t = np.zeros((P, TABLE.width), np.float32)
    t[:, TABLE["eps"]] = [EPS, 1e-5, 64e-5, 128 * EPS]
    p, f = np.arange(P)[:, None], np.arange(P)[None, :]
    t[:, TABLE["ident"]], t[:, TABLE["ones"]] = p == f, 1.0
    t[:, TABLE["incl_t"]], t[:, TABLE["upper"]], t[:, TABLE["strict"]] = f >= p, f > p, p > f
    t[:, TABLE["level"]] = np.concatenate([(p // (2 * b) == f // (2 * b)) & (p % (2 * b) >= b) & (f % (2 * b) < b)
                                           for b in (1 << n for n in range(LEVELS))], axis=1)
    token = np.arange(SEQ)[None, :]
    ret = []
    for h in range(HEADS):
        gamma, d = 1.0 - 2.0 ** (-5.0 - h), token - p
        m = np.where(d >= 0, gamma ** np.maximum(d, 0), 0.0) * 64 ** -0.5
        ret += [m, m[:, :P]]
    t[:, TABLE["ret"]] = np.concatenate(ret, axis=1)
    dist = np.concatenate([p - f, P + p - token], axis=1)
    count = (dist >= 0) * ((dist <= 128) * 1 + (dist % 4 == 0) + (dist % 16 == 0))
    t[:, TABLE["count"]], t[:, TABLE["bias_dil"]] = count, np.where(count > 0, 0.0, -1e30)
    t[:, TABLE["bias"]] = np.where(dist >= 0, 0.0, -1e30)
    for half, theta, dim in ((32, 10000.0, 64), (64, 10000.0, 128), (8, 500000.0, 16)):
        inv = np.float32(theta) ** (-np.arange(0, dim, 2, dtype=np.float32) / np.float32(dim))
        ang = (np.arange(SEQ, dtype=np.float32)[:, None] * inv[None, :]).reshape(TT, P, half).transpose(1, 0, 2)
        t[:, TABLE[f"cos{half}"]], t[:, TABLE[f"sin{half}"]] = (g(ang).reshape(P, -1) for g in (np.cos, np.sin))
    n = np.arange(CMP_PAD)[None, None, :]
    seen = (n < CMP_N) & (16 * n + 31 <= (p + P * np.arange(TT)[None, :])[:, :, None])
    t[:, TABLE["cmp_mask"]] = seen.reshape(P, -1)
    t[:, TABLE["cmp_bias"]] = np.where(seen, 0.0, -1e30).reshape(P, -1)
    t[:, TABLE["pair_ones"]] = p // 64 == f // 64
    t[:, TABLE["pair_sel"]] = p // 64 == np.arange(2)[None, :]
    t[:, TABLE["cmp_block"]] = p // CMP_PAD == np.arange(8)[None, :]
    t[:, TABLE["slots"]] = np.arange(SEQ)[None, :]
    e = np.arange(EXPERTS)
    t[:, TABLE["lower8"]] = (e[None, :] < e[:, None]).reshape(1, -1)
    return t


def kernel(**inputs):
    import concourse.bacc as bacc
    from concourse.bass_utils import run_bass_kernel_spmd

    a = {name: np.asarray(v) for name, v in inputs.items()}
    steps = sum(STEPS[kind] for kind, _ in NETWORK)
    stream = np.empty((steps, P, STEP), np.float32)
    for g, step in enumerate(stream_steps(a)):
        stream[g] = step
    arrays = {"x": np.ascontiguousarray(a["x"]), "stream": stream, "columns": pack_columns(a), "rows": pack_rows(a),
              "tables": shape_tables(), "gains": np.stack([a["final_norm"], a["final_norm_2"], a["o_norm_ffn_2"].reshape(-1)])}
    marks = {}
    for _ in range(2):
        nc = bacc.Bacc("TRN2", target_bir_lowering=False, num_devices=1)
        args = [nc.dram_tensor(f"in_{n}", v.shape, F32, kind="ExternalInput").ap() for n, v in arrays.items()]
        out = nc.dram_tensor("result", a["x"].shape, F32, kind="ExternalOutput").ap()
        network_kernel(nc, *args, out, marks)
    r = run_bass_kernel_spmd(nc, [{f"in_{n}": v for n, v in arrays.items()}], core_ids=[0])
    return r.results[0]["result"]
```
